# Optimizing a Trainium2 kernel written in Bass

```python
import math
import jax, jax.numpy as jnp
from jax import lax
import numpy as np

D_MODEL = 1024
BATCH = 1
SEQ = 512
DEPTH = 1

D_FF = 2816
RMS_EPS = 1e-6
N_DIR = 2
D_HYENA = 512
HYENA_ORDER = 2
HYENA_BANDS = 16
HYENA_EMB = 2 * HYENA_BANDS + 1
HYENA_FFN = 64
HYENA_MIN_DECAY = abs(math.log(1e-2)) / 1.5
HYENA_MAX_DECAY = abs(math.log(1e-2)) / 0.3
FILTER_EPS = 1e-6
D_RWKV = 512
RWKV_HEAD = 64
RWKV_HEADS = D_RWKV // RWKV_HEAD
DECAY_LORA = 64
AAA_LORA = 64
GATE_LORA = 160
GN_EPS = 64e-5
N_HY_IN = 3 * D_HYENA
N_RW_IN = 3 * D_RWKV + N_DIR * (DECAY_LORA + AAA_LORA) + GATE_LORA
N_GATE = 2 * D_MODEL
N_IN = N_HY_IN + N_RW_IN + N_GATE


def _rmsnorm(x, g):
    xf = x.astype(jnp.float32)
    y = xf * lax.rsqrt(jnp.mean(xf * xf, axis=-1, keepdims=True) + RMS_EPS)
    return (y * g.astype(jnp.float32)).astype(x.dtype)

def _swiglu(h, w_gu, w_down):
    gate, up = jnp.split(h @ w_gu, 2, axis=-1)
    return (jax.nn.silu(gate) * up) @ w_down

def _centred_conv3(u, w, b):
    up = jnp.pad(u, ((0, 0), (1, 1), (0, 0)))
    return w[0] * up[:, :-2] + w[1] * up[:, 1:-1] + w[2] * up[:, 2:] + b

def _centred_token_shift(u, mu):
    prev = jnp.pad(u, ((0, 0), (1, 0), (0, 0)))[:, :-1]
    nxt = jnp.pad(u, ((0, 0), (0, 1), (0, 0)))[:, 1:]
    return u + mu[0] * (prev - u) + mu[1] * (nxt - u)

def _hyena_filters(L, w1, b1, w2, b2, w3, b3, freq, decay):
    f32 = jnp.float32
    pos = jnp.arange(L, dtype=f32)
    t = (pos / max(L - 1, 1))[:, None]
    ang = (2.0 * math.pi / L) * pos[:, None]
    bands = jnp.linspace(1e-4, HYENA_BANDS - 1, HYENA_BANDS, dtype=f32)[None, :]
    feats = jnp.concatenate([t, jnp.cos(bands * ang), -jnp.sin(bands * ang)], axis=-1)
    fr = freq.astype(f32)
    h = jnp.sin(fr * (feats @ w1.astype(f32) + b1.astype(f32)))
    h = jnp.sin(fr * (h @ w2.astype(f32) + b2.astype(f32)))
    h = h @ w3.astype(f32) + b3.astype(f32)
    h = h.reshape(L, N_DIR, HYENA_ORDER, D_HYENA)
    h = h * jnp.exp(-t[:, :, None, None] * jnp.abs(decay.astype(f32))[None])
    fwd, bwd = h[:, 0], h[:, 1]
    zero = jnp.zeros((1, HYENA_ORDER, D_HYENA), f32)
    k = jnp.concatenate([fwd, zero, jnp.flip(bwd[1:], axis=0)], axis=0)
    k = k * lax.rsqrt(jnp.sum(k * k, axis=0, keepdims=True) + FILTER_EPS)
    return k

def _long_conv(z, k_f, d, L):
    zf = jnp.fft.rfft(z, n=2 * L, axis=1)
    y = jnp.fft.irfft(zf * k_f[None], n=2 * L, axis=1)[:, :L]
    return y + d * z

def _hyena_branch(u, conv_w, conv_b, w1, b1, w2, b2, w3, b3, freq, decay, bias_d, w_o):
    out_dtype = u.dtype
    L = u.shape[1]
    uc = _centred_conv3(u, conv_w, conv_b).astype(jnp.float32)
    x1, x2, v = jnp.split(uc, 3, axis=-1)
    k = _hyena_filters(L, w1, b1, w2, b2, w3, b3, freq, decay)
    k_f = jnp.fft.rfft(k, axis=0)
    d = bias_d.astype(jnp.float32)
    z = x1 * _long_conv(v, k_f[:, 0], d[0], L)
    z = x2 * _long_conv(z, k_f[:, 1], d[1], L)
    return z.astype(out_dtype) @ w_o

def _time_major_pair(fwd, bwd):
    return jnp.moveaxis(jnp.stack([fwd, jnp.flip(bwd, axis=1)], axis=0), 2, 0)

def _rwkv7_step(S, inp):
    r, w, k, v, kk, a = inp
    sa = jnp.einsum('dbhij,dbhj->dbhi', S, -kk)
    S = S * w[..., None, :] + sa[..., None] * (kk * a)[..., None, :] + v[..., None] * k[..., None, :]
    y = jnp.einsum('dbhij,dbhj->dbhi', S, r)
    return S, y

def _rwkv7_branch(u, mu, w0, w2, a0, a2, g2, k_k, k_a, r_k, ln_w, ln_b, w_o):
    out_dtype = u.dtype
    B, L, _ = u.shape
    H, N = RWKV_HEADS, RWKV_HEAD
    f32 = jnp.float32
    u = _centred_token_shift(u, mu).astype(f32)
    splits = [D_RWKV, 2 * D_RWKV, 3 * D_RWKV, 3 * D_RWKV + N_DIR * DECAY_LORA,
              3 * D_RWKV + N_DIR * (DECAY_LORA + AAA_LORA)]
    r, k, v, wd, ad, gd = jnp.split(u, splits, axis=-1)
    wd = wd.reshape(B, L, N_DIR, DECAY_LORA)
    ad = ad.reshape(B, L, N_DIR, AAA_LORA)
    w = -jax.nn.softplus(-(w0 + jnp.einsum('bldr,drc->bldc', jnp.tanh(wd), w2))) - 0.5
    decay = jnp.exp(-jnp.exp(w))
    a = jax.nn.sigmoid(a0 + jnp.einsum('bldr,drc->bldc', ad, a2))
    g = jax.nn.sigmoid(gd) @ g2
    kk = (k * k_k).reshape(B, L, H, N)
    kk = kk / jnp.maximum(jnp.sqrt(jnp.sum(kk * kk, axis=-1, keepdims=True)), 1e-12)
    k_dir = k[:, :, None, :] * (1.0 + (a - 1.0) * k_a)

    def heads(t):
        return t.reshape(t.shape[:-1] + (H, N))

    r_h, v_h = heads(r), heads(v)
    decay_h, a_h, k_h = heads(decay), heads(a), heads(k_dir)
    seq = (_time_major_pair(r_h, r_h),
           _time_major_pair(decay_h[:, :, 0], decay_h[:, :, 1]),
           _time_major_pair(k_h[:, :, 0], k_h[:, :, 1]),
           _time_major_pair(v_h, v_h),
           _time_major_pair(kk, kk),
           _time_major_pair(a_h[:, :, 0], a_h[:, :, 1]))
    S0 = jnp.zeros((N_DIR, B, H, N, N), f32)
    _, ys = lax.scan(_rwkv7_step, S0, seq)
    y = jnp.moveaxis(ys[:, 0] + jnp.flip(ys[:, 1], axis=0), 0, 1)
    mean = jnp.mean(y, axis=-1, keepdims=True)
    var = jnp.mean(jnp.square(y - mean), axis=-1, keepdims=True)
    y = ((y - mean) * lax.rsqrt(var + GN_EPS)).reshape(B, L, D_RWKV) * ln_w + ln_b
    bonus = jnp.sum(r_h[:, :, None] * k_h * r_k, axis=-1, keepdims=True)
    y = y + (jnp.sum(bonus, axis=2) * v_h).reshape(B, L, D_RWKV)
    y = y * g
    return y.astype(out_dtype) @ w_o

def first_inputs(seed: int = 0) -> dict:
    key = jax.random.key(seed)
    ks = jax.random.split(key, 35)
    f32 = jnp.float32

    def nrm(i, shape, scale):
        return scale * jax.random.normal(ks[i], shape, f32)

    hy_decay_base = jnp.linspace(HYENA_MIN_DECAY, HYENA_MAX_DECAY, D_HYENA, dtype=f32)
    rw_w0_base = jnp.linspace(-6.0, -1.0, D_RWKV, dtype=f32)
    return {
        "x": nrm(0, (BATCH, SEQ, D_MODEL), 1.0),
        "ffn1_norm": 1.0 + nrm(1, (D_MODEL,), 0.05),
        "ffn1_w_gu": nrm(2, (D_MODEL, 2 * D_FF), D_MODEL ** -0.5),
        "ffn1_w_down": nrm(3, (D_FF, D_MODEL), D_FF ** -0.5),
        "mix_norm": 1.0 + nrm(4, (D_MODEL,), 0.05),
        "w_in": nrm(5, (D_MODEL, N_IN), D_MODEL ** -0.5),
        "hy_conv_w": nrm(6, (3, N_HY_IN), 3 ** -0.5),
        "hy_conv_b": nrm(7, (N_HY_IN,), 0.02),
        "hy_ffn_w1": nrm(8, (HYENA_EMB, HYENA_FFN), HYENA_EMB ** -0.5),
        "hy_ffn_b1": nrm(9, (HYENA_FFN,), 0.1),
        "hy_ffn_w2": nrm(10, (HYENA_FFN, HYENA_FFN), HYENA_FFN ** -0.5),
        "hy_ffn_b2": nrm(11, (HYENA_FFN,), 0.1),
        "hy_ffn_w3": nrm(12, (HYENA_FFN, N_DIR * HYENA_ORDER * D_HYENA), HYENA_FFN ** -0.5),
        "hy_ffn_b3": nrm(13, (N_DIR * HYENA_ORDER * D_HYENA,), 0.1),
        "hy_sin_freq": 1.0 + nrm(14, (HYENA_FFN,), 0.1),
        "hy_decay": hy_decay_base + nrm(15, (N_DIR, HYENA_ORDER, D_HYENA), 0.1),
        "hy_bias_d": nrm(16, (HYENA_ORDER, D_HYENA), 0.5),
        "hy_out": nrm(17, (D_HYENA, D_MODEL), D_HYENA ** -0.5),
        "rw_mu": jax.random.uniform(ks[18], (2, N_RW_IN), f32, 0.0, 0.5),
        "rw_w0": rw_w0_base + nrm(19, (N_DIR, D_RWKV), 0.1),
        "rw_w2": nrm(20, (N_DIR, DECAY_LORA, D_RWKV), 0.1),
        "rw_a0": nrm(21, (N_DIR, D_RWKV), 0.3),
        "rw_a2": nrm(22, (N_DIR, AAA_LORA, D_RWKV), 0.1),
        "rw_g2": nrm(23, (GATE_LORA, D_RWKV), GATE_LORA ** -0.5),
        "rw_k_k": 0.85 + nrm(24, (D_RWKV,), 0.05),
        "rw_k_a": 1.0 + nrm(25, (D_RWKV,), 0.05),
        "rw_r_k": nrm(26, (RWKV_HEADS, RWKV_HEAD), 0.1),
        "rw_ln_w": 1.0 + nrm(27, (D_RWKV,), 0.05),
        "rw_ln_b": nrm(28, (D_RWKV,), 0.02),
        "rw_out": nrm(29, (D_RWKV, D_MODEL), D_RWKV ** -0.5),
        "w_out": nrm(30, (D_MODEL, D_MODEL), D_MODEL ** -0.5),
        "ffn2_norm": 1.0 + nrm(31, (D_MODEL,), 0.05),
        "ffn2_w_gu": nrm(32, (D_MODEL, 2 * D_FF), D_MODEL ** -0.5),
        "ffn2_w_down": nrm(33, (D_FF, D_MODEL), D_FF ** -0.5),
        "final_norm": 1.0 + nrm(34, (D_MODEL,), 0.05),
    }

def first_block(x, ffn1_norm, ffn1_w_gu, ffn1_w_down, mix_norm, w_in, hy_conv_w, hy_conv_b,
              hy_ffn_w1, hy_ffn_b1, hy_ffn_w2, hy_ffn_b2, hy_ffn_w3, hy_ffn_b3, hy_sin_freq,
              hy_decay, hy_bias_d, hy_out, rw_mu, rw_w0, rw_w2, rw_a0, rw_a2, rw_g2, rw_k_k,
              rw_k_a, rw_r_k, rw_ln_w, rw_ln_b, rw_out, w_out, ffn2_norm, ffn2_w_gu,
              ffn2_w_down, final_norm):
    split_at = [N_HY_IN, N_HY_IN + N_RW_IN, N_HY_IN + N_RW_IN + D_MODEL]
    for _ in range(DEPTH):
        x = x + 0.5 * _swiglu(_rmsnorm(x, ffn1_norm), ffn1_w_gu, ffn1_w_down)
        h = _rmsnorm(x, mix_norm)
        u_hy, u_rw, g_hy, g_rw = jnp.split(h @ w_in, split_at, axis=-1)
        y_hy = _hyena_branch(u_hy, hy_conv_w, hy_conv_b, hy_ffn_w1, hy_ffn_b1, hy_ffn_w2,
                             hy_ffn_b2, hy_ffn_w3, hy_ffn_b3, hy_sin_freq, hy_decay,
                             hy_bias_d, hy_out)
        y_rw = _rwkv7_branch(u_rw, rw_mu, rw_w0, rw_w2, rw_a0, rw_a2, rw_g2, rw_k_k, rw_k_a,
                             rw_r_k, rw_ln_w, rw_ln_b, rw_out)
        merged = jax.nn.sigmoid(g_hy) * y_hy + jax.nn.sigmoid(g_rw) * y_rw
        x = x + merged @ w_out
        x = x + 0.5 * _swiglu(_rmsnorm(x, ffn2_norm), ffn2_w_gu, ffn2_w_down)
    return _rmsnorm(x, final_norm)


DEPTH_2 = 2

N_A = DEPTH_2 // 2
N_B = DEPTH_2 - N_A

A_HEADS = 8
A_QK_DIM = D_MODEL // 2 // A_HEADS
A_V_DIM = D_MODEL // A_HEADS
A_QK_W = A_HEADS * A_QK_DIM
A_V_W = A_HEADS * A_V_DIM
A_IN_WIDTH = 2 * A_QK_W + A_V_W + 2 * A_HEADS + A_V_W
A_CHUNK = 128

B_HEADS = 8
B_Q_LORA = 384
B_KV_LORA = 256
B_NOPE = 128
B_ROPE = 64
B_V = 128
B_QBLOCK = 128
ROPE_THETA = 10000.0

D_FF_2 = 4 * D_MODEL
EPS = 1e-6


def rmsnorm(x, g):
    xf = x.astype(jnp.float32)
    y = xf * lax.rsqrt(jnp.mean(xf * xf, axis=-1, keepdims=True) + EPS)
    return (y * g.astype(jnp.float32)).astype(x.dtype)

def modulate(h, shift, scale):
    return h * (1 + scale[:, None, :]) + shift[:, None, :]

def rope_tables(positions):
    half = B_ROPE // 2
    inv = ROPE_THETA ** (-jnp.arange(half, dtype=jnp.float32) / half)
    ang = positions.astype(jnp.float32)[..., None] * inv
    return jnp.cos(ang), jnp.sin(ang)

def apply_rope(x, cos, sin):
    xf = x.astype(jnp.float32)
    x1, x2 = jnp.split(xf, 2, axis=-1)
    out = jnp.concatenate([x1 * cos - x2 * sin, x2 * cos + x1 * sin], axis=-1)
    return out.astype(x.dtype)

def mlstm_chunkwise(q, k, v, i_pre, f_pre):
    B_, H, S, dk = q.shape
    dv = v.shape[-1]
    L = A_CHUNK
    nc = S // L
    f32 = jnp.float32
    qf = q.astype(f32)
    kf = k.astype(f32) * (dk ** -0.5)
    vf = v.astype(f32)
    lf = jax.nn.log_sigmoid(f_pre.astype(f32))
    ig = i_pre.astype(f32)

    def chunks(a):
        return jnp.moveaxis(a.reshape(B_, H, nc, L, *a.shape[3:]), 2, 0)

    qc, kc, vc, ic = chunks(qf), chunks(kf), chunks(vf), chunks(ig)
    bc = jnp.cumsum(chunks(lf), axis=-1)
    tri = jnp.tril(jnp.ones((L, L), dtype=bool))

    def step(carry, xs):
        C, n, m = carry
        qb, kb, vb, ib, bb = xs
        log_d = bb[..., :, None] - bb[..., None, :] + ib[..., None, :]
        log_d = jnp.where(tri, log_d, -jnp.inf)
        log_inter = bb + m[..., None]
        m_t = jnp.maximum(log_inter, jnp.max(log_d, axis=-1))
        w_intra = jnp.exp(log_d - m_t[..., None])
        w_inter = jnp.exp(log_inter - m_t)
        s = jnp.einsum('bhtd,bhsd->bhts', qb, kb) * w_intra
        num = (w_inter[..., None] * jnp.einsum('bhtd,bhde->bhte', qb, C)
               + jnp.einsum('bhts,bhse->bhte', s, vb))
        den = w_inter * jnp.einsum('bhtd,bhd->bht', qb, n) + jnp.sum(s, axis=-1)
        h = num / jnp.maximum(jnp.abs(den), jnp.exp(-m_t))[..., None]
        b_last = bb[..., -1]
        log_w = b_last[..., None] - bb + ib
        m_new = jnp.maximum(b_last + m, jnp.max(log_w, axis=-1))
        w = jnp.exp(log_w - m_new[..., None])
        decay = jnp.exp(b_last + m - m_new)
        C_new = decay[..., None, None] * C + jnp.einsum('bhs,bhsd,bhse->bhde', w, kb, vb)
        n_new = decay[..., None] * n + jnp.einsum('bhs,bhsd->bhd', w, kb)
        return (C_new, n_new, m_new), h

    init = (jnp.zeros((B_, H, dk, dv), f32), jnp.zeros((B_, H, dk), f32), jnp.zeros((B_, H), f32))
    _, hc = lax.scan(step, init, (qc, kc, vc, ic, bc))
    return jnp.moveaxis(hc, 0, 2).reshape(B_, H, S, dv).astype(q.dtype)

def mlstm_mixer(h, w_in, gate_b, head_g, w_out):
    B_, S, _ = h.shape
    proj = h @ w_in
    splits = [A_QK_W, 2 * A_QK_W, 2 * A_QK_W + A_V_W, 2 * A_QK_W + A_V_W + A_HEADS,
              2 * A_QK_W + A_V_W + 2 * A_HEADS]
    q, k, v, ig, fg, og = jnp.split(proj, splits, axis=-1)
    heads = lambda a, d: a.reshape(B_, S, A_HEADS, d).transpose(0, 2, 1, 3)
    i_pre = (ig + gate_b[0]).transpose(0, 2, 1)
    f_pre = (fg + gate_b[1]).transpose(0, 2, 1)
    hh = mlstm_chunkwise(heads(q, A_QK_DIM), heads(k, A_QK_DIM), heads(v, A_V_DIM), i_pre, f_pre)
    hh = rmsnorm(hh.transpose(0, 2, 1, 3), head_g).reshape(B_, S, A_V_W)
    return (hh * jax.nn.sigmoid(og)) @ w_out

def mla_shared_kv(x, shift, scale, g_in, w_a, g_latent, w_b, cos, sin):
    B_, S, _ = x.shape
    h = modulate(rmsnorm(x, g_in), shift, scale)
    kv = h @ w_a
    c_kv, k_rope = jnp.split(kv, [B_KV_LORA], axis=-1)
    c_kv = rmsnorm(c_kv, g_latent)
    kvb = (c_kv @ w_b).reshape(B_, S, B_HEADS, B_NOPE + B_V)
    k_nope, v = jnp.split(kvb, [B_NOPE], axis=-1)
    k_rope = apply_rope(k_rope, cos, sin)
    return k_nope, k_rope, v

def causal_mla_attention(q_nope, q_rope, k_nope, k_rope, v):
    B_, S, H, _ = q_nope.shape
    nb = S // B_QBLOCK
    scale = (B_NOPE + B_ROPE) ** -0.5
    qn = jnp.moveaxis(q_nope.reshape(B_, nb, B_QBLOCK, H, B_NOPE), 1, 0)
    qr = jnp.moveaxis(q_rope.reshape(B_, nb, B_QBLOCK, H, B_ROPE), 1, 0)
    kpos = jnp.arange(S, dtype=jnp.int32)
    starts = jnp.arange(nb, dtype=jnp.int32) * B_QBLOCK

    def block(args):
        qn_b, qr_b, start = args
        s = (jnp.einsum('bqhd,bkhd->bhqk', qn_b, k_nope)
             + jnp.einsum('bqhd,bkd->bhqk', qr_b, k_rope)).astype(jnp.float32) * scale
        qpos = start + jnp.arange(B_QBLOCK, dtype=jnp.int32)
        s = jnp.where(kpos[None, :] <= qpos[:, None], s, -jnp.inf)
        p = jax.nn.softmax(s, axis=-1)
        return jnp.einsum('bhqk,bkhd->bqhd', p.astype(v.dtype), v)

    o = lax.map(block, (qn, qr, starts))
    return jnp.moveaxis(o, 0, 1).reshape(B_, S, H, B_V)

def mla_mixer(h, w_q_a, g_q_latent, w_q_b, w_out, k_nope, k_rope, v, cos, sin):
    B_, S, _ = h.shape
    cq = rmsnorm(h @ w_q_a, g_q_latent)
    q = (cq @ w_q_b).reshape(B_, S, B_HEADS, B_NOPE + B_ROPE)
    q_nope, q_rope = jnp.split(q, [B_NOPE], axis=-1)
    q_rope = apply_rope(q_rope, cos[:, :, None, :], sin[:, :, None, :])
    o = causal_mla_attention(q_nope, q_rope, k_nope, k_rope, v)
    return o.reshape(B_, S, B_HEADS * B_V) @ w_out

def sqrelu_mlp(h, w1, w2):
    return jnp.square(jax.nn.relu(h @ w1)) @ w2

def second_inputs(seed: int = 0) -> dict:
    key = jax.random.key(seed)
    ks = jax.random.split(key, 24)
    f32 = jnp.float32

    def nrm(k, shape, fan_in, s=1.0):
        return s * (fan_in ** -0.5) * jax.random.normal(k, shape, f32)

    def gain(k, shape):
        return 1.0 + 0.02 * jax.random.normal(k, shape, f32)

    x = jax.random.normal(ks[0], (BATCH, SEQ, D_MODEL), f32)
    c = jax.random.normal(ks[1], (BATCH, D_MODEL), f32)
    positions = (jax.random.randint(ks[2], (BATCH, 1), 0, 4096, dtype=jnp.int32)
                 + jnp.arange(SEQ, dtype=jnp.int32)[None, :])
    ada_w = nrm(ks[3], (DEPTH_2, D_MODEL, 6 * D_MODEL), D_MODEL, 0.5)
    ada_b = 0.02 * jax.random.normal(ks[4], (DEPTH_2, 6 * D_MODEL), f32)
    norm_g = gain(ks[5], (DEPTH_2, 4, D_MODEL))
    a_w_in = nrm(ks[6], (N_A, D_MODEL, A_IN_WIDTH), D_MODEL)
    kg1, kg2 = jax.random.split(ks[7])
    i_bias = 0.1 * jax.random.normal(kg1, (N_A, A_HEADS), f32)
    f_bias = jnp.linspace(3.0, 6.0, A_HEADS, dtype=f32)[None, :] + 0.1 * jax.random.normal(kg2, (N_A, A_HEADS), f32)
    a_gate_b = jnp.stack([i_bias, f_bias], axis=1)
    a_head_g = gain(ks[8], (N_A, A_HEADS, A_V_DIM))
    a_w_out = nrm(ks[9], (N_A, A_V_W, D_MODEL), A_V_W)
    kv_ada_w = nrm(ks[10], (D_MODEL, 2 * D_MODEL), D_MODEL, 0.5)
    kv_ada_b = 0.02 * jax.random.normal(ks[11], (2 * D_MODEL,), f32)
    kv_norm_g = gain(ks[12], (D_MODEL,))
    kv_w_a = nrm(ks[13], (D_MODEL, B_KV_LORA + B_ROPE), D_MODEL)
    kv_latent_g = gain(ks[14], (B_KV_LORA,))
    kv_w_b = nrm(ks[15], (B_KV_LORA, B_HEADS * (B_NOPE + B_V)), B_KV_LORA)
    b_w_q_a = nrm(ks[16], (N_B, D_MODEL, B_Q_LORA), D_MODEL)
    b_q_latent_g = gain(ks[17], (N_B, B_Q_LORA))
    b_w_q_b = nrm(ks[18], (N_B, B_Q_LORA, B_HEADS * (B_NOPE + B_ROPE)), B_Q_LORA)
    b_w_out = nrm(ks[19], (N_B, B_HEADS * B_V, D_MODEL), B_HEADS * B_V)
    mlp_w1 = nrm(ks[20], (DEPTH_2, D_MODEL, D_FF_2), D_MODEL)
    mlp_w2 = nrm(ks[21], (DEPTH_2, D_FF_2, D_MODEL), D_FF_2)
    return {"x": x, "c": c, "positions": positions, "ada_w": ada_w, "ada_b": ada_b,
            "norm_g": norm_g, "a_w_in": a_w_in, "a_gate_b": a_gate_b, "a_head_g": a_head_g,
            "a_w_out": a_w_out, "kv_ada_w": kv_ada_w, "kv_ada_b": kv_ada_b, "kv_norm_g": kv_norm_g,
            "kv_w_a": kv_w_a, "kv_latent_g": kv_latent_g, "kv_w_b": kv_w_b, "b_w_q_a": b_w_q_a,
            "b_q_latent_g": b_q_latent_g, "b_w_q_b": b_w_q_b, "b_w_out": b_w_out,
            "mlp_w1": mlp_w1, "mlp_w2": mlp_w2}

def second_block(x, c, positions, ada_w, ada_b, norm_g, a_w_in, a_gate_b, a_head_g, a_w_out,
              kv_ada_w, kv_ada_b, kv_norm_g, kv_w_a, kv_latent_g, kv_w_b, b_w_q_a, b_q_latent_g,
              b_w_q_b, b_w_out, mlp_w1, mlp_w2):
    cond = jax.nn.silu(c)
    cos, sin = rope_tables(positions)
    shared_kv = None
    for l in range(DEPTH_2):
        ada = cond @ ada_w[l] + ada_b[l]
        sh1, sc1, g1, sh2, sc2, g2 = jnp.split(ada, 6, axis=-1)
        h = modulate(rmsnorm(x, norm_g[l, 0]), sh1, sc1)
        if l < N_A:
            y = mlstm_mixer(h, a_w_in[l], a_gate_b[l], a_head_g[l], a_w_out[l])
        else:
            if shared_kv is None:
                kv_shift, kv_scale = jnp.split(cond @ kv_ada_w + kv_ada_b, 2, axis=-1)
                shared_kv = mla_shared_kv(x, kv_shift, kv_scale, kv_norm_g, kv_w_a, kv_latent_g,
                                          kv_w_b, cos, sin)
            k_nope, k_rope, v = shared_kv
            j = l - N_A
            y = mla_mixer(h, b_w_q_a[j], b_q_latent_g[j], b_w_q_b[j], b_w_out[j],
                          k_nope, k_rope, v, cos, sin)
        x = x + g1[:, None, :] * rmsnorm(y, norm_g[l, 1])
        h = modulate(rmsnorm(x, norm_g[l, 2]), sh2, sc2)
        y = sqrelu_mlp(h, mlp_w1[l], mlp_w2[l])
        x = x + g2[:, None, :] * rmsnorm(y, norm_g[l, 3])
    return x


def setup_inputs(seed=0):
    out = dict(first_inputs(seed))
    for name, value in second_inputs(seed + 1).items():
        if name != "x":
            out[name + "_2"] = value
    return out


def reference(
    x, ffn1_norm, ffn1_w_gu, ffn1_w_down, mix_norm, w_in, hy_conv_w, hy_conv_b, hy_ffn_w1,
    hy_ffn_b1, hy_ffn_w2, hy_ffn_b2, hy_ffn_w3, hy_ffn_b3, hy_sin_freq, hy_decay, hy_bias_d,
    hy_out, rw_mu, rw_w0, rw_w2, rw_a0, rw_a2, rw_g2, rw_k_k, rw_k_a, rw_r_k, rw_ln_w, rw_ln_b,
    rw_out, w_out, ffn2_norm, ffn2_w_gu, ffn2_w_down, final_norm, c_2, positions_2, ada_w_2,
    ada_b_2, norm_g_2, a_w_in_2, a_gate_b_2, a_head_g_2, a_w_out_2, kv_ada_w_2, kv_ada_b_2,
    kv_norm_g_2, kv_w_a_2, kv_latent_g_2, kv_w_b_2, b_w_q_a_2, b_q_latent_g_2, b_w_q_b_2,
    b_w_out_2, mlp_w1_2, mlp_w2_2,
):
    x = first_block(
        x, ffn1_norm, ffn1_w_gu, ffn1_w_down, mix_norm, w_in, hy_conv_w, hy_conv_b, hy_ffn_w1,
        hy_ffn_b1, hy_ffn_w2, hy_ffn_b2, hy_ffn_w3, hy_ffn_b3, hy_sin_freq, hy_decay, hy_bias_d,
        hy_out, rw_mu, rw_w0, rw_w2, rw_a0, rw_a2, rw_g2, rw_k_k, rw_k_a, rw_r_k, rw_ln_w,
        rw_ln_b, rw_out, w_out, ffn2_norm, ffn2_w_gu, ffn2_w_down, final_norm,
    )
    return second_block(
        x, c_2, positions_2, ada_w_2, ada_b_2, norm_g_2, a_w_in_2, a_gate_b_2, a_head_g_2,
        a_w_out_2, kv_ada_w_2, kv_ada_b_2, kv_norm_g_2, kv_w_a_2, kv_latent_g_2, kv_w_b_2,
        b_w_q_a_2, b_q_latent_g_2, b_w_q_b_2, b_w_out_2, mlp_w1_2, mlp_w2_2,
    )


_drawn_inputs = setup_inputs


def setup_inputs(seed=0):
    import zlib

    import numpy as np

    out = dict(_drawn_inputs(seed))
    spreads = {}
    factors = {'rw_w2': 3.657,
     'rw_k_k': 5.124,
     'rw_k_a': 3.487,
     'rw_ln_w': 4.85,
     'rw_ln_b': 8.0,
     'ffn2_norm': 3.066,
     'norm_g_2': 3.071,
     'a_head_g_2': 8.0,
     'kv_ada_b_2': 3.66,
     'kv_norm_g_2': 8.0,
     'kv_latent_g_2': 8.0,
     'b_q_latent_g_2': 8.0}
    for name, (base, spread) in spreads.items():
        noise = np.random.default_rng([zlib.crc32(name.encode()), seed]).standard_normal(out[name].shape)
        drawn = base * np.exp(spread * noise) if base else spread * noise
        out[name] = __import__('jax').numpy.asarray(drawn.astype(out[name].dtype))
    for name, factor in factors.items():
        out[name] = (out[name] * factor).astype(out[name].dtype)
    return out
```

```python
import math
from contextlib import ExitStack

import numpy as np
import concourse.bass as bass
from concourse import mybir


F32 = mybir.dt.float32
ACT = mybir.ActivationFunctionType
ALU = mybir.AluOpType
AX = mybir.AxisListType
P = 128

D = 1024
L = 512
DT = D // P
TT = L // P
D_FF = 2816
D_HY = 512
HT = D_HY // P
N_HY = 3 * D_HY
D_RW = 512
RT = D_RW // P
N_RW = 3 * D_RW + 2 * 64 + 2 * 64 + 160
EMB = 33
FILT = 64
EPS = 1e-6
GN_EPS = 64e-5
CH = 64
NCH = L // CH
LEVELS = 6
LH = L // 2
HCH = LH // CH
LOG_DECAY_MAX = -math.exp(-0.5)

A_HEADS = 8
A_QK = 64
A_IN = 3088
B_HEADS = 8
Q_LORA = 384
KV_LORA = 256
NOPE = 128
ROPE = 64
D_FF2 = 4096

TWO_PI = 2 * math.pi
ROUND = 1.5 * 2.0**23
PI_A = 6.28125
PI_B = float(np.float32(np.float32((TWO_PI - PI_A) * 2**20).astype(np.int64) / 2**20))
PI_C = TWO_PI - PI_A - PI_B

VECTORS = [
    ("ffn1_norm", 8, 128), ("mix_norm", 8, 128), ("hy_conv_w", 36, 128), ("hy_conv_b", 12, 128),
    ("hy_ffn_b1", 1, 64), ("hy_ffn_b2", 1, 64), ("hy_sin_freq", 1, 64), ("hy_bias_d", 8, 128),
    ("rw_w0", 8, 128), ("rw_a0", 8, 128), ("rw_k_k", 4, 128), ("rw_k_a", 4, 128),
    ("rw_r_k", 4, 128), ("rw_ln_w", 4, 128), ("rw_ln_b", 4, 128), ("ffn2_norm", 8, 128),
    ("final_norm", 8, 128), ("ada_b_2", 96, 128), ("norm_g_2", 64, 128),
    ("a_head_g_2", 8, 128), ("kv_ada_b_2", 16, 128), ("kv_norm_g_2", 8, 128),
    ("kv_latent_g_2", 2, 128), ("b_q_latent_g_2", 3, 128), ("c_2", 8, 128),
    ("a_gate_b_2", 2, 8),
]
MU_ROWS = N_RW // P
COL = {}
_at = 0
for _name, _rows, _ in VECTORS:
    COL[_name] = _at
    _at += _rows
COL["rw_mu"] = _at
_at += 2 * (MU_ROWS + 1)
ROW_TILES = -(-_at // P)


class Kept:
    pass


class Steps:

    def __init__(self, sem):
        self.sem, self.n = sem, 0

    def mark(self, ins):
        ins.then_inc(self.sem, 1)
        self.n += 1
        return self.n


MOST_SEMAPHORES = 20


class Semaphores:

    used = 0
    numbers = set()

    @classmethod
    def room(cls, nc, n=MOST_SEMAPHORES):
        if cls.used + n > cls.limit:
            first, last = min(cls.numbers), max(cls.numbers)
            with nc.Block() as block:
                @block.gpsimd
                def _(pool):
                    pool.sem_clear(range(first, last + 1))
            cls.used = 0

    @classmethod
    def start(cls, nc):
        cls.used, cls.numbers, cls.limit = 0, set(), nc.free_len()

    @classmethod
    def take(cls, nc, stack, name):
        sem = stack.enter_context(nc.semaphore(name))
        cls.used += 1
        cls.numbers.add(sem.num)
        return sem


def opened(nc, stack, tag):
    Semaphores.room(nc)
    sb = lambda name, shape: stack.enter_context(nc.sbuf_tensor(f"{tag}_{name}", shape, F32))
    pb = lambda name, shape: stack.enter_context(nc.psum_tensor(f"{tag}_{name}", shape, F32))
    sem = lambda name: Semaphores.take(nc, stack, f"{tag}_{name}")
    return sb, pb, sem


def col(e, name, i=0, parts=P, base=0):
    c = COL[name] + i
    return e.cols[base:base + parts, c:c + 1]



def load_constants(nc, e, I):
    with ExitStack() as s:
        sb, pb, sem = opened(nc, s, "init")
        rows = sb("rows", [P, ROW_TILES, P])
        xin = sb("xin", [P, TT, D])
        ps = pb("ps", [P, 8, L])
        rows_zero, rows_in, x_in, tables_in = sem("rows_zero"), sem("rows_in"), sem("x_in"), sem("tables_in")
        vec_t, vec_c, x_t, x_c = sem("vec_t"), sem("vec_c"), sem("x_t"), sem("x_c")
        block = s.enter_context(nc.Block())
        pieces = []
        for name, n, width in VECTORS:
            flat = I[name]
            shape = "abcdef"[:len(flat.shape)]
            flat = flat.rearrange(f"{' '.join(shape)} -> ({' '.join(shape)})") if len(flat.shape) > 1 else flat
            view = flat.rearrange("(n w) -> n w", w=width)
            at = 0
            while at < n:
                row = COL[name] + at
                k = min(n - at, P - row % P)
                pieces.append((row, k, width, view[at:at + k, :]))
                at += k
        for m in range(2):
            row = COL["rw_mu"] + m * (MU_ROWS + 1)
            pieces.append((row, MU_ROWS, P, I["rw_mu"][m, 0:MU_ROWS * P].rearrange("(n w) -> n w", w=P)))
            pieces.append((row + MU_ROWS, 1, N_RW - MU_ROWS * P, I["rw_mu"][m:m + 1, MU_ROWS * P:N_RW]))
        split = []
        for row, k, width, src in pieces:
            first = min(k, P - row % P)
            split.append((row, first, width, src[0:first, :]))
            if first < k:
                split.append((row + first, k - first, width, src[first:k, :]))

        @block.sync
        def _(sp):
            xv = I["x"][0].rearrange("(t p) d -> p t d", p=P)
            sp.dma_start(e.ident[:, :], I["c_ident"]).then_inc(tables_in, 16)
            sp.dma_start(e.heads[:, :], I["c_heads"]).then_inc(tables_in, 16)
            for t in range(TT):
                sp.dma_start(xin[:, t, :], xv[:, t, :]).then_inc(x_in, 16)
            sp.wait_ge(rows_zero, 1)
            for row, k, width, src in split:
                sp.dma_start(rows[row % P:row % P + k, row // P, 0:width], src).then_inc(rows_in, 16)

        @block.vector
        def _(dve):
            nc.vector.memset(rows[:, :, :], 0.0).then_inc(rows_zero, 1)
            nc.vector.memset(e.ones[:, :], 1.0)
            for k in range(DT):
                dve.wait_ge(x_t, k + 1)
                nc.vector.tensor_copy(e.x[:, k, :], ps[:, k % 4, :]).then_inc(x_c, 1)
            dve.wait_ge(vec_t, 1)
            nc.vector.tensor_copy(e.cols[:, :], ps[:, 4, 0:ROW_TILES * P]).then_inc(vec_c, 1)

        @block.tensor
        def _(pe):
            pe.wait_ge(tables_in, 32)
            pe.wait_ge(x_in, 16 * TT)
            for k in range(DT):
                if k >= 4:
                    pe.wait_ge(x_c, k - 3)
                for t in range(TT):
                    last = nc.tensor.transpose(ps[:, k % 4, t * P:(t + 1) * P],
                                               xin[:, t, k * P:(k + 1) * P], e.ident[:, :])
                last.then_inc(x_t, 1)
            pe.wait_ge(rows_in, 16 * len(split))
            for r in range(ROW_TILES):
                last = nc.tensor.transpose(ps[:, 4, r * P:(r + 1) * P], rows[:, r, :], e.ident[:, :])
            last.then_inc(vec_t, 1)



def norm_stage(nc, e, tag, src, n, dst, gain, eps=EPS, shift=None, scale=None,
               gate=None, onto=None):
    with ExitStack() as s:
        sb, pb, sem = opened(nc, s, tag)
        sq = sb("sq", [P, 2, L])
        rs = sb("rs", [P, 2, L])
        g1 = sb("g1", [P, n])
        ps = pb("ps", [P, L])
        sq_ready, sq_used, sum_done = sem("sq_ready"), sem("sq_used"), sem("sum_done")
        inv_ready, rs_ready, steps, out_done = sem("inv_ready"), sem("rs_ready"), sem("steps"), sem("out")
        block = s.enter_context(nc.Block())

        @block.scalar
        def _(act):
            for k in range(n):
                if k >= 2:
                    act.wait_ge(sq_used, k - 1)
                nc.scalar.activation(sq[:, k % 2, :], src[:, k, :], ACT.Square).then_inc(sq_ready, 1)
            act.wait_ge(inv_ready, 1)
            nc.scalar.activation(rs[:, 1, :], rs[:, 0, :], ACT.Sqrt).then_inc(rs_ready, 1)
            if shift is not None:
                for k in range(n):
                    act.wait_ge(out_done, k + 1)
                    nc.scalar.activation(dst[:, k, :], dst[:, k, :], ACT.Identity, bias=shift(k))

        @block.tensor
        def _(pe):
            for k in range(n):
                pe.wait_ge(sq_ready, k + 1)
                last = nc.tensor.matmul(ps[:, :], e.ones[:, :], sq[:, k % 2, :], start=k == 0, stop=k == n - 1)
                last.then_inc(sq_used, 1)

        @block.vector
        def _(dve):
            st = Steps(steps)
            if scale is not None:
                for k in range(n):
                    st.mark(nc.vector.scalar_tensor_tensor(g1[:, k:k + 1], scale(k), 1.0, gain(k),
                                                           ALU.add, ALU.mult))
            if gate is not None:
                for k in range(n):
                    st.mark(nc.vector.tensor_tensor(g1[:, k:k + 1], gate(k), gain(k), ALU.mult))
            dve.wait_ge(sq_used, n)
            dve.wait_ge(steps, st.mark(nc.vector.tensor_scalar(rs[:, 0, :], ps[:, :], 1.0 / (n * P), eps,
                                                               ALU.mult, ALU.add)))
            nc.vector.reciprocal(rs[:, 0, :], rs[:, 0, :]).then_inc(inv_ready, 1)
            dve.wait_ge(rs_ready, 1)
            for k in range(n):
                g = gain(k) if scale is None and gate is None else g1[:, k:k + 1]
                nc.vector.scalar_tensor_tensor(dst[:, k, :], src[:, k, :], g, rs[:, 1, :],
                                               ALU.mult, ALU.mult).then_inc(out_done, 1)

        @block.gpsimd
        def _(pool):
            if onto is not None:
                for k in range(n):
                    pool.wait_ge(out_done, k + 1)
                    nc.gpsimd.tensor_tensor(onto[:, k, :], onto[:, k, :], dst[:, k, :], ALU.add)



def stream_weights(sp, load, slots, groups, per_slot, loaded, mm_done):
    for i in range(slots):
        load(i, i).then_inc(loaded[i], 16)
    if groups > 1:
        with sp.Fori(1, groups) as g:
            for i in range(slots):
                sp.wait_ge(mm_done, (g - 1) * (slots * per_slot) + (i + 1) * per_slot)
                load(i, g * slots + i).then_inc(loaded[i], 16)


def project(nc, e, tag, w, k_tiles, rhs, groups, slots, per_slot, evac, on="scalar", width=P, tail=P,
            setup=None):
    with ExitStack() as s:
        sb, pb, sem = opened(nc, s, tag)
        ring = sb("ring", [P, slots, k_tiles, per_slot * width])
        nb = slots * per_slot
        ps = pb("ps", [P, nb, L])
        loaded = [sem(f"loaded{i}") for i in range(slots)]
        mm_done, bank_free = sem("mm_done"), sem("bank_free")
        local = setup(sb, sem) if setup else None
        block = s.enter_context(nc.Block())
        wv = w.rearrange("(k p) n -> p k n", p=P)
        step = per_slot * width

        @block.sync
        def _(sp):
            def load(i, c):
                return sp.dma_start(ring[:, i, :, :], wv[:, :, bass.ds(c * step, step)])
            stream_weights(sp, load, slots, groups, per_slot, loaded, mm_done)

        @block.tensor
        def _(pe):
            with pe.Fori(0, groups) as g:
                for i in range(slots):
                    pe.wait_ge(loaded[i], g * 16 + 16)
                    for t in range(per_slot):
                        b = i * per_slot + t
                        pe.wait_ge(bank_free, g * nb + (b + 1))
                        for k in range(k_tiles):
                            last = nc.tensor.matmul(ps[0:width, b, :], ring[:, i, k, t * width:(t + 1) * width],
                                                    rhs[:, k, :], start=k == 0, stop=k == k_tiles - 1)
                        last.then_inc(mm_done, 1)

        def take_out(eng):
            eng.sem_inc(bank_free, nb)
            with eng.Fori(0, groups) as g:
                for b in range(nb):
                    eng.wait_ge(mm_done, g * nb + (b + 1))
                    evac(g * nb + b, ps[0:width, b, :]).then_inc(bank_free, 1)

        if on == "scalar":
            @block.scalar
            def _(act):
                take_out(act)
        else:
            @block.vector
            def _(dve):
                take_out(dve)


def tile_at(t, j):
    return t[:, bass.ds(j, 1), :].rearrange("p a n -> p (a n)")


def swiglu_up(nc, e, tag, w_gu, h, ff):
    with ExitStack() as s:
        sb, pb, sem = opened(nc, s, tag)
        slots = 2
        groups = D_FF // P // slots
        ring = sb("ring", [P, slots, DT, 2, P])
        silu = sb("silu", [P, slots, L])
        ps = pb("ps", [P, 2 * slots, L])
        loaded = [sem(f"loaded{i}") for i in range(slots)]
        mm_done, gate_free, up_free = sem("mm_done"), sem("gate_free"), sem("up_free")
        block = s.enter_context(nc.Block())
        wv = w_gu.rearrange("(k p) (two n) -> p k two n", p=P, two=2)

        @block.sync
        def _(sp):
            def load(i, c):
                sp.dma_start(ring[:, i, :, 0, :], wv[:, :, 0, bass.ds(c * P, P)]).then_inc(loaded[i], 16)
                return sp.dma_start(ring[:, i, :, 1, :], wv[:, :, 1, bass.ds(c * P, P)])
            stream_weights(sp, load, slots, groups, 2, loaded, mm_done)

        @block.tensor
        def _(pe):
            with pe.Fori(0, groups) as g:
                for i in range(slots):
                    pe.wait_ge(loaded[i], g * 32 + 32)
                    for t, free in ((0, gate_free), (1, up_free)):
                        pe.wait_ge(free, g * slots + (i + 1))
                        for k in range(DT):
                            last = nc.tensor.matmul(ps[:, 2 * i + t, :], ring[:, i, k, t, :], h[:, k, :],
                                                    start=k == 0, stop=k == DT - 1)
                        last.then_inc(mm_done, 1)

        @block.scalar
        def _(act):
            act.sem_inc(gate_free, slots)
            with act.Fori(0, groups) as g:
                for i in range(slots):
                    act.wait_ge(mm_done, g * 2 * slots + (2 * i + 1))
                    act.wait_ge(up_free, g * slots + (i + 1))
                    nc.scalar.activation(silu[:, i, :], ps[:, 2 * i, :], ACT.Silu).then_inc(gate_free, 1)

        @block.vector
        def _(dve):
            dve.sem_inc(up_free, slots)
            with dve.Fori(0, groups) as g:
                for i in range(slots):
                    dve.wait_ge(mm_done, g * 2 * slots + (2 * i + 2))
                    dve.wait_ge(gate_free, g * slots + (slots + i + 1))
                    nc.vector.tensor_tensor(tile_at(ff, g * slots + i), silu[:, i, :], ps[:, 2 * i + 1, :],
                                            ALU.mult).then_inc(up_free, 1)


def add_to_x(nc, e, factor):
    def evac(j, bank):
        xt = tile_at(e.x, j)
        return nc.vector.scalar_tensor_tensor(xt, bank, factor, xt, ALU.mult, ALU.add)
    return evac


def ffn_swiglu(nc, e, tag, norm, w_gu, w_down):
    with ExitStack() as s:
        h = s.enter_context(nc.sbuf_tensor(f"{tag}_h", [P, DT, L], F32))
        ff = s.enter_context(nc.sbuf_tensor(f"{tag}_ff", [P, D_FF // P, L], F32))
        norm_stage(nc, e, f"{tag}_norm", e.x, DT, h, lambda k: col(e, norm, k))
        swiglu_up(nc, e, f"{tag}_up", w_gu, h, ff)
        project(nc, e, f"{tag}_down", w_down, D_FF // P, ff, 4, 2, 1, add_to_x(nc, e, 0.5), on="vector")


def copy_to(nc, dst, func=ACT.Copy):
    return lambda j, bank: nc.scalar.activation(tile_at(dst, j), bank, func)


def load_tables(nc, tag, pairs):
    with ExitStack() as s:
        sb, pb, sem = opened(nc, s, tag)
        loaded = sem("loaded")
        block = s.enter_context(nc.Block())

        @block.sync
        def _(sp):
            for dst, src in pairs:
                sp.dma_start(dst, src).then_inc(loaded, 16)
            sp.wait_ge(loaded, 16 * len(pairs))



def shape_tables():
    f32 = np.float32
    t = {"c_ident": np.eye(P, dtype=f32)}
    half = np.arange(P) // CH
    t["c_heads"] = (half[:, None] == half[None, :]).astype(f32)
    ang = 2 * np.pi * ((2 * np.arange(L)[None, :] + 1) * np.arange(L)[:, None] % (4 * L)) / (4 * L)
    t["c_cos"], t["c_sin"] = np.cos(ang).astype(f32), np.sin(ang).astype(f32)
    t["c_cosT"], t["c_sinT"] = np.ascontiguousarray(t["c_cos"].T), np.ascontiguousarray(t["c_sin"].T)
    pos = np.arange(L, dtype=f32)
    tt = (pos / f32(L - 1))[:, None]
    w = (f32(TWO_PI / L) * pos)[:, None]
    bands = np.linspace(1e-4, 15, 16).astype(f32)[None, :]
    feats = np.concatenate([tt, np.cos(bands * w), -np.sin(bands * w)], axis=-1).astype(f32)
    t["c_feats"] = np.ascontiguousarray(feats.T)
    t["c_negt"] = np.ascontiguousarray(-tt.reshape(TT, P).T)
    nz = np.ones((P, TT), f32)
    nz[0, 0] = 0
    t["c_notfirst"] = nz
    i = np.arange(P)
    r, c = i[:, None], i[None, :]
    lev = []
    for k in range(LEVELS):
        b = 2**k
        lev.append((r // (2 * b) == c // (2 * b)) & (r // b % 2 == 1) & (c // b % 2 == 0))
    lower = np.stack(lev).astype(f32)
    t["c_levels"] = np.ascontiguousarray(
        np.stack([lower, lower.transpose(0, 2, 1)]).transpose(2, 0, 1, 3).reshape(P, -1))
    sC, tC = i % CH, i % CH
    strict, incl = sC[:, None] < tC[None, :CH], sC[:, None] <= tC[None, :CH]
    fwd = np.concatenate([strict, incl], 1)
    strict, incl = sC[:, None] > tC[None, :CH], sC[:, None] >= tC[None, :CH]
    bwd = np.concatenate([strict, incl], 1)
    t["c_scan"] = np.ascontiguousarray(np.concatenate([fwd, bwd], 1).astype(f32))
    reset = np.ones((P, L), f32)
    reset[:, ::CH] = 0
    t["c_reset"] = reset
    t["c_causal"] = (r <= c).astype(f32)
    t["c_causal_row"] = np.where(c <= r, 0, -1e30).astype(f32)
    sel = np.zeros((A_HEADS, A_HEADS, P), f32)
    for h in range(A_HEADS):
        sel[h, h, :] = 1
    t["c_sel"] = sel.reshape(A_HEADS, -1)
    inv = (10000.0 ** (-np.arange(32, dtype=f32).astype(np.float64) / 32)).astype(f32)
    t["c_invfreq"] = np.tile(inv, 4).reshape(P, 1)
    return t



def hyena_filter_mlp(nc, e, I, h2):
    with ExitStack() as s:
        sb, pb, sem = opened(nc, s, "hyf")
        feats, w1, w2 = sb("feats", [EMB, L]), sb("w1", [EMB, FILT]), sb("w2", [FILT, FILT])
        h1, y, n = sb("h1", [FILT, L]), sb("y", [FILT, L]), sb("n", [FILT, L])
        ps = pb("ps", [FILT, 2, L])
        loaded, z_ready, y_ready, sin_ready = sem("loaded"), sem("z"), sem("y"), sem("sin")
        steps = sem("steps")
        block = s.enter_context(nc.Block())

        @block.sync
        def _(sp):
            sp.dma_start(feats[:, :], I["c_feats"]).then_inc(loaded, 16)
            sp.dma_start(w1[:, :], I["hy_ffn_w1"]).then_inc(loaded, 16)
            sp.dma_start(w2[:, :], I["hy_ffn_w2"]).then_inc(loaded, 16)

        @block.tensor
        def _(pe):
            pe.wait_ge(loaded, 48)
            nc.tensor.matmul(ps[:, 0, :], w1[:, :], feats[:, :], start=True, stop=True).then_inc(z_ready, 1)
            pe.wait_ge(sin_ready, 1)
            nc.tensor.matmul(ps[:, 1, :], w2[:, :], h1[:, :], start=True, stop=True).then_inc(z_ready, 1)

        @block.vector
        def _(dve):
            st = Steps(steps)

            def then(ins):
                dve.wait_ge(steps, st.mark(ins))

            nc.vector.memset(h2[FILT:FILT + 1, :], 1.0)
            for layer, bias in enumerate(("hy_ffn_b1", "hy_ffn_b2")):
                dve.wait_ge(z_ready, layer + 1)
                then(nc.vector.tensor_scalar(y[:, :], ps[:, layer, :], col(e, bias, 0, FILT),
                                             col(e, "hy_sin_freq", 0, FILT), ALU.add, ALU.mult))
                then(nc.vector.tensor_scalar(n[:, :], y[:, :], 1 / TWO_PI, ROUND, ALU.mult, ALU.add))
                then(nc.vector.tensor_scalar(n[:, :], n[:, :], ROUND, None, ALU.subtract))
                for part in (PI_A, PI_B, PI_C):
                    then(nc.vector.scalar_tensor_tensor(y[:, :], n[:, :], -part, y[:, :], ALU.mult, ALU.add))
                nc.vector.tensor_scalar(y[:, :], y[:, :], math.pi, -math.pi, ALU.min, ALU.max)\
                    .then_inc(y_ready, 1)
                if layer == 0:
                    dve.wait_ge(sin_ready, 1)

        @block.scalar
        def _(act):
            for layer, dst in enumerate((h1, h2)):
                act.wait_ge(y_ready, layer + 1)
                nc.scalar.activation(dst[0:FILT, :], y[:, :], ACT.Sin).then_inc(sin_ready, 1)


def hyena_spectra(nc, e, I, h2, cos, sin, spec):
    with ExitStack() as s:
        sb, pb, sem = opened(nc, s, "hys")
        w3 = sb("w3", [FILT + 1, 4, D_HY])
        dec = sb("dec", [P, 4, D_HY])
        negt, notfirst = sb("negt", [P, TT]), sb("notfirst", [P, TT])
        env = sb("env", [P, 2, D_HY])
        fb = sb("fb", [P, 2, D_HY])
        sq = sb("sq", [P, 2, D_HY])
        ab = sb("ab", [P, 2, TT, D_HY])
        rs = sb("rs", [P, 2, D_HY])
        ps = pb("ps", [P, 2, D_HY])
        pn = pb("pn", [P, D_HY])
        pk = pb("pk", [P, 2, D_HY])
        loaded, dec_abs, env_ready, raw_done = sem("loaded"), sem("dec_abs"), sem("env_ready"), sem("raw_done")
        fb_ready, sq_ready, sq_used, ab_ready = sem("fb_ready"), sem("sq_ready"), sem("sq_used"), sem("ab_ready")
        inv_ready, rs_ready, k_done, k_out = sem("inv_ready"), sem("rs_ready"), sem("k_done"), sem("k_out")
        steps = sem("steps")
        block = s.enter_context(nc.Block())
        N = 2 * TT

        @block.sync
        def _(sp):
            sp.dma_start(w3[0:FILT, :, :], I["hy_ffn_w3"].rearrange("k (g c) -> k g c", g=4)).then_inc(loaded, 16)
            sp.dma_start(w3[FILT:FILT + 1, :, :],
                         I["hy_ffn_b3"].rearrange("(o g c) -> o g c", o=1, g=4)).then_inc(loaded, 16)
            decay = I["hy_decay"].rearrange("d o c -> (d o) c")
            sp.dma_start(dec[:, :, :], decay.partition_broadcast(P)).then_inc(loaded, 16)
            sp.dma_start(negt[:, :], I["c_negt"]).then_inc(loaded, 16)
            sp.dma_start(notfirst[:, :], I["c_notfirst"]).then_inc(loaded, 16)

        @block.tensor
        def _(pe):
            pe.wait_ge(loaded, 80)
            for o in range(2):
                for t in range(TT):
                    n = o * TT + t
                    for d in range(2):
                        if n > 0:
                            pe.wait_ge(fb_ready, 2 * (n - 1) + d + 1)
                        nc.tensor.matmul(ps[:, d, :], h2[:, t * P:(t + 1) * P], w3[:, 2 * d + o, :],
                                         start=True, stop=True).then_inc(raw_done, 1)
                    for d in range(2):
                        pe.wait_ge(sq_ready, 2 * n + d + 1)
                        nc.tensor.matmul(pn[:, :], e.ones[:, :], sq[:, d, :], start=t == 0 and d == 0,
                                         stop=t == TT - 1 and d == 1).then_inc(sq_used, 1)
                pe.wait_ge(ab_ready, 2 * TT * (o + 1))
                for j in range(2 * TT):
                    m = o * 2 * TT + j
                    part, f = j // TT, j % TT
                    table = (cos, sin)[part]
                    if m >= 2:
                        pe.wait_ge(k_out, m - 1)
                    for t in range(TT):
                        last = nc.tensor.matmul(pk[:, m % 2, :], table[:, t, f * P:(f + 1) * P],
                                                ab[:, part, t, :], start=t == 0, stop=t == TT - 1)
                    last.then_inc(k_done, 1)

        @block.scalar
        def _(act):
            act.wait_ge(loaded, 80)
            nc.scalar.activation(dec[:, :, :], dec[:, :, :], ACT.Abs).then_inc(dec_abs, 1)
            act.wait_ge(dec_abs, 1)
            for o in range(2):
                for t in range(TT):
                    n = o * TT + t
                    for d in range(2):
                        if n > 0:
                            act.wait_ge(fb_ready, 2 * (n - 1) + d + 1)
                        nc.scalar.activation(env[:, d, :], dec[:, 2 * d + o, :], ACT.Exp,
                                             scale=negt[:, t:t + 1]).then_inc(env_ready, 1)
                    for d in range(2):
                        act.wait_ge(fb_ready, 2 * n + d + 1)
                        if n > 0:
                            act.wait_ge(sq_used, 2 * (n - 1) + d + 1)
                        nc.scalar.activation(sq[:, d, :], fb[:, d, :], ACT.Square).then_inc(sq_ready, 1)
                act.wait_ge(inv_ready, o + 1)
                nc.scalar.activation(rs[:, 1, :], rs[:, 0, :], ACT.Sqrt).then_inc(rs_ready, 1)

        @block.vector
        def _(dve):
            st = Steps(steps)
            for o in range(2):
                if o == 1:
                    dve.wait_ge(k_done, 2 * TT)
                for t in range(TT):
                    n = o * TT + t
                    for d in range(2):
                        dve.wait_ge(raw_done, 2 * n + d + 1)
                        dve.wait_ge(env_ready, 2 * n + d + 1)
                        if n > 0:
                            dve.wait_ge(sq_ready, 2 * (n - 1) + d + 1)
                            dve.wait_ge(ab_ready, 2 * n)
                        scalar = 1.0 if d == 0 else notfirst[:, t:t + 1]
                        nc.vector.scalar_tensor_tensor(fb[:, d, :], ps[:, d, :], scalar, env[:, d, :],
                                                       ALU.mult, ALU.mult).then_inc(fb_ready, 1)
                    dve.wait_ge(fb_ready, 2 * n + 2)
                    nc.vector.tensor_tensor(ab[:, 0, t, :], fb[:, 0, :], fb[:, 1, :], ALU.add).then_inc(ab_ready, 1)
                    nc.vector.tensor_tensor(ab[:, 1, t, :], fb[:, 0, :], fb[:, 1, :], ALU.subtract)\
                        .then_inc(ab_ready, 1)
                dve.wait_ge(sq_used, 2 * TT * (o + 1))
                dve.wait_ge(steps, st.mark(nc.vector.tensor_scalar(rs[:, 0, :], pn[:, :], EPS, None, ALU.add)))
                nc.vector.reciprocal(rs[:, 0, :], rs[:, 0, :]).then_inc(inv_ready, 1)
                dve.wait_ge(rs_ready, o + 1)
                for j in range(2 * TT):
                    m = o * 2 * TT + j
                    dve.wait_ge(k_done, m + 1)
                    nc.vector.scalar_tensor_tensor(spec[:, o, j // TT, j % TT, :], pk[:, m % 2, :], 1.0 / L,
                                                   rs[:, 1, :], ALU.mult, ALU.mult).then_inc(k_out, 1)


def hyena_conv3(nc, e, u, uc):
    with ExitStack() as s:
        sb, pb, sem = opened(nc, s, "hyc")
        mid, left = sem("mid"), sem("left")
        block = s.enter_context(nc.Block())
        n = N_HY // P

        @block.scalar
        def _(act):
            for j in range(n):
                nc.scalar.activation(uc[:, j, :], u[:, j, :], ACT.Identity, bias=col(e, "hy_conv_b", j),
                                     scale=col(e, "hy_conv_w", n + j)).then_inc(mid, 1)

        @block.vector
        def _(dve):
            for j in range(n):
                dve.wait_ge(mid, j + 1)
                nc.vector.scalar_tensor_tensor(uc[:, j, 1:L], u[:, j, 0:L - 1], col(e, "hy_conv_w", j),
                                               uc[:, j, 1:L], ALU.mult, ALU.add).then_inc(left, 1)
                dve.wait_ge(left, j + 1)
                nc.vector.scalar_tensor_tensor(uc[:, j, 0:L - 1], u[:, j, 1:L], col(e, "hy_conv_w", 2 * n + j),
                                               uc[:, j, 0:L - 1], ALU.mult, ALU.add)


def hyena_long_conv(nc, e, o, z, gate, dst, cos, sin, cosT, sinT, spec):
    with ExitStack() as s:
        sb, pb, sem = opened(nc, s, f"hyl{o}")
        zt = sb("zt", [P, TT, D_HY])
        zf = sb("zf", [P, 2, D_HY])
        yf = sb("yf", [P, 2, TT, D_HY])
        tmp = sb("tmp", [P, 4, D_HY])
        dz = sb("dz", [P, HT, L])
        pt = pb("pt", [P, 2, D_HY])
        pf = pb("pf", [P, 2, D_HY])
        po = pb("po", [P, 2, L])
        turned, zt_ready, f_done, f_out = sem("turned"), sem("zt_ready"), sem("f_done"), sem("f_out")
        prod, yf_ready, o_done, o_out, sum_ready = sem("prod"), sem("yf"), sem("o_done"), sem("o_out"), sem("sum")
        block = s.enter_context(nc.Block())

        @block.tensor
        def _(pe):
            for t in range(TT):
                if t >= 2:
                    pe.wait_ge(zt_ready, t - 1)
                for c in range(HT):
                    last = nc.tensor.transpose(pt[:, t % 2, c * P:(c + 1) * P], z[:, c, t * P:(t + 1) * P],
                                               e.ident[:, :])
                last.then_inc(turned, 1)
            pe.wait_ge(zt_ready, TT)
            for f in range(TT):
                for part, table in enumerate((cos, sin)):
                    if f > 0:
                        pe.wait_ge(f_out, 2 * (f - 1) + part + 1)
                    for t in range(TT):
                        last = nc.tensor.matmul(pf[:, part, :], table[:, t, f * P:(f + 1) * P], zt[:, t, :],
                                                start=t == 0, stop=t == TT - 1)
                    last.then_inc(f_done, 1)
            pe.wait_ge(yf_ready, 2 * TT)
            for c in range(HT):
                if c >= 2:
                    pe.wait_ge(o_out, c - 1)
                for part, table in enumerate((cosT, sinT)):
                    for f in range(TT):
                        last = nc.tensor.matmul(po[:, c % 2, :], yf[:, part, f, c * P:(c + 1) * P],
                                                table[:, f, :], start=part + f == 0,
                                                stop=part == 1 and f == TT - 1)
                last.then_inc(o_done, 1)

        @block.scalar
        def _(act):
            for t in range(TT):
                act.wait_ge(turned, t + 1)
                nc.scalar.activation(zt[:, t, :], pt[:, t % 2, :], ACT.Copy).then_inc(zt_ready, 1)
            for f in range(TT):
                for part in range(2):
                    act.wait_ge(f_done, 2 * f + part + 1)
                    if f > 0:
                        act.wait_ge(prod, 4 * f)
                    nc.scalar.activation(zf[:, part, :], pf[:, part, :], ACT.Copy).then_inc(f_out, 1)

        @block.vector
        def _(dve):
            for f in range(TT):
                dve.wait_ge(f_out, 2 * f + 2)
                kr, ks = spec[:, o, 0, f, :], spec[:, o, 1, f, :]
                if f > 0:
                    dve.wait_ge(yf_ready, 2 * f)
                for i, (a, b) in enumerate(((0, kr), (1, ks), (0, ks), (1, kr))):
                    nc.vector.tensor_tensor(tmp[:, i, :], zf[:, a, :], b, ALU.mult).then_inc(prod, 1)
            for c in range(HT):
                dve.wait_ge(o_done, c + 1)
                nc.vector.scalar_tensor_tensor(dz[:, c, :], z[:, c, :], col(e, "hy_bias_d", o * HT + c),
                                               po[:, c % 2, :], ALU.mult, ALU.add).then_inc(o_out, 1)
                dve.wait_ge(o_out, c + 1)
                nc.vector.tensor_tensor(dst[:, c, :], dz[:, c, :], gate[:, c, :], ALU.mult)

        @block.gpsimd
        def _(pool):
            for f in range(TT):
                pool.wait_ge(prod, 4 * f + 4)
                nc.gpsimd.tensor_tensor(yf[:, 0, f, :], tmp[:, 0, :], tmp[:, 1, :], ALU.subtract)\
                    .then_inc(yf_ready, 1)
                nc.gpsimd.tensor_tensor(yf[:, 1, f, :], tmp[:, 2, :], tmp[:, 3, :], ALU.add)\
                    .then_inc(yf_ready, 1)


def hyena_branch(nc, e, I, h, merged):
    with ExitStack() as s:
        keep = lambda name, shape: s.enter_context(nc.sbuf_tensor(f"hy_{name}", shape, F32))
        z2 = keep("z2", [P, HT, L])
        with ExitStack() as s2:
            part = lambda name, shape: s2.enter_context(nc.sbuf_tensor(f"hy_{name}", shape, F32))
            cos, sin = part("cos", [P, TT, L]), part("sin", [P, TT, L])
            spec = part("spec", [P, 2, 2, TT, D_HY])
            table = lambda name: I[name].rearrange("(t p) f -> p t f", p=P)
            load_tables(nc, "dft", [(cos[:, :, :], table("c_cos")), (sin[:, :, :], table("c_sin"))])
            with nc.sbuf_tensor("hy_h2", [FILT + 1, L], F32) as h2:
                hyena_filter_mlp(nc, e, I, h2)
                hyena_spectra(nc, e, I, h2, cos, sin, spec)
            uc = part("uc", [P, N_HY // P, L])
            with nc.sbuf_tensor("hy_u", [P, N_HY // P, L], F32) as u:
                project(nc, e, "hy_in", I["w_in"][:, 0:N_HY], DT, h, 3, 2, 2, copy_to(nc, u))
                hyena_conv3(nc, e, u, uc)
            cosT, sinT = part("cosT", [P, TT, L]), part("sinT", [P, TT, L])
            load_tables(nc, "idft", [(cosT[:, :, :], table("c_cosT")), (sinT[:, :, :], table("c_sinT"))])
            x1, x2, v = uc[:, 0:HT, :], uc[:, HT:2 * HT, :], uc[:, 2 * HT:3 * HT, :]
            hyena_long_conv(nc, e, 0, v, x1, x1, cos, sin, cosT, sinT, spec)
            hyena_long_conv(nc, e, 1, x1, x2, z2, cos, sin, cosT, sinT, spec)
        gated_output(nc, e, "hy", I["w_in"][:, N_HY + N_RW:N_HY + N_RW + D], h, I["hy_out"], HT, z2, merged, False)


def gated_output(nc, e, tag, w_gate, h, w_o, k_tiles, z, merged, add):
    with nc.sbuf_tensor(f"{tag}_sig", [P, DT, L], F32) as g:
        project(nc, e, f"{tag}_gate", w_gate, DT, h, 2, 2, 2, copy_to(nc, g, ACT.Sigmoid))

        def evac(j, bank):
            dst = tile_at(g if add else merged, j)
            return nc.vector.tensor_tensor(dst, tile_at(g, j), bank, ALU.mult)
        project(nc, e, f"{tag}_out", w_o, k_tiles, z, 2, 2, 2, evac, on="vector")
        if add:
            with nc.Block() as block:
                @block.vector
                def _(dve):
                    for k in range(DT):
                        nc.vector.tensor_tensor(merged[:, k, :], merged[:, k, :], g[:, k, :], ALU.add)



def rwkv_inputs(nc, e, I, h, rkv, lora):
    n = MU_ROWS + 1
    rest = N_RW - MU_ROWS * P
    with ExitStack() as s:
        u = s.enter_context(nc.sbuf_tensor("rw_u", [P, n, L], F32))
        w = I["w_in"]
        project(nc, e, "rw_in", w[:, N_HY:N_HY + MU_ROWS * P], DT, h, 5, 3, 1, copy_to(nc, u))
        project(nc, e, "rw_in2", w[:, N_HY + MU_ROWS * P:N_HY + N_RW], DT, h, 1, 1, 1,
                lambda j, bank: nc.scalar.activation(u[0:rest, MU_ROWS, :], bank, ACT.Copy), width=rest)
        keep = s.enter_context(nc.sbuf_tensor("rw_keep", [P, n], F32))
        with ExitStack() as s2:
            sb, pb, sem = opened(nc, s2, "shift")
            kept, mid, left = sem("kept"), sem("mid"), sem("left")
            block = s2.enter_context(nc.Block())
            mu = COL["rw_mu"]

            def shifted(j):
                p = P if j < MU_ROWS else rest
                return p, (rkv[:, j, :] if j < 3 * RT else lora[0:p, j - 3 * RT, :])

            @block.vector
            def _(dve):
                nc.vector.tensor_tensor(keep[:, :], e.cols[:, mu:mu + n], e.cols[:, mu + n:mu + 2 * n],
                                        ALU.add).then_inc(kept, 1)
                dve.wait_ge(kept, 1)
                nc.vector.tensor_scalar(keep[:, :], keep[:, :], -1.0, 1.0, ALU.mult, ALU.add).then_inc(kept, 1)
                for j in range(n):
                    p, us = shifted(j)
                    dve.wait_ge(mid, j + 1)
                    nc.vector.scalar_tensor_tensor(us[:, 1:L], u[0:p, j, 0:L - 1],
                                                   e.cols[0:p, mu + j:mu + j + 1], us[:, 1:L],
                                                   ALU.mult, ALU.add).then_inc(left, 1)
                    dve.wait_ge(left, j + 1)
                    nc.vector.scalar_tensor_tensor(us[:, 0:L - 1], u[0:p, j, 1:L],
                                                   e.cols[0:p, mu + n + j:mu + n + j + 1],
                                                   us[:, 0:L - 1], ALU.mult, ALU.add)

            @block.scalar
            def _(act):
                act.wait_ge(kept, 2)
                for j in range(n):
                    p, us = shifted(j)
                    nc.scalar.activation(us, u[0:p, j, :], ACT.Copy,
                                         scale=keep[0:p, j:j + 1]).then_inc(mid, 1)


def rwkv_features(nc, e, I, rkv, lora, lw, a, g, kk, bonus):
    r, k, v = rkv[:, 0:RT, :], rkv[:, RT:2 * RT, :], rkv[:, 2 * RT:3 * RT, :]
    us = lora
    WD, AD, GD = 0, 1, 2
    rest = N_RW - MU_ROWS * P
    with ExitStack() as s:
        sb, pb, sem = opened(nc, s, "rwf")
        w2, a2 = sb("w2", [P, D_RW]), sb("a2", [P, D_RW])
        g2, g2b = sb("g2", [P, D_RW]), sb("g2b", [rest, D_RW])
        kks = sb("kks", [P, RT, L])
        sq = sb("sq", [P, 2, L])
        nrm = sb("nrm", [P, 2, L])
        kd = sb("kd", [P, 2, L])
        rk = sb("rk", [P, 2, L])
        ps = pb("ps", [P, 4, L])
        pn = pb("pn", [P, 2, L])
        loaded, act_in, done, taken = sem("loaded"), sem("act_in"), sem("done"), sem("taken")
        kks_ready, sq_ready, n_done, n_root, steps = sem("kks"), sem("sq"), sem("n_done"), sem("n_root"), sem("steps")
        rk_ready, b_done, b_out, lw_done, kk_done = sem("rk"), sem("b_done"), sem("b_out"), sem("lw"), sem("kk_done")
        block = s.enter_context(nc.Block())

        @block.sync
        def _(sp):
            sp.dma_start(w2[:, :], I["rw_w2"].rearrange("d r c -> (d r) c")).then_inc(loaded, 16)
            sp.dma_start(a2[:, :], I["rw_a2"].rearrange("d r c -> (d r) c")).then_inc(loaded, 16)
            sp.dma_start(g2[:, :], I["rw_g2"][0:P, :]).then_inc(loaded, 16)
            sp.dma_start(g2b[:, :], I["rw_g2"][P:P + rest, :]).then_inc(loaded, 16)

        jobs = [("w", d, c) for d in range(2) for c in range(RT)] + \
               [("a", d, c) for d in range(2) for c in range(RT)] + [("g", 0, c) for c in range(RT)]

        @block.tensor
        def _(pe):
            pe.wait_ge(loaded, 64)
            pe.wait_ge(act_in, 3)
            for n, (kind, d, c) in enumerate(jobs):
                if n >= 4:
                    pe.wait_ge(taken, n - 3)
                cs = slice(c * P, (c + 1) * P)
                hd = slice(64 * d, 64 * d + 64)
                if kind == "g":
                    nc.tensor.matmul(ps[:, n % 4, :], g2[:, cs], us[:, GD, :], start=True, stop=False)
                    last = nc.tensor.matmul(ps[:, n % 4, :], g2b[:, cs], us[0:rest, GD + 1, :], start=False, stop=True)
                else:
                    wt, src = (w2, WD) if kind == "w" else (a2, AD)
                    last = nc.tensor.matmul(ps[:, n % 4, :], wt[hd, cs], us[hd, src, :], start=True, stop=True)
                last.then_inc(done, 1)
            for c in range(RT):
                pe.wait_ge(sq_ready, c + 1)
                if c >= 2:
                    pe.wait_ge(n_root, c - 1)
                nc.tensor.matmul(pn[:, c % 2, :], e.heads[:, :], sq[:, c % 2, :], start=True, stop=True)\
                    .then_inc(n_done, 1)
            for c in range(RT):
                pe.wait_ge(rk_ready, c + 1)
                if c >= 2:
                    pe.wait_ge(b_out, c - 1)
                else:
                    pe.wait_ge(n_root, RT)
                nc.tensor.matmul(pn[:, c % 2, :], e.heads[:, :], rk[:, c % 2, :], start=True, stop=True)\
                    .then_inc(b_done, 1)

        @block.scalar
        def _(act):
            nc.scalar.activation(us[:, WD, :], us[:, WD, :], ACT.Tanh).then_inc(act_in, 1)
            nc.scalar.activation(us[:, GD, :], us[:, GD, :], ACT.Sigmoid).then_inc(act_in, 1)
            nc.scalar.activation(us[0:rest, GD + 1, :], us[0:rest, GD + 1, :], ACT.Sigmoid).then_inc(act_in, 1)
            for n, (kind, d, c) in enumerate(jobs):
                act.wait_ge(done, n + 1)
                if kind == "g":
                    ins = nc.scalar.activation(g[:, c, :], ps[:, n % 4, :], ACT.Copy)
                else:
                    dst, bias = (lw, "rw_w0") if kind == "w" else (a, "rw_a0")
                    ins = nc.scalar.activation(dst[:, d, c, :], ps[:, n % 4, :], ACT.Sigmoid,
                                               bias=col(e, bias, d * RT + c))
                ins.then_inc(taken, 1)
            for c in range(RT):
                act.wait_ge(kks_ready, c + 1)
                if c >= 2:
                    act.wait_ge(n_done, c - 1)
                nc.scalar.activation(sq[:, c % 2, :], kks[:, c, :], ACT.Square).then_inc(sq_ready, 1)
            for c in range(RT):
                act.wait_ge(n_done, c + 1)
                if c >= 2:
                    act.wait_ge(kk_done, c - 1)
                nc.scalar.activation(nrm[:, c % 2, :], pn[:, c % 2, :], ACT.Sqrt).then_inc(n_root, 1)

        @block.gpsimd
        def _(pool):
            for c in range(RT):
                nc.gpsimd.tensor_scalar(kks[:, c, :], k[:, c, :], col(e, "rw_k_k", c), None, ALU.mult)\
                    .then_inc(kks_ready, 1)
            for d in range(2):
                for c in range(RT):
                    pool.wait_ge(taken, d * RT + c + 1)
                    nc.gpsimd.tensor_scalar(lw[:, d, c, :], lw[:, d, c, :], LOG_DECAY_MAX, None, ALU.mult)

        @block.vector
        def _(dve):
            st = Steps(steps)

            def then(ins):
                dve.wait_ge(steps, st.mark(ins))

            for c in range(RT):
                dve.wait_ge(n_root, c + 1)
                then(nc.vector.tensor_scalar(nrm[:, c % 2, :], nrm[:, c % 2, :], 1e-12, None, ALU.max))
                then(nc.vector.reciprocal(nrm[:, c % 2, :], nrm[:, c % 2, :]))
                nc.vector.tensor_tensor(kk[:, c, :], kks[:, c, :], nrm[:, c % 2, :], ALU.mult).then_inc(kk_done, 1)
            dve.wait_ge(taken, 4 * RT)
            for c in range(RT):
                then(nc.vector.scalar_tensor_tensor(kd[:, 0, :], a[:, 0, c, :], -2.0, a[:, 1, c, :],
                                                    ALU.add, ALU.add))
                then(nc.vector.tensor_scalar(kd[:, 0, :], kd[:, 0, :], col(e, "rw_k_a", c), 2.0,
                                             ALU.mult, ALU.add))
                then(nc.vector.tensor_tensor(kd[:, 0, :], kd[:, 0, :], k[:, c, :], ALU.mult))
                if c >= 2:
                    dve.wait_ge(b_done, c - 1)
                nc.vector.scalar_tensor_tensor(rk[:, c % 2, :], kd[:, 0, :], col(e, "rw_r_k", c), r[:, c, :],
                                               ALU.mult, ALU.mult).then_inc(rk_ready, 1)
                dve.wait_ge(rk_ready, c + 1)
            for c in range(RT):
                dve.wait_ge(b_done, c + 1)
                nc.vector.tensor_tensor(bonus[:, c, :], pn[:, c % 2, :], v[:, c, :], ALU.mult).then_inc(b_out, 1)


def rwkv_scaled(nc, e, d, half, rkv, lw, a, kk, reset, ar, kb, pend):
    toks = slice(half * LH, half * LH + LH)
    r, k = rkv[:, 0:RT, toks], rkv[:, RT:2 * RT, toks]
    lw, a, kk = lw[:, :, :, toks], a[:, :, :, toks], kk[:, :, toks]
    chunks = lambda t: t.rearrange("p (n c) -> p n c", c=CH)
    with ExitStack() as s:
        sb, pb, sem = opened(nc, s, f"rws{d}{half}")
        inc, exc = sb("inc", [P, 2, LH]), sb("exc", [P, 2, LH])
        kd = sb("kd", [P, 2, LH])
        steps, pin, pout, kd_ready, kd_used = sem("steps"), sem("logs"), sem("powers"), sem("kd"), sem("kd_used")
        pn, pn_used = sem("inverse"), sem("pn_used")
        block = s.enter_context(nc.Block())
        inv = sb("inv", [P, 2, LH])

        @block.gpsimd
        def _(pool):
            for c in range(RT):
                b = c % 2
                if c >= 2:
                    pool.wait_ge(kd_used, c - 1)
                nc.gpsimd.tensor_scalar(kd[:, b, :], a[:, d, c, :], -1.0, col(e, "rw_k_a", c),
                                        ALU.add, ALU.mult).then_inc(kd_ready, 1)
                pool.wait_ge(kd_ready, 3 * c + 1)
                nc.gpsimd.tensor_scalar(kd[:, b, :], kd[:, b, :], 1.0, None, ALU.add).then_inc(kd_ready, 1)
                pool.wait_ge(kd_ready, 3 * c + 2)
                nc.gpsimd.tensor_tensor(kd[:, b, :], kd[:, b, :], k[:, c, :], ALU.mult).then_inc(kd_ready, 1)

        @block.scalar
        def _(act):
            for c in range(RT):
                b = c % 2
                act.wait_ge(pin, c + 1)
                if c >= 2:
                    act.wait_ge(pn_used, c - 1)
                nc.scalar.activation(inv[:, b, :], inc[:, b, :], ACT.Exp, scale=-1.0).then_inc(pn, 1)
                act.wait_ge(pn, c + 1)
                nc.scalar.activation(inc[:, b, :], inc[:, b, :], ACT.Exp).then_inc(pout, 1)
                nc.scalar.activation(exc[:, b, :], exc[:, b, :], ACT.Exp).then_inc(pout, 1)

        @block.vector
        def _(dve):
            st = Steps(steps)

            def then(ins):
                dve.wait_ge(steps, st.mark(ins))

            def logs(c):
                b = c % 2
                pre = (inc, exc)[d]
                w = lw[:, d, c, :]
                then(nc.vector.tensor_tensor_scan(pre[:, b, :], reset[:, 0:LH], w, 0.0, ALU.mult, ALU.add))
                if d == 0:
                    nc.vector.tensor_tensor(exc[:, b, :], inc[:, b, :], w, ALU.subtract).then_inc(pin, 1)
                else:
                    whole = chunks(pre[:, b, :])[:, :, CH - 1:CH]
                    then(nc.vector.tensor_copy(pend[:, c, :], whole.rearrange("p n o -> p (n o)")))
                    then(nc.vector.tensor_tensor(chunks(exc[:, b, :]), pend[:, c, :].unsqueeze(2).to_broadcast([P, HCH, CH]),
                                                 chunks(pre[:, b, :]), ALU.subtract))
                    nc.vector.tensor_tensor(inc[:, b, :], exc[:, b, :], w, ALU.add).then_inc(pin, 1)

            def products(c):
                b = c % 2
                dve.wait_ge(pout, 2 * c + 2)
                dve.wait_ge(kd_ready, 3 * c + 3)
                nc.vector.scalar_tensor_tensor(ar[:, c, :, 0:CH], chunks(kk[:, c, :]), -1.0, chunks(exc[:, b, :]),
                                               ALU.mult, ALU.mult)
                nc.vector.tensor_tensor(ar[:, c, :, CH:2 * CH], chunks(r[:, c, :]), chunks(inc[:, b, :]), ALU.mult)
                nc.vector.tensor_tensor(kb[:, c, :, 0:CH], chunks(kd[:, b, :]), chunks(inv[:, b, :]),
                                        ALU.mult).then_inc(kd_used, 1)
                at = CH - 1 if d == 0 else 0
                nc.vector.tensor_copy(pend[:, c, :].unsqueeze(2), chunks(inc[:, b, :])[:, :, at:at + 1])
                then(nc.vector.tensor_tensor(kb[:, c, :, CH:2 * CH], chunks(kk[:, c, :]), chunks(a[:, d, c, :]),
                                             ALU.mult))
                nc.vector.tensor_tensor(kb[:, c, :, CH:2 * CH], kb[:, c, :, CH:2 * CH], chunks(inv[:, b, :]),
                                        ALU.mult).then_inc(pn_used, 1)
                dve.wait_ge(pn_used, c + 1)

            logs(0)
            for c in range(RT):
                if c + 1 < RT:
                    logs(c + 1)
                products(c)


def rwkv_matrices(nc, e, d, half, rkv, ar, kb, scan_mask, gt, kbt, vu, bv):
    v = rkv[:, 2 * RT:3 * RT, half * LH:half * LH + LH]
    with ExitStack() as s:
        sb, pb, sem = opened(nc, s, f"rwm{d}{half}")
        pg = pb("pg", [P, 2, 2, HCH, P])
        pk, pv, pbv = pb("pk", [P, HCH, P]), pb("pv", [CH, HCH, P]), pb("pbv", [P, 2, L])
        g_done, k_done, v_done = sem("g_done"), sem("k_done"), sem("v_done")
        g_out, k_out, v_out = sem("g_out"), sem("k_out"), sem("v_out")
        b_done, b_out = sem("b_done"), sem("b_out")
        block = s.enter_context(nc.Block())
        hs = [slice(0, 64), slice(64, 128)]

        @block.tensor
        def _(pe):
            def b_times_v(c):
                pe.wait_ge(g_out, 2 * c + 2)
                pe.wait_ge(v_out, c + 1)
                if c >= 2:
                    pe.wait_ge(b_out, c - 1)
                for ch in range(HCH):
                    for hd in range(2):
                        last = nc.tensor.matmul(pbv[hs[hd], c % 2, ch * CH:(ch + 1) * CH], gt[0:CH, c, ch, hd, 0:CH],
                                                vu[0:CH, c, ch, hs[hd]], start=True, stop=True)
                last.then_inc(b_done, 1)

            for c in range(RT):
                for hd in range(2):
                    if c >= 2:
                        pe.wait_ge(g_out, 2 * (c - 2) + hd + 1)
                    for ch in range(HCH):
                        last = nc.tensor.matmul(pg[:, c % 2, hd, ch, :], kb[hs[hd], c, ch, :], ar[hs[hd], c, ch, :],
                                                start=True, stop=True)
                    last.then_inc(g_done, 1)
                if c > 0:
                    pe.wait_ge(k_out, c)
                    pe.wait_ge(v_out, c)
                for ch in range(HCH):
                    last = nc.tensor.transpose(pk[:, ch, :], kb[:, c, ch, :], e.ident[:, :])
                last.then_inc(k_done, 1)
                for ch in range(HCH):
                    last = nc.tensor.transpose(pv[:, ch, :], v[:, c, ch * CH:(ch + 1) * CH], e.ident[:, :])
                last.then_inc(v_done, 1)
                if c > 0:
                    b_times_v(c - 1)
            b_times_v(RT - 1)

        @block.scalar
        def _(act):
            for c in range(RT):
                act.wait_ge(k_done, c + 1)
                nc.scalar.activation(kbt[:, c, :, :], pk[:, :, :], ACT.Copy).then_inc(k_out, 1)
                act.wait_ge(v_done, c + 1)
                nc.scalar.activation(vu[0:CH, c, :, :], pv[:, :, :], ACT.Copy).then_inc(v_out, 1)
                act.wait_ge(b_done, c + 1)
                nc.scalar.activation(bv[:, :, c, :], pbv[:, c % 2, 0:LH].rearrange("p (n i) -> p n i", n=HCH),
                                     ACT.Copy).then_inc(b_out, 1)

        @block.vector
        def _(dve):
            for c in range(RT):
                for hd in range(2):
                    dve.wait_ge(g_done, 2 * c + hd + 1)
                    mask = scan_mask[:, d, :].unsqueeze(1).to_broadcast([P, HCH, P])
                    nc.vector.tensor_tensor(gt[:, c, :, hd, :], pg[:, c % 2, hd, :, :], mask, ALU.mult)\
                        .then_inc(g_out, 1)


def rwkv_inverse(nc, e, d, half, gt, levels, xt, spare):
    with ExitStack() as s:
        sb, pb, sem = opened(nc, s, f"rwi{d}{half}")
        at, a = spare[:, 0:2, :, :], spare[:, 2:4, :, :]
        x, w = (sb(n, [P, 2, 4, P]) for n in ("x", "w"))
        pw, pt, px = (pb(n, [P, 2, 4, P]) for n in ("pw", "pt", "px"))
        zeroed, at_ready, a_turned, a_ready = sem("zeroed"), sem("at"), sem("a_turned"), sem("a")
        start_ready, w_done, w_out = sem("start"), sem("w_done"), sem("w_out")
        t_done, t_out, x_done, x_out, steps = sem("t_done"), sem("t_out"), sem("x_done"), sem("x_out"), sem("steps")
        block = s.enter_context(nc.Block())
        rounds = RT // 2
        K = LEVELS - 1
        below, above = (levels[:, d, :, :], levels[:, 1 - d, :, :])
        mask4 = lambda m: m.unsqueeze(1).to_broadcast([P, 4, P])

        @block.tensor
        def _(pe):
            for c in range(rounds):
                for q in range(2):
                    pe.wait_ge(at_ready, 2 * c + q + 1)
                    if c > 0:
                        pe.wait_ge(x_out, (K - 1) * (2 * (c - 1) + q + 1))
                    for m in range(4):
                        last = nc.tensor.transpose(px[:, q, m, :], at[:, q, m, :], e.ident[:, :])
                    last.then_inc(a_turned, 1)
                for k in range(K):
                    for q in range(2):
                        i = (c * K + k) * 2 + q
                        if k == 0:
                            pe.wait_ge(start_ready, 2 * c + q + 1)
                        else:
                            pe.wait_ge(t_out, i - 1)
                            pe.wait_ge(x_out, (c * (K - 1) + k - 1) * 2 + q + 1)
                        for m in range(4):
                            last = nc.tensor.matmul(pw[:, q, m, :], a[:, q, m, :], xt[:, 2 * c + q, m, :],
                                                    start=True, stop=True)
                        last.then_inc(w_done, 1)
                    for q in range(2):
                        i = (c * K + k) * 2 + q
                        pe.wait_ge(w_out, i + 1)
                        for m in range(4):
                            last = nc.tensor.matmul(pt[:, q, m, :], x[:, q, m, :], w[:, q, m, :],
                                                    start=True, stop=True)
                        last.then_inc(t_done, 1)
                        if k < K - 1:
                            for m in range(4):
                                last = nc.tensor.matmul(px[:, q, m, :], w[:, q, m, :], x[:, q, m, :],
                                                        start=True, stop=True)
                            last.then_inc(x_done, 1)

        @block.scalar
        def _(act):
            for c in range(rounds):
                for q in range(2):
                    act.wait_ge(a_turned, 2 * c + q + 1)
                    if c > 0:
                        act.wait_ge(w_done, 2 * K * c)
                    nc.scalar.activation(a[:, q, :, :], px[:, q, :, :], ACT.Copy).then_inc(a_ready, 1)

        @block.vector
        def _(dve):
            st = Steps(steps)
            nc.vector.memset(at[:, :, :, :], 0.0).then_inc(zeroed, 1)
            dve.wait_ge(zeroed, 1)
            for c in range(rounds):
                for q in range(2):
                    if c > 0:
                        dve.wait_ge(start_ready, 2 * c)
                    for hd in range(2):
                        hs = slice(64 * hd, 64 * hd + 64)
                        ins = nc.vector.tensor_copy(at[hs, q, :, hs], gt[CH:P, 2 * c + q, :, hd, 0:CH])
                        st.mark(ins) if hd == 0 else ins.then_inc(at_ready, 1)
                for q in range(2):
                    dve.wait_ge(a_ready, 2 * c + q + 1)
                    dve.wait_ge(at_ready, 2 * c + q + 1)
                    dve.wait_ge(steps, st.n)
                    if c > 0:
                        dve.wait_ge(t_done, 2 * K * (c - 1) + 2 * K)
                    xq, xtq = x[:, q, :, :], xt[:, 2 * c + q, :, :]
                    st.mark(nc.vector.tensor_tensor(xq, a[:, q, :, :], mask4(below[:, 0, :]), ALU.mult))
                    st.mark(nc.vector.tensor_tensor(xtq, at[:, q, :, :], mask4(above[:, 0, :]), ALU.mult))
                    dve.wait_ge(steps, st.n)
                    st.mark(nc.vector.tensor_tensor(xq, xq, mask4(e.ident[:, :]), ALU.add))
                    nc.vector.tensor_tensor(xtq, xtq, mask4(e.ident[:, :]), ALU.add).then_inc(start_ready, 1)
                    dve.wait_ge(steps, st.n)
                for k in range(K):
                    for q in range(2):
                        i = (c * K + k) * 2 + q
                        dve.wait_ge(w_done, i + 1)
                        if i >= 2:
                            dve.wait_ge(t_done, i - 1)
                        nc.vector.tensor_tensor(w[:, q, :, :], pw[:, q, :, :], mask4(above[:, k + 1, :]),
                                                ALU.mult).then_inc(w_out, 1)
                    for q in range(2):
                        i = (c * K + k) * 2 + q
                        xq, xtq = x[:, q, :, :], xt[:, 2 * c + q, :, :]
                        dve.wait_ge(t_done, i + 1)
                        nc.vector.tensor_tensor(xtq, xtq, pt[:, q, :, :], ALU.add).then_inc(t_out, 1)
                        if k < K - 1:
                            dve.wait_ge(x_done, (c * (K - 1) + k) * 2 + q + 1)
                            nc.vector.tensor_tensor(xq, xq, px[:, q, :, :], ALU.add).then_inc(x_out, 1)


def rwkv_chain(nc, e, d, half, state, ar, gt, kbt, xt, vu, bv, pend, y):
    with ExitStack() as s:
        sb, pb, sem = opened(nc, s, f"rwc{d}{half}")
        first = half == d
        rhs = sb("rhs", [P, RT, CH])
        grown = sb("grown", [P, RT, CH])
        pr, pu, py, pt = (pb(n, [P, RT, CH]) for n in ("pr", "pu", "py", "pt"))
        zeroed, r_done, r_out, u_done, u_out = sem("zeroed"), sem("r_done"), sem("r_out"), sem("u_done"), sem("u_out")
        u_out2, y_done, y_out = sem("u_out2"), sem("y_done"), sem("y_out")
        t_done, grown_ready, state_ready = sem("t_done"), sem("grown"), sem("state_ready")
        block = s.enter_context(nc.Block())
        order = list(range(HCH)) if d == 0 else list(range(HCH - 1, -1, -1))
        hs = [slice(0, 64), slice(64, 128)]

        @block.tensor
        def _(pe):
            if first:
                pe.wait_ge(zeroed, 1)
            for n, ch in enumerate(order):
                if n > 0:
                    pe.wait_ge(state_ready, n)
                    pe.wait_ge(r_out, n)
                for c in range(RT):
                    for hd in range(2):
                        last = nc.tensor.matmul(pr[hs[hd], c, :], ar[hs[hd], c, ch, 0:CH], state[hs[hd], c, :],
                                                start=True, stop=True)
                last.then_inc(r_done, 1)
                pe.wait_ge(r_out, n + 1)
                if n > 0:
                    pe.wait_ge(u_out, n)
                    pe.wait_ge(u_out2, n)
                for c in range(RT):
                    last = nc.tensor.matmul(pu[:, c, :], xt[:, c, ch, :], rhs[:, c, :], start=True, stop=True)
                last.then_inc(u_done, 1)
                pe.wait_ge(u_out, n + 1)
                pe.wait_ge(u_out2, n + 1)
                if n > 0:
                    pe.wait_ge(grown_ready, n)
                for c in range(RT):
                    for hd in range(2):
                        last = nc.tensor.matmul(pt[hs[hd], c, :], kbt[:, c, ch, hs[hd]], vu[:, c, ch, hs[hd]],
                                                start=True, stop=True)
                last.then_inc(t_done, 1)
                if n > 0:
                    pe.wait_ge(y_out, n)
                for c in range(RT):
                    for hd in range(2):
                        nc.tensor.matmul(py[hs[hd], c, :], vu[:, c, ch, hs[hd]], gt[:, c, ch, hd, CH:2 * CH],
                                         start=True, stop=False)
                        last = nc.tensor.matmul(py[hs[hd], c, :], state[hs[hd], c, :], ar[hs[hd], c, ch, CH:2 * CH],
                                                start=False, stop=True)
                last.then_inc(y_done, 1)

        @block.scalar
        def _(act):
            for n, ch in enumerate(order):
                act.wait_ge(u_done, n + 1)
                nc.scalar.activation(vu[CH:P, :, ch, 0:CH], pu[0:CH, :, :], ACT.Copy).then_inc(u_out, 1)

        @block.vector
        def _(dve):
            if first:
                nc.vector.memset(state[:, :, :], 0.0).then_inc(zeroed, 1)
                dve.wait_ge(zeroed, 1)
            for n, ch in enumerate(order):
                dve.wait_ge(r_done, n + 1)
                if n > 0:
                    dve.wait_ge(u_done, n)
                nc.vector.tensor_tensor(rhs[:, :, :], bv[:, ch, :, :], pr[:, :, :], ALU.add).then_inc(r_out, 1)
                dve.wait_ge(u_done, n + 1)
                nc.vector.tensor_copy(vu[CH:P, :, ch, CH:P], pu[CH:P, :, :]).then_inc(u_out2, 1)
                dve.wait_ge(t_done, n + 1)
                if n > 0:
                    dve.wait_ge(state_ready, n)
                nc.vector.tensor_tensor(grown[:, :, :], state[:, :, :], pt[:, :, :], ALU.add)\
                    .then_inc(grown_ready, 1)
                dve.wait_ge(y_done, n + 1)
                dve.wait_ge(grown_ready, n + 1)
                decay = pend[:, :, ch:ch + 1].to_broadcast([P, RT, CH])
                nc.vector.tensor_tensor(state[:, :, :], grown[:, :, :], decay, ALU.mult).then_inc(state_ready, 1)
                ys = y[:, :, half * LH + ch * CH:half * LH + (ch + 1) * CH]
                if d == 0:
                    nc.vector.tensor_copy(ys, py[:, :, :]).then_inc(y_out, 1)
                else:
                    nc.vector.tensor_tensor(ys, ys, py[:, :, :], ALU.add).then_inc(y_out, 1)


def rwkv_group_norm(nc, e, y, bonus, g):
    with ExitStack() as s:
        sb, pb, sem = opened(nc, s, "rwn")
        cen, sq, rs = sb("cen", [P, RT, L]), sb("sq", [P, RT, L]), sb("rs", [P, RT, L])
        ps, pv = pb("ps", [P, 2, L]), pb("pv", [P, 2, L])
        m_done, cen_ready, sq_ready, v_done = sem("m_done"), sem("cen"), sem("sq"), sem("v_done")
        inv_ready, rs_ready, steps = sem("inv"), sem("rs_ready"), sem("steps")
        block = s.enter_context(nc.Block())

        @block.tensor
        def _(pe):
            for c in range(RT):
                if c >= 2:
                    pe.wait_ge(cen_ready, c - 1)
                nc.tensor.matmul(ps[:, c % 2, :], e.heads[:, :], y[:, c, :], start=True, stop=True).then_inc(m_done, 1)
            for c in range(RT):
                pe.wait_ge(sq_ready, c + 1)
                if c >= 2:
                    pe.wait_ge(inv_ready, c - 1)
                nc.tensor.matmul(pv[:, c % 2, :], e.heads[:, :], sq[:, c, :], start=True, stop=True).then_inc(v_done, 1)

        @block.scalar
        def _(act):
            for c in range(RT):
                act.wait_ge(cen_ready, c + 1)
                nc.scalar.activation(sq[:, c, :], cen[:, c, :], ACT.Square).then_inc(sq_ready, 1)
            for c in range(RT):
                act.wait_ge(inv_ready, c + 1)
                nc.scalar.activation(rs[:, c, :], rs[:, c, :], ACT.Sqrt).then_inc(rs_ready, 1)

        @block.vector
        def _(dve):
            st = Steps(steps)

            def then(ins):
                dve.wait_ge(steps, st.mark(ins))

            for c in range(RT):
                dve.wait_ge(m_done, c + 1)
                nc.vector.scalar_tensor_tensor(cen[:, c, :], ps[:, c % 2, :], -1.0 / CH, y[:, c, :],
                                               ALU.mult, ALU.add).then_inc(cen_ready, 1)
            for c in range(RT):
                dve.wait_ge(v_done, c + 1)
                then(nc.vector.tensor_scalar(rs[:, c, :], pv[:, c % 2, :], 1.0 / CH, GN_EPS, ALU.mult, ALU.add))
                nc.vector.reciprocal(rs[:, c, :], rs[:, c, :]).then_inc(inv_ready, 1)
            for c in range(RT):
                dve.wait_ge(rs_ready, c + 1)
                dve.wait_ge(cen_ready, c + 1)
                then(nc.vector.scalar_tensor_tensor(cen[:, c, :], cen[:, c, :], col(e, "rw_ln_w", c), rs[:, c, :],
                                                    ALU.mult, ALU.mult))
                then(nc.vector.scalar_tensor_tensor(cen[:, c, :], cen[:, c, :], col(e, "rw_ln_b", c),
                                                    bonus[:, c, :], ALU.add, ALU.add))
                nc.vector.tensor_tensor(y[:, c, :], cen[:, c, :], g[:, c, :], ALU.mult)


def rwkv_branch(nc, e, I, merged):
    with ExitStack() as s:
        keep = lambda name, shape: s.enter_context(nc.sbuf_tensor(f"rw_{name}", shape, F32))
        y = keep("y", [P, RT, L])
        with ExitStack() as s2:
            part = lambda name, shape: s2.enter_context(nc.sbuf_tensor(f"rw_{name}", shape, F32))
            rkv = part("rkv", [P, 3 * RT, L])
            lw, a = part("lw", [P, 2, RT, L]), part("a", [P, 2, RT, L])
            g, kk, bonus = (part(n, [P, RT, L]) for n in ("g", "kk", "bonus"))
            with nc.sbuf_tensor("rw_lora", [P, 4, L], F32) as lora, nc.sbuf_tensor("rw_h", [P, DT, L], F32) as h:
                norm_stage(nc, e, "mix2", e.x, DT, h, lambda k: col(e, "mix_norm", k))
                rwkv_inputs(nc, e, I, h, rkv, lora)
                rwkv_features(nc, e, I, rkv, lora, lw, a, g, kk, bonus)
            with ExitStack() as s3:
                scan = lambda name, shape: s3.enter_context(nc.sbuf_tensor(f"rw_{name}", shape, F32))
                gt = scan("gt", [P, RT, HCH, 2, P])
                kbt, vu, xt, ar, kb = (scan(n, [P, RT, HCH, P]) for n in ("kbt", "vu", "xt", "ar", "kb"))
                pend = scan("pend", [P, RT, HCH])
                state = scan("state", [P, RT, CH])
                bv = scan("bv", [P, HCH, RT, CH])
                reset, scan_mask = scan("reset", [P, L]), scan("scan_mask", [P, 2, P])
                levels = scan("levels", [P, 2, LEVELS, P])
                load_tables(nc, "scan_tables", [
                    (reset[:, :], I["c_reset"]),
                    (scan_mask[:, :, :], I["c_scan"].rearrange("p (d t) -> p d t", d=2)),
                    (levels[:, :, :, :], I["c_levels"].rearrange("p (a k t) -> p a k t", a=2, k=LEVELS))])
                for d in range(2):
                    for half in ((0, 1), (1, 0))[d]:
                        rwkv_scaled(nc, e, d, half, rkv, lw, a, kk, reset, ar, kb, pend)
                        rwkv_matrices(nc, e, d, half, rkv, ar, kb, scan_mask, gt, kbt, vu, bv)
                        rwkv_inverse(nc, e, d, half, gt, levels, xt, kb)
                        rwkv_chain(nc, e, d, half, state, ar, gt, kbt, xt, vu, bv, pend, y)
            rwkv_group_norm(nc, e, y, bonus, g)
        h = keep("h3", [P, DT, L])
        norm_stage(nc, e, "mix3", e.x, DT, h, lambda k: col(e, "mix_norm", k))
        gated_output(nc, e, "rw", I["w_in"][:, N_HY + N_RW + D:N_HY + N_RW + 2 * D], h, I["rw_out"], RT, y, merged, True)



def silu_condition(nc, e, cond):
    with ExitStack() as s:
        s.enter_context(nc.Block()).scalar(
            lambda act: nc.scalar.activation(cond[:, :], e.cols[:, COL["c_2"]:COL["c_2"] + DT], ACT.Silu))


def condition(nc, e, tag, w, n_tiles, bias, cond, dst):
    wide = 4 * P
    n = n_tiles // 4
    with ExitStack() as s:
        sb, pb, sem = opened(nc, s, tag)
        ring = sb("ring", [P, 2, DT, wide])
        acc = sb("acc", [P, 2, wide])
        ps = pb("ps", [P, n_tiles])
        loaded = [sem(f"loaded{i}") for i in range(2)]
        acc_done, summed, steps = sem("acc_done"), sem("summed"), sem("steps")
        block = s.enter_context(nc.Block())
        wv = w.rearrange("(k p) n -> p k n", p=P)

        @block.sync
        def _(sp):
            for c in range(n):
                if c >= 2:
                    sp.wait_ge(acc_done, c - 1)
                sp.dma_start(ring[:, c % 2, :, :], wv[:, :, c * wide:(c + 1) * wide]).then_inc(loaded[c % 2], 16)

        @block.vector
        def _(dve):
            st = Steps(steps)
            for c in range(n):
                b = c % 2
                dve.wait_ge(loaded[b], 16 * (c // 2 + 1))
                if c >= 2:
                    dve.wait_ge(summed, c - 1)
                dve.wait_ge(steps, st.mark(nc.vector.tensor_scalar(acc[:, b, :], ring[:, b, 0, :], cond[:, 0:1],
                                                                   None, ALU.mult)))
                for k in range(1, DT):
                    ins = nc.vector.scalar_tensor_tensor(acc[:, b, :], ring[:, b, k, :], cond[:, k:k + 1],
                                                         acc[:, b, :], ALU.mult, ALU.add)
                    if k < DT - 1:
                        dve.wait_ge(steps, st.mark(ins))
                    else:
                        ins.then_inc(acc_done, 1)
            dve.wait_ge(summed, n)
            nc.vector.tensor_tensor(dst[:, :], ps[:, :], e.cols[:, bias:bias + n_tiles], ALU.add)

        @block.tensor
        def _(pe):
            for c in range(n):
                pe.wait_ge(acc_done, c + 1)
                for j in range(4):
                    last = nc.tensor.matmul(ps[:, 4 * c + j:4 * c + j + 1], acc[:, c % 2, j * P:(j + 1) * P],
                                            e.ones[:, 0:1], start=True, stop=True)
                last.then_inc(summed, 1)


def project_tokens(nc, e, tag, w, k_tiles, lhs, n_chunks, dst, columns):
    with ExitStack() as s:
        sb, pb, sem = opened(nc, s, tag)
        ring = sb("ring", [P, 2, k_tiles, 512])
        ps = pb("ps", [P, 4, 512])
        loaded = [sem(f"loaded{i}") for i in range(2)]
        mm_done, taken = sem("mm_done"), sem("taken")
        block = s.enter_context(nc.Block())
        parts = [columns(c) for c in range(n_chunks)]

        @block.sync
        def _(sp):
            for c in range(n_chunks):
                if c >= 2:
                    sp.wait_ge(mm_done, TT * (c - 1))
                step = 512 // len(parts[c])
                for i, at in enumerate(parts[c]):
                    sp.dma_start(ring[:, c % 2, :, i * step:(i + 1) * step],
                                 w.rearrange("(k p) n -> p k n", p=P)[:, :, at:at + step]).then_inc(loaded[c % 2], 16)

        @block.tensor
        def _(pe):
            for c in range(n_chunks):
                pe.wait_ge(loaded[c % 2], 16 * len(parts[c]) * (c // 2 + 1))
                for t in range(TT):
                    n = c * TT + t
                    if n >= 4:
                        pe.wait_ge(taken, n - 3)
                    for k in range(k_tiles):
                        last = nc.tensor.matmul(ps[:, n % 4, :], lhs[:, k, t * P:(t + 1) * P], ring[:, c % 2, k, :],
                                                start=k == 0, stop=k == k_tiles - 1)
                    last.then_inc(mm_done, 1)

        @block.scalar
        def _(act):
            for c in range(n_chunks):
                for t in range(TT):
                    n = c * TT + t
                    act.wait_ge(mm_done, n + 1)
                    nc.scalar.activation(dst[:, t, c * 512:(c + 1) * 512], ps[:, n % 4, :], ACT.Copy).then_inc(taken, 1)


def mlstm_gates(nc, e, I, h, rows, ccol):
    H = A_HEADS
    with ExitStack() as s:
        sb, pb, sem = opened(nc, s, "mg")
        w = sb("w", [P, DT, 2 * H])
        ones, zeros = sb("ones", [H, L]), sb("zeros", [H, L])
        ig, f, af, m, F, M = (sb(n, [H, L]) for n in ("ig", "f", "af", "m", "cf", "mx"))
        pi, pf, pc = pb("pi", [H, L]), pb("pf", [H, L]), pb("pc", [P, TT, H])
        loaded, mm_done, act_done, dve_done = sem("loaded"), sem("mm_done"), sem("act_done"), sem("dve_done")
        steps, turned, in_done = sem("steps"), sem("turned"), sem("in_done")
        block = s.enter_context(nc.Block())
        at = 2 * H * A_QK + A_HEADS * P

        @block.sync
        def _(sp):
            sp.dma_start(w[:, :, :], I["a_w_in_2"][0, :, at:at + 2 * H].rearrange("(k p) n -> p k n", p=P))\
                .then_inc(loaded, 16)

        @block.tensor
        def _(pe):
            pe.wait_ge(loaded, 16)
            for g, ps in enumerate((pi, pf)):
                for k in range(DT):
                    last = nc.tensor.matmul(ps[:, :], w[:, k, g * H:(g + 1) * H], h[:, k, :],
                                            start=k == 0, stop=k == DT - 1)
                last.then_inc(mm_done, 1)
            pe.wait_ge(dve_done, 2)
            for t in range(TT):
                last = nc.tensor.transpose(pc[:, t, :], ig[:, t * P:(t + 1) * P], e.ident[0:H, 0:H])
            last.then_inc(turned, 1)

        @block.scalar
        def _(act):
            b = COL["a_gate_b_2"]
            act.wait_ge(mm_done, 1)
            nc.scalar.activation(ig[:, :], pi[:, :], ACT.Identity, bias=e.cols[0:H, b:b + 1]).then_inc(act_done, 1)
            act.wait_ge(mm_done, 2)
            nc.scalar.activation(f[:, :], pf[:, :], ACT.Identity, bias=e.cols[0:H, b + 1:b + 2]).then_inc(act_done, 1)
            act.wait_ge(act_done, 2)
            nc.scalar.activation(af[:, :], f[:, :], ACT.Abs).then_inc(act_done, 1)
            act.wait_ge(act_done, 3)
            nc.scalar.activation(af[:, :], af[:, :], ACT.Exp, scale=-1.0).then_inc(act_done, 1)
            act.wait_ge(act_done, 4)
            nc.scalar.activation(af[:, :], af[:, :], ACT.Ln, bias=1.0).then_inc(act_done, 1)
            act.wait_ge(dve_done, 1)
            nc.scalar.activation(rows[:, 1, :], m[:, :], ACT.Exp, scale=-1.0)
            act.wait_ge(turned, 1)
            nc.scalar.activation(ccol[:, :, :], pc[:, :, :], ACT.Copy)

        @block.vector
        def _(dve):
            st = Steps(steps)

            def then(ins):
                dve.wait_ge(steps, st.mark(ins))

            then(nc.vector.memset(ones[:, :], 1.0))
            then(nc.vector.memset(zeros[:, :], 0.0))
            dve.wait_ge(act_done, 5)
            then(nc.vector.scalar_tensor_tensor(f[:, :], f[:, :], 0.0, af[:, :], ALU.min, ALU.subtract))
            then(nc.vector.tensor_tensor_scan(F[:, :], ones[:, :], f[:, :], 0.0, ALU.mult, ALU.add))
            then(nc.vector.tensor_tensor(ig[:, :], ig[:, :], F[:, :], ALU.subtract))
            then(nc.vector.tensor_tensor_scan(M[:, :], zeros[:, :], ig[:, :], 0.0, ALU.add, ALU.max))
            nc.vector.tensor_tensor(m[:, :], F[:, :], M[:, :], ALU.add).then_inc(dve_done, 1)
            nc.vector.tensor_scalar(rows[:, 0, :], M[:, :], -1.0, None, ALU.mult).then_inc(dve_done, 1)


def mlstm_heads(nc, e, I, qk, v, rows, ccol, out):
    H = A_HEADS
    with ExitStack() as s:
        sb, pb, sem = opened(nc, s, "mh")
        sel, causal = sb("sel", [H, H, P]), sb("causal", [P, P])
        dT, pT = sb("dT", [P, 2, L]), sb("pT", [P, 2, L])
        negM, floor, den = sb("negM", [P, 2, L]), sb("floor", [P, 2, L]), sb("den", [P, 2, L])
        pm, pe_, pS, pn, pd = (pb("pm", [P, L]), pb("pe", [P, L]), pb("pS", [P, 2, L]),
                               pb("pn", [P, 2, L]), pb("pd", [P, 2, L]))
        loaded, rows_done, rows_out, s_done = sem("loaded"), sem("rows_done"), sem("rows_out"), sem("s_done")
        arg_ready, d_ready, p_ready, p_masked = sem("arg"), sem("d_ready"), sem("p_ready"), sem("p_masked")
        used, head_done, abs_ready, out_done, steps = (sem("used"), sem("head_done"), sem("abs"),
                                                       sem("out_done"), sem("steps"))
        block = s.enter_context(nc.Block())
        units = [(h, j) for h in range(H) for j in range(TT)]

        @block.sync
        def _(sp):
            sp.dma_start(sel[:, :, :], I["c_sel"].rearrange("k (h p) -> k h p", h=H)).then_inc(loaded, 16)
            sp.dma_start(causal[:, :], I["c_causal"]).then_inc(loaded, 16)

        @block.tensor
        def _(pe):
            def scores(n):
                h, j = units[n]
                hs = slice(64 * (h % 2), 64 * (h % 2) + 64)
                if j == 0:
                    if h > 0:
                        pe.wait_ge(rows_out, 2 * h)
                    nc.tensor.matmul(pm[:, :], sel[:, h, :], rows[:, 0, :], start=True, stop=True)
                    nc.tensor.matmul(pe_[:, :], sel[:, h, :], rows[:, 1, :], start=True, stop=True)\
                        .then_inc(rows_done, 1)
                if n >= 2:
                    pe.wait_ge(p_ready, n - 1)
                nc.tensor.matmul(pS[:, n % 2, j * P:L], qk[hs, H // 2 + h // 2, j * P:(j + 1) * P],
                                 qk[hs, h // 2, j * P:L], start=True, stop=True).then_inc(s_done, 1)

            pe.wait_ge(loaded, 32)
            scores(0)
            for n, (h, j) in enumerate(units):
                if n + 1 < len(units):
                    scores(n + 1)
                pe.wait_ge(p_masked, n + 1)
                if j == 0 and h >= 2:
                    pe.wait_ge(out_done, h - 1)
                first, last_j = j == 0, j == TT - 1
                nc.tensor.matmul(pn[:, h % 2, j * P:L], v[:, j, h * P:(h + 1) * P], pT[:, n % 2, j * P:L],
                                 start=first, stop=last_j)
                last = nc.tensor.matmul(pd[:, h % 2, j * P:L], e.ones[:, :], pT[:, n % 2, j * P:L],
                                        start=first, stop=last_j)
                last.then_inc(used, 1)
                if last_j:
                    pass

        @block.scalar
        def _(act):
            for n, (h, j) in enumerate(units):
                if j == 0:
                    act.wait_ge(rows_done, h + 1)
                    if h >= 2:
                        act.wait_ge(out_done, h - 1)
                    nc.scalar.activation(negM[:, h % 2, :], pm[:, :], ACT.Copy).then_inc(rows_out, 1)
                    nc.scalar.activation(floor[:, h % 2, :], pe_[:, :], ACT.Copy).then_inc(rows_out, 1)
                act.wait_ge(arg_ready, n + 1)
                nc.scalar.activation(dT[:, n % 2, j * P:L], dT[:, n % 2, j * P:L], ACT.Exp).then_inc(d_ready, 1)
                if j == TT - 1:
                    act.wait_ge(used, n + 1)
                    nc.scalar.activation(den[:, h % 2, :], pd[:, h % 2, :], ACT.Abs).then_inc(abs_ready, 1)

        @block.vector
        def _(dve):
            st = Steps(steps)

            def then(ins):
                dve.wait_ge(steps, st.mark(ins))

            def finish(h):
                d = den[:, h % 2, :]
                dve.wait_ge(abs_ready, h + 1)
                then(nc.vector.tensor_tensor(d, d, floor[:, h % 2, :], ALU.max))
                then(nc.vector.reciprocal(d, d))
                nc.vector.tensor_tensor(out[:, h, :], pn[:, h % 2, :], d, ALU.mult).then_inc(out_done, 1)

            for n, (h, j) in enumerate(units):
                if j == 0:
                    dve.wait_ge(rows_out, 2 * h + 2)
                if n >= 2:
                    dve.wait_ge(p_ready, n - 1)
                nc.vector.tensor_scalar(dT[:, n % 2, j * P:L], negM[:, h % 2, j * P:L], ccol[:, j, h:h + 1], 0.0,
                                        ALU.add, ALU.min).then_inc(arg_ready, 1)
                dve.wait_ge(d_ready, n + 1)
                dve.wait_ge(s_done, n + 1)
                if n >= 2:
                    dve.wait_ge(used, n - 1)
                nc.vector.scalar_tensor_tensor(pT[:, n % 2, j * P:L], pS[:, n % 2, j * P:L], A_QK**-0.5,
                                               dT[:, n % 2, j * P:L], ALU.mult, ALU.mult).then_inc(p_ready, 1)
                if j == TT - 1:
                    finish(h)

        @block.gpsimd
        def _(pool):
            pool.wait_ge(loaded, 32)
            for n, (h, j) in enumerate(units):
                pool.wait_ge(p_ready, n + 1)
                diag = pT[:, n % 2, j * P:(j + 1) * P]
                nc.gpsimd.tensor_tensor(diag, diag, causal[:, :], ALU.mult).then_inc(p_masked, 1)


def head_norm_gate(nc, e, hh, og):
    n = A_HEADS
    with ExitStack() as s:
        sb, pb, sem = opened(nc, s, "hn")
        sq, rs = sb("sq", [P, 2, L]), sb("rs", [P, 2, L])
        ps = pb("ps", [P, 2, L])
        sq_ready, v_done, inv_ready, rs_ready, done, steps = (sem("sq"), sem("v_done"), sem("inv"),
                                                              sem("rs_ready"), sem("done"), sem("steps"))
        block = s.enter_context(nc.Block())

        @block.tensor
        def _(pe):
            for k in range(n):
                pe.wait_ge(sq_ready, k + 1)
                if k >= 2:
                    pe.wait_ge(inv_ready, k - 1)
                nc.tensor.matmul(ps[:, k % 2, :], e.ones[:, :], sq[:, k % 2, :], start=True, stop=True)\
                    .then_inc(v_done, 1)

        @block.scalar
        def _(act):
            for k in range(n):
                if k >= 2:
                    act.wait_ge(v_done, k - 1)
                nc.scalar.activation(sq[:, k % 2, :], hh[:, k, :], ACT.Square).then_inc(sq_ready, 1)
                if k >= 1:
                    act.wait_ge(inv_ready, k)
                    nc.scalar.activation(rs[:, (k - 1) % 2, :], rs[:, (k - 1) % 2, :], ACT.Sqrt).then_inc(rs_ready, 1)
            act.wait_ge(inv_ready, n)
            nc.scalar.activation(rs[:, (n - 1) % 2, :], rs[:, (n - 1) % 2, :], ACT.Sqrt).then_inc(rs_ready, 1)

        @block.vector
        def _(dve):
            st = Steps(steps)

            def then(ins):
                dve.wait_ge(steps, st.mark(ins))

            def finish(k):
                dve.wait_ge(rs_ready, k + 1)
                then(nc.vector.scalar_tensor_tensor(hh[:, k, :], hh[:, k, :], col(e, "a_head_g_2", k),
                                                    rs[:, k % 2, :], ALU.mult, ALU.mult))
                then(nc.vector.tensor_tensor(hh[:, k, :], hh[:, k, :], og[:, k, :], ALU.mult))

            for k in range(n):
                dve.wait_ge(v_done, k + 1)
                then(nc.vector.tensor_scalar(rs[:, k % 2, :], ps[:, k % 2, :], 1.0 / P, EPS, ALU.mult, ALU.add))
                nc.vector.reciprocal(rs[:, k % 2, :], rs[:, k % 2, :]).then_inc(inv_ready, 1)
                if k >= 1:
                    finish(k - 1)
            finish(n - 1)


def mlstm_mixer(nc, e, I, h, y):
    H = A_HEADS
    with ExitStack() as s:
        keep = lambda name, shape: s.enter_context(nc.sbuf_tensor(f"ml_{name}", shape, F32))
        w = I["a_w_in_2"][0]
        hh, og = keep("hh", [P, H, L]), keep("og", [P, H, L])
        with ExitStack() as s2:
            part = lambda name, shape: s2.enter_context(nc.sbuf_tensor(f"ml_{name}", shape, F32))
            qk, v = part("qk", [P, H, L]), part("v", [P, TT, H * P])
            rows, ccol = part("rows", [H, 2, L]), part("ccol", [P, TT, H])
            project(nc, e, "ml_qk", w[:, 0:2 * H * A_QK], DT, h, 2, 2, 2, copy_to(nc, qk))
            project_tokens(nc, e, "ml_v", w, DT, h, 2, v, lambda c: [2 * H * A_QK + 512 * c])
            mlstm_gates(nc, e, I, h, rows, ccol)
            at = 2 * H * A_QK + H * P + 2 * H
            project(nc, e, "ml_og", w[:, at:at + H * P], DT, h, 2, 2, 2, copy_to(nc, og, ACT.Sigmoid))
            mlstm_heads(nc, e, I, qk, v, rows, ccol, hh)
        head_norm_gate(nc, e, hh, og)
        project(nc, e, "ml_out", I["a_w_out_2"][0], H, hh, 2, 2, 2, copy_to(nc, y))


def sqrelu_up(nc, e, tag, w1, h, ff):
    with ExitStack() as s:
        sb, pb, sem = opened(nc, s, tag)
        slots, per = 2, 2
        nb = slots * per
        groups = D_FF2 // P // nb
        ring = sb("ring", [P, slots, DT, per * P])
        pos = sb("pos", [P, nb, L])
        ps = pb("ps", [P, nb, L])
        loaded = [sem(f"loaded{i}") for i in range(slots)]
        mm_done, relu_ready, bank_free = sem("mm_done"), sem("relu_ready"), sem("bank_free")
        block = s.enter_context(nc.Block())
        wv = w1.rearrange("(k p) n -> p k n", p=P)

        @block.sync
        def _(sp):
            def load(i, c):
                return sp.dma_start(ring[:, i, :, :], wv[:, :, bass.ds(c * per * P, per * P)])
            stream_weights(sp, load, slots, groups, per, loaded, mm_done)

        @block.tensor
        def _(pe):
            with pe.Fori(0, groups) as g:
                for i in range(slots):
                    pe.wait_ge(loaded[i], g * 16 + 16)
                    for t in range(per):
                        b = i * per + t
                        pe.wait_ge(bank_free, g * nb + (b + 1))
                        for k in range(DT):
                            last = nc.tensor.matmul(ps[:, b, :], ring[:, i, k, t * P:(t + 1) * P], h[:, k, :],
                                                    start=k == 0, stop=k == DT - 1)
                        last.then_inc(mm_done, 1)

        @block.scalar
        def _(act):
            with act.Fori(0, groups) as g:
                for b in range(nb):
                    act.wait_ge(mm_done, g * nb + (b + 1))
                    act.wait_ge(bank_free, g * nb + (b + 1))
                    nc.scalar.activation(pos[:, b, :], ps[:, b, :], ACT.Relu).then_inc(relu_ready, 1)

        @block.vector
        def _(dve):
            dve.sem_inc(bank_free, nb)
            with dve.Fori(0, groups) as g:
                for b in range(nb):
                    dve.wait_ge(relu_ready, g * nb + (b + 1))
                    nc.vector.scalar_tensor_tensor(tile_at(ff, g * nb + b), ps[:, b, :], 0.0, pos[:, b, :],
                                                   ALU.max, ALU.mult).then_inc(bank_free, 1)


def rope_tables(nc, e, I, cosr, sinr):
    with ExitStack() as s:
        sb, pb, sem = opened(nc, s, "rope")
        pos = s.enter_context(nc.sbuf_tensor("rope_pos", [P, L], mybir.dt.int32))
        inv, ang, n, r = sb("inv", [P, 1]), sb("ang", [P, L]), sb("n", [P, L]), sb("r", [P, L])
        loaded, steps, r_ready, abs_ready, c_ready = sem("loaded"), sem("steps"), sem("r"), sem("abs"), sem("c")
        block = s.enter_context(nc.Block())

        @block.sync
        def _(sp):
            sp.dma_start(pos[:, :], I["positions_2"][0, :].partition_broadcast(P)).then_inc(loaded, 16)
            sp.dma_start(inv[:, :], I["c_invfreq"]).then_inc(loaded, 16)

        @block.vector
        def _(dve):
            st = Steps(steps)

            def then(ins):
                dve.wait_ge(steps, st.mark(ins))

            dve.wait_ge(loaded, 32)
            then(nc.vector.tensor_copy(ang[:, :], pos[:, :]))
            then(nc.vector.tensor_scalar(ang[:, :], ang[:, :], inv[:, 0:1], None, ALU.mult))
            then(nc.vector.tensor_scalar(n[:, :], ang[:, :], 1 / TWO_PI, ROUND, ALU.mult, ALU.add))
            then(nc.vector.tensor_scalar(n[:, :], n[:, :], ROUND, None, ALU.subtract))
            for part in (PI_A, PI_B, PI_C):
                then(nc.vector.scalar_tensor_tensor(ang[:, :], n[:, :], -part, ang[:, :], ALU.mult, ALU.add))
            nc.vector.tensor_scalar(ang[:, :], ang[:, :], math.pi, -math.pi, ALU.min, ALU.max).then_inc(r_ready, 1)
            dve.wait_ge(abs_ready, 1)
            nc.vector.tensor_scalar(r[:, :], r[:, :], -1.0, math.pi / 2, ALU.mult, ALU.add).then_inc(c_ready, 1)

        @block.scalar
        def _(act):
            act.wait_ge(r_ready, 1)
            nc.scalar.activation(sinr[:, :], ang[:, :], ACT.Sin)
            nc.scalar.activation(r[:, :], ang[:, :], ACT.Abs).then_inc(abs_ready, 1)
            act.wait_ge(c_ready, 1)
            nc.scalar.activation(cosr[:, :], r[:, :], ACT.Sin)


def rotate(nc, dve, steps, st, p1, p2, cosr, sinr, parts, t1, t2, t3, t4):
    cs, sn = cosr[0:parts, :], sinr[0:parts, :]
    st.mark(nc.vector.tensor_tensor(t1, p1, cs, ALU.mult))
    st.mark(nc.vector.tensor_tensor(t2, p2, sn, ALU.mult))
    st.mark(nc.vector.tensor_tensor(t3, p2, cs, ALU.mult))
    dve.wait_ge(steps, st.mark(nc.vector.tensor_tensor(t4, p1, sn, ALU.mult)))


def mla_keys_a(nc, e, I, h, ckv, cosr, sinr, kr):
    with ExitStack() as s:
        sb, pb, sem = opened(nc, s, "ka")
        w = sb("w", [P, DT, KV_LORA + ROPE])
        t1, t2, t3, t4 = (sb(n, [32, L]) for n in ("t1", "t2", "t3", "t4"))
        pc, p1, p2 = pb("pc", [P, 2, L]), pb("p1", [32, L]), pb("p2", [32, L])
        loaded, c_done, r_done, steps = sem("loaded"), sem("c_done"), sem("r_done"), sem("steps")
        block = s.enter_context(nc.Block())

        @block.sync
        def _(sp):
            sp.dma_start(w[:, :, :], I["kv_w_a_2"].rearrange("(k p) n -> p k n", p=P)).then_inc(loaded, 16)

        @block.tensor
        def _(pe):
            pe.wait_ge(loaded, 16)
            for ps, at, m in ((p1[:, :], KV_LORA, 32), (p2[:, :], KV_LORA + 32, 32),
                              (pc[:, 0, :], 0, P), (pc[:, 1, :], P, P)):
                for k in range(DT):
                    last = nc.tensor.matmul(ps, w[:, k, at:at + m], h[:, k, :], start=k == 0, stop=k == DT - 1)
                last.then_inc(r_done if m == 32 else c_done, 1)

        @block.scalar
        def _(act):
            for j in range(2):
                act.wait_ge(c_done, j + 1)
                nc.scalar.activation(ckv[:, j, :], pc[:, j, :], ACT.Copy)

        @block.vector
        def _(dve):
            st = Steps(steps)
            dve.wait_ge(r_done, 2)
            rotate(nc, dve, steps, st, p1[:, :], p2[:, :], cosr, sinr, 32, t1[:, :], t2[:, :], t3[:, :], t4[:, :])
            nc.vector.tensor_tensor(kr[0:32, :], t1[:, :], t2[:, :], ALU.subtract)
            nc.vector.tensor_tensor(kr[32:64, :], t3[:, :], t4[:, :], ALU.add)


def mla_queries(nc, e, I, cq, cosr, sinr, qn, qr):
    H, KT = B_HEADS, Q_LORA // P
    with ExitStack() as s:
        sb, pb, sem = opened(nc, s, "qb")
        w = sb("w", [P, KT, H, NOPE + ROPE])
        wr = sb("wr", [P, KT, 2, H, 32])
        t = sb("t", [P, 4, L])
        pn, pr = pb("pn", [P, 2, L]), pb("pr", [P, 2, 2, L])
        loaded, sorted_, n_done, n_out = sem("loaded"), sem("sorted"), sem("n_done"), sem("n_out")
        r_done, steps = sem("r_done"), sem("steps")
        block = s.enter_context(nc.Block())

        @block.sync
        def _(sp):
            sp.dma_start(w[:, :, :, :], I["b_w_q_b_2"][0].rearrange("(k p) (h n) -> p k h n", p=P, h=H))\
                .then_inc(loaded, 16)

        @block.gpsimd
        def _(pool):
            pool.wait_ge(loaded, 16)
            for k in range(KT):
                for half in range(2):
                    at = NOPE + 32 * half
                    nc.gpsimd.tensor_copy(wr[:, k, half, :, :], w[:, k, :, at:at + 32]).then_inc(sorted_, 1)

        @block.tensor
        def _(pe):
            pe.wait_ge(loaded, 16)
            pe.wait_ge(sorted_, 2 * KT)
            for g in range(2):
                for half in range(2):
                    for k in range(KT):
                        last = nc.tensor.matmul(pr[:, g, half, :],
                                                wr[:, k, half, 4 * g:4 * g + 4, :].rearrange("p h n -> p (h n)"),
                                                cq[:, k, :], start=k == 0, stop=k == KT - 1)
                last.then_inc(r_done, 1)
            for h in range(H):
                if h >= 2:
                    pe.wait_ge(n_out, h - 1)
                for k in range(KT):
                    last = nc.tensor.matmul(pn[:, h % 2, :], w[:, k, h, 0:NOPE], cq[:, k, :],
                                            start=k == 0, stop=k == KT - 1)
                last.then_inc(n_done, 1)

        @block.scalar
        def _(act):
            for h in range(H):
                act.wait_ge(n_done, h + 1)
                nc.scalar.activation(qn[:, h, :], pn[:, h % 2, :], ACT.Copy).then_inc(n_out, 1)

        @block.vector
        def _(dve):
            st = Steps(steps)
            for g in range(2):
                dve.wait_ge(r_done, g + 1)
                rotate(nc, dve, steps, st, pr[:, g, 0, :], pr[:, g, 1, :], cosr, sinr, P,
                       t[:, 0, :], t[:, 1, :], t[:, 2, :], t[:, 3, :])
                for i in range(4):
                    hp = slice(32 * i, 32 * i + 32)
                    st.mark(nc.vector.tensor_tensor(qr[0:32, 4 * g + i, :], t[hp, 0, :], t[hp, 1, :], ALU.subtract))
                    st.mark(nc.vector.tensor_tensor(qr[32:64, 4 * g + i, :], t[hp, 2, :], t[hp, 3, :], ALU.add))
                dve.wait_ge(steps, st.n)


def mla_attention(nc, e, I, qn, qr, kn, kr, v, out):
    H = B_HEADS
    scale = (NOPE + ROPE) ** -0.5
    with ExitStack() as s:
        sb, pb, sem = opened(nc, s, "at")
        mask = sb("mask", [P, P])
        mx, nm, total, inv = (sb(n, [P, 2]) for n in ("mx", "nm", "total", "inv"))
        p, pT = sb("p", [P, 2, L]), sb("pT", [P, 2, L])
        pS, pt, po = pb("pS", [P, 2, L]), pb("pt", [P, 2, L]), pb("po", [P, 2, L])
        loaded, s_done, nm_ready, p_ready = sem("loaded"), sem("s_done"), sem("nm"), sem("p_ready")
        p_normed, turned, pT_ready, used = sem("p_normed"), sem("turned"), sem("pT_ready"), sem("used")
        out_done, steps = sem("out_done"), sem("steps")
        block = s.enter_context(nc.Block())
        units = [(h, i) for h in range(H) for i in range(TT)]
        N = len(units)

        @block.sync
        def _(sp):
            sp.dma_start(mask[:, :], I["c_causal_row"]).then_inc(loaded, 16)

        @block.tensor
        def _(pe):
            def scores(n):
                h, i = units[n]
                w = (i + 1) * P
                if n >= 2:
                    pe.wait_ge(p_ready, n - 1)
                ts = slice(i * P, (i + 1) * P)
                nc.tensor.matmul(pS[:, n % 2, 0:w], qn[:, h, ts], kn[:, h, 0:w], start=True, stop=False)
                nc.tensor.matmul(pS[:, n % 2, 0:w], qr[0:ROPE, h, ts], kr[0:ROPE, 0:w], start=False, stop=True)\
                    .then_inc(s_done, 1)

            def turn(n):
                h, i = units[n]
                pe.wait_ge(p_normed, n + 1)
                if n >= 2:
                    pe.wait_ge(pT_ready, n - 1)
                for j in range(i + 1):
                    js = slice(j * P, (j + 1) * P)
                    last = nc.tensor.transpose(pt[:, n % 2, js], p[:, n % 2, js], e.ident[:, :])
                last.then_inc(turned, 1)

            def values(n):
                h, i = units[n]
                pe.wait_ge(pT_ready, n + 1)
                if i == 0 and h >= 2:
                    pe.wait_ge(out_done, h - 1)
                for j in range(i + 1):
                    last = nc.tensor.matmul(po[:, h % 2, i * P:(i + 1) * P], v[:, j, h * P:(h + 1) * P],
                                            pT[:, n % 2, j * P:(j + 1) * P], start=j == 0, stop=j == i)
                last.then_inc(used, 1)

            for n in range(N + 2):
                if n < N:
                    scores(n)
                if 1 <= n <= N:
                    turn(n - 1)
                if n >= 2:
                    values(n - 2)

        @block.vector
        def _(dve):
            st = Steps(steps)

            def then(ins):
                dve.wait_ge(steps, st.mark(ins))

            def maximum(n):
                h, i = units[n]
                b = n % 2
                dve.wait_ge(s_done, n + 1)
                diag = pS[:, b, i * P:(i + 1) * P]
                then(nc.vector.tensor_tensor(diag, diag, mask[:, :], ALU.add))
                then(nc.vector.reduce_max(mx[:, b:b + 1], pS[:, b, 0:(i + 1) * P], AX.X))
                if n >= 2:
                    dve.wait_ge(p_ready, n - 1)
                nc.vector.tensor_scalar(nm[:, b:b + 1], mx[:, b:b + 1], -scale, None, ALU.mult).then_inc(nm_ready, 1)

            def normalise(n):
                h, i = units[n]
                b = n % 2
                dve.wait_ge(p_ready, n + 1)
                then(nc.vector.reciprocal(inv[:, b:b + 1], total[:, b:b + 1]))
                nc.vector.tensor_scalar(p[:, b, 0:(i + 1) * P], p[:, b, 0:(i + 1) * P], inv[:, b:b + 1], None,
                                        ALU.mult).then_inc(p_normed, 1)

            dve.wait_ge(loaded, 16)
            maximum(0)
            for n in range(N):
                if n + 1 < N:
                    maximum(n + 1)
                normalise(n)

        @block.scalar
        def _(act):
            def copies(n):
                h, i = units[n]
                act.wait_ge(turned, n + 1)
                if n >= 2:
                    act.wait_ge(used, n - 1)
                nc.scalar.activation(pT[:, n % 2, 0:(i + 1) * P], pt[:, n % 2, 0:(i + 1) * P], ACT.Copy)\
                    .then_inc(pT_ready, 1)

            def take_out(n):
                h, i = units[n]
                if i == TT - 1:
                    act.wait_ge(used, n + 1)
                    nc.scalar.activation(out[:, h, :], po[:, h % 2, :], ACT.Copy).then_inc(out_done, 1)

            for n in range(N):
                h, i = units[n]
                b = n % 2
                act.wait_ge(nm_ready, n + 1)
                if n >= 2:
                    act.wait_ge(turned, n - 1)
                nc.scalar.activation(p[:, b, 0:(i + 1) * P], pS[:, b, 0:(i + 1) * P], ACT.Exp, bias=nm[:, b:b + 1],
                                     scale=scale, accum_out=total[:, b:b + 1]).then_inc(p_ready, 1)
                if n >= 1:
                    copies(n - 1)
                if n >= 3:
                    take_out(n - 3)
            copies(N - 1)
            for n in range(N - 3, N):
                take_out(n)


def mla_mixer(nc, e, I, kvada, h, y):
    H = B_HEADS
    with ExitStack() as s:
        keep = lambda name, shape: s.enter_context(nc.sbuf_tensor(f"mla_{name}", shape, F32))
        out = keep("out", [P, H, L])
        kn, v, kr = keep("kn", [P, H, L]), keep("v", [P, TT, H * P]), keep("kr", [ROPE, L])
        qn, qr = keep("qn", [P, H, L]), keep("qr", [ROPE, H, L])
        cosr, sinr = keep("cos", [P, L]), keep("sin", [P, L])
        rope_tables(nc, e, I, cosr, sinr)
        with ExitStack() as s2:
            part = lambda name, shape: s2.enter_context(nc.sbuf_tensor(f"mla_{name}", shape, F32))
            hk, ckv = part("hk", [P, DT, L]), part("ckv", [P, 2, L])
            norm_stage(nc, e, "kv_norm", e.x, DT, hk, lambda k: col(e, "kv_norm_g_2", k),
                       shift=lambda k: kvada[:, k:k + 1], scale=lambda k: kvada[:, DT + k:DT + k + 1])
            mla_keys_a(nc, e, I, hk, ckv, cosr, sinr, kr)
            norm_stage(nc, e, "kv_latent", ckv, 2, ckv, lambda k: col(e, "kv_latent_g_2", k))
            wb = I["kv_w_b_2"]
            k_of = wb.rearrange("k (h two n) -> k h two n", h=H, two=2)
            with ExitStack() as s3:
                sb, pb, sem = opened(nc, s3, "kb")
                w = sb("w", [P, 2, H, P])
                ps = pb("ps", [P, 2, L])
                loaded, done, taken = sem("loaded"), sem("done"), sem("taken")
                block = s3.enter_context(nc.Block())

                @block.sync
                def _(sp):
                    for k in range(2):
                        sp.dma_start(w[:, k, :, :], k_of[k * P:(k + 1) * P, :, 0, :]).then_inc(loaded, 16)

                @block.tensor
                def _(pe):
                    pe.wait_ge(loaded, 32)
                    for hd in range(H):
                        if hd >= 2:
                            pe.wait_ge(taken, hd - 1)
                        for k in range(2):
                            last = nc.tensor.matmul(ps[:, hd % 2, :], w[:, k, hd, :], ckv[:, k, :],
                                                    start=k == 0, stop=k == 1)
                        last.then_inc(done, 1)

                @block.scalar
                def _(act):
                    for hd in range(H):
                        act.wait_ge(done, hd + 1)
                        nc.scalar.activation(kn[:, hd, :], ps[:, hd % 2, :], ACT.Copy).then_inc(taken, 1)
            project_tokens(nc, e, "kv_v", wb, 2, ckv, 2, v, lambda c: [2 * P * (4 * c + i) + P for i in range(4)])
        with nc.sbuf_tensor("mla_cq", [P, Q_LORA // P, L], F32) as cq:
            project(nc, e, "q_a", I["b_w_q_a_2"][0], DT, h, 1, 3, 1, copy_to(nc, cq))
            norm_stage(nc, e, "q_latent", cq, Q_LORA // P, cq, lambda k: col(e, "b_q_latent_g_2", k))
            mla_queries(nc, e, I, cq, cosr, sinr, qn, qr)
        mla_attention(nc, e, I, qn, qr, kn, kr, v, out)
        project(nc, e, "mla_out", I["b_w_out_2"][0], H, out, 2, 2, 2, copy_to(nc, y))


def second_block(nc, e, I):
    with ExitStack() as s:
        keep = lambda name, shape: s.enter_context(nc.sbuf_tensor(f"sb_{name}", shape, F32))
        cond, kvada = keep("cond", [P, DT]), keep("kvada", [P, 2 * DT])
        ada = keep("ada", [P, 2, 6 * DT])
        silu_condition(nc, e, cond)
        for l in range(2):
            condition(nc, e, f"ada{l}", I["ada_w_2"][l], 6 * DT, COL["ada_b_2"] + l * 6 * DT, cond, ada[:, l, :])
        condition(nc, e, "kvada", I["kv_ada_w_2"], 2 * DT, COL["kv_ada_b_2"], cond, kvada)
        for l in range(2):
            part = lambda i: (lambda k: ada[:, l, i * DT + k:i * DT + k + 1])
            gain = lambda i: (lambda k: col(e, "norm_g_2", (4 * l + i) * DT + k))
            with ExitStack() as s2:
                h = s2.enter_context(nc.sbuf_tensor(f"l{l}_h", [P, DT, L], F32))
                y = s2.enter_context(nc.sbuf_tensor(f"l{l}_y", [P, DT, L], F32))
                norm_stage(nc, e, f"l{l}_in", e.x, DT, h, gain(0), shift=part(0), scale=part(1))
                if l == 0:
                    mlstm_mixer(nc, e, I, h, y)
                else:
                    mla_mixer(nc, e, I, kvada, h, y)
                norm_stage(nc, e, f"l{l}_mixed", y, DT, y, gain(1), gate=part(2), onto=e.x)
                norm_stage(nc, e, f"l{l}_mid", e.x, DT, h, gain(2), shift=part(3), scale=part(4))
                with nc.sbuf_tensor(f"l{l}_ff", [P, D_FF2 // P, L], F32) as ff:
                    sqrelu_up(nc, e, f"l{l}_up", I["mlp_w1_2"][l], h, ff)
                    project(nc, e, f"l{l}_down", I["mlp_w2_2"][l], D_FF2 // P, ff, 4, 2, 1, copy_to(nc, y))
                norm_stage(nc, e, f"l{l}_out", y, DT, y, gain(3), gate=part(5), onto=e.x)


def store_output(nc, e, out):
    with ExitStack() as s:
        sb, pb, sem = opened(nc, s, "store")
        rows = sb("rows", [P, TT, D])
        ps = pb("ps", [P, 4, L])
        turned, taken, stored = sem("turned"), sem("taken"), sem("stored")
        block = s.enter_context(nc.Block())

        @block.tensor
        def _(pe):
            for n in range(2 * TT):
                t, half = n // 2, n % 2
                if n >= 4:
                    pe.wait_ge(taken, n - 3)
                for i in range(4):
                    last = nc.tensor.transpose(ps[:, n % 4, i * P:(i + 1) * P],
                                               e.x[:, 4 * half + i, t * P:(t + 1) * P], e.ident[:, :])
                last.then_inc(turned, 1)

        @block.scalar
        def _(act):
            for n in range(2 * TT):
                t, half = n // 2, n % 2
                act.wait_ge(turned, n + 1)
                nc.scalar.activation(rows[:, t, half * 512:(half + 1) * 512], ps[:, n % 4, :], ACT.Copy)\
                    .then_inc(taken, 1)

        @block.sync
        def _(sp):
            for t in range(TT):
                sp.wait_ge(taken, 2 * t + 2)
                sp.dma_start(out[0, t * P:(t + 1) * P, :], rows[:, t, :]).then_inc(stored, 16)
            sp.wait_ge(stored, 16 * TT)



def program(nc, I, out):
    with ExitStack() as s:
        e = Kept()
        Semaphores.start(nc)
        keep = lambda name, shape: s.enter_context(nc.sbuf_tensor(name, shape, F32))
        e.x = keep("resid", [P, DT, L])
        e.ident, e.ones, e.heads = keep("ident", [P, P]), keep("ones", [P, P]), keep("heads", [P, P])
        e.cols = keep("cols", [P, ROW_TILES * P])
        load_constants(nc, e, I)
        ffn_swiglu(nc, e, "ffn1", "ffn1_norm", I["ffn1_w_gu"], I["ffn1_w_down"])
        with ExitStack() as s2:
            part = lambda name, shape: s2.enter_context(nc.sbuf_tensor(name, shape, F32))
            merged = part("merged", [P, DT, L])
            with nc.sbuf_tensor("h_mix", [P, DT, L], F32) as h:
                norm_stage(nc, e, "mix", e.x, DT, h, lambda k: col(e, "mix_norm", k))
                hyena_branch(nc, e, I, h, merged)
            rwkv_branch(nc, e, I, merged)
            project(nc, e, "mix_out", I["w_out"], DT, merged, 2, 2, 2, add_to_x(nc, e, 1.0), on="vector")
        ffn_swiglu(nc, e, "ffn2", "ffn2_norm", I["ffn2_w_gu"], I["ffn2_w_down"])
        norm_stage(nc, e, "final", e.x, DT, e.x, lambda k: col(e, "final_norm", k))
        second_block(nc, e, I)
        store_output(nc, e, out)




_OUT = (1, L, D)


def kernel(**inputs):
    import concourse.bacc as bacc
    from concourse.bass_utils import run_bass_kernel_spmd

    nc = bacc.Bacc("TRN2", target_bir_lowering=False, num_devices=1)
    arrays, aps = {}, {}
    for name, a in list(inputs.items()) + list(shape_tables().items()):
        a = np.ascontiguousarray(a)
        arrays[f"in_{name}"] = a
        aps[name] = nc.dram_tensor(f"in_{name}", a.shape, mybir.dt.from_np(a.dtype), kind="ExternalInput").ap()
    out = nc.dram_tensor("out_0", _OUT, F32, kind="ExternalOutput").ap()
    program(nc, aps, out)
    return run_bass_kernel_spmd(nc, [arrays], core_ids=[0]).results[0]["out_0"]
```

```python
import math
from contextlib import ExitStack

import numpy as np
import concourse.bass as bass
from concourse import mybir


F32 = mybir.dt.float32
F32R = mybir.dt.float32r
ACT = mybir.ActivationFunctionType
ALU = mybir.AluOpType
AX = mybir.AxisListType
P = 128

D = 1024
L = 512
DT = D // P
TT = L // P
D_FF = 2816
D_HY = 512
HT = D_HY // P
N_HY = 3 * D_HY
D_RW = 512
RT = D_RW // P
N_RW = 3 * D_RW + 2 * 64 + 2 * 64 + 160
EMB = 33
FILT = 64
EPS = 1e-6
GN_EPS = 64e-5
CH = 64
NCH = L // CH
LEVELS = 6
LH = L // 2
HCH = LH // CH
LOG_DECAY_MAX = -math.exp(-0.5)

A_HEADS = 8
A_QK = 64
A_IN = 3088
B_HEADS = 8
Q_LORA = 384
KV_LORA = 256
NOPE = 128
ROPE = 64
D_FF2 = 4096

TWO_PI = 2 * math.pi
ROUND = 1.5 * 2.0**23
PI_A = 6.28125
PI_B = float(np.float32(np.float32((TWO_PI - PI_A) * 2**20).astype(np.int64) / 2**20))
PI_C = TWO_PI - PI_A - PI_B

VECTORS = [
    ("ffn1_norm", 8, 128), ("mix_norm", 8, 128), ("hy_conv_w", 36, 128), ("hy_conv_b", 12, 128),
    ("hy_ffn_b1", 1, 64), ("hy_ffn_b2", 1, 64), ("hy_sin_freq", 1, 64), ("hy_bias_d", 8, 128),
    ("rw_w0", 8, 128), ("rw_a0", 8, 128), ("rw_k_k", 4, 128), ("rw_k_a", 4, 128),
    ("rw_r_k", 4, 128), ("rw_ln_w", 4, 128), ("rw_ln_b", 4, 128), ("ffn2_norm", 8, 128),
    ("final_norm", 8, 128), ("ada_b_2", 96, 128), ("norm_g_2", 64, 128),
    ("a_head_g_2", 8, 128), ("kv_ada_b_2", 16, 128), ("kv_norm_g_2", 8, 128),
    ("kv_latent_g_2", 2, 128), ("b_q_latent_g_2", 3, 128), ("c_2", 8, 128),
    ("a_gate_b_2", 2, 8),
]
MU_ROWS = N_RW // P
COL = {}
_at = 0
for _name, _rows, _ in VECTORS:
    COL[_name] = _at
    _at += _rows
COL["rw_mu"] = _at
_at += 2 * (MU_ROWS + 1)
ROW_TILES = -(-_at // P)


class Kept:
    pass


class Steps:

    def __init__(self, sem):
        self.sem, self.n = sem, 0

    def mark(self, ins):
        ins.then_inc(self.sem, 1)
        self.n += 1
        return self.n


MOST_SEMAPHORES = 30


class Semaphores:

    used = 0
    numbers = set()

    @classmethod
    def room(cls, nc, n=MOST_SEMAPHORES):
        if cls.used + n > cls.limit:
            first, last = min(cls.numbers), max(cls.numbers)
            with nc.Block() as block:
                @block.gpsimd
                def _(pool):
                    pool.sem_clear(range(first, last + 1))
            cls.used = 0

    @classmethod
    def start(cls, nc):
        cls.used, cls.numbers, cls.limit = 0, set(), nc.free_len()

    @classmethod
    def take(cls, nc, stack, name):
        sem = stack.enter_context(nc.semaphore(name))
        cls.used += 1
        cls.numbers.add(sem.num)
        return sem


def opened(nc, stack, tag):
    Semaphores.room(nc)
    sb = lambda name, shape: stack.enter_context(nc.sbuf_tensor(f"{tag}_{name}", shape, F32))
    pb = lambda name, shape: stack.enter_context(nc.psum_tensor(f"{tag}_{name}", shape, F32))
    sem = lambda name: Semaphores.take(nc, stack, f"{tag}_{name}")
    return sb, pb, sem


def col(e, name, i=0, parts=P, base=0):
    c = COL[name] + i
    return e.cols[base:base + parts, c:c + 1]



def load_constants(nc, e, I):
    with ExitStack() as s:
        sb, pb, sem = opened(nc, s, "init")
        rows = sb("rows", [P, ROW_TILES, P])
        xin = sb("xin", [P, TT, D])
        ps = pb("ps", [P, 8, L])
        rows_zero, rows_in, x_in, tables_in = sem("rows_zero"), sem("rows_in"), sem("x_in"), sem("tables_in")
        vec_t, vec_c, x_t, x_c = sem("vec_t"), sem("vec_c"), sem("x_t"), sem("x_c")
        block = s.enter_context(nc.Block())
        pieces = []
        for name, n, width in VECTORS:
            flat = I[name]
            shape = "abcdef"[:len(flat.shape)]
            flat = flat.rearrange(f"{' '.join(shape)} -> ({' '.join(shape)})") if len(flat.shape) > 1 else flat
            view = flat.rearrange("(n w) -> n w", w=width)
            at = 0
            while at < n:
                row = COL[name] + at
                k = min(n - at, P - row % P)
                pieces.append((row, k, width, view[at:at + k, :]))
                at += k
        for m in range(2):
            row = COL["rw_mu"] + m * (MU_ROWS + 1)
            pieces.append((row, MU_ROWS, P, I["rw_mu"][m, 0:MU_ROWS * P].rearrange("(n w) -> n w", w=P)))
            pieces.append((row + MU_ROWS, 1, N_RW - MU_ROWS * P, I["rw_mu"][m:m + 1, MU_ROWS * P:N_RW]))
        split = []
        for row, k, width, src in pieces:
            first = min(k, P - row % P)
            split.append((row, first, width, src[0:first, :]))
            if first < k:
                split.append((row + first, k - first, width, src[first:k, :]))

        @block.sync
        def _(sp):
            xv = I["x"][0].rearrange("(t p) d -> p t d", p=P)
            sp.dma_start(e.ident[:, :], I["c_ident"]).then_inc(tables_in, 16)
            sp.dma_start(e.heads[:, :], I["c_heads"]).then_inc(tables_in, 16)
            for t in range(TT):
                sp.dma_start(xin[:, t, :], xv[:, t, :]).then_inc(x_in, 16)
            sp.wait_ge(rows_zero, 1)
            for row, k, width, src in split:
                sp.dma_start(rows[row % P:row % P + k, row // P, 0:width], src).then_inc(rows_in, 16)

        @block.vector
        def _(dve):
            nc.vector.memset(rows[:, :, :], 0.0).then_inc(rows_zero, 1)
            nc.vector.memset(e.ones[:, :], 1.0)
            for k in range(DT):
                dve.wait_ge(x_t, k + 1)
                nc.vector.tensor_copy(e.x[:, k, :], ps[:, k % 4, :]).then_inc(x_c, 1)
            dve.wait_ge(vec_t, 1)
            nc.vector.tensor_copy(e.cols[:, :], ps[:, 4, 0:ROW_TILES * P]).then_inc(vec_c, 1)

        @block.tensor
        def _(pe):
            pe.wait_ge(tables_in, 32)
            pe.wait_ge(x_in, 16 * TT)
            for k in range(DT):
                if k >= 4:
                    pe.wait_ge(x_c, k - 3)
                for t in range(TT):
                    last = nc.tensor.transpose(ps[:, k % 4, t * P:(t + 1) * P],
                                               xin[:, t, k * P:(k + 1) * P], e.ident[:, :])
                last.then_inc(x_t, 1)
            pe.wait_ge(rows_in, 16 * len(split))
            for r in range(ROW_TILES):
                last = nc.tensor.transpose(ps[:, 4, r * P:(r + 1) * P], rows[:, r, :], e.ident[:, :])
            last.then_inc(vec_t, 1)



def norm_stage(nc, e, tag, src, n, dst, gain, eps=EPS, shift=None, scale=None,
               gate=None, onto=None):
    with ExitStack() as s:
        sb, pb, sem = opened(nc, s, tag)
        sq = sb("sq", [P, 2, L])
        rs = sb("rs", [P, 2, L])
        g1 = sb("g1", [P, n])
        ps = pb("ps", [P, L])
        sq_ready, sq_used, sum_done = sem("sq_ready"), sem("sq_used"), sem("sum_done")
        inv_ready, rs_ready, steps, out_done = sem("inv_ready"), sem("rs_ready"), sem("steps"), sem("out")
        block = s.enter_context(nc.Block())

        @block.scalar
        def _(act):
            for k in range(n):
                if k >= 2:
                    act.wait_ge(sq_used, k - 1)
                nc.scalar.activation(sq[:, k % 2, :], src[:, k, :], ACT.Square).then_inc(sq_ready, 1)
            act.wait_ge(inv_ready, 1)
            nc.scalar.activation(rs[:, 1, :], rs[:, 0, :], ACT.Sqrt).then_inc(rs_ready, 1)
            if shift is not None:
                for k in range(n):
                    act.wait_ge(out_done, k + 1)
                    nc.scalar.activation(dst[:, k, :], dst[:, k, :], ACT.Identity, bias=shift(k))

        @block.tensor
        def _(pe):
            for k in range(n):
                pe.wait_ge(sq_ready, k + 1)
                last = nc.tensor.matmul(ps[:, :], e.ones[:, :], sq[:, k % 2, :], start=k == 0, stop=k == n - 1)
                last.then_inc(sq_used, 1)

        @block.vector
        def _(dve):
            st = Steps(steps)
            if scale is not None:
                for k in range(n):
                    st.mark(nc.vector.scalar_tensor_tensor(g1[:, k:k + 1], scale(k), 1.0, gain(k),
                                                           ALU.add, ALU.mult))
            if gate is not None:
                for k in range(n):
                    st.mark(nc.vector.tensor_tensor(g1[:, k:k + 1], gate(k), gain(k), ALU.mult))
            dve.wait_ge(sq_used, n)
            dve.wait_ge(steps, st.mark(nc.vector.tensor_scalar(rs[:, 0, :], ps[:, :], 1.0 / (n * P), eps,
                                                               ALU.mult, ALU.add)))
            nc.vector.reciprocal(rs[:, 0, :], rs[:, 0, :]).then_inc(inv_ready, 1)
            dve.wait_ge(rs_ready, 1)
            for k in range(n):
                g = gain(k) if scale is None and gate is None else g1[:, k:k + 1]
                nc.vector.scalar_tensor_tensor(dst[:, k, :], src[:, k, :], g, rs[:, 1, :],
                                               ALU.mult, ALU.mult).then_inc(out_done, 1)

        @block.gpsimd
        def _(pool):
            if onto is not None:
                for k in range(n):
                    pool.wait_ge(out_done, k + 1)
                    nc.gpsimd.tensor_tensor(onto[:, k, :], onto[:, k, :], dst[:, k, :], ALU.add)



def norm_programs(nc, e, sb, pb, sem, src, n, hi, lo, gain, shift=None, scale=None, scratch=None):
    N = SimpleParts()
    sq = scratch if scratch is not None else sb("n_sq", [P, 4, L])
    pair = sb("n_pair", [P, 2, L])
    t, rs = sq[:, 0:3, :], sq[:, 3, :]
    u, turn = (pair, 2) if shift is not None else (t, 3)
    g1 = sb("n_g1", [P, n])
    ps = pb("n_ps", [P, L])
    sq_ready, pair_ready, summed = sem("n_sq"), sem("n_pair"), sem("n_summed")
    inv_ready, rs_ready, steps = sem("n_inv"), sem("n_rs"), sem("n_steps")
    t_ready, hi_ready, lo_done = sem("n_t"), sem("n_hi"), sem("n_lo")
    N.ready, N.count = lo_done, n

    def act_sums(eng):
        for k in range(n):
            if k >= 4:
                eng.wait_ge(pair_ready, k // 2 - 1)
            nc.scalar.activation(sq[:, k % 4, :], src[:, k, :], ACT.Square).then_inc(sq_ready, 1)

    def act_parts(eng):
        eng.wait_ge(inv_ready, 1)
        nc.scalar.activation(rs, rs, ACT.Sqrt).then_inc(rs_ready, 1)
        for k in range(n):
            eng.wait_ge(t_ready, k + 1)
            if shift is None:
                nc.scalar.activation(hi[:, k, :], t[:, k % 3, :], ACT.Copy).then_inc(hi_ready, 1)
            else:
                nc.scalar.activation(hi[:, k, :], t[:, k % 3, :], ACT.Identity, bias=shift(k))
                if k >= 2:
                    eng.wait_ge(lo_done, k - 1)
                nc.scalar.activation(u[:, k % 2, :], t[:, k % 3, :], ACT.Identity, bias=shift(k))\
                    .then_inc(hi_ready, 1)

    def pe(eng):
        for k in range(n // 2 + n % 2):
            eng.wait_ge(pair_ready, k + 1)
            nc.tensor.matmul(ps[:, :], e.ones[:, :], pair[:, k % 2, :], start=k == 0, stop=k == n // 2 + n % 2 - 1)\
                .then_inc(summed, 1)

    def dve_sums(eng):
        st = Steps(steps)
        if scale is not None:
            for k in range(n):
                st.mark(nc.vector.scalar_tensor_tensor(g1[:, k:k + 1], scale(k), 1.0, gain(k), ALU.add, ALU.mult))
        for k in range(n // 2 + n % 2):
            eng.wait_ge(sq_ready, min(2 * k + 2, n))
            if k >= 2:
                eng.wait_ge(summed, k - 1)
            if 2 * k + 1 < n:
                ins = nc.vector.tensor_tensor(pair[:, k % 2, :], sq[:, 2 * (k % 2), :], sq[:, 2 * (k % 2) + 1, :], ALU.add)
            else:
                ins = nc.vector.tensor_copy(pair[:, k % 2, :], sq[:, 2 * (k % 2), :])
            ins.then_inc(pair_ready, 1)
        eng.wait_ge(summed, n // 2 + n % 2)
        eng.wait_ge(steps, st.mark(nc.vector.tensor_scalar(rs, ps[:, :], 1.0 / (n * P), EPS,
                                                           ALU.mult, ALU.add)))
        nc.vector.reciprocal(rs, rs).then_inc(inv_ready, 1)

    def dve_parts(eng):
        eng.wait_ge(rs_ready, 1)

        def lower(k):
            eng.wait_ge(hi_ready, k + 1)
            nc.vector.tensor_tensor(lo[:, k, :], u[:, k % turn, :], hi[:, k, :].bitcast(F32), ALU.subtract)\
                .then_inc(lo_done, 1)

        for k in range(n):
            g = gain(k) if scale is None else g1[:, k:k + 1]
            if k >= 3:
                eng.wait_ge(lo_done if u is t else hi_ready, k - 2)
            nc.vector.scalar_tensor_tensor(t[:, k % 3, :], src[:, k, :], g, rs, ALU.mult, ALU.mult)\
                .then_inc(t_ready, 1)
            if k >= 1:
                lower(k - 1)
        lower(n - 1)

    N.act, N.pe, N.dve = (act_sums, act_parts), pe, (dve_sums, dve_parts)
    return N


def cut_programs(nc, e, sb, pb, sem, src, n, hi, lo, scratch=None):
    N = SimpleParts()
    hi_ready, lo_done = sem("c_hi"), sem("c_lo")
    N.ready, N.count = lo_done, n

    def act(eng):
        for k in range(n):
            nc.scalar.activation(hi[:, k, :], src[:, k, :], ACT.Copy).then_inc(hi_ready, 1)

    def dve(eng):
        for k in range(n):
            eng.wait_ge(hi_ready, k + 1)
            nc.vector.tensor_tensor(lo[:, k, :], src[:, k, :], hi[:, k, :].bitcast(F32), ALU.subtract)\
                .then_inc(lo_done, 1)

    nothing = lambda eng: None
    N.act, N.pe, N.dve = (act, nothing), nothing, (dve, nothing)
    return N


class SimpleParts:
    pass



def staggered(eng, groups, slots, ahead, behind):
    if groups > 1:
        with eng.Fori(0, groups - 1) as g:
            for i in range(slots):
                ahead(g * slots + (i + 1), g + (i + 1) // slots, (i + 1) % slots)
                behind(g * slots + i, g, i)
    for i in range(slots):
        c = (groups - 1) * slots + i
        if i + 1 < slots:
            ahead(c + 1, groups - 1, i + 1)
        behind(c, groups - 1, i)


def tile_at(t, j):
    return t[:, bass.ds(j, 1), :].rearrange("p a n -> p (a n)")


def gemm(nc, e, tag, w, kt, x, groups, slots, per, kind, dst=None, func=ACT.Copy, factor=1.0, gate=None,
         width=P, before=None, side=None):
    with ExitStack() as s:
        sb, pb, sem = opened(nc, s, tag)
        sbr = lambda name, shape: s.enter_context(nc.sbuf_tensor(f"{tag}_{name}", shape, F32R))
        xh, xl = x
        wide = per * width
        nb = slots * per
        pair = kind == "swiglu"
        raw = sb("raw", [P, slots, kt, wide])
        wh, wl = sbr("wh", [P, slots, kt, wide]), sbr("wl", [P, slots, kt, wide])
        ps = pb("ps", [P, nb, L])
        loaded = [sem(f"loaded{i}") for i in range(slots)]
        hi_ready, lo_ready, mm_done, bank_free = sem("hi_ready"), sem("lo_ready"), sem("mm_done"), sem("bank_free")
        n_buf = slots if pair else nb
        scratch = None
        if kind in ("swiglu", "sqrelu"):
            scratch = sb("factors", [P, 2 * n_buf, L])
            f1, f2 = scratch[:, 0:n_buf, :], scratch[:, n_buf:, :]
            f1_ready, f2_free = sem("f1_ready"), sem("f2_free")
        first = before(sb, pb, sem, scratch) if before else None
        if side:
            assert slots == 2
            side_w, side_cols, cond, side_out = side
            sraw, acc = sb("sraw", [P, DT // 2, side_cols]), sb("acc", [P, side_cols])
            n_side = side_cols // P
            sps = pb("sps", [P, (groups + 1) * n_side])
            side_step, side_sum = sem("side_step"), sem("side_sum")
            side_in, loads_before = e.side_in, e.side_loads
            e.side_loads += groups * slots
        block = s.enter_context(nc.Block())
        if pair:
            wv = w.rearrange("(k p) (two n) -> p k two n", p=P, two=2)
        else:
            wv = w.rearrange("(k p) n -> p k n", p=P)

        @block.sync
        def _(sp):
            def load(c, i):
                if pair:
                    for t in range(2):
                        sp.dma_start(raw[:, i, :, t * P:(t + 1) * P], wv[:, :, t, bass.ds(c * P, P)])\
                            .then_inc(loaded[i], 16)
                else:
                    sp.dma_start(raw[:, i, :, :], wv[:, :, bass.ds(c * wide, wide)]).then_inc(loaded[i], 16)

            for i in range(slots):
                load(i, i)
            if groups > 1:
                with sp.Fori(1, groups) as g:
                    for i in range(slots):
                        sp.wait_ge(lo_ready, (g - 1) * slots + (i + 1))
                        load(g * slots + i, i)

        @block.tensor
        def _(pe):
            def side_sums(at, steps_done):
                pe.wait_ge(side_step, steps_done)
                for j in range(n_side):
                    last = nc.tensor.matmul(sps[:, bass.ds(at + j, 1)], acc[:, j * P:(j + 1) * P],
                                            e.ones[:, 0:1], start=True, stop=True)
                last.then_inc(side_sum, 1)

            pe.sem_inc(mm_done, nb)
            if first:
                first.pe(pe)
            with pe.Fori(0, groups) as g:
                for i in range(slots):
                    c = g * slots + i
                    pe.wait_ge(hi_ready, c + 1)
                    ws = [slice(t * width, (t + 1) * width) for t in range(per)]
                    banks = [ps[0:width, i * per + t, :] for t in range(per)]

                    def free(t):
                        if pair:
                            pe.wait_ge((f1_ready, bank_free)[t], c + 1)
                        else:
                            pe.wait_ge(bank_free, g * nb + (i * per + t + 1))

                    def upper_passes(k, t):
                        nc.tensor.matmul(banks[t], wh[:, i, k, ws[t]], xh[:, k, :], start=k == 0, stop=False)
                        nc.tensor.matmul(banks[t], wh[:, i, k, ws[t]], xl[:, k, :], start=False, stop=False)

                    def lower_pass(t):
                        for k in range(kt):
                            last = nc.tensor.matmul(banks[t], wl[:, i, k, ws[t]], xh[:, k, :],
                                                    start=False, stop=k == kt - 1)
                        last.then_inc(mm_done, 1)

                    if first and i == 0:
                        for t in range(per):
                            free(t)
                        for k in range(kt):
                            pe.wait_ge(first.ready, k + 1)
                            for t in range(per):
                                upper_passes(k, t)
                        pe.wait_ge(lo_ready, c + 1)
                        for t in range(per):
                            lower_pass(t)
                    else:
                        for t in range(per):
                            free(t)
                            for k in range(kt):
                                upper_passes(k, t)
                            if t == 0:
                                pe.wait_ge(lo_ready, c + 1)
                            lower_pass(t)
                    if side and i == 0:
                        side_sums(g * n_side, g * DT + 1)
            if side:
                side_sums(groups * n_side, groups * DT + 1)

        @block.scalar
        def _(act):
            if pair:
                act.sem_inc(f1_ready, slots)
            if kind == "copy":
                act.sem_inc(bank_free, nb)
            def upper(c, g, i):
                act.wait_ge(loaded[i], g * 16 * (2 if pair else 1) + 16 * (2 if pair else 1))
                act.wait_ge(mm_done, c * per + per)
                nc.scalar.activation(wh[:, i, :, :], raw[:, i, :, :], ACT.Copy).then_inc(hi_ready, 1)

            def take_out(c, g, i):
                if kind == "copy":
                    for t in range(per):
                        act.wait_ge(mm_done, c * per + (nb + t + 1))
                        nc.scalar.activation(tile_at(dst, c * per + t)[0:width, :], ps[0:width, i * per + t, :], func)\
                            .then_inc(bank_free, 1)
                elif pair:
                    act.wait_ge(mm_done, c * 2 + (nb + 1))
                    act.wait_ge(bank_free, c + 1)
                    nc.scalar.activation(f1[:, i, :], ps[:, 2 * i, :], ACT.Silu).then_inc(f1_ready, 1)
                elif kind == "sqrelu":
                    for t in range(per):
                        act.wait_ge(mm_done, c * per + (nb + t + 1))
                        act.wait_ge(bank_free, c * per + (t + 1))
                        nc.scalar.activation(f1[:, i * per + t, :], ps[:, i * per + t, :], ACT.Relu)\
                            .then_inc(f1_ready, 1)

            if first:
                first.act[0](act)
            upper(0, 0, 0)
            if first:
                first.act[1](act)
            if kind in ("copy", "swiglu", "sqrelu"):
                staggered(act, groups, slots, upper, take_out)
            else:
                staggered(act, groups, slots, upper, lambda c, g, i: None)

        @block.vector
        def _(dve):
            if kind != "copy":
                dve.sem_inc(bank_free, slots if pair else nb)

            def lower(c, g, i):
                dve.wait_ge(hi_ready, c + 1)
                nc.vector.tensor_tensor(wl[:, i, :, :], raw[:, i, :, :], wh[:, i, :, :].bitcast(F32), ALU.subtract)\
                    .then_inc(lo_ready, 1)

            def both_parts(j, i, a, bank, op0, a_ready):
                dve.wait_ge(f1_ready, a_ready)
                dve.wait_ge(f2_free, j + 1)
                nc.vector.scalar_tensor_tensor(tile_at(dst[0], j), bank, op0, a, ALU.max if op0 == 0.0 else ALU.mult,
                                               ALU.mult)
                nc.vector.scalar_tensor_tensor(f2[:, i, :], bank, op0, a, ALU.max if op0 == 0.0 else ALU.mult,
                                               ALU.mult).then_inc(bank_free, 1)

            def take_out(c, g, i):
                if pair:
                    dve.wait_ge(mm_done, c * 2 + (nb + 2))
                    both_parts(c, i, f1[:, i, :], ps[:, 2 * i + 1, :], 1.0, c + (slots + 1))
                elif kind == "sqrelu":
                    for t in range(per):
                        b = i * per + t
                        both_parts(c * per + t, b, f1[:, b, :], ps[:, b, :], 0.0, c * per + (t + 1))
                elif kind in ("add", "gate"):
                    for t in range(per):
                        bank = ps[0:width, i * per + t, :]
                        d = tile_at(dst, c * per + t)
                        dve.wait_ge(mm_done, c * per + (nb + t + 1))
                        if kind == "add":
                            nc.vector.scalar_tensor_tensor(d, bank, factor, d, ALU.mult, ALU.add).then_inc(bank_free, 1)
                        elif factor == 0:
                            nc.vector.tensor_tensor(d, tile_at(gate, c * per + t), bank, ALU.mult).then_inc(bank_free, 1)
                        else:
                            gt = tile_at(gate, c * per + t)
                            nc.vector.tensor_tensor(gt, gt, bank, ALU.mult).then_inc(bank_free, 1)
                            dve.wait_ge(bank_free, c * per + (nb + t + 1))
                            nc.vector.tensor_tensor(d, d, gt, ALU.add)
                if side:
                    dve.wait_ge(side_in, c * 16 + 16 * (loads_before + 1))
                    if i == 0:
                        dve.wait_ge(side_sum, g + 1)
                    for kk in range(DT // 2):
                        k = i * (DT // 2) + kk
                        factor_k = cond[:, k:k + 1]
                        if k == 0:
                            ins = nc.vector.tensor_scalar(acc[:, :], sraw[:, kk, :], factor_k, None, ALU.mult)
                        else:
                            dve.wait_ge(side_step, g * DT + (k + 1))
                            ins = nc.vector.scalar_tensor_tensor(acc[:, :], sraw[:, kk, :], factor_k, acc[:, :],
                                                                 ALU.mult, ALU.add)
                        ins.then_inc(side_step, 1)

            if side:
                nc.vector.memset(acc[:, :], 0.0).then_inc(side_step, 1)
            if first:
                first.dve[0](dve)
            lower(0, 0, 0)
            if first:
                first.dve[1](dve)
            staggered(dve, groups, slots, lower, take_out)
            if side:
                dve.wait_ge(side_sum, groups + 1)
                nc.vector.tensor_copy(side_out, sps[:, n_side:])

        if kind in ("swiglu", "sqrelu") or side:
            @block.gpsimd
            def _(pool):
                if kind in ("swiglu", "sqrelu"):
                    pool.sem_inc(f2_free, n_buf)
                with pool.Fori(0, groups) as g:
                    for i in range(slots):
                        if side:
                            pool.wait_ge(side_step, g * DT + (DT // 2 * i + 1))
                            pool.dma_start(sraw[:, :, :], side_w.rearrange("(two k p) n -> two p k n", two=2, p=P)
                                           [i, :, :, bass.ds(g * side_cols, side_cols)]).then_inc(side_in, 16)
                        if kind in ("swiglu", "sqrelu"):
                            for b in range(i * n_buf // slots, (i + 1) * n_buf // slots):
                                pool.wait_ge(bank_free, g * n_buf + (n_buf + b + 1))
                                d = tile_at(dst[1], g * n_buf + b)
                                nc.gpsimd.tensor_tensor(d, f2[:, b, :], tile_at(dst[0], g * n_buf + b).bitcast(F32),
                                                        ALU.subtract).then_inc(f2_free, 1)


def gemm_tokens(nc, e, tag, w, kt, x, n_chunks, dst, columns):
    with ExitStack() as s:
        sb, pb, sem = opened(nc, s, tag)
        raw = sb("raw", [P, 2, kt, 512])
        wh, wl = (s.enter_context(nc.sbuf_tensor(f"{tag}_{n}", [P, 2, kt, 512], F32R)) for n in ("wh", "wl"))
        ps = pb("ps", [P, 4, 512])
        loaded = [sem(f"loaded{i}") for i in range(2)]
        hi_ready, lo_ready, mm_done, taken = sem("hi_ready"), sem("lo_ready"), sem("mm_done"), sem("taken")
        block = s.enter_context(nc.Block())
        parts = [columns(c) for c in range(n_chunks)]
        assert n_chunks <= 2
        xh, xl = x

        @block.sync
        def _(sp):
            for c in range(n_chunks):
                step = 512 // len(parts[c])
                for i, at in enumerate(parts[c]):
                    sp.dma_start(raw[:, c, :, i * step:(i + 1) * step],
                                 w.rearrange("(k p) n -> p k n", p=P)[:, :, at:at + step]).then_inc(loaded[c], 16)

        @block.tensor
        def _(pe):
            for c in range(n_chunks):
                pe.wait_ge(lo_ready, c + 1)
                for t in range(TT):
                    n = c * TT + t
                    if n >= 4:
                        pe.wait_ge(taken, n - 3)
                    ts = slice(t * P, (t + 1) * P)
                    for k in range(kt):
                        nc.tensor.matmul(ps[:, n % 4, :], xh[:, k, ts], wh[:, c, k, :], start=k == 0, stop=False)
                        nc.tensor.matmul(ps[:, n % 4, :], xh[:, k, ts], wl[:, c, k, :], start=False, stop=False)
                        last = nc.tensor.matmul(ps[:, n % 4, :], xl[:, k, ts], wh[:, c, k, :], start=False,
                                                stop=k == kt - 1)
                    last.then_inc(mm_done, 1)

        @block.scalar
        def _(act):
            for c in range(n_chunks):
                act.wait_ge(loaded[c], 16 * len(parts[c]))
                nc.scalar.activation(wh[:, c, :, :], raw[:, c, :, :], ACT.Copy).then_inc(hi_ready, 1)
            for n in range(n_chunks * TT):
                act.wait_ge(mm_done, n + 1)
                nc.scalar.activation(dst[:, n % TT, n // TT * 512:(n // TT + 1) * 512], ps[:, n % 4, :], ACT.Copy)\
                    .then_inc(taken, 1)

        @block.vector
        def _(dve):
            for c in range(n_chunks):
                dve.wait_ge(hi_ready, c + 1)
                nc.vector.tensor_tensor(wl[:, c, :, :], raw[:, c, :, :], wh[:, c, :, :].bitcast(F32), ALU.subtract)\
                    .then_inc(lo_ready, 1)


def two_parts(nc, stack, name, n):
    return [stack.enter_context(nc.sbuf_tensor(f"{name}_{p}", [P, n, L], F32R)) for p in ("hi", "lo")]


def normed(nc, e, src, n, x, gain, shift=None, scale=None):
    return lambda *a: norm_programs(nc, e, *a[:3], src, n, x[0], x[1], gain, shift, scale, *a[3:])


def cut(nc, e, src, n, x):
    return lambda *a: cut_programs(nc, e, *a[:3], src, n, x[0], x[1])


def ffn_swiglu(nc, e, tag, norm, w_gu, w_down, side_up, side_down):
    with ExitStack() as s:
        ff = two_parts(nc, s, f"{tag}_ff", D_FF // P)
        with ExitStack() as s2:
            h = two_parts(nc, s2, f"{tag}_h", DT)
            gemm(nc, e, f"{tag}_up", w_gu, DT, h, D_FF // P // 2, 2, 2, "swiglu", dst=ff, side=side_up,
                 before=normed(nc, e, e.x, DT, h, lambda k: col(e, norm, k)))
        gemm(nc, e, f"{tag}_down", w_down, D_FF // P, ff, 4, 2, 1, "add", dst=e.x, factor=0.5, side=side_down)


def load_tables(nc, tag, pairs):
    with ExitStack() as s:
        sb, pb, sem = opened(nc, s, tag)
        loaded = sem("loaded")
        block = s.enter_context(nc.Block())

        @block.sync
        def _(sp):
            for dst, src in pairs:
                sp.dma_start(dst, src).then_inc(loaded, 16)
            sp.wait_ge(loaded, 16 * len(pairs))



def shape_tables():
    f32 = np.float32
    t = {"c_ident": np.eye(P, dtype=f32)}
    half = np.arange(P) // CH
    t["c_heads"] = (half[:, None] == half[None, :]).astype(f32)
    ang = 2 * np.pi * ((2 * np.arange(L)[None, :] + 1) * np.arange(L)[:, None] % (4 * L)) / (4 * L)
    t["c_cos"], t["c_sin"] = np.cos(ang).astype(f32), np.sin(ang).astype(f32)
    t["c_cosT"], t["c_sinT"] = np.ascontiguousarray(t["c_cos"].T), np.ascontiguousarray(t["c_sin"].T)
    pos = np.arange(L, dtype=f32)
    tt = (pos / f32(L - 1))[:, None]
    w = (f32(TWO_PI / L) * pos)[:, None]
    bands = np.linspace(1e-4, 15, 16).astype(f32)[None, :]
    feats = np.concatenate([tt, np.cos(bands * w), -np.sin(bands * w)], axis=-1).astype(f32)
    t["c_feats"] = np.ascontiguousarray(feats.T)
    t["c_negt"] = np.ascontiguousarray(-tt.reshape(TT, P).T)
    nz = np.ones((P, TT), f32)
    nz[0, 0] = 0
    t["c_notfirst"] = nz
    i = np.arange(P)
    r, c = i[:, None], i[None, :]
    lev = []
    for k in range(LEVELS):
        b = 2**k
        lev.append((r // (2 * b) == c // (2 * b)) & (r // b % 2 == 1) & (c // b % 2 == 0))
    lower = np.stack(lev).astype(f32)
    t["c_levels"] = np.ascontiguousarray(
        np.stack([lower, lower.transpose(0, 2, 1)]).transpose(2, 0, 1, 3).reshape(P, -1))
    sC, tC = i % CH, i % CH
    strict, incl = sC[:, None] < tC[None, :CH], sC[:, None] <= tC[None, :CH]
    fwd = np.concatenate([strict, incl], 1)
    strict, incl = sC[:, None] > tC[None, :CH], sC[:, None] >= tC[None, :CH]
    bwd = np.concatenate([strict, incl], 1)
    t["c_scan"] = np.ascontiguousarray(np.concatenate([fwd, bwd], 1).astype(f32))
    reset = np.ones((P, L), f32)
    reset[:, ::CH] = 0
    t["c_reset"] = reset
    t["c_causal"] = (r <= c).astype(f32)
    t["c_causal_row"] = np.where(c <= r, 0, -1e30).astype(f32)
    sel = np.zeros((A_HEADS, A_HEADS, P), f32)
    for h in range(A_HEADS):
        sel[h, h, :] = 1
    t["c_sel"] = sel.reshape(A_HEADS, -1)
    inv = (10000.0 ** (-np.arange(32, dtype=f32).astype(np.float64) / 32)).astype(f32)
    t["c_invfreq"] = np.tile(inv, 4).reshape(P, 1)
    return t



def hyena_filter_mlp(nc, e, I, h2):
    with ExitStack() as s:
        sb, pb, sem = opened(nc, s, "hyf")
        feats, w1, w2 = sb("feats", [EMB, L]), sb("w1", [EMB, FILT]), sb("w2", [FILT, FILT])
        h1, y, n = sb("h1", [FILT, L]), sb("y", [FILT, L]), sb("n", [FILT, L])
        ps = pb("ps", [FILT, 2, L])
        loaded, z_ready, y_ready, sin_ready = sem("loaded"), sem("z"), sem("y"), sem("sin")
        steps = sem("steps")
        block = s.enter_context(nc.Block())

        @block.sync
        def _(sp):
            sp.dma_start(feats[:, :], I["c_feats"]).then_inc(loaded, 16)
            sp.dma_start(w1[:, :], I["hy_ffn_w1"]).then_inc(loaded, 16)
            sp.dma_start(w2[:, :], I["hy_ffn_w2"]).then_inc(loaded, 16)

        @block.tensor
        def _(pe):
            pe.wait_ge(loaded, 48)
            nc.tensor.matmul(ps[:, 0, :], w1[:, :], feats[:, :], start=True, stop=True).then_inc(z_ready, 1)
            pe.wait_ge(sin_ready, 1)
            nc.tensor.matmul(ps[:, 1, :], w2[:, :], h1[:, :], start=True, stop=True).then_inc(z_ready, 1)

        @block.vector
        def _(dve):
            st = Steps(steps)

            def then(ins):
                dve.wait_ge(steps, st.mark(ins))

            nc.vector.memset(h2[FILT:FILT + 1, :], 1.0)
            for layer, bias in enumerate(("hy_ffn_b1", "hy_ffn_b2")):
                dve.wait_ge(z_ready, layer + 1)
                then(nc.vector.tensor_scalar(y[:, :], ps[:, layer, :], col(e, bias, 0, FILT),
                                             col(e, "hy_sin_freq", 0, FILT), ALU.add, ALU.mult))
                then(nc.vector.tensor_scalar(n[:, :], y[:, :], 1 / TWO_PI, ROUND, ALU.mult, ALU.add))
                then(nc.vector.tensor_scalar(n[:, :], n[:, :], ROUND, None, ALU.subtract))
                for part in (PI_A, PI_B, PI_C):
                    then(nc.vector.scalar_tensor_tensor(y[:, :], n[:, :], -part, y[:, :], ALU.mult, ALU.add))
                nc.vector.tensor_scalar(y[:, :], y[:, :], math.pi, -math.pi, ALU.min, ALU.max)\
                    .then_inc(y_ready, 1)
                if layer == 0:
                    dve.wait_ge(sin_ready, 1)

        @block.scalar
        def _(act):
            for layer, dst in enumerate((h1, h2)):
                act.wait_ge(y_ready, layer + 1)
                nc.scalar.activation(dst[0:FILT, :], y[:, :], ACT.Sin).then_inc(sin_ready, 1)


def hyena_spectra(nc, e, I, h2, cos, sin, spec):
    with ExitStack() as s:
        sb, pb, sem = opened(nc, s, "hys")
        w3 = sb("w3", [FILT + 1, 4, D_HY])
        dec = sb("dec", [P, 4, D_HY])
        negt, notfirst = sb("negt", [P, TT]), sb("notfirst", [P, TT])
        env = sb("env", [P, 2, D_HY])
        fb = sb("fb", [P, 2, D_HY])
        sq = sb("sq", [P, 2, D_HY])
        ab = sb("ab", [P, 2, TT, D_HY])
        rs = sb("rs", [P, 2, D_HY])
        ps = pb("ps", [P, 2, D_HY])
        pn = pb("pn", [P, D_HY])
        pk = pb("pk", [P, 2, D_HY])
        loaded, dec_abs, env_ready, raw_done = sem("loaded"), sem("dec_abs"), sem("env_ready"), sem("raw_done")
        fb_ready, sq_ready, sq_used, ab_ready = sem("fb_ready"), sem("sq_ready"), sem("sq_used"), sem("ab_ready")
        inv_ready, rs_ready, k_done, k_out = sem("inv_ready"), sem("rs_ready"), sem("k_done"), sem("k_out")
        steps = sem("steps")
        block = s.enter_context(nc.Block())
        N = 2 * TT

        @block.sync
        def _(sp):
            sp.dma_start(w3[0:FILT, :, :], I["hy_ffn_w3"].rearrange("k (g c) -> k g c", g=4)).then_inc(loaded, 16)
            sp.dma_start(w3[FILT:FILT + 1, :, :],
                         I["hy_ffn_b3"].rearrange("(o g c) -> o g c", o=1, g=4)).then_inc(loaded, 16)
            decay = I["hy_decay"].rearrange("d o c -> (d o) c")
            sp.dma_start(dec[:, :, :], decay.partition_broadcast(P)).then_inc(loaded, 16)
            sp.dma_start(negt[:, :], I["c_negt"]).then_inc(loaded, 16)
            sp.dma_start(notfirst[:, :], I["c_notfirst"]).then_inc(loaded, 16)

        @block.tensor
        def _(pe):
            pe.wait_ge(loaded, 80)
            for o in range(2):
                for t in range(TT):
                    n = o * TT + t
                    for d in range(2):
                        if n > 0:
                            pe.wait_ge(fb_ready, 2 * (n - 1) + d + 1)
                        nc.tensor.matmul(ps[:, d, :], h2[:, t * P:(t + 1) * P], w3[:, 2 * d + o, :],
                                         start=True, stop=True).then_inc(raw_done, 1)
                    for d in range(2):
                        pe.wait_ge(sq_ready, 2 * n + d + 1)
                        nc.tensor.matmul(pn[:, :], e.ones[:, :], sq[:, d, :], start=t == 0 and d == 0,
                                         stop=t == TT - 1 and d == 1).then_inc(sq_used, 1)
                pe.wait_ge(ab_ready, 2 * TT * (o + 1))
                for j in range(2 * TT):
                    m = o * 2 * TT + j
                    part, f = j // TT, j % TT
                    table = (cos, sin)[part]
                    if m >= 2:
                        pe.wait_ge(k_out, m - 1)
                    for t in range(TT):
                        last = nc.tensor.matmul(pk[:, m % 2, :], table[:, t, f * P:(f + 1) * P],
                                                ab[:, part, t, :], start=t == 0, stop=t == TT - 1)
                    last.then_inc(k_done, 1)

        @block.scalar
        def _(act):
            act.wait_ge(loaded, 80)
            nc.scalar.activation(dec[:, :, :], dec[:, :, :], ACT.Abs).then_inc(dec_abs, 1)
            act.wait_ge(dec_abs, 1)
            for o in range(2):
                for t in range(TT):
                    n = o * TT + t
                    for d in range(2):
                        if n > 0:
                            act.wait_ge(fb_ready, 2 * (n - 1) + d + 1)
                        nc.scalar.activation(env[:, d, :], dec[:, 2 * d + o, :], ACT.Exp,
                                             scale=negt[:, t:t + 1]).then_inc(env_ready, 1)
                    for d in range(2):
                        act.wait_ge(fb_ready, 2 * n + d + 1)
                        if n > 0:
                            act.wait_ge(sq_used, 2 * (n - 1) + d + 1)
                        nc.scalar.activation(sq[:, d, :], fb[:, d, :], ACT.Square).then_inc(sq_ready, 1)
                act.wait_ge(inv_ready, o + 1)
                nc.scalar.activation(rs[:, 1, :], rs[:, 0, :], ACT.Sqrt).then_inc(rs_ready, 1)

        @block.vector
        def _(dve):
            st = Steps(steps)
            for o in range(2):
                if o == 1:
                    dve.wait_ge(k_done, 2 * TT)
                for t in range(TT):
                    n = o * TT + t
                    for d in range(2):
                        dve.wait_ge(raw_done, 2 * n + d + 1)
                        dve.wait_ge(env_ready, 2 * n + d + 1)
                        if n > 0:
                            dve.wait_ge(sq_ready, 2 * (n - 1) + d + 1)
                            dve.wait_ge(ab_ready, 2 * n)
                        scalar = 1.0 if d == 0 else notfirst[:, t:t + 1]
                        nc.vector.scalar_tensor_tensor(fb[:, d, :], ps[:, d, :], scalar, env[:, d, :],
                                                       ALU.mult, ALU.mult).then_inc(fb_ready, 1)
                    dve.wait_ge(fb_ready, 2 * n + 2)
                    nc.vector.tensor_tensor(ab[:, 0, t, :], fb[:, 0, :], fb[:, 1, :], ALU.add).then_inc(ab_ready, 1)
                    nc.vector.tensor_tensor(ab[:, 1, t, :], fb[:, 0, :], fb[:, 1, :], ALU.subtract)\
                        .then_inc(ab_ready, 1)
                dve.wait_ge(sq_used, 2 * TT * (o + 1))
                dve.wait_ge(steps, st.mark(nc.vector.tensor_scalar(rs[:, 0, :], pn[:, :], EPS, None, ALU.add)))
                nc.vector.reciprocal(rs[:, 0, :], rs[:, 0, :]).then_inc(inv_ready, 1)
                dve.wait_ge(rs_ready, o + 1)
                for j in range(2 * TT):
                    m = o * 2 * TT + j
                    dve.wait_ge(k_done, m + 1)
                    nc.vector.scalar_tensor_tensor(spec[:, o, j // TT, j % TT, :], pk[:, m % 2, :], 1.0 / L,
                                                   rs[:, 1, :], ALU.mult, ALU.mult).then_inc(k_out, 1)


def hyena_conv3(nc, e, u, uc):
    with ExitStack() as s:
        sb, pb, sem = opened(nc, s, "hyc")
        mid, left = sem("mid"), sem("left")
        block = s.enter_context(nc.Block())
        n = N_HY // P

        @block.scalar
        def _(act):
            for j in range(n):
                nc.scalar.activation(uc[:, j, :], u[:, j, :], ACT.Identity, bias=col(e, "hy_conv_b", j),
                                     scale=col(e, "hy_conv_w", n + j)).then_inc(mid, 1)

        @block.vector
        def _(dve):
            for j in range(n):
                dve.wait_ge(mid, j + 1)
                nc.vector.scalar_tensor_tensor(uc[:, j, 1:L], u[:, j, 0:L - 1], col(e, "hy_conv_w", j),
                                               uc[:, j, 1:L], ALU.mult, ALU.add).then_inc(left, 1)
                dve.wait_ge(left, j + 1)
                nc.vector.scalar_tensor_tensor(uc[:, j, 0:L - 1], u[:, j, 1:L], col(e, "hy_conv_w", 2 * n + j),
                                               uc[:, j, 0:L - 1], ALU.mult, ALU.add)


def hyena_long_conv(nc, e, o, z, gate, dst, cos, sin, cosT, sinT, spec):
    with ExitStack() as s:
        sb, pb, sem = opened(nc, s, f"hyl{o}")
        zt = sb("zt", [P, TT, D_HY])
        zf = sb("zf", [P, 2, D_HY])
        yf = sb("yf", [P, 2, TT, D_HY])
        tmp = sb("tmp", [P, 4, D_HY])
        dz = sb("dz", [P, HT, L])
        pt = pb("pt", [P, 2, D_HY])
        pf = pb("pf", [P, 2, D_HY])
        po = pb("po", [P, 2, L])
        turned, zt_ready, f_done, f_out = sem("turned"), sem("zt_ready"), sem("f_done"), sem("f_out")
        prod, yf_ready, o_done, o_out, sum_ready = sem("prod"), sem("yf"), sem("o_done"), sem("o_out"), sem("sum")
        block = s.enter_context(nc.Block())

        @block.tensor
        def _(pe):
            for t in range(TT):
                if t >= 2:
                    pe.wait_ge(zt_ready, t - 1)
                for c in range(HT):
                    last = nc.tensor.transpose(pt[:, t % 2, c * P:(c + 1) * P], z[:, c, t * P:(t + 1) * P],
                                               e.ident[:, :])
                last.then_inc(turned, 1)
            pe.wait_ge(zt_ready, TT)
            for f in range(TT):
                for part, table in enumerate((cos, sin)):
                    if f > 0:
                        pe.wait_ge(f_out, 2 * (f - 1) + part + 1)
                    for t in range(TT):
                        last = nc.tensor.matmul(pf[:, part, :], table[:, t, f * P:(f + 1) * P], zt[:, t, :],
                                                start=t == 0, stop=t == TT - 1)
                    last.then_inc(f_done, 1)
            pe.wait_ge(yf_ready, 2 * TT)
            for c in range(HT):
                if c >= 2:
                    pe.wait_ge(o_out, c - 1)
                for part, table in enumerate((cosT, sinT)):
                    for f in range(TT):
                        last = nc.tensor.matmul(po[:, c % 2, :], yf[:, part, f, c * P:(c + 1) * P],
                                                table[:, f, :], start=part + f == 0,
                                                stop=part == 1 and f == TT - 1)
                last.then_inc(o_done, 1)

        @block.scalar
        def _(act):
            for t in range(TT):
                act.wait_ge(turned, t + 1)
                nc.scalar.activation(zt[:, t, :], pt[:, t % 2, :], ACT.Copy).then_inc(zt_ready, 1)
            for f in range(TT):
                for part in range(2):
                    act.wait_ge(f_done, 2 * f + part + 1)
                    if f > 0:
                        act.wait_ge(prod, 4 * f)
                    nc.scalar.activation(zf[:, part, :], pf[:, part, :], ACT.Copy).then_inc(f_out, 1)

        @block.vector
        def _(dve):
            for f in range(TT):
                dve.wait_ge(f_out, 2 * f + 2)
                kr, ks = spec[:, o, 0, f, :], spec[:, o, 1, f, :]
                if f > 0:
                    dve.wait_ge(yf_ready, 2 * f)
                for i, (a, b) in enumerate(((0, kr), (1, ks), (0, ks), (1, kr))):
                    nc.vector.tensor_tensor(tmp[:, i, :], zf[:, a, :], b, ALU.mult).then_inc(prod, 1)
            for c in range(HT):
                dve.wait_ge(o_done, c + 1)
                nc.vector.scalar_tensor_tensor(dz[:, c, :], z[:, c, :], col(e, "hy_bias_d", o * HT + c),
                                               po[:, c % 2, :], ALU.mult, ALU.add).then_inc(o_out, 1)
                dve.wait_ge(o_out, c + 1)
                nc.vector.tensor_tensor(dst[:, c, :], dz[:, c, :], gate[:, c, :], ALU.mult)

        @block.gpsimd
        def _(pool):
            for f in range(TT):
                pool.wait_ge(prod, 4 * f + 4)
                nc.gpsimd.tensor_tensor(yf[:, 0, f, :], tmp[:, 0, :], tmp[:, 1, :], ALU.subtract)\
                    .then_inc(yf_ready, 1)
                nc.gpsimd.tensor_tensor(yf[:, 1, f, :], tmp[:, 2, :], tmp[:, 3, :], ALU.add)\
                    .then_inc(yf_ready, 1)


def hyena_branch(nc, e, I, h, merged):
    with ExitStack() as s:
        keep = lambda name, shape: s.enter_context(nc.sbuf_tensor(f"hy_{name}", shape, F32))
        z2 = keep("z2", [P, HT, L])
        with ExitStack() as s2:
            part = lambda name, shape: s2.enter_context(nc.sbuf_tensor(f"hy_{name}", shape, F32))
            uc = part("uc", [P, N_HY // P, L])
            with nc.sbuf_tensor("hy_u", [P, N_HY // P, L], F32) as u:
                gemm(nc, e, "hy_in", I["w_in"][:, 0:N_HY], DT, h, 3, 2, 2, "copy", dst=u,
                     before=normed(nc, e, e.x, DT, h, lambda k: col(e, "mix_norm", k)))
                hyena_conv3(nc, e, u, uc)
            cos, sin = part("cos", [P, TT, L]), part("sin", [P, TT, L])
            spec = part("spec", [P, 2, 2, TT, D_HY])
            table = lambda name: I[name].rearrange("(t p) f -> p t f", p=P)
            load_tables(nc, "dft", [(cos[:, :, :], table("c_cos")), (sin[:, :, :], table("c_sin"))])
            with nc.sbuf_tensor("hy_h2", [FILT + 1, L], F32) as h2:
                hyena_filter_mlp(nc, e, I, h2)
                hyena_spectra(nc, e, I, h2, cos, sin, spec)
            cosT, sinT = part("cosT", [P, TT, L]), part("sinT", [P, TT, L])
            load_tables(nc, "idft", [(cosT[:, :, :], table("c_cosT")), (sinT[:, :, :], table("c_sinT"))])
            x1, x2, v = uc[:, 0:HT, :], uc[:, HT:2 * HT, :], uc[:, 2 * HT:3 * HT, :]
            hyena_long_conv(nc, e, 0, v, x1, x1, cos, sin, cosT, sinT, spec)
            hyena_long_conv(nc, e, 1, x1, x2, z2, cos, sin, cosT, sinT, spec)
        gated_output(nc, e, "hy", I["w_in"][:, N_HY + N_RW:N_HY + N_RW + D], h, None, I["hy_out"], HT, z2, merged, 0)


def gated_output(nc, e, tag, w_gate, h, before, w_o, k_tiles, z, merged, add):
    with ExitStack() as s:
        g = s.enter_context(nc.sbuf_tensor(f"{tag}_sig", [P, DT, L], F32))
        gemm(nc, e, f"{tag}_gate", w_gate, DT, h, 2, 2, 2, "copy", dst=g, func=ACT.Sigmoid, before=before)
        zp = two_parts(nc, s, f"{tag}_z", k_tiles)
        gemm(nc, e, f"{tag}_out", w_o, k_tiles, zp, 2, 2, 2, "gate", dst=merged, gate=g, factor=add,
             before=cut(nc, e, z, k_tiles, zp))



def rwkv_inputs(nc, e, I, h, rkv, lora):
    n = MU_ROWS + 1
    rest = N_RW - MU_ROWS * P
    with ExitStack() as s:
        u = s.enter_context(nc.sbuf_tensor("rw_u", [P, n, L], F32))
        w = I["w_in"]
        gemm(nc, e, "rw_in", w[:, N_HY:N_HY + n * P], DT, h, n // 4, 2, 2, "copy", dst=u,
             before=normed(nc, e, e.x, DT, h, lambda k: col(e, "mix_norm", k)))
        keep = s.enter_context(nc.sbuf_tensor("rw_keep", [P, n], F32))
        with ExitStack() as s2:
            sb, pb, sem = opened(nc, s2, "shift")
            kept, mid, left = sem("kept"), sem("mid"), sem("left")
            block = s2.enter_context(nc.Block())
            mu = COL["rw_mu"]

            def shifted(j):
                p = P if j < MU_ROWS else rest
                return p, (rkv[:, j, :] if j < 3 * RT else lora[0:p, j - 3 * RT, :])

            @block.vector
            def _(dve):
                nc.vector.tensor_tensor(keep[:, :], e.cols[:, mu:mu + n], e.cols[:, mu + n:mu + 2 * n],
                                        ALU.add).then_inc(kept, 1)
                dve.wait_ge(kept, 1)
                nc.vector.tensor_scalar(keep[:, :], keep[:, :], -1.0, 1.0, ALU.mult, ALU.add).then_inc(kept, 1)
                for j in range(n):
                    p, us = shifted(j)
                    dve.wait_ge(mid, j + 1)
                    nc.vector.scalar_tensor_tensor(us[:, 1:L], u[0:p, j, 0:L - 1],
                                                   e.cols[0:p, mu + j:mu + j + 1], us[:, 1:L],
                                                   ALU.mult, ALU.add).then_inc(left, 1)
                    dve.wait_ge(left, j + 1)
                    nc.vector.scalar_tensor_tensor(us[:, 0:L - 1], u[0:p, j, 1:L],
                                                   e.cols[0:p, mu + n + j:mu + n + j + 1],
                                                   us[:, 0:L - 1], ALU.mult, ALU.add)

            @block.scalar
            def _(act):
                act.wait_ge(kept, 2)
                for j in range(n):
                    p, us = shifted(j)
                    nc.scalar.activation(us, u[0:p, j, :], ACT.Copy,
                                         scale=keep[0:p, j:j + 1]).then_inc(mid, 1)


def rwkv_features(nc, e, I, rkv, lora, lw, a, g, kk, bonus):
    r, k, v = rkv[:, 0:RT, :], rkv[:, RT:2 * RT, :], rkv[:, 2 * RT:3 * RT, :]
    us = lora
    WD, AD, GD = 0, 1, 2
    rest = N_RW - MU_ROWS * P
    with ExitStack() as s:
        sb, pb, sem = opened(nc, s, "rwf")
        w2, a2 = sb("w2", [P, D_RW]), sb("a2", [P, D_RW])
        g2, g2b = sb("g2", [P, D_RW]), sb("g2b", [rest, D_RW])
        kks = sb("kks", [P, RT, L])
        sq = sb("sq", [P, RT, L])
        nrm = sb("nrm", [P, RT, L])
        kd = sb("kd", [P, 2, L])
        rk = sb("rk", [P, 2, L])
        ps = pb("ps", [P, 4, L])
        pn = pb("pn", [P, RT, L])
        loaded, act_in, done, taken = sem("loaded"), sem("act_in"), sem("done"), sem("taken")
        kks_ready, sq_ready, n_done, n_root, steps = sem("kks"), sem("sq"), sem("n_done"), sem("n_root"), sem("steps")
        rk_ready, b_done, b_out = sem("rk"), sem("b_done"), sem("b_out")
        block = s.enter_context(nc.Block())

        @block.sync
        def _(sp):
            sp.dma_start(w2[:, :], I["rw_w2"].rearrange("d r c -> (d r) c")).then_inc(loaded, 16)
            sp.dma_start(a2[:, :], I["rw_a2"].rearrange("d r c -> (d r) c")).then_inc(loaded, 16)
            sp.dma_start(g2[:, :], I["rw_g2"][0:P, :]).then_inc(loaded, 16)
            sp.dma_start(g2b[:, :], I["rw_g2"][P:P + rest, :]).then_inc(loaded, 16)

        jobs = [("a", d, c) for c in range(RT) for d in range(2)] + \
               [("w", d, c) for d in range(2) for c in range(RT)] + [("g", 0, c) for c in range(RT)]

        @block.tensor
        def _(pe):
            for c in range(RT):
                pe.wait_ge(sq_ready, c + 1)
                nc.tensor.matmul(pn[:, c, :], e.heads[:, :], sq[:, c, :], start=True, stop=True)\
                    .then_inc(n_done, 1)
            pe.wait_ge(loaded, 64)
            for n, (kind, d, c) in enumerate(jobs):
                if n >= 4:
                    pe.wait_ge(taken, n - 3)
                cs = slice(c * P, (c + 1) * P)
                hd = slice(64 * d, 64 * d + 64)
                if kind == "g":
                    pe.wait_ge(act_in, 3)
                    nc.tensor.matmul(ps[:, n % 4, :], g2[:, cs], us[:, GD, :], start=True, stop=False)
                    last = nc.tensor.matmul(ps[:, n % 4, :], g2b[:, cs], us[0:rest, GD + 1, :], start=False, stop=True)
                else:
                    wt, src = (w2, WD) if kind == "w" else (a2, AD)
                    if kind == "w":
                        pe.wait_ge(act_in, 1)
                    last = nc.tensor.matmul(ps[:, n % 4, :], wt[hd, cs], us[hd, src, :], start=True, stop=True)
                last.then_inc(done, 1)
            for c in range(RT):
                pe.wait_ge(rk_ready, c + 1)
                pe.wait_ge(n_root, c + 1)
                nc.tensor.matmul(pn[:, c, :], e.heads[:, :], rk[:, c % 2, :], start=True, stop=True)\
                    .then_inc(b_done, 1)

        @block.scalar
        def _(act):
            for c in range(RT):
                nc.scalar.activation(sq[:, c, :], k[:, c, :], ACT.Square, scale=col(e, "rw_k_k", c))\
                    .then_inc(sq_ready, 1)
            for c in range(RT):
                act.wait_ge(n_done, c + 1)
                nc.scalar.activation(nrm[:, c, :], pn[:, c, :], ACT.Sqrt).then_inc(n_root, 1)
            nc.scalar.activation(us[:, WD, :], us[:, WD, :], ACT.Tanh).then_inc(act_in, 1)
            nc.scalar.activation(us[:, GD, :], us[:, GD, :], ACT.Sigmoid).then_inc(act_in, 1)
            nc.scalar.activation(us[0:rest, GD + 1, :], us[0:rest, GD + 1, :], ACT.Sigmoid).then_inc(act_in, 1)
            for n, (kind, d, c) in enumerate(jobs):
                act.wait_ge(done, n + 1)
                if kind == "g":
                    ins = nc.scalar.activation(g[:, c, :], ps[:, n % 4, :], ACT.Copy)
                else:
                    dst, bias = (lw, "rw_w0") if kind == "w" else (a, "rw_a0")
                    ins = nc.scalar.activation(dst[:, d, c, :], ps[:, n % 4, :], ACT.Sigmoid,
                                               bias=col(e, bias, d * RT + c))
                ins.then_inc(taken, 1)

        @block.gpsimd
        def _(pool):
            for c in range(RT):
                nc.gpsimd.tensor_scalar(kks[:, c, :], k[:, c, :], col(e, "rw_k_k", c), None, ALU.mult)\
                    .then_inc(kks_ready, 1)
            for d in range(2):
                for c in range(RT):
                    pool.wait_ge(taken, 2 * RT + d * RT + c + 1)
                    nc.gpsimd.tensor_scalar(lw[:, d, c, :], lw[:, d, c, :], LOG_DECAY_MAX, None, ALU.mult)

        @block.vector
        def _(dve):
            st = Steps(steps)

            def then(ins):
                dve.wait_ge(steps, st.mark(ins))

            for c in range(RT):
                dve.wait_ge(n_root, c + 1)
                then(nc.vector.tensor_scalar(nrm[:, c, :], nrm[:, c, :], 1e-12, None, ALU.max))
                then(nc.vector.reciprocal(nrm[:, c, :], nrm[:, c, :]))
                dve.wait_ge(kks_ready, c + 1)
                nc.vector.tensor_tensor(kk[:, c, :], kks[:, c, :], nrm[:, c, :], ALU.mult)
            for c in range(RT):
                dve.wait_ge(taken, 2 * c + 2)
                then(nc.vector.scalar_tensor_tensor(kd[:, 0, :], a[:, 0, c, :], -2.0, a[:, 1, c, :],
                                                    ALU.add, ALU.add))
                then(nc.vector.tensor_scalar(kd[:, 0, :], kd[:, 0, :], col(e, "rw_k_a", c), 2.0,
                                             ALU.mult, ALU.add))
                then(nc.vector.tensor_tensor(kd[:, 0, :], kd[:, 0, :], k[:, c, :], ALU.mult))
                if c >= 2:
                    dve.wait_ge(b_done, c - 1)
                nc.vector.scalar_tensor_tensor(rk[:, c % 2, :], kd[:, 0, :], col(e, "rw_r_k", c), r[:, c, :],
                                               ALU.mult, ALU.mult).then_inc(rk_ready, 1)
                dve.wait_ge(rk_ready, c + 1)
            for c in range(RT):
                dve.wait_ge(b_done, c + 1)
                nc.vector.tensor_tensor(bonus[:, c, :], pn[:, c, :], v[:, c, :], ALU.mult).then_inc(b_out, 1)


class Scaled:
    pass


def scaled_programs(nc, e, sb, sem, d, half, nb, rkv, lw, a, kk, reset, ar, kb, pend):
    toks = slice(half * LH, half * LH + LH)
    r, k = rkv[:, 0:RT, toks], rkv[:, RT:2 * RT, toks]
    lw, a, kk = lw[:, :, :, toks], a[:, :, :, toks], kk[:, :, toks]
    chunks = lambda t: t.rearrange("p (n c) -> p n c", c=CH)
    N = Scaled()
    inc, exc, kd, inv = (sb(f"s_{n}", [P, nb, LH]) for n in ("inc", "exc", "kd", "inv"))
    steps, pin, pout, kd_ready, kd_used = (sem("s_steps"), sem("s_logs"), sem("s_powers"), sem("s_kd"),
                                           sem("s_kd_used"))
    pn, pn_used = sem("s_inverse"), sem("s_pn_used")
    st = Steps(steps)

    def pool_program(pool):
        for c in range(RT):
            b = c % nb
            if c >= nb:
                pool.wait_ge(kd_used, c - nb + 1)
            nc.gpsimd.tensor_scalar(kd[:, b, :], a[:, d, c, :], -1.0, col(e, "rw_k_a", c),
                                    ALU.add, ALU.mult).then_inc(kd_ready, 1)
            pool.wait_ge(kd_ready, 3 * c + 1)
            nc.gpsimd.tensor_scalar(kd[:, b, :], kd[:, b, :], 1.0, None, ALU.add).then_inc(kd_ready, 1)
            pool.wait_ge(kd_ready, 3 * c + 2)
            nc.gpsimd.tensor_tensor(kd[:, b, :], kd[:, b, :], k[:, c, :], ALU.mult).then_inc(kd_ready, 1)

    def act_program(act, c):
        b = c % nb
        act.wait_ge(pin, c + 1)
        if c >= nb:
            act.wait_ge(pn_used, c - nb + 1)
        nc.scalar.activation(inv[:, b, :], inc[:, b, :], ACT.Exp, scale=-1.0).then_inc(pn, 1)
        act.wait_ge(pn, c + 1)
        nc.scalar.activation(inc[:, b, :], inc[:, b, :], ACT.Exp).then_inc(pout, 1)
        nc.scalar.activation(exc[:, b, :], exc[:, b, :], ACT.Exp).then_inc(pout, 1)

    def then(dve, ins):
        dve.wait_ge(steps, st.mark(ins))

    def logs(dve, c):
        b = c % nb
        pre = (inc, exc)[d]
        w = lw[:, d, c, :]
        then(dve, nc.vector.tensor_tensor_scan(pre[:, b, :], reset[:, 0:LH], w, 0.0, ALU.mult, ALU.add))
        if d == 0:
            nc.vector.tensor_tensor(exc[:, b, :], inc[:, b, :], w, ALU.subtract).then_inc(pin, 1)
        else:
            whole = chunks(pre[:, b, :])[:, :, CH - 1:CH]
            then(dve, nc.vector.tensor_copy(pend[:, c, :], whole.rearrange("p n o -> p (n o)")))
            then(dve, nc.vector.tensor_tensor(chunks(exc[:, b, :]), pend[:, c, :].unsqueeze(2).to_broadcast([P, HCH, CH]),
                                         chunks(pre[:, b, :]), ALU.subtract))
            nc.vector.tensor_tensor(inc[:, b, :], exc[:, b, :], w, ALU.add).then_inc(pin, 1)

    def products(dve, c):
        b = c % nb
        dve.wait_ge(pout, 2 * c + 2)
        dve.wait_ge(kd_ready, 3 * c + 3)
        nc.vector.scalar_tensor_tensor(ar[:, c, :, 0:CH], chunks(kk[:, c, :]), -1.0, chunks(exc[:, b, :]),
                                       ALU.mult, ALU.mult)
        nc.vector.tensor_tensor(ar[:, c, :, CH:2 * CH], chunks(r[:, c, :]), chunks(inc[:, b, :]), ALU.mult)
        nc.vector.tensor_tensor(kb[:, c, :, 0:CH], chunks(kd[:, b, :]), chunks(inv[:, b, :]),
                                ALU.mult).then_inc(kd_used, 1)
        at = CH - 1 if d == 0 else 0
        nc.vector.tensor_copy(pend[:, c, :].unsqueeze(2), chunks(inc[:, b, :])[:, :, at:at + 1])
        then(dve, nc.vector.tensor_tensor(kb[:, c, :, CH:2 * CH], chunks(kk[:, c, :]), chunks(a[:, d, c, :]),
                                     ALU.mult))
        nc.vector.tensor_tensor(kb[:, c, :, CH:2 * CH], kb[:, c, :, CH:2 * CH], chunks(inv[:, b, :]),
                                ALU.mult).then_inc(pn_used, 1)
        dve.wait_ge(pn_used, c + 1)

    N.pool, N.act, N.logs, N.products = pool_program, act_program, logs, products
    return N


def rwkv_scaled(nc, e, d, half, *operands):
    with ExitStack() as s:
        sb, pb, sem = opened(nc, s, f"rws{d}{half}")
        N = scaled_programs(nc, e, sb, sem, d, half, 1, *operands)
        block = s.enter_context(nc.Block())
        block.gpsimd(N.pool)

        @block.scalar
        def _(act):
            for c in range(RT):
                N.act(act, c)

        @block.vector
        def _(dve):
            for c in range(RT):
                N.logs(dve, c)
                N.products(dve, c)


def rwkv_matrices(nc, e, d, half, rkv, ar, kb, scan_mask, gt, kbt, vu, bv):
    v = rkv[:, 2 * RT:3 * RT, half * LH:half * LH + LH]
    with ExitStack() as s:
        sb, pb, sem = opened(nc, s, f"rwm{d}{half}")
        pg = pb("pg", [P, 2, 2, HCH, P])
        pk, pv, pbv = pb("pk", [P, HCH, P]), pb("pv", [CH, HCH, P]), pb("pbv", [P, 2, L])
        g_done, k_done, v_done = sem("g_done"), sem("k_done"), sem("v_done")
        g_out, k_out, v_out = sem("g_out"), sem("k_out"), sem("v_out")
        b_done, b_out = sem("b_done"), sem("b_out")
        block = s.enter_context(nc.Block())
        hs = [slice(0, 64), slice(64, 128)]

        @block.tensor
        def _(pe):
            def b_times_v(c):
                pe.wait_ge(g_out, 2 * c + 2)
                pe.wait_ge(v_out, c + 1)
                if c >= 2:
                    pe.wait_ge(b_out, c - 1)
                for ch in range(HCH):
                    for hd in range(2):
                        last = nc.tensor.matmul(pbv[hs[hd], c % 2, ch * CH:(ch + 1) * CH], gt[0:CH, c, ch, hd, 0:CH],
                                                vu[0:CH, c, ch, hs[hd]], start=True, stop=True)
                last.then_inc(b_done, 1)

            for c in range(RT):
                for hd in range(2):
                    if c >= 2:
                        pe.wait_ge(g_out, 2 * (c - 2) + hd + 1)
                    for ch in range(HCH):
                        last = nc.tensor.matmul(pg[:, c % 2, hd, ch, :], kb[hs[hd], c, ch, :], ar[hs[hd], c, ch, :],
                                                start=True, stop=True)
                    last.then_inc(g_done, 1)
                if c > 0:
                    pe.wait_ge(k_out, c)
                    pe.wait_ge(v_out, c)
                for ch in range(HCH):
                    last = nc.tensor.transpose(pk[:, ch, :], kb[:, c, ch, :], e.ident[:, :])
                last.then_inc(k_done, 1)
                for ch in range(HCH):
                    last = nc.tensor.transpose(pv[:, ch, :], v[:, c, ch * CH:(ch + 1) * CH], e.ident[:, :])
                last.then_inc(v_done, 1)
                if c > 0:
                    b_times_v(c - 1)
            b_times_v(RT - 1)

        @block.scalar
        def _(act):
            for c in range(RT):
                act.wait_ge(k_done, c + 1)
                nc.scalar.activation(kbt[:, c, :, :], pk[:, :, :], ACT.Copy).then_inc(k_out, 1)
                act.wait_ge(v_done, c + 1)
                nc.scalar.activation(vu[0:CH, c, :, :], pv[:, :, :], ACT.Copy).then_inc(v_out, 1)
                act.wait_ge(b_done, c + 1)
                nc.scalar.activation(bv[:, :, c, :], pbv[:, c % 2, 0:LH].rearrange("p (n i) -> p n i", n=HCH),
                                     ACT.Copy).then_inc(b_out, 1)

        @block.vector
        def _(dve):
            for c in range(RT):
                for hd in range(2):
                    dve.wait_ge(g_done, 2 * c + hd + 1)
                    mask = scan_mask[:, d, :].unsqueeze(1).to_broadcast([P, HCH, P])
                    nc.vector.tensor_tensor(gt[:, c, :, hd, :], pg[:, c % 2, hd, :, :], mask, ALU.mult)\
                        .then_inc(g_out, 1)


def rwkv_inverse(nc, e, d, half, gt, levels, xt, spare, xw):
    with ExitStack() as s:
        sb, pb, sem = opened(nc, s, f"rwi{d}{half}")
        at, a = spare[:, 0:2, :, :], spare[:, 2:4, :, :]
        x, w = xw[:, 0:2, :, :], xw[:, 2:4, :, :]
        pw, pt, px = (pb(n, [P, 2, 4, P]) for n in ("pw", "pt", "px"))
        zeroed, at_ready, a_turned, a_ready = sem("zeroed"), sem("at"), sem("a_turned"), sem("a")
        start_ready, w_done, w_out = sem("start"), sem("w_done"), sem("w_out")
        t_done, t_out, x_done, x_out, steps = sem("t_done"), sem("t_out"), sem("x_done"), sem("x_out"), sem("steps")
        block = s.enter_context(nc.Block())
        rounds = RT // 2
        K = LEVELS - 1
        below, above = (levels[:, d, :, :], levels[:, 1 - d, :, :])
        mask4 = lambda m: m.unsqueeze(1).to_broadcast([P, 4, P])

        @block.tensor
        def _(pe):
            for c in range(rounds):
                for q in range(2):
                    pe.wait_ge(at_ready, 2 * c + q + 1)
                    if c > 0:
                        pe.wait_ge(x_out, (K - 1) * (2 * (c - 1) + q + 1))
                    for m in range(4):
                        last = nc.tensor.transpose(px[:, q, m, :], at[:, q, m, :], e.ident[:, :])
                    last.then_inc(a_turned, 1)
                for k in range(K):
                    for q in range(2):
                        i = (c * K + k) * 2 + q
                        if k == 0:
                            pe.wait_ge(start_ready, 2 * c + q + 1)
                        else:
                            pe.wait_ge(t_out, i - 1)
                            pe.wait_ge(x_out, (c * (K - 1) + k - 1) * 2 + q + 1)
                        for m in range(4):
                            last = nc.tensor.matmul(pw[:, q, m, :], a[:, q, m, :], xt[:, 2 * c + q, m, :],
                                                    start=True, stop=True)
                        last.then_inc(w_done, 1)
                    for q in range(2):
                        i = (c * K + k) * 2 + q
                        pe.wait_ge(w_out, i + 1)
                        for m in range(4):
                            last = nc.tensor.matmul(pt[:, q, m, :], x[:, q, m, :], w[:, q, m, :],
                                                    start=True, stop=True)
                        last.then_inc(t_done, 1)
                        if k < K - 1:
                            for m in range(4):
                                last = nc.tensor.matmul(px[:, q, m, :], w[:, q, m, :], x[:, q, m, :],
                                                        start=True, stop=True)
                            last.then_inc(x_done, 1)

        @block.scalar
        def _(act):
            for c in range(rounds):
                for q in range(2):
                    act.wait_ge(a_turned, 2 * c + q + 1)
                    if c > 0:
                        act.wait_ge(w_done, 2 * K * c)
                    nc.scalar.activation(a[:, q, :, :], px[:, q, :, :], ACT.Copy).then_inc(a_ready, 1)

        @block.vector
        def _(dve):
            st = Steps(steps)
            nc.vector.memset(at[:, :, :, :], 0.0).then_inc(zeroed, 1)
            dve.wait_ge(zeroed, 1)
            for c in range(rounds):
                for q in range(2):
                    if c > 0:
                        dve.wait_ge(start_ready, 2 * c)
                    for hd in range(2):
                        hs = slice(64 * hd, 64 * hd + 64)
                        ins = nc.vector.tensor_copy(at[hs, q, :, hs], gt[CH:P, 2 * c + q, :, hd, 0:CH])
                        st.mark(ins) if hd == 0 else ins.then_inc(at_ready, 1)
                for q in range(2):
                    dve.wait_ge(a_ready, 2 * c + q + 1)
                    dve.wait_ge(at_ready, 2 * c + q + 1)
                    dve.wait_ge(steps, st.n)
                    if c > 0:
                        dve.wait_ge(t_done, 2 * K * (c - 1) + 2 * K)
                    xq, xtq = x[:, q, :, :], xt[:, 2 * c + q, :, :]
                    st.mark(nc.vector.tensor_tensor(xq, a[:, q, :, :], mask4(below[:, 0, :]), ALU.mult))
                    st.mark(nc.vector.tensor_tensor(xtq, at[:, q, :, :], mask4(above[:, 0, :]), ALU.mult))
                    dve.wait_ge(steps, st.n)
                    st.mark(nc.vector.tensor_tensor(xq, xq, mask4(e.ident[:, :]), ALU.add))
                    nc.vector.tensor_tensor(xtq, xtq, mask4(e.ident[:, :]), ALU.add).then_inc(start_ready, 1)
                    dve.wait_ge(steps, st.n)
                for k in range(K):
                    for q in range(2):
                        i = (c * K + k) * 2 + q
                        dve.wait_ge(w_done, i + 1)
                        if i >= 2:
                            dve.wait_ge(t_done, i - 1)
                        nc.vector.tensor_tensor(w[:, q, :, :], pw[:, q, :, :], mask4(above[:, k + 1, :]),
                                                ALU.mult).then_inc(w_out, 1)
                    for q in range(2):
                        i = (c * K + k) * 2 + q
                        xq, xtq = x[:, q, :, :], xt[:, 2 * c + q, :, :]
                        dve.wait_ge(t_done, i + 1)
                        nc.vector.tensor_tensor(xtq, xtq, pt[:, q, :, :], ALU.add).then_inc(t_out, 1)
                        if k < K - 1:
                            dve.wait_ge(x_done, (c * (K - 1) + k) * 2 + q + 1)
                            nc.vector.tensor_tensor(xq, xq, px[:, q, :, :], ALU.add).then_inc(x_out, 1)


def rwkv_chain(nc, e, d, half, state, ar, gt, kbt, xt, vu, bv, pend, y, following):
    with ExitStack() as s:
        sb, pb, sem = opened(nc, s, f"rwc{d}{half}")
        first = half == d
        rhs = sb("rhs", [P, RT, CH])
        grown = sb("grown", [P, RT, CH])
        pr, pu, py, pt = (pb(n, [P, RT, CH]) for n in ("pr", "pu", "py", "pt"))
        zeroed, r_done, r_out, u_done, u_out = sem("zeroed"), sem("r_done"), sem("r_out"), sem("u_done"), sem("u_out")
        u_out2, y_done, y_out = sem("u_out2"), sem("y_done"), sem("y_out")
        t_done, grown_ready, state_ready = sem("t_done"), sem("grown"), sem("state_ready")
        ahead = scaled_programs(nc, e, sb, sem, *following) if following else None
        block = s.enter_context(nc.Block())
        order = list(range(HCH)) if d == 0 else list(range(HCH - 1, -1, -1))
        hs = [slice(0, 64), slice(64, 128)]

        @block.tensor
        def _(pe):
            if first:
                pe.wait_ge(zeroed, 1)
            for n, ch in enumerate(order):
                if n > 0:
                    pe.wait_ge(state_ready, n)
                    pe.wait_ge(r_out, n)
                for c in range(RT):
                    for hd in range(2):
                        last = nc.tensor.matmul(pr[hs[hd], c, :], ar[hs[hd], c, ch, 0:CH], state[hs[hd], c, :],
                                                start=True, stop=True)
                last.then_inc(r_done, 1)
                pe.wait_ge(r_out, n + 1)
                if n > 0:
                    pe.wait_ge(u_out, n)
                    pe.wait_ge(u_out2, n)
                for c in range(RT):
                    last = nc.tensor.matmul(pu[:, c, :], xt[:, c, ch, :], rhs[:, c, :], start=True, stop=True)
                last.then_inc(u_done, 1)
                pe.wait_ge(u_out, n + 1)
                pe.wait_ge(u_out2, n + 1)
                if n > 0:
                    pe.wait_ge(grown_ready, n)
                for c in range(RT):
                    for hd in range(2):
                        last = nc.tensor.matmul(pt[hs[hd], c, :], kbt[:, c, ch, hs[hd]], vu[:, c, ch, hs[hd]],
                                                start=True, stop=True)
                last.then_inc(t_done, 1)
                if n > 0:
                    pe.wait_ge(y_out, n)
                for c in range(RT):
                    for hd in range(2):
                        nc.tensor.matmul(py[hs[hd], c, :], vu[:, c, ch, hs[hd]], gt[:, c, ch, hd, CH:2 * CH],
                                         start=True, stop=False)
                        last = nc.tensor.matmul(py[hs[hd], c, :], state[hs[hd], c, :], ar[hs[hd], c, ch, CH:2 * CH],
                                                start=False, stop=True)
                last.then_inc(y_done, 1)

        @block.scalar
        def _(act):
            for n, ch in enumerate(order):
                act.wait_ge(u_done, n + 1)
                nc.scalar.activation(vu[CH:P, :, ch, 0:CH], pu[0:CH, :, :], ACT.Copy).then_inc(u_out, 1)
                if ahead:
                    ahead.act(act, n)

        @block.vector
        def _(dve):
            if first:
                nc.vector.memset(state[:, :, :], 0.0).then_inc(zeroed, 1)
                dve.wait_ge(zeroed, 1)
            for n, ch in enumerate(order):
                dve.wait_ge(r_done, n + 1)
                if n > 0:
                    dve.wait_ge(u_done, n)
                nc.vector.tensor_tensor(rhs[:, :, :], bv[:, ch, :, :], pr[:, :, :], ALU.add).then_inc(r_out, 1)
                if ahead:
                    ahead.logs(dve, n)
                dve.wait_ge(u_done, n + 1)
                nc.vector.tensor_copy(vu[CH:P, :, ch, CH:P], pu[CH:P, :, :]).then_inc(u_out2, 1)
                dve.wait_ge(t_done, n + 1)
                if n > 0:
                    dve.wait_ge(state_ready, n)
                nc.vector.tensor_tensor(grown[:, :, :], state[:, :, :], pt[:, :, :], ALU.add)\
                    .then_inc(grown_ready, 1)
                dve.wait_ge(y_done, n + 1)
                dve.wait_ge(grown_ready, n + 1)
                decay = pend[:, :, ch:ch + 1].to_broadcast([P, RT, CH])
                nc.vector.tensor_tensor(state[:, :, :], grown[:, :, :], decay, ALU.mult).then_inc(state_ready, 1)
                ys = y[:, :, half * LH + ch * CH:half * LH + (ch + 1) * CH]
                if d == 0:
                    nc.vector.tensor_copy(ys, py[:, :, :]).then_inc(y_out, 1)
                else:
                    nc.vector.tensor_tensor(ys, ys, py[:, :, :], ALU.add).then_inc(y_out, 1)
                if ahead:
                    ahead.products(dve, n)

        if ahead:
            block.gpsimd(ahead.pool)


def rwkv_group_norm(nc, e, y, bonus, g):
    with ExitStack() as s:
        sb, pb, sem = opened(nc, s, "rwn")
        cen, sq, rs = sb("cen", [P, RT, L]), sb("sq", [P, RT, L]), sb("rs", [P, RT, L])
        ps, pv = pb("ps", [P, 2, L]), pb("pv", [P, 2, L])
        m_done, cen_ready, sq_ready, v_done = sem("m_done"), sem("cen"), sem("sq"), sem("v_done")
        inv_ready, rs_ready, steps = sem("inv"), sem("rs_ready"), sem("steps")
        block = s.enter_context(nc.Block())

        @block.tensor
        def _(pe):
            for c in range(RT):
                if c >= 2:
                    pe.wait_ge(cen_ready, c - 1)
                nc.tensor.matmul(ps[:, c % 2, :], e.heads[:, :], y[:, c, :], start=True, stop=True).then_inc(m_done, 1)
            for c in range(RT):
                pe.wait_ge(sq_ready, c + 1)
                if c >= 2:
                    pe.wait_ge(inv_ready, c - 1)
                nc.tensor.matmul(pv[:, c % 2, :], e.heads[:, :], sq[:, c, :], start=True, stop=True).then_inc(v_done, 1)

        @block.scalar
        def _(act):
            for c in range(RT):
                act.wait_ge(cen_ready, c + 1)
                nc.scalar.activation(sq[:, c, :], cen[:, c, :], ACT.Square).then_inc(sq_ready, 1)
            for c in range(RT):
                act.wait_ge(inv_ready, c + 1)
                nc.scalar.activation(rs[:, c, :], rs[:, c, :], ACT.Sqrt).then_inc(rs_ready, 1)

        @block.vector
        def _(dve):
            st = Steps(steps)

            def then(ins):
                dve.wait_ge(steps, st.mark(ins))

            for c in range(RT):
                dve.wait_ge(m_done, c + 1)
                nc.vector.scalar_tensor_tensor(cen[:, c, :], ps[:, c % 2, :], -1.0 / CH, y[:, c, :],
                                               ALU.mult, ALU.add).then_inc(cen_ready, 1)
            for c in range(RT):
                dve.wait_ge(v_done, c + 1)
                then(nc.vector.tensor_scalar(rs[:, c, :], pv[:, c % 2, :], 1.0 / CH, GN_EPS, ALU.mult, ALU.add))
                nc.vector.reciprocal(rs[:, c, :], rs[:, c, :]).then_inc(inv_ready, 1)
            for c in range(RT):
                dve.wait_ge(rs_ready, c + 1)
                dve.wait_ge(cen_ready, c + 1)
                then(nc.vector.scalar_tensor_tensor(cen[:, c, :], cen[:, c, :], col(e, "rw_ln_w", c), rs[:, c, :],
                                                    ALU.mult, ALU.mult))
                then(nc.vector.scalar_tensor_tensor(cen[:, c, :], cen[:, c, :], col(e, "rw_ln_b", c),
                                                    bonus[:, c, :], ALU.add, ALU.add))
                nc.vector.tensor_tensor(y[:, c, :], cen[:, c, :], g[:, c, :], ALU.mult)


def rwkv_branch(nc, e, I, merged):
    with ExitStack() as s:
        keep = lambda name, shape: s.enter_context(nc.sbuf_tensor(f"rw_{name}", shape, F32))
        y = keep("y", [P, RT, L])
        with ExitStack() as s2:
            part = lambda name, shape: s2.enter_context(nc.sbuf_tensor(f"rw_{name}", shape, F32))
            rkv = part("rkv", [P, 3 * RT, L])
            lora = y
            with ExitStack() as s3:
                rwkv_inputs(nc, e, I, two_parts(nc, s3, "rw_h", DT), rkv, lora)
            lw, a = part("lw", [P, 2, RT, L]), part("a", [P, 2, RT, L])
            g, kk, bonus = (part(n, [P, RT, L]) for n in ("g", "kk", "bonus"))
            rwkv_features(nc, e, I, rkv, lora, lw, a, g, kk, bonus)
            with ExitStack() as s3:
                scan = lambda name, shape: s3.enter_context(nc.sbuf_tensor(f"rw_{name}", shape, F32))
                gt = scan("gt", [P, RT, HCH, 2, P])
                kbt, vu, xt, kb = (scan(n, [P, RT, HCH, P]) for n in ("kbt", "vu", "xt", "kb"))
                place = [scan(f"place{i}", [P, RT, HCH, P]) for i in range(2)]
                pend = [scan(f"pend{i}", [P, RT, HCH]) for i in range(2)]
                state = scan("state", [P, RT, CH])
                bv = scan("bv", [P, HCH, RT, CH])
                reset, scan_mask = scan("reset", [P, L]), scan("scan_mask", [P, 2, P])
                levels = scan("levels", [P, 2, LEVELS, P])
                load_tables(nc, "scan_tables", [
                    (reset[:, :], I["c_reset"]),
                    (scan_mask[:, :, :], I["c_scan"].rearrange("p (d t) -> p d t", d=2)),
                    (levels[:, :, :, :], I["c_levels"].rearrange("p (a k t) -> p a k t", a=2, k=LEVELS))])
                units = [(0, 0), (0, 1), (1, 1), (1, 0)]
                inputs = lambda n: (rkv, lw, a, kk, reset, place[n % 2], kb, pend[n % 2])
                rwkv_scaled(nc, e, *units[0], *inputs(0))
                for n, (d, half) in enumerate(units):
                    ar = place[n % 2]
                    rwkv_matrices(nc, e, d, half, rkv, ar, kb, scan_mask, gt, kbt, vu, bv)
                    rwkv_inverse(nc, e, d, half, gt, levels, xt, kb, place[(n + 1) % 2])
                    following = (*units[n + 1], 1, *inputs(n + 1)) if n + 1 < len(units) else None
                    rwkv_chain(nc, e, d, half, state, ar, gt, kbt, xt, vu, bv, pend[n % 2], y, following)
            rwkv_group_norm(nc, e, y, bonus, g)
        h = two_parts(nc, s, "rw_h3", DT)
        gated_output(nc, e, "rw", I["w_in"][:, N_HY + N_RW + D:N_HY + N_RW + 2 * D], h,
                     normed(nc, e, e.x, DT, h, lambda k: col(e, "mix_norm", k)), I["rw_out"], RT, y, merged, 1)



def silu_condition(nc, e, cond):
    with ExitStack() as s:
        s.enter_context(nc.Block()).scalar(
            lambda act: nc.scalar.activation(cond[:, :], e.cols[:, COL["c_2"]:COL["c_2"] + DT], ACT.Silu))


def add_condition_bias(nc, e):
    with ExitStack() as s:
        block = s.enter_context(nc.Block())

        @block.vector
        def _(dve):
            for dst, name, at in ((e.ada[:, 0, :], "ada_b_2", 0), (e.kvada[:, :], "kv_ada_b_2", 0)):
                n = dst.shape[-1]
                nc.vector.tensor_tensor(dst, dst, e.cols[:, COL[name] + at:COL[name] + at + n], ALU.add)


def add_condition_bias_1(nc, e):
    with ExitStack() as s:
        block = s.enter_context(nc.Block())

        @block.vector
        def _(dve):
            at = COL["ada_b_2"] + 6 * DT
            nc.vector.tensor_tensor(e.ada[:, 1, :], e.ada[:, 1, :], e.cols[:, at:at + 6 * DT], ALU.add)


def mlstm_gates(nc, e, I, h, rows, ccol):
    H = A_HEADS
    with ExitStack() as s:
        sb, pb, sem = opened(nc, s, "mg")
        raw = sb("raw", [P, 2, DT, P])
        wh, wl = (s.enter_context(nc.sbuf_tensor(f"mg_{n}", [P, 2, DT, P], F32R)) for n in ("wh", "wl"))
        ones, zeros = sb("ones", [H, L]), sb("zeros", [H, L])
        ig, f, af, m, F, M = (sb(n, [H, L]) for n in ("ig", "f", "af", "m", "cf", "mx"))
        pi, pf, pc = pb("pi", [P, L]), pb("pf", [P, L]), pb("pc", [P, TT, H])
        loaded, mm_done, act_done, dve_done = sem("loaded"), sem("mm_done"), sem("act_done"), sem("dve_done")
        steps, turned, hi_ready, lo_ready = sem("steps"), sem("turned"), sem("hi_ready"), sem("lo_ready")
        xh, xl = h
        block = s.enter_context(nc.Block())
        at = 2 * H * A_QK + A_HEADS * P

        @block.sync
        def _(sp):
            for g in range(2):
                sp.dma_start(raw[:, g, :, :], I["a_w_in_2"][0, :, at + g * H:at + g * H + P]
                             .rearrange("(k p) n -> p k n", p=P)).then_inc(loaded, 16)

        @block.tensor
        def _(pe):
            pe.wait_ge(lo_ready, 1)
            for g, ps in enumerate((pi, pf)):
                for k in range(DT):
                    nc.tensor.matmul(ps[:, :], wh[:, g, k, :], xh[:, k, :], start=k == 0, stop=False)
                    nc.tensor.matmul(ps[:, :], wh[:, g, k, :], xl[:, k, :], start=False, stop=False)
                    last = nc.tensor.matmul(ps[:, :], wl[:, g, k, :], xh[:, k, :], start=False, stop=k == DT - 1)
                last.then_inc(mm_done, 1)
            pe.wait_ge(dve_done, 2)
            for t in range(TT):
                last = nc.tensor.transpose(pc[:, t, :], ig[:, t * P:(t + 1) * P], e.ident[0:H, 0:H])
            last.then_inc(turned, 1)

        @block.scalar
        def _(act):
            act.wait_ge(loaded, 32)
            nc.scalar.activation(wh[:, :, :, :], raw[:, :, :, :], ACT.Copy).then_inc(hi_ready, 1)
            b = COL["a_gate_b_2"]
            act.wait_ge(mm_done, 1)
            nc.scalar.activation(ig[:, :], pi[0:H, :], ACT.Identity, bias=e.cols[0:H, b:b + 1]).then_inc(act_done, 1)
            act.wait_ge(mm_done, 2)
            nc.scalar.activation(f[:, :], pf[0:H, :], ACT.Identity, bias=e.cols[0:H, b + 1:b + 2]).then_inc(act_done, 1)
            act.wait_ge(act_done, 2)
            nc.scalar.activation(af[:, :], f[:, :], ACT.Abs).then_inc(act_done, 1)
            act.wait_ge(act_done, 3)
            nc.scalar.activation(af[:, :], af[:, :], ACT.Exp, scale=-1.0).then_inc(act_done, 1)
            act.wait_ge(act_done, 4)
            nc.scalar.activation(af[:, :], af[:, :], ACT.Ln, bias=1.0).then_inc(act_done, 1)
            act.wait_ge(dve_done, 1)
            nc.scalar.activation(rows[:, 1, :], m[:, :], ACT.Exp, scale=-1.0)
            act.wait_ge(turned, 1)
            nc.scalar.activation(ccol[:, :, :], pc[:, :, :], ACT.Copy)

        @block.vector
        def _(dve):
            st = Steps(steps)

            def then(ins):
                dve.wait_ge(steps, st.mark(ins))

            dve.wait_ge(hi_ready, 1)
            nc.vector.tensor_tensor(wl[:, :, :, :], raw[:, :, :, :], wh[:, :, :, :].bitcast(F32), ALU.subtract)\
                .then_inc(lo_ready, 1)
            then(nc.vector.memset(ones[:, :], 1.0))
            then(nc.vector.memset(zeros[:, :], 0.0))
            dve.wait_ge(act_done, 5)
            then(nc.vector.scalar_tensor_tensor(f[:, :], f[:, :], 0.0, af[:, :], ALU.min, ALU.subtract))
            then(nc.vector.tensor_tensor_scan(F[:, :], ones[:, :], f[:, :], 0.0, ALU.mult, ALU.add))
            then(nc.vector.tensor_tensor(ig[:, :], ig[:, :], F[:, :], ALU.subtract))
            then(nc.vector.tensor_tensor_scan(M[:, :], zeros[:, :], ig[:, :], 0.0, ALU.add, ALU.max))
            nc.vector.tensor_tensor(m[:, :], F[:, :], M[:, :], ALU.add).then_inc(dve_done, 1)
            nc.vector.tensor_scalar(rows[:, 0, :], M[:, :], -1.0, None, ALU.mult).then_inc(dve_done, 1)


def mlstm_heads(nc, e, I, qk, v, rows, ccol, out):
    H = A_HEADS
    with ExitStack() as s:
        sb, pb, sem = opened(nc, s, "mh")
        sel, causal = sb("sel", [H, H, P]), sb("causal", [P, P])
        dT, pT = sb("dT", [P, 3, L]), sb("pT", [P, 3, L])
        negM, floor, den = sb("negM", [P, 2, L]), sb("floor", [P, 2, L]), sb("den", [P, 2, L])
        pm, pe_, pS, pn, pd = (pb("pm", [P, L]), pb("pe", [P, L]), pb("pS", [P, 2, L]),
                               pb("pn", [P, 2, L]), pb("pd", [P, 2, L]))
        loaded, rows_done, rows_out, s_done = sem("loaded"), sem("rows_done"), sem("rows_out"), sem("s_done")
        arg_ready, d_ready, p_ready, p_masked = sem("arg"), sem("d_ready"), sem("p_ready"), sem("p_masked")
        used, head_done, abs_ready, out_done, steps = (sem("used"), sem("head_done"), sem("abs"),
                                                       sem("out_done"), sem("steps"))
        block = s.enter_context(nc.Block())
        units = [(h, j) for h in range(H) for j in range(TT)]

        @block.sync
        def _(sp):
            sp.dma_start(sel[:, :, :], I["c_sel"].rearrange("k (h p) -> k h p", h=H)).then_inc(loaded, 16)
            sp.dma_start(causal[:, :], I["c_causal"]).then_inc(loaded, 16)

        @block.tensor
        def _(pe):
            def broadcast(h):
                if h > 0:
                    pe.wait_ge(rows_out, 2 * h)
                nc.tensor.matmul(pm[:, :], sel[:, h, :], rows[:, 0, :], start=True, stop=True)
                nc.tensor.matmul(pe_[:, :], sel[:, h, :], rows[:, 1, :], start=True, stop=True)\
                    .then_inc(rows_done, 1)

            def scores(n):
                h, j = units[n]
                hs = slice(64 * (h % 2), 64 * (h % 2) + 64)
                if n >= 2:
                    pe.wait_ge(p_ready, n - 1)
                nc.tensor.matmul(pS[:, n % 2, j * P:L], qk[hs, H // 2 + h // 2, j * P:(j + 1) * P],
                                 qk[hs, h // 2, j * P:L], start=True, stop=True).then_inc(s_done, 1)

            pe.wait_ge(loaded, 32)
            broadcast(0)
            scores(0)
            scores(1)
            for n, (h, j) in enumerate(units):
                if j == 1 and h + 1 < H:
                    broadcast(h + 1)
                if n + 2 < len(units):
                    scores(n + 2)
                pe.wait_ge(p_masked, n + 1)
                if j == 0 and h >= 2:
                    pe.wait_ge(out_done, h - 1)
                first, last_j = j == 0, j == TT - 1
                nc.tensor.matmul(pn[:, h % 2, j * P:L], v[:, j, h * P:(h + 1) * P], pT[:, n % 3, j * P:L],
                                 start=first, stop=last_j)
                last = nc.tensor.matmul(pd[:, h % 2, j * P:L], e.ones[:, :], pT[:, n % 3, j * P:L],
                                        start=first, stop=last_j)
                last.then_inc(used, 1)

        @block.scalar
        def _(act):
            def take_rows(h):
                act.wait_ge(rows_done, h + 1)
                if h >= 2:
                    act.wait_ge(out_done, h - 1)
                nc.scalar.activation(negM[:, h % 2, :], pm[:, :], ACT.Copy).then_inc(rows_out, 1)
                nc.scalar.activation(floor[:, h % 2, :], pe_[:, :], ACT.Copy).then_inc(rows_out, 1)

            def take_sum(h):
                act.wait_ge(used, TT * (h + 1))
                nc.scalar.activation(den[:, h % 2, :], pd[:, h % 2, :], ACT.Abs).then_inc(abs_ready, 1)

            take_rows(0)
            for n, (h, j) in enumerate(units):
                act.wait_ge(arg_ready, n + 1)
                nc.scalar.activation(dT[:, n % 3, j * P:L], dT[:, n % 3, j * P:L], ACT.Exp).then_inc(d_ready, 1)
                if j == 1 and h > 0:
                    take_sum(h - 1)
                if j == 2 and h + 1 < H:
                    take_rows(h + 1)
            take_sum(H - 1)

        @block.vector
        def _(dve):
            st = Steps(steps)

            def then(ins):
                dve.wait_ge(steps, st.mark(ins))

            def finish(h):
                d = den[:, h % 2, :]
                dve.wait_ge(abs_ready, h + 1)
                then(nc.vector.tensor_tensor(d, d, floor[:, h % 2, :], ALU.max))
                then(nc.vector.reciprocal(d, d))
                nc.vector.tensor_tensor(out[:, h, :], pn[:, h % 2, :], d, ALU.mult).then_inc(out_done, 1)

            def argument(n):
                h, j = units[n]
                if j == 0:
                    dve.wait_ge(rows_out, 2 * h + 2)
                if n >= 3:
                    dve.wait_ge(p_ready, n - 2)
                nc.vector.tensor_scalar(dT[:, n % 3, j * P:L], negM[:, h % 2, j * P:L], ccol[:, j, h:h + 1], 0.0,
                                        ALU.add, ALU.min).then_inc(arg_ready, 1)

            argument(0)
            argument(1)
            for n, (h, j) in enumerate(units):
                dve.wait_ge(d_ready, n + 1)
                dve.wait_ge(s_done, n + 1)
                if n >= 3:
                    dve.wait_ge(used, n - 2)
                nc.vector.scalar_tensor_tensor(pT[:, n % 3, j * P:L], pS[:, n % 2, j * P:L], A_QK**-0.5,
                                               dT[:, n % 3, j * P:L], ALU.mult, ALU.mult).then_inc(p_ready, 1)
                if n + 2 < len(units):
                    argument(n + 2)
                if j == 1 and h > 0:
                    finish(h - 1)
            finish(H - 1)

        @block.gpsimd
        def _(pool):
            pool.wait_ge(loaded, 32)
            for n, (h, j) in enumerate(units):
                pool.wait_ge(p_ready, n + 1)
                diag = pT[:, n % 3, j * P:(j + 1) * P]
                nc.gpsimd.tensor_tensor(diag, diag, causal[:, :], ALU.mult).then_inc(p_masked, 1)


def head_norm_gate(nc, e, hh, og):
    n = A_HEADS
    with ExitStack() as s:
        sb, pb, sem = opened(nc, s, "hn")
        sq, rs = sb("sq", [P, 2, L]), sb("rs", [P, 2, L])
        ps = pb("ps", [P, 2, L])
        sq_ready, v_done, inv_ready, rs_ready, done, steps = (sem("sq"), sem("v_done"), sem("inv"),
                                                              sem("rs_ready"), sem("done"), sem("steps"))
        block = s.enter_context(nc.Block())

        @block.tensor
        def _(pe):
            for k in range(n):
                pe.wait_ge(sq_ready, k + 1)
                if k >= 2:
                    pe.wait_ge(inv_ready, k - 1)
                nc.tensor.matmul(ps[:, k % 2, :], e.ones[:, :], sq[:, k % 2, :], start=True, stop=True)\
                    .then_inc(v_done, 1)

        @block.scalar
        def _(act):
            for k in range(n):
                if k >= 2:
                    act.wait_ge(v_done, k - 1)
                nc.scalar.activation(sq[:, k % 2, :], hh[:, k, :], ACT.Square).then_inc(sq_ready, 1)
                if k >= 1:
                    act.wait_ge(inv_ready, k)
                    nc.scalar.activation(rs[:, (k - 1) % 2, :], rs[:, (k - 1) % 2, :], ACT.Sqrt).then_inc(rs_ready, 1)
            act.wait_ge(inv_ready, n)
            nc.scalar.activation(rs[:, (n - 1) % 2, :], rs[:, (n - 1) % 2, :], ACT.Sqrt).then_inc(rs_ready, 1)

        @block.vector
        def _(dve):
            st = Steps(steps)

            def then(ins):
                dve.wait_ge(steps, st.mark(ins))

            def finish(k):
                dve.wait_ge(rs_ready, k + 1)
                then(nc.vector.scalar_tensor_tensor(hh[:, k, :], hh[:, k, :], col(e, "a_head_g_2", k),
                                                    rs[:, k % 2, :], ALU.mult, ALU.mult))
                then(nc.vector.tensor_tensor(hh[:, k, :], hh[:, k, :], og[:, k, :], ALU.mult))

            for k in range(n):
                dve.wait_ge(v_done, k + 1)
                then(nc.vector.tensor_scalar(rs[:, k % 2, :], ps[:, k % 2, :], 1.0 / P, EPS, ALU.mult, ALU.add))
                nc.vector.reciprocal(rs[:, k % 2, :], rs[:, k % 2, :]).then_inc(inv_ready, 1)
                if k >= 1:
                    finish(k - 1)
            finish(n - 1)


def mlstm_mixer(nc, e, I, h, before, y, side):
    H = A_HEADS
    with ExitStack() as s:
        part = lambda name, shape: s.enter_context(nc.sbuf_tensor(f"ml_{name}", shape, F32))
        w = I["a_w_in_2"][0]
        qk, v = part("qk", [P, H, L]), part("v", [P, TT, H * P])
        rows, ccol = part("rows", [H, 2, L]), part("ccol", [P, TT, H])
        gemm(nc, e, "ml_qk", w[:, 0:2 * H * A_QK], DT, h, 2, 2, 2, "copy", dst=qk, before=before)
        gemm_tokens(nc, e, "ml_v", w, DT, h, 2, v, lambda c: [2 * H * A_QK + 512 * c])
        mlstm_gates(nc, e, I, h, rows, ccol)
        at = 2 * H * A_QK + H * P + 2 * H
        og = part("og", [P, H, L])
        gemm(nc, e, "ml_og", w[:, at:at + H * P], DT, h, 4, 2, 1, "copy", dst=og, func=ACT.Sigmoid, side=side)
        mlstm_heads(nc, e, I, qk, v, rows, ccol, y)
        head_norm_gate(nc, e, y, og)
        hp = two_parts(nc, s, "ml_hp", H)
        gemm(nc, e, "ml_out", I["a_w_out_2"][0], H, hp, 2, 2, 2, "copy", dst=y, before=cut(nc, e, y, H, hp))


def rope_tables(nc, e, I, cosr, sinr):
    with ExitStack() as s:
        sb, pb, sem = opened(nc, s, "rope")
        pos = s.enter_context(nc.sbuf_tensor("rope_pos", [P, L], mybir.dt.int32))
        inv, ang, n, r = sb("inv", [P, 1]), sb("ang", [P, L]), sb("n", [P, L]), sb("r", [P, L])
        loaded, steps, r_ready, abs_ready, c_ready = sem("loaded"), sem("steps"), sem("r"), sem("abs"), sem("c")
        block = s.enter_context(nc.Block())

        @block.sync
        def _(sp):
            sp.dma_start(pos[:, :], I["positions_2"][0, :].partition_broadcast(P)).then_inc(loaded, 16)
            sp.dma_start(inv[:, :], I["c_invfreq"]).then_inc(loaded, 16)

        @block.vector
        def _(dve):
            st = Steps(steps)

            def then(ins):
                dve.wait_ge(steps, st.mark(ins))

            dve.wait_ge(loaded, 32)
            then(nc.vector.tensor_copy(ang[:, :], pos[:, :]))
            then(nc.vector.tensor_scalar(ang[:, :], ang[:, :], inv[:, 0:1], None, ALU.mult))
            then(nc.vector.tensor_scalar(n[:, :], ang[:, :], 1 / TWO_PI, ROUND, ALU.mult, ALU.add))
            then(nc.vector.tensor_scalar(n[:, :], n[:, :], ROUND, None, ALU.subtract))
            for part in (PI_A, PI_B, PI_C):
                then(nc.vector.scalar_tensor_tensor(ang[:, :], n[:, :], -part, ang[:, :], ALU.mult, ALU.add))
            nc.vector.tensor_scalar(ang[:, :], ang[:, :], math.pi, -math.pi, ALU.min, ALU.max).then_inc(r_ready, 1)
            dve.wait_ge(abs_ready, 1)
            nc.vector.tensor_scalar(r[:, :], r[:, :], -1.0, math.pi / 2, ALU.mult, ALU.add).then_inc(c_ready, 1)

        @block.scalar
        def _(act):
            act.wait_ge(r_ready, 1)
            nc.scalar.activation(sinr[:, :], ang[:, :], ACT.Sin)
            nc.scalar.activation(r[:, :], ang[:, :], ACT.Abs).then_inc(abs_ready, 1)
            act.wait_ge(c_ready, 1)
            nc.scalar.activation(cosr[:, :], r[:, :], ACT.Sin)


def rotate(nc, dve, steps, st, p1, p2, cosr, sinr, parts, t1, t2, t3, t4):
    cs, sn = cosr[0:parts, :], sinr[0:parts, :]
    st.mark(nc.vector.tensor_tensor(t1, p1, cs, ALU.mult))
    st.mark(nc.vector.tensor_tensor(t2, p2, sn, ALU.mult))
    st.mark(nc.vector.tensor_tensor(t3, p2, cs, ALU.mult))
    dve.wait_ge(steps, st.mark(nc.vector.tensor_tensor(t4, p1, sn, ALU.mult)))


def three_passes(nc, ps, wh, wl, xh, xl, kt):
    for k in range(kt):
        nc.tensor.matmul(ps, wh(k), xh(k), start=k == 0, stop=False)
        nc.tensor.matmul(ps, wh(k), xl(k), start=False, stop=False)
        last = nc.tensor.matmul(ps, wl(k), xh(k), start=False, stop=k == kt - 1)
    return last


def mla_keys_a(nc, e, I, h, before, ckv, cosr, sinr, kr):
    with ExitStack() as s:
        sb, pb, sem = opened(nc, s, "ka")
        raw = sb("raw", [P, DT, 4, P])
        wh, wl = (s.enter_context(nc.sbuf_tensor(f"ka_{n}", [P, DT, 4, P], F32R)) for n in ("wh", "wl"))
        t1, t2, t3, t4 = (sb(n, [32, L]) for n in ("t1", "t2", "t3", "t4"))
        ps = pb("ps", [P, 4, L])
        loaded, hi_ready, lo_ready = sem("loaded"), sem("hi_ready"), sem("lo_ready")
        c_done, r_done, steps = sem("c_done"), sem("r_done"), sem("steps")
        first = before(sb, pb, sem)
        block = s.enter_context(nc.Block())

        @block.sync
        def _(sp):
            w = I["kv_w_a_2"].rearrange("(k p) n -> p k n", p=P)
            sp.dma_start(raw[:, :, 0:2, :], w[:, :, 0:2 * P].rearrange("p k (c n) -> p k c n", c=2)).then_inc(loaded, 16)
            for half in range(2):
                at = KV_LORA + 32 * half
                sp.dma_start(raw[:, :, 2 + half, 0:32], w[:, :, at:at + 32]).then_inc(loaded, 16)
                sp.dma_start(raw[:, :, 2 + half, 32:P], w[:, :, 0:P - 32]).then_inc(loaded, 16)

        @block.tensor
        def _(pe):
            first.pe(pe)
            pe.wait_ge(first.ready, first.count)
            pe.wait_ge(lo_ready, 1)
            for j in (2, 3, 0, 1):
                three_passes(nc, ps[:, j, :], lambda k: wh[:, k, j, :], lambda k: wl[:, k, j, :],
                             lambda k: h[0][:, k, :], lambda k: h[1][:, k, :], DT)\
                    .then_inc(r_done if j >= 2 else c_done, 1)

        @block.scalar
        def _(act):
            first.act[0](act)
            act.wait_ge(loaded, 16 * 5)
            nc.scalar.activation(wh[:, :, :, :], raw[:, :, :, :], ACT.Copy).then_inc(hi_ready, 1)
            first.act[1](act)
            for j in range(2):
                act.wait_ge(c_done, j + 1)
                nc.scalar.activation(ckv[:, j, :], ps[:, j, :], ACT.Copy)

        @block.vector
        def _(dve):
            first.dve[0](dve)
            dve.wait_ge(hi_ready, 1)
            nc.vector.tensor_tensor(wl[:, :, :, :], raw[:, :, :, :], wh[:, :, :, :].bitcast(F32), ALU.subtract)\
                .then_inc(lo_ready, 1)
            first.dve[1](dve)
            st = Steps(steps)
            dve.wait_ge(r_done, 2)
            rotate(nc, dve, steps, st, ps[0:32, 2, :], ps[0:32, 3, :], cosr, sinr, 32,
                   t1[:, :], t2[:, :], t3[:, :], t4[:, :])
            nc.vector.tensor_tensor(kr[0:32, :], t1[:, :], t2[:, :], ALU.subtract)
            nc.vector.tensor_tensor(kr[32:64, :], t3[:, :], t4[:, :], ALU.add)


def mla_queries(nc, e, I, cq, before, cosr, sinr, qn, qr):
    H, KT = B_HEADS, Q_LORA // P
    with ExitStack() as s:
        sb, pb, sem = opened(nc, s, "qb")
        raw = sb("raw", [P, KT, H, NOPE + ROPE])
        rope = sb("rope", [P, KT, 2, H, 32])
        wh, wl = (s.enter_context(nc.sbuf_tensor(f"qb_{n}", [P, KT, H, NOPE], F32R)) for n in ("wh", "wl"))
        rh, rl = (s.enter_context(nc.sbuf_tensor(f"qb_{n}", [P, KT, 2, H, 32], F32R)) for n in ("rh", "rl"))
        t = sb("t", [P, 4, L])
        pn, pr = pb("pn", [P, 2, L]), pb("pr", [P, 2, 2, L])
        loaded, sorted_, n_done, n_out = sem("loaded"), sem("sorted"), sem("n_done"), sem("n_out")
        hi_ready, lo_ready, r_done, steps = sem("hi_ready"), sem("lo_ready"), sem("r_done"), sem("steps")
        first = before(sb, pb, sem)
        block = s.enter_context(nc.Block())

        @block.sync
        def _(sp):
            sp.dma_start(raw[:, :, :, :], I["b_w_q_b_2"][0].rearrange("(k p) (h n) -> p k h n", p=P, h=H))\
                .then_inc(loaded, 16)

        @block.gpsimd
        def _(pool):
            pool.wait_ge(loaded, 16)
            for k in range(KT):
                for half in range(2):
                    at = NOPE + 32 * half
                    nc.gpsimd.tensor_copy(rope[:, k, half, :, :], raw[:, k, :, at:at + 32]).then_inc(sorted_, 1)

        @block.tensor
        def _(pe):
            first.pe(pe)
            pe.wait_ge(first.ready, first.count)
            xh, xl = (lambda k: cq[0][:, k, :]), (lambda k: cq[1][:, k, :])
            pe.wait_ge(lo_ready, 2)
            for g in range(2):
                for half in range(2):
                    of = lambda w: (lambda k: w[:, k, half, 4 * g:4 * g + 4, :].rearrange("p h n -> p (h n)"))
                    last = three_passes(nc, pr[:, g, half, :], of(rh), of(rl), xh, xl, KT)
                last.then_inc(r_done, 1)
            for h in range(H):
                if h >= 2:
                    pe.wait_ge(n_out, h - 1)
                three_passes(nc, pn[:, h % 2, :], lambda k: wh[:, k, h, :], lambda k: wl[:, k, h, :], xh, xl, KT)\
                    .then_inc(n_done, 1)

        @block.scalar
        def _(act):
            first.act[0](act)
            act.wait_ge(loaded, 16)
            for k in range(KT):
                ins = nc.scalar.activation(wh[:, k, :, :], raw[:, k, :, 0:NOPE], ACT.Copy)
            ins.then_inc(hi_ready, 1)
            act.wait_ge(sorted_, 2 * KT)
            nc.scalar.activation(rh[:, :, :, :, :], rope[:, :, :, :, :], ACT.Copy).then_inc(hi_ready, 1)
            first.act[1](act)
            for h in range(H):
                act.wait_ge(n_done, h + 1)
                nc.scalar.activation(qn[:, h, :], pn[:, h % 2, :], ACT.Copy).then_inc(n_out, 1)

        @block.vector
        def _(dve):
            first.dve[0](dve)
            dve.wait_ge(hi_ready, 1)
            for k in range(KT):
                ins = nc.vector.tensor_tensor(wl[:, k, :, :], raw[:, k, :, 0:NOPE], wh[:, k, :, :].bitcast(F32),
                                              ALU.subtract)
            ins.then_inc(lo_ready, 1)
            dve.wait_ge(hi_ready, 2)
            nc.vector.tensor_tensor(rl[:, :, :, :, :], rope[:, :, :, :, :], rh[:, :, :, :, :].bitcast(F32),
                                    ALU.subtract).then_inc(lo_ready, 1)
            first.dve[1](dve)
            st = Steps(steps)
            for g in range(2):
                dve.wait_ge(r_done, g + 1)
                rotate(nc, dve, steps, st, pr[:, g, 0, :], pr[:, g, 1, :], cosr, sinr, P,
                       t[:, 0, :], t[:, 1, :], t[:, 2, :], t[:, 3, :])
                for i in range(4):
                    hp = slice(32 * i, 32 * i + 32)
                    st.mark(nc.vector.tensor_tensor(qr[0:32, 4 * g + i, :], t[hp, 0, :], t[hp, 1, :], ALU.subtract))
                    st.mark(nc.vector.tensor_tensor(qr[32:64, 4 * g + i, :], t[hp, 2, :], t[hp, 3, :], ALU.add))
                dve.wait_ge(steps, st.n)


def mla_attention(nc, e, I, qn, qr, kn, kr, v, out):
    H = B_HEADS
    scale = (NOPE + ROPE) ** -0.5
    with ExitStack() as s:
        sb, pb, sem = opened(nc, s, "at")
        mask = sb("mask", [P, P])
        mx, nm, total, inv = (sb(n, [P, 3]) for n in ("mx", "nm", "total", "inv"))
        p, pT = sb("p", [P, 3, L]), sb("pT", [P, 3, L])
        pS, pt, po = pb("pS", [P, 3, L]), pb("pt", [P, 3, L]), pb("po", [P, 2, L])
        loaded, s_done, nm_ready, p_ready = sem("loaded"), sem("s_done"), sem("nm"), sem("p_ready")
        p_normed, turned, pT_ready, used = sem("p_normed"), sem("turned"), sem("pT_ready"), sem("used")
        out_done, steps = sem("out_done"), sem("steps")
        block = s.enter_context(nc.Block())
        units = [(h, i) for h in range(H) for i in range(TT)]
        N = len(units)

        @block.sync
        def _(sp):
            sp.dma_start(mask[:, :], I["c_causal_row"]).then_inc(loaded, 16)

        @block.tensor
        def _(pe):
            def scores(n):
                h, i = units[n]
                w = (i + 1) * P
                if n >= 3:
                    pe.wait_ge(p_ready, n - 2)
                ts = slice(i * P, (i + 1) * P)
                nc.tensor.matmul(pS[:, n % 3, 0:w], qn[:, h, ts], kn[:, h, 0:w], start=True, stop=False)
                nc.tensor.matmul(pS[:, n % 3, 0:w], qr[0:ROPE, h, ts], kr[0:ROPE, 0:w], start=False, stop=True)\
                    .then_inc(s_done, 1)

            def turn(n):
                h, i = units[n]
                pe.wait_ge(p_normed, n + 1)
                if n >= 3:
                    pe.wait_ge(pT_ready, n - 2)
                for j in range(i + 1):
                    js = slice(j * P, (j + 1) * P)
                    last = nc.tensor.transpose(pt[:, n % 3, js], p[:, n % 3, js], e.ident[:, :])
                last.then_inc(turned, 1)

            def values(n):
                h, i = units[n]
                pe.wait_ge(pT_ready, n + 1)
                if i == 0 and h >= 2:
                    pe.wait_ge(out_done, h - 1)
                for j in range(i + 1):
                    last = nc.tensor.matmul(po[:, h % 2, i * P:(i + 1) * P], v[:, j, h * P:(h + 1) * P],
                                            pT[:, n % 3, j * P:(j + 1) * P], start=j == 0, stop=j == i)
                last.then_inc(used, 1)

            for n in range(N + 3):
                if n < N:
                    scores(n)
                if 2 <= n < N + 2:
                    turn(n - 2)
                if n >= 3:
                    values(n - 3)

        @block.vector
        def _(dve):
            st = Steps(steps)

            def then(ins):
                dve.wait_ge(steps, st.mark(ins))

            def maximum(n):
                h, i = units[n]
                b = n % 3
                dve.wait_ge(s_done, n + 1)
                diag = pS[:, b, i * P:(i + 1) * P]
                then(nc.vector.tensor_tensor(diag, diag, mask[:, :], ALU.add))
                then(nc.vector.reduce_max(mx[:, b:b + 1], pS[:, b, 0:(i + 1) * P], AX.X))
                if n >= 3:
                    dve.wait_ge(p_ready, n - 2)
                nc.vector.tensor_scalar(nm[:, b:b + 1], mx[:, b:b + 1], -scale, None, ALU.mult).then_inc(nm_ready, 1)

            def normalise(n):
                h, i = units[n]
                b = n % 3
                dve.wait_ge(p_ready, n + 1)
                then(nc.vector.reciprocal(inv[:, b:b + 1], total[:, b:b + 1]))
                nc.vector.tensor_scalar(p[:, b, 0:(i + 1) * P], p[:, b, 0:(i + 1) * P], inv[:, b:b + 1], None,
                                        ALU.mult).then_inc(p_normed, 1)

            dve.wait_ge(loaded, 16)
            maximum(0)
            maximum(1)
            for n in range(N):
                normalise(n)
                if n + 2 < N:
                    maximum(n + 2)

        @block.scalar
        def _(act):
            def copies(n):
                h, i = units[n]
                act.wait_ge(turned, n + 1)
                if n >= 3:
                    act.wait_ge(used, n - 2)
                nc.scalar.activation(pT[:, n % 3, 0:(i + 1) * P], pt[:, n % 3, 0:(i + 1) * P], ACT.Copy)\
                    .then_inc(pT_ready, 1)

            def take_out(n):
                h, i = units[n]
                if i == TT - 1:
                    act.wait_ge(used, n + 1)
                    nc.scalar.activation(out[:, h, :], po[:, h % 2, :], ACT.Copy).then_inc(out_done, 1)

            for n in range(N):
                h, i = units[n]
                b = n % 3
                act.wait_ge(nm_ready, n + 1)
                if n >= 3:
                    act.wait_ge(turned, n - 2)
                nc.scalar.activation(p[:, b, 0:(i + 1) * P], pS[:, b, 0:(i + 1) * P], ACT.Exp, bias=nm[:, b:b + 1],
                                     scale=scale, accum_out=total[:, b:b + 1]).then_inc(p_ready, 1)
                if n >= 2:
                    copies(n - 2)
                if n >= 4:
                    take_out(n - 4)
            copies(N - 2)
            copies(N - 1)
            for n in range(N - 4, N):
                take_out(n)


def mla_keys_b(nc, e, w_b, ckv, kn):
    H = B_HEADS
    with ExitStack() as s:
        sb, pb, sem = opened(nc, s, "kb")
        raw = sb("raw", [P, 2, H, P])
        wh, wl = (s.enter_context(nc.sbuf_tensor(f"kb_{n}", [P, 2, H, P], F32R)) for n in ("wh", "wl"))
        ps = pb("ps", [P, 2, L])
        loaded, hi_ready, lo_ready, done, taken = sem("loaded"), sem("hi_ready"), sem("lo_ready"), sem("done"), sem("taken")
        block = s.enter_context(nc.Block())
        k_of = w_b.rearrange("k (h two n) -> k h two n", h=H, two=2)

        @block.sync
        def _(sp):
            for k in range(2):
                sp.dma_start(raw[:, k, :, :], k_of[k * P:(k + 1) * P, :, 0, :]).then_inc(loaded, 16)

        @block.tensor
        def _(pe):
            pe.wait_ge(lo_ready, 1)
            for h in range(H):
                if h >= 2:
                    pe.wait_ge(taken, h - 1)
                three_passes(nc, ps[:, h % 2, :], lambda k: wh[:, k, h, :], lambda k: wl[:, k, h, :],
                             lambda k: ckv[0][:, k, :], lambda k: ckv[1][:, k, :], 2).then_inc(done, 1)

        @block.scalar
        def _(act):
            act.wait_ge(loaded, 32)
            nc.scalar.activation(wh[:, :, :, :], raw[:, :, :, :], ACT.Copy).then_inc(hi_ready, 1)
            for h in range(H):
                act.wait_ge(done, h + 1)
                nc.scalar.activation(kn[:, h, :], ps[:, h % 2, :], ACT.Copy).then_inc(taken, 1)

        @block.vector
        def _(dve):
            dve.wait_ge(hi_ready, 1)
            nc.vector.tensor_tensor(wl[:, :, :, :], raw[:, :, :, :], wh[:, :, :, :].bitcast(F32), ALU.subtract)\
                .then_inc(lo_ready, 1)


def prepare(nc, tag, before):
    with ExitStack() as s:
        sb, pb, sem = opened(nc, s, tag)
        first = before(sb, pb, sem)
        block = s.enter_context(nc.Block())
        block.scalar(lambda act: [part(act) for part in first.act])
        block.tensor(first.pe)
        block.vector(lambda dve: [part(dve) for part in first.dve])


def mla_mixer(nc, e, I, before, y):
    H = B_HEADS
    with ExitStack() as s:
        keep = lambda name, shape: s.enter_context(nc.sbuf_tensor(f"mla_{name}", shape, F32))
        cosr, sinr = keep("cos", [P, L]), keep("sin", [P, L])
        kr, cq = keep("kr", [ROPE, L]), keep("cq", [P, Q_LORA // P, L])
        rope_tables(nc, e, I, cosr, sinr)
        with ExitStack() as s2:
            h = two_parts(nc, s2, "mla_h", DT)
            gemm(nc, e, "q_a", I["b_w_q_a_2"][0], DT, h, 1, 3, 1, "copy", dst=cq, before=before(h))
        kn, v = keep("kn", [P, H, L]), keep("v", [P, TT, H * P])
        with ExitStack() as s2:
            ckv = s2.enter_context(nc.sbuf_tensor("mla_ckv", [P, 2, L], F32))
            with ExitStack() as s3:
                hk = two_parts(nc, s3, "mla_hk", DT)
                mla_keys_a(nc, e, I, hk, normed(nc, e, e.x, DT, hk, lambda k: col(e, "kv_norm_g_2", k),
                                                shift=lambda k: e.kvada[:, k:k + 1],
                                                scale=lambda k: e.kvada[:, DT + k:DT + k + 1]),
                           ckv, cosr, sinr, kr)
            cp = two_parts(nc, s2, "mla_cp", 2)
            prepare(nc, "kv_latent", normed(nc, e, ckv, 2, cp, lambda k: col(e, "kv_latent_g_2", k)))
            mla_keys_b(nc, e, I["kv_w_b_2"], cp, kn)
            gemm_tokens(nc, e, "kv_v", I["kv_w_b_2"], 2, cp, 2, v,
                        lambda c: [2 * P * (4 * c + i) + P for i in range(4)])
        qn, qr = keep("qn", [P, H, L]), keep("qr", [ROPE, H, L])
        with ExitStack() as s2:
            qp = two_parts(nc, s2, "mla_qp", Q_LORA // P)
            mla_queries(nc, e, I, qp, normed(nc, e, cq, Q_LORA // P, qp, lambda k: col(e, "b_q_latent_g_2", k)),
                        cosr, sinr, qn, qr)
        mla_attention(nc, e, I, qn, qr, kn, kr, v, y)
    with ExitStack() as s:
        yp = two_parts(nc, s, "mla_yp", H)
        gemm(nc, e, "mla_out", I["b_w_out_2"][0], H, yp, 2, 2, 2, "copy", dst=y, before=cut(nc, e, y, H, yp))


def second_block(nc, e, I, side):
    add_condition_bias(nc, e)
    for l in range(2):
        part = lambda i: (lambda k: e.ada[:, l, i * DT + k:i * DT + k + 1])
        gain = lambda i: (lambda k: col(e, "norm_g_2", (4 * l + i) * DT + k))
        with ExitStack() as s:
            y = s.enter_context(nc.sbuf_tensor(f"l{l}_y", [P, DT, L], F32))
            before = lambda h: normed(nc, e, e.x, DT, h, gain(0), shift=part(0), scale=part(1))
            if l == 0:
                with ExitStack() as s2:
                    h = two_parts(nc, s2, "ml_h", DT)
                    mlstm_mixer(nc, e, I, h, before(h), y, side)
                    add_condition_bias_1(nc, e)
            else:
                mla_mixer(nc, e, I, before, y)
            norm_stage(nc, e, f"l{l}_mixed", y, DT, y, gain(1), gate=part(2), onto=e.x)
            h = two_parts(nc, s, f"l{l}_h2", DT)
            ff = two_parts(nc, s, f"l{l}_ff", D_FF2 // P // 2)
            for half in range(2):
                cols = slice(half * D_FF2 // 2, (half + 1) * D_FF2 // 2)
                gemm(nc, e, f"l{l}_up{half}", I["mlp_w1_2"][l][:, cols], DT, h, 4, 2, 2, "sqrelu", dst=ff,
                     before=normed(nc, e, e.x, DT, h, gain(2), shift=part(3), scale=part(4)) if half == 0 else None)
                gemm(nc, e, f"l{l}_down{half}", I["mlp_w2_2"][l][cols, :], D_FF2 // P // 2, ff, 4, 2, 1,
                     "copy" if half == 0 else "add", dst=y)
            norm_stage(nc, e, f"l{l}_out", y, DT, y, gain(3), gate=part(5), onto=e.x)


def store_output(nc, e, out):
    with ExitStack() as s:
        sb, pb, sem = opened(nc, s, "store")
        rows = sb("rows", [P, TT, D])
        ps = pb("ps", [P, 4, L])
        turned, taken, stored = sem("turned"), sem("taken"), sem("stored")
        block = s.enter_context(nc.Block())

        @block.tensor
        def _(pe):
            for n in range(2 * TT):
                t, half = n // 2, n % 2
                if n >= 4:
                    pe.wait_ge(taken, n - 3)
                for i in range(4):
                    last = nc.tensor.transpose(ps[:, n % 4, i * P:(i + 1) * P],
                                               e.x[:, 4 * half + i, t * P:(t + 1) * P], e.ident[:, :])
                last.then_inc(turned, 1)

        @block.scalar
        def _(act):
            for n in range(2 * TT):
                t, half = n // 2, n % 2
                act.wait_ge(turned, n + 1)
                nc.scalar.activation(rows[:, t, half * 512:(half + 1) * 512], ps[:, n % 4, :], ACT.Copy)\
                    .then_inc(taken, 1)

        @block.sync
        def _(sp):
            for t in range(TT):
                sp.wait_ge(taken, 2 * t + 2)
                sp.dma_start(out[0, t * P:(t + 1) * P, :], rows[:, t, :]).then_inc(stored, 16)
            sp.wait_ge(stored, 16 * TT)



def program(nc, I, out):
    with ExitStack() as s:
        e = Kept()
        e.side_in, e.side_loads = s.enter_context(nc.semaphore("side_in")), 0
        Semaphores.start(nc)
        keep = lambda name, shape: s.enter_context(nc.sbuf_tensor(name, shape, F32))
        e.x = keep("resid", [P, DT, L])
        e.ident, e.ones, e.heads = keep("ident", [P, P]), keep("ones", [P, P]), keep("heads", [P, P])
        e.cols = keep("cols", [P, ROW_TILES * P])
        load_constants(nc, e, I)
        e.cond, e.kvada, e.ada = keep("cond", [P, DT]), keep("kvada", [P, 2 * DT]), keep("ada", [P, 2, 6 * DT])
        silu_condition(nc, e, e.cond)
        most, rest = 33, 6 * DT - 16
        side = lambda w, at, n, cols, dst: (w[:, at * P:(at + n) * P], cols, e.cond, dst[:, at:at + n])
        ada0, ada1, kvada = I["ada_w_2"][0], I["ada_w_2"][1], I["kv_ada_w_2"]
        ffn_swiglu(nc, e, "ffn1", "ffn1_norm", I["ffn1_w_gu"], I["ffn1_w_down"],
                   side(ada0, 0, most, 3 * P, e.ada[:, 0, :]), side(ada0, rest, 16, 4 * P, e.ada[:, 0, :]))
        with ExitStack() as s2:
            part = lambda name, shape: s2.enter_context(nc.sbuf_tensor(name, shape, F32))
            merged = part("merged", [P, DT, L])
            with ExitStack() as s3:
                hyena_branch(nc, e, I, two_parts(nc, s3, "h_mix", DT), merged)
            rwkv_branch(nc, e, I, merged)
            mp = two_parts(nc, s2, "merged", DT)
            gemm(nc, e, "mix_out", I["w_out"], DT, mp, 2, 2, 2, "add", dst=e.x, before=cut(nc, e, merged, DT, mp))
        ffn_swiglu(nc, e, "ffn2", "ffn2_norm", I["ffn2_w_gu"], I["ffn2_w_down"],
                   side(ada1, 0, most, 3 * P, e.ada[:, 1, :]), side(kvada, 0, 2 * DT, 4 * P, e.kvada))
        norm_stage(nc, e, "final", e.x, DT, e.x, lambda k: col(e, "final_norm", k))
        second_block(nc, e, I, side(ada1, rest, 16, 4 * P, e.ada[:, 1, :]))
        store_output(nc, e, out)




_OUT = (1, L, D)


def kernel(**inputs):
    import concourse.bacc as bacc
    from concourse.bass_utils import run_bass_kernel_spmd

    nc = bacc.Bacc("TRN2", target_bir_lowering=False, num_devices=1)
    arrays, aps = {}, {}
    for name, a in list(inputs.items()) + list(shape_tables().items()):
        a = np.ascontiguousarray(a)
        arrays[f"in_{name}"] = a
        aps[name] = nc.dram_tensor(f"in_{name}", a.shape, mybir.dt.from_np(a.dtype), kind="ExternalInput").ap()
    out = nc.dram_tensor("out_0", _OUT, F32, kind="ExternalOutput").ap()
    program(nc, aps, out)
    return run_bass_kernel_spmd(nc, [arrays], core_ids=[0]).results[0]["out_0"]
```

```python
import math
from contextlib import ExitStack

import numpy as np
import concourse.bass as bass
from concourse import mybir


F32 = mybir.dt.float32
F32R = mybir.dt.float32r
ACT = mybir.ActivationFunctionType
ALU = mybir.AluOpType
AX = mybir.AxisListType
P = 128

D = 1024
L = 512
DT = D // P
TT = L // P
D_FF = 2816
D_HY = 512
HT = D_HY // P
N_HY = 3 * D_HY
D_RW = 512
RT = D_RW // P
N_RW = 3 * D_RW + 2 * 64 + 2 * 64 + 160
EMB = 33
FILT = 64
EPS = 1e-6
GN_EPS = 64e-5
CH = 64
NCH = L // CH
LEVELS = 6
LH = L // 2
HCH = LH // CH
LOG_DECAY_MAX = -math.exp(-0.5)

A_HEADS = 8
A_QK = 64
A_IN = 3088
B_HEADS = 8
Q_LORA = 384
KV_LORA = 256
NOPE = 128
ROPE = 64
D_FF2 = 4096

TWO_PI = 2 * math.pi
ROUND = 1.5 * 2.0**23
PI_A = 6.28125
PI_B = float(np.float32(np.float32((TWO_PI - PI_A) * 2**20).astype(np.int64) / 2**20))
PI_C = TWO_PI - PI_A - PI_B

VECTORS = [
    ("ffn1_norm", 8, 128), ("mix_norm", 8, 128), ("hy_conv_w", 36, 128), ("hy_conv_b", 12, 128),
    ("hy_ffn_b1", 1, 64), ("hy_ffn_b2", 1, 64), ("hy_sin_freq", 1, 64), ("hy_bias_d", 8, 128),
    ("rw_w0", 8, 128), ("rw_a0", 8, 128), ("rw_k_k", 4, 128), ("rw_k_a", 4, 128),
    ("rw_r_k", 4, 128), ("rw_ln_w", 4, 128), ("rw_ln_b", 4, 128), ("ffn2_norm", 8, 128),
    ("final_norm", 8, 128), ("ada_b_2", 96, 128), ("norm_g_2", 64, 128),
    ("a_head_g_2", 8, 128), ("kv_ada_b_2", 16, 128), ("kv_norm_g_2", 8, 128),
    ("kv_latent_g_2", 2, 128), ("b_q_latent_g_2", 3, 128), ("c_2", 8, 128),
    ("a_gate_b_2", 2, 8),
]
MU_ROWS = N_RW // P
COL = {}
_at = 0
for _name, _rows, _ in VECTORS:
    COL[_name] = _at
    _at += _rows
COL["rw_mu"] = _at
_at += 2 * (MU_ROWS + 1)
ROW_TILES = -(-_at // P)


class Kept:
    pass


class Steps:

    def __init__(self, sem):
        self.sem, self.n = sem, 0

    def mark(self, ins):
        ins.then_inc(self.sem, 1)
        self.n += 1
        return self.n


MOST_SEMAPHORES = 30


class Semaphores:

    used = 0
    numbers = set()

    @classmethod
    def room(cls, nc, n=MOST_SEMAPHORES):
        if cls.used + n > cls.limit:
            first, last = min(cls.numbers), max(cls.numbers)
            with nc.Block() as block:
                @block.gpsimd
                def _(pool):
                    pool.sem_clear(range(first, last + 1))
            cls.used = 0

    @classmethod
    def start(cls, nc):
        cls.used, cls.numbers, cls.limit = 0, set(), nc.free_len()

    @classmethod
    def take(cls, nc, stack, name):
        sem = stack.enter_context(nc.semaphore(name))
        cls.used += 1
        cls.numbers.add(sem.num)
        return sem


def opened(nc, stack, tag):
    Semaphores.room(nc)
    sb = lambda name, shape: stack.enter_context(nc.sbuf_tensor(f"{tag}_{name}", shape, F32))
    pb = lambda name, shape: stack.enter_context(nc.psum_tensor(f"{tag}_{name}", shape, F32))
    sem = lambda name: Semaphores.take(nc, stack, f"{tag}_{name}")
    return sb, pb, sem


def col_at(t, c):
    return t[:, bass.ds(c, 1)]


def col(e, name, i=0, parts=P, base=0):
    c = COL[name] + i
    return e.cols[base:base + parts, c:c + 1]



def load_constants(nc, e, I):
    with ExitStack() as s:
        sb, pb, sem = opened(nc, s, "init")
        rows = sb("rows", [P, ROW_TILES, P])
        xin = sb("xin", [P, TT, D])
        ps = pb("ps", [P, 8, L])
        rows_zero, rows_in, x_in, tables_in = sem("rows_zero"), sem("rows_in"), sem("x_in"), sem("tables_in")
        vec_t, vec_c, x_t, x_c = sem("vec_t"), sem("vec_c"), sem("x_t"), sem("x_c")
        block = s.enter_context(nc.Block())
        pieces = []
        for name, n, width in VECTORS:
            flat = I[name]
            shape = "abcdef"[:len(flat.shape)]
            flat = flat.rearrange(f"{' '.join(shape)} -> ({' '.join(shape)})") if len(flat.shape) > 1 else flat
            view = flat.rearrange("(n w) -> n w", w=width)
            at = 0
            while at < n:
                row = COL[name] + at
                k = min(n - at, P - row % P)
                pieces.append((row, k, width, view[at:at + k, :]))
                at += k
        for m in range(2):
            row = COL["rw_mu"] + m * (MU_ROWS + 1)
            pieces.append((row, MU_ROWS, P, I["rw_mu"][m, 0:MU_ROWS * P].rearrange("(n w) -> n w", w=P)))
            pieces.append((row + MU_ROWS, 1, N_RW - MU_ROWS * P, I["rw_mu"][m:m + 1, MU_ROWS * P:N_RW]))
        split = []
        for row, k, width, src in pieces:
            first = min(k, P - row % P)
            split.append((row, first, width, src[0:first, :]))
            if first < k:
                split.append((row + first, k - first, width, src[first:k, :]))

        @block.sync
        def _(sp):
            xv = I["x"][0].rearrange("(t p) d -> p t d", p=P)
            sp.dma_start(e.ident[:, :], I["c_ident"]).then_inc(tables_in, 16)
            sp.dma_start(e.heads[:, :], I["c_heads"]).then_inc(tables_in, 16)
            for t in range(TT):
                sp.dma_start(xin[:, t, :], xv[:, t, :]).then_inc(x_in, 16)
            sp.wait_ge(rows_zero, 1)
            for row, k, width, src in split:
                sp.dma_start(rows[row % P:row % P + k, row // P, 0:width], src).then_inc(rows_in, 16)

        @block.vector
        def _(dve):
            nc.vector.memset(rows[:, :, :], 0.0).then_inc(rows_zero, 1)
            nc.vector.memset(e.ones[:, :], 1.0)
            for k in range(DT):
                dve.wait_ge(x_t, k + 1)
                nc.vector.tensor_copy(e.x[:, k, :], ps[:, k % 4, :]).then_inc(x_c, 1)
            dve.wait_ge(vec_t, 1)
            nc.vector.tensor_copy(e.cols[:, :], ps[:, 4, 0:ROW_TILES * P]).then_inc(vec_c, 1)

        @block.tensor
        def _(pe):
            pe.wait_ge(tables_in, 32)
            pe.wait_ge(x_in, 16 * TT)
            for k in range(DT):
                if k >= 4:
                    pe.wait_ge(x_c, k - 3)
                for t in range(TT):
                    last = nc.tensor.transpose(ps[:, k % 4, t * P:(t + 1) * P],
                                               xin[:, t, k * P:(k + 1) * P], e.ident[:, :])
                last.then_inc(x_t, 1)
            pe.wait_ge(rows_in, 16 * len(split))
            for r in range(ROW_TILES):
                last = nc.tensor.transpose(ps[:, 4, r * P:(r + 1) * P], rows[:, r, :], e.ident[:, :])
            last.then_inc(vec_t, 1)



def norm_stage(nc, e, tag, src, n, dst, gain, eps=EPS, shift=None, scale=None,
               gate=None, onto=None):
    with ExitStack() as s:
        sb, pb, sem = opened(nc, s, tag)
        sq, pair = sb("sq", [P, 4, L]), sb("pair", [P, 2, L])
        rs = sb("rs", [P, 2, L])
        g1 = sb("g1", [P, n])
        ps = pb("ps", [P, L])
        sq_ready, pair_ready, summed = sem("sq_ready"), sem("pair_ready"), sem("summed")
        inv_ready, rs_ready, steps, out_done = sem("inv_ready"), sem("rs_ready"), sem("steps"), sem("out")
        block = s.enter_context(nc.Block())

        @block.scalar
        def _(act):
            for k in range(n):
                if k >= 4:
                    act.wait_ge(pair_ready, k // 2 - 1)
                nc.scalar.activation(sq[:, k % 4, :], src[:, k, :], ACT.Square).then_inc(sq_ready, 1)
            act.wait_ge(inv_ready, 1)
            nc.scalar.activation(rs[:, 1, :], rs[:, 0, :], ACT.Sqrt).then_inc(rs_ready, 1)
            if shift is not None:
                for k in range(n):
                    act.wait_ge(out_done, k + 1)
                    nc.scalar.activation(dst[:, k, :], dst[:, k, :], ACT.Identity, bias=shift(k))

        @block.tensor
        def _(pe):
            for k in range(n // 2):
                pe.wait_ge(pair_ready, k + 1)
                nc.tensor.matmul(ps[:, :], e.ones[:, :], pair[:, k % 2, :], start=k == 0, stop=k == n // 2 - 1)\
                    .then_inc(summed, 1)

        @block.vector
        def _(dve):
            st = Steps(steps)
            if scale is not None:
                for k in range(n):
                    st.mark(nc.vector.scalar_tensor_tensor(g1[:, k:k + 1], scale(k), 1.0, gain(k),
                                                           ALU.add, ALU.mult))
            if gate is not None:
                for k in range(n):
                    st.mark(nc.vector.tensor_tensor(g1[:, k:k + 1], gate(k), gain(k), ALU.mult))
            for k in range(n // 2):
                dve.wait_ge(sq_ready, 2 * k + 2)
                if k >= 2:
                    dve.wait_ge(summed, k - 1)
                nc.vector.tensor_tensor(pair[:, k % 2, :], sq[:, 2 * (k % 2), :], sq[:, 2 * (k % 2) + 1, :],
                                        ALU.add).then_inc(pair_ready, 1)
            dve.wait_ge(summed, n // 2)
            dve.wait_ge(steps, st.mark(nc.vector.tensor_scalar(rs[:, 0, :], ps[:, :], 1.0 / (n * P), eps,
                                                               ALU.mult, ALU.add)))
            nc.vector.reciprocal(rs[:, 0, :], rs[:, 0, :]).then_inc(inv_ready, 1)
            dve.wait_ge(rs_ready, 1)
            for k in range(n):
                g = gain(k) if scale is None and gate is None else g1[:, k:k + 1]
                nc.vector.scalar_tensor_tensor(dst[:, k, :], src[:, k, :], g, rs[:, 1, :],
                                               ALU.mult, ALU.mult).then_inc(out_done, 1)
                if onto is not None and k % 2 == 1:
                    dve.wait_ge(out_done, k)
                    nc.vector.tensor_tensor(onto[:, k - 1, :], onto[:, k - 1, :], dst[:, k - 1, :], ALU.add)

        @block.gpsimd
        def _(pool):
            if onto is not None:
                for k in range(1, n, 2):
                    pool.wait_ge(out_done, k + 1)
                    nc.gpsimd.tensor_tensor(onto[:, k, :], onto[:, k, :], dst[:, k, :], ALU.add)



def norm_programs(nc, e, sb, pb, sem, src, n, hi, lo, gain, shift=None, scale=None, root=None,
                  known=False, scratch=None):
    N = SimpleParts()
    N.count = n
    sq = scratch if scratch is not None else sb("n_sq", [P, 4, L])
    pair = sb("n_pair", [P, 2, L])
    t, rs = sq[:, 0:3, :], sq[:, 3, :] if root is None else root
    u, turn = (pair, 2) if shift is not None else (t, 3)
    g1 = sb("n_g1", [P, n])
    ps = pb("n_ps", [P, L])
    sq_ready, pair_ready, summed = sem("n_sq"), sem("n_pair"), sem("n_summed")
    inv_ready, rs_ready, steps = sem("n_inv"), sem("n_rs"), sem("n_steps")
    t_ready, hi_ready = sem("n_t"), sem("n_hi")
    lo_done = [sem("n_lo_even"), sem("n_lo_odd")]

    def wait_part(eng, k):
        eng.wait_ge(lo_done[k % 2], k // 2 + 1)

    def lower(eng, engine, k):
        eng.wait_ge(hi_ready, k + 1)
        engine.tensor_tensor(lo[:, k, :], u[:, k % turn, :], hi[:, k, :].bitcast(F32), ALU.subtract)\
            .then_inc(lo_done[k % 2], 1)

    def act_sums(eng):
        for k in range(0 if known else n):
            if k >= 4:
                eng.wait_ge(pair_ready, k // 2 - 1)
            nc.scalar.activation(sq[:, k % 4, :], src[:, k, :], ACT.Square).then_inc(sq_ready, 1)

    def act_parts(eng):
        if not known:
            eng.wait_ge(inv_ready, 1)
            nc.scalar.activation(rs, rs, ACT.Sqrt).then_inc(rs_ready, 1)
        for k in range(n):
            eng.wait_ge(t_ready, k + 1)
            if shift is None:
                nc.scalar.activation(hi[:, k, :], t[:, k % 3, :], ACT.Copy).then_inc(hi_ready, 1)
            else:
                nc.scalar.activation(hi[:, k, :], t[:, k % 3, :], ACT.Identity, bias=shift(k))
                if k >= 2:
                    wait_part(eng, k - 2)
                nc.scalar.activation(u[:, k % 2, :], t[:, k % 3, :], ACT.Identity, bias=shift(k))\
                    .then_inc(hi_ready, 1)

    def pe(eng):
        for k in range(0 if known else n // 2 + n % 2):
            eng.wait_ge(pair_ready, k + 1)
            nc.tensor.matmul(ps[:, :], e.ones[:, :], pair[:, k % 2, :], start=k == 0, stop=k == n // 2 + n % 2 - 1)\
                .then_inc(summed, 1)

    st = Steps(steps)

    def dve_sums(eng):
        if scale is not None:
            for k in range(n):
                st.mark(nc.vector.scalar_tensor_tensor(g1[:, k:k + 1], scale(k), 1.0, gain(k), ALU.add, ALU.mult))
        if known:
            return
        for k in range(n // 2 + n % 2):
            eng.wait_ge(sq_ready, min(2 * k + 2, n))
            if k >= 2:
                eng.wait_ge(summed, k - 1)
            if 2 * k + 1 < n:
                ins = nc.vector.tensor_tensor(pair[:, k % 2, :], sq[:, 2 * (k % 2), :], sq[:, 2 * (k % 2) + 1, :], ALU.add)
            else:
                ins = nc.vector.tensor_copy(pair[:, k % 2, :], sq[:, 2 * (k % 2), :])
            ins.then_inc(pair_ready, 1)

    def dve_parts(eng):
        if not known:
            eng.wait_ge(summed, n // 2 + n % 2)
            eng.wait_ge(steps, st.mark(nc.vector.tensor_scalar(rs, ps[:, :], 1.0 / (n * P), EPS,
                                                               ALU.mult, ALU.add)))
            nc.vector.reciprocal(rs, rs).then_inc(inv_ready, 1)
            eng.wait_ge(rs_ready, 1)
        elif scale is not None:
            eng.wait_ge(steps, st.n)

        for k in range(n):
            g = gain(k) if scale is None else g1[:, k:k + 1]
            if k >= 3:
                if u is t:
                    wait_part(eng, k - 3)
                else:
                    eng.wait_ge(hi_ready, k - 2)
            nc.vector.scalar_tensor_tensor(t[:, k % 3, :], src[:, k, :], g, rs, ALU.mult, ALU.mult)\
                .then_inc(t_ready, 1)
            if k % 2 == 1:
                lower(eng, nc.vector, k - 1)
        if n % 2 == 1:
            lower(eng, nc.vector, n - 1)

    def pool(eng):
        for k in range(1, n, 2):
            lower(eng, nc.gpsimd, k)

    N.act, N.pe, N.dve, N.pool, N.wait_part = (act_sums, act_parts), pe, (dve_sums, dve_parts), pool, wait_part
    if known:
        N.act = (lambda eng: (act_sums(eng), act_parts(eng)), lambda eng: None)
        N.dve = (lambda eng: (dve_sums(eng), dve_parts(eng)), lambda eng: None)
    return N


def cut_programs(nc, e, sb, pb, sem, src, n, hi, lo, scratch=None):
    N = SimpleParts()
    N.count = n
    hi_ready, lo_done = sem("c_hi"), [sem("c_lo_even"), sem("c_lo_odd")]

    def wait_part(eng, k):
        eng.wait_ge(lo_done[k % 2], k // 2 + 1)

    def lower(eng, engine, k):
        eng.wait_ge(hi_ready, k + 1)
        engine.tensor_tensor(lo[:, k, :], src[:, k, :], hi[:, k, :].bitcast(F32), ALU.subtract)\
            .then_inc(lo_done[k % 2], 1)

    def act(eng):
        for k in range(n):
            nc.scalar.activation(hi[:, k, :], src[:, k, :], ACT.Copy).then_inc(hi_ready, 1)

    def dve(eng):
        for k in range(0, n, 2):
            lower(eng, nc.vector, k)

    def pool(eng):
        for k in range(1, n, 2):
            lower(eng, nc.gpsimd, k)

    nothing = lambda eng: None
    N.act, N.pe, N.dve, N.pool, N.wait_part = (act, nothing), nothing, (dve, nothing), pool, wait_part
    return N


class SimpleParts:
    pass



def staggered(eng, groups, slots, ahead, behind):
    if groups > 1:
        with eng.Fori(0, groups - 1) as g:
            for i in range(slots):
                behind(g * slots + i, g, i)
                ahead(g * slots + (slots + i), g + 1, i)
    for i in range(slots):
        behind((groups - 1) * slots + i, groups - 1, i)


class Stream:

    def __init__(self, nc, e, stack, tag, size):
        self.nc, self.e, self.loads, self.loaded = nc, e, e.loads, e.loaded
        self.raw = stack.enter_context(nc.sbuf_tensor(f"{tag}_stream", [P, 2, size], F32))
        self.prepared = False

    def slot(self, i, kt, wide):
        return self.raw[:, i, 0:kt * wide].rearrange("p (k n) -> p k n", k=kt)

    def load(self, sp, w, kt, wide, i):
        sp.dma_start(self.slot(i, kt, wide), w.rearrange("(k p) n -> p k n", p=P)[:, :, i * wide:(i + 1) * wide])\
            .then_inc(self.loaded[i], 16)


def tile_at(t, j):
    return t[:, bass.ds(j, 1), :].rearrange("p a n -> p (a n)")


def gemm(nc, e, tag, w, kt, x, groups, slots, per, kind, dst=None, func=ACT.Copy, factor=1.0, gate=None,
         width=P, before=None, side=None, stream=None, following=None,
         also=None, taps=None):
    with ExitStack() as s:
        sb, pb, sem = opened(nc, s, tag)
        sbr = lambda name, shape: s.enter_context(nc.sbuf_tensor(f"{tag}_{name}", shape, F32R))
        xh, xl = x
        wide = per * width
        nb = slots * per
        pair = kind == "swiglu"
        if stream:
            raw = [stream.slot(i, kt, wide) for i in range(slots)]
            loaded, loads_at = stream.loaded, list(stream.loads)
            preloaded, stream.prepared = stream.prepared, following is not None
            for i in range(2):
                stream.loads[i] += groups + (following is not None)
        else:
            raw_slots = sb("raw", [P, slots, kt, wide])
            raw = [raw_slots[:, i, :, :] for i in range(slots)]
            loaded, loads_at, preloaded = [sem(f"loaded{i}") for i in range(slots)], [0] * slots, False
        if preloaded:
            loads_at = [n - 1 for n in loads_at]
            for i in range(2):
                stream.loads[i] -= 1
        wh, wl = sbr("wh", [P, slots, kt, wide]), sbr("wl", [P, slots, kt, wide])
        ps = pb("ps", [P, nb, L])
        hi_ready, lo_ready, mm_done, bank_free = sem("hi_ready"), sem("lo_ready"), sem("mm_done"), sem("bank_free")
        n_buf = slots if pair else nb
        scratch = None
        if kind in ("swiglu", "sqrelu"):
            scratch = sb("factors", [P, 2 * n_buf, L])
            f1, f2 = scratch[:, 0:n_buf, :], scratch[:, n_buf:, :]
            f1_ready, f2_free = sem("f1_ready"), sem("f2_free")
        first = before(sb, pb, sem, scratch) if before else None
        on_the_way = also(sb, pb, sem) if also else None
        tapped = sem("tapped") if taps else None
        if side:
            assert slots == 2
            side_w, side_cols, cond, side_out = side
            sraw, acc = sb("sraw", [P, DT // 2, side_cols]), sb("acc", [P, side_cols])
            n_side = side_cols // P
            sps = pb("sps", [P, (groups + 1) * n_side])
            side_step, side_sum = sem("side_step"), sem("side_sum")
            side_in, loads_before = e.side_in, e.side_loads
            e.side_loads += groups * slots
        block = s.enter_context(nc.Block())
        if pair:
            wv = w.rearrange("(k p) (two n) -> p k two n", p=P, two=2)
        else:
            wv = w.rearrange("(k p) n -> p k n", p=P)

        @block.sync
        def _(sp):
            def load(c, i):
                if pair:
                    for t in range(2):
                        sp.dma_start(raw[i][:, :, t * P:(t + 1) * P], wv[:, :, t, bass.ds(c * P, P)])\
                            .then_inc(loaded[i], 16)
                else:
                    sp.dma_start(raw[i], wv[:, :, bass.ds(c * wide, wide)]).then_inc(loaded[i], 16)

            for i in range(slots):
                if not preloaded:
                    load(i, i)
            if groups > 1:
                with sp.Fori(1, groups) as g:
                    for i in range(slots):
                        sp.wait_ge(lo_ready, (g - 1) * slots + (i + 1))
                        load(g * slots + i, i)
            if following:
                for i in range(slots):
                    sp.wait_ge(lo_ready, (groups - 1) * slots + i + 1)
                    stream.load(sp, *following, i)
            if also:
                on_the_way[0](sp)

        @block.tensor
        def _(pe):
            def side_sums(at, steps_done):
                pe.wait_ge(side_step, steps_done)
                for j in range(n_side):
                    last = nc.tensor.matmul(sps[:, bass.ds(at + j, 1)], acc[:, j * P:(j + 1) * P],
                                            e.ones[:, 0:1], start=True, stop=True)
                last.then_inc(side_sum, 1)

            pe.sem_inc(mm_done, nb)
            if first:
                first.pe(pe)
            with pe.Fori(0, groups) as g:
                for i in range(slots):
                    c = g * slots + i
                    pe.wait_ge(hi_ready, c + 1)
                    ws = [slice(t * width, (t + 1) * width) for t in range(per)]
                    banks = [ps[0:width, i * per + t, :] for t in range(per)]

                    def free(t):
                        if pair:
                            pe.wait_ge((f1_ready, bank_free)[t], c + 1)
                        else:
                            pe.wait_ge(bank_free, g * nb + (i * per + t + 1))

                    def upper_passes(k, t):
                        nc.tensor.matmul(banks[t], wh[:, i, k, ws[t]], xh[:, k, :], start=k == 0, stop=False)
                        nc.tensor.matmul(banks[t], wh[:, i, k, ws[t]], xl[:, k, :], start=False, stop=False)

                    def lower_pass(t):
                        for k in range(kt):
                            last = nc.tensor.matmul(banks[t], wl[:, i, k, ws[t]], xh[:, k, :],
                                                    start=False, stop=k == kt - 1)
                        last.then_inc(mm_done, 1)

                    if first and i == 0:
                        for t in range(per):
                            free(t)
                        for k in range(kt):
                            first.wait_part(pe, k)
                            for t in range(per):
                                upper_passes(k, t)
                        pe.wait_ge(lo_ready, c + 1)
                        for t in range(per):
                            lower_pass(t)
                    else:
                        for t in range(per):
                            free(t)
                            for k in range(kt):
                                upper_passes(k, t)
                            if t == 0:
                                pe.wait_ge(lo_ready, c + 1)
                            lower_pass(t)
                    if side and i == 0:
                        side_sums(g * n_side, g * DT + 1)
            if side:
                side_sums(groups * n_side, groups * DT + 1)

        @block.scalar
        def _(act):
            if pair:
                act.sem_inc(f1_ready, slots)
            if kind == "copy":
                act.sem_inc(bank_free, nb)
            def upper(c, g, i):
                act.wait_ge(loaded[i], g * 16 * (2 if pair else 1) + 16 * ((2 if pair else 1) + loads_at[i]))
                act.wait_ge(mm_done, c * per + per)
                nc.scalar.activation(wh[:, i, :, :], raw[i], ACT.Copy).then_inc(hi_ready, 1)

            def take_out(c, g, i):
                if kind == "copy":
                    for t in range(per):
                        act.wait_ge(mm_done, c * per + (nb + t + 1))
                        if taps:
                            result, now, _, _, bias = taps
                            j = c * per + t
                            if bias:
                                nc.scalar.activation(result(j), ps[:, i * per + t, :], ACT.Identity, bias=bias(j),
                                                     scale=now(j))
                            else:
                                nc.scalar.activation(result(j), ps[:, i * per + t, :], ACT.Copy, scale=now(j))
                        nc.scalar.activation(tile_at(dst, c * per + t)[0:width, :], ps[0:width, i * per + t, :], func)\
                            .then_inc(bank_free, 1)
                elif pair:
                    act.wait_ge(mm_done, c * 2 + (nb + 1))
                    act.wait_ge(bank_free, c + 1)
                    nc.scalar.activation(f1[:, i, :], ps[:, 2 * i, :], ACT.Silu).then_inc(f1_ready, 1)
                elif kind == "sqrelu":
                    for t in range(per):
                        act.wait_ge(mm_done, c * per + (nb + t + 1))
                        act.wait_ge(bank_free, c * per + (t + 1))
                        nc.scalar.activation(f1[:, i * per + t, :], ps[:, i * per + t, :], ACT.Relu)\
                            .then_inc(f1_ready, 1)

            if first:
                first.act[0](act)
            for i in range(slots):
                upper(i, 0, i)
            if first:
                first.act[1](act)
            if kind in ("copy", "swiglu", "sqrelu"):
                staggered(act, groups, slots, upper, take_out)
            else:
                staggered(act, groups, slots, upper, lambda c, g, i: None)
            if also:
                on_the_way[1](act)

        @block.vector
        def _(dve):
            if kind != "copy":
                dve.sem_inc(bank_free, slots if pair else nb)

            def lower(c, g, i):
                dve.wait_ge(hi_ready, c + 1)
                nc.vector.tensor_tensor(wl[:, i, :, :], raw[i], wh[:, i, :, :].bitcast(F32), ALU.subtract)\
                    .then_inc(lo_ready, 1)

            def both_parts(j, i, a, bank, op0, a_ready):
                dve.wait_ge(f1_ready, a_ready)
                dve.wait_ge(f2_free, j + 1)
                nc.vector.scalar_tensor_tensor(tile_at(dst[0], j), bank, op0, a, ALU.max if op0 == 0.0 else ALU.mult,
                                               ALU.mult)
                nc.vector.scalar_tensor_tensor(f2[:, i, :], bank, op0, a, ALU.max if op0 == 0.0 else ALU.mult,
                                               ALU.mult).then_inc(bank_free, 1)

            def take_out(c, g, i):
                if pair:
                    dve.wait_ge(mm_done, c * 2 + (nb + 2))
                    both_parts(c, i, f1[:, i, :], ps[:, 2 * i + 1, :], 1.0, c + (slots + 1))
                elif kind == "sqrelu":
                    for t in range(per):
                        b = i * per + t
                        both_parts(c * per + t, b, f1[:, b, :], ps[:, b, :], 0.0, c * per + (t + 1))
                elif taps:
                    result, _, before_, after_, _ = taps
                    for t in range(per):
                        j = c * per + t
                        out, u = result(j), tile_at(dst, j)
                        dve.wait_ge(bank_free, j + (nb + 1))
                        nc.vector.scalar_tensor_tensor(out[:, 1:L], u[:, 0:L - 1], before_(j), out[:, 1:L],
                                                       ALU.mult, ALU.add).then_inc(tapped, 1)
                        dve.wait_ge(tapped, j + 1)
                        nc.vector.scalar_tensor_tensor(out[:, 0:L - 1], u[:, 1:L], after_(j), out[:, 0:L - 1],
                                                       ALU.mult, ALU.add)
                elif kind in ("add", "gate"):
                    for t in range(per):
                        bank = ps[0:width, i * per + t, :]
                        d = tile_at(dst, c * per + t)
                        dve.wait_ge(mm_done, c * per + (nb + t + 1))
                        if kind == "add":
                            nc.vector.scalar_tensor_tensor(d, bank, factor, d, ALU.mult, ALU.add).then_inc(bank_free, 1)
                        elif factor == 0:
                            nc.vector.tensor_tensor(d, tile_at(gate, c * per + t), bank, ALU.mult).then_inc(bank_free, 1)
                        else:
                            gt = tile_at(gate, c * per + t)
                            nc.vector.tensor_tensor(gt, gt, bank, ALU.mult).then_inc(bank_free, 1)
                            dve.wait_ge(bank_free, c * per + (nb + t + 1))
                            nc.vector.tensor_tensor(d, d, gt, ALU.add)
                if side:
                    dve.wait_ge(side_in, c * 16 + 16 * (loads_before + 1))
                    if i == 0:
                        dve.wait_ge(side_sum, g + 1)
                    for kk in range(DT // 2):
                        k = i * (DT // 2) + kk
                        factor_k = cond[:, k:k + 1]
                        if k == 0:
                            ins = nc.vector.tensor_scalar(acc[:, :], sraw[:, kk, :], factor_k, None, ALU.mult)
                        else:
                            dve.wait_ge(side_step, g * DT + (k + 1))
                            ins = nc.vector.scalar_tensor_tensor(acc[:, :], sraw[:, kk, :], factor_k, acc[:, :],
                                                                 ALU.mult, ALU.add)
                        ins.then_inc(side_step, 1)

            if side:
                nc.vector.memset(acc[:, :], 0.0).then_inc(side_step, 1)
            if first:
                first.dve[0](dve)
            lower(0, 0, 0)
            if first:
                first.dve[1](dve)
            for i in range(1, slots):
                lower(i, 0, i)
            staggered(dve, groups, slots, lower, take_out)
            if side:
                dve.wait_ge(side_sum, groups + 1)
                nc.vector.tensor_copy(side_out, sps[:, n_side:])
            if also:
                on_the_way[2](dve)

        if kind not in ("swiglu", "sqrelu") and not side:
            if first:
                block.gpsimd(first.pool)
        else:
            @block.gpsimd
            def _(pool):
                if first:
                    first.pool(pool)
                if kind in ("swiglu", "sqrelu"):
                    pool.sem_inc(f2_free, n_buf)
                with pool.Fori(0, groups) as g:
                    for i in range(slots):
                        if side:
                            pool.wait_ge(side_step, g * DT + (DT // 2 * i + 1))
                            pool.dma_start(sraw[:, :, :], side_w.rearrange("(two k p) n -> two p k n", two=2, p=P)
                                           [i, :, :, bass.ds(g * side_cols, side_cols)]).then_inc(side_in, 16)
                        if kind in ("swiglu", "sqrelu"):
                            for b in range(i * n_buf // slots, (i + 1) * n_buf // slots):
                                pool.wait_ge(bank_free, g * n_buf + (n_buf + b + 1))
                                d = tile_at(dst[1], g * n_buf + b)
                                nc.gpsimd.tensor_tensor(d, f2[:, b, :], tile_at(dst[0], g * n_buf + b).bitcast(F32),
                                                        ALU.subtract).then_inc(f2_free, 1)


def gemm_tokens(nc, e, tag, w, kt, x, n_chunks, dst, at):
    with ExitStack() as s:
        sb, pb, sem = opened(nc, s, tag)
        raw = sb("raw", [P, n_chunks, kt, 512])
        wh, wl = (s.enter_context(nc.sbuf_tensor(f"{tag}_{n}", [P, n_chunks, kt, 512], F32R)) for n in ("wh", "wl"))
        ps = pb("ps", [P, n_chunks * TT, 512])
        pieces = [(c, k) for c in range(n_chunks) for k in range(0, kt, 2)]
        loaded = [sem(f"loaded{i}") for i in range(len(pieces))]
        hi_ready, lo_ready, mm_done = sem("hi_ready"), sem("lo_ready"), sem("mm_done")
        block = s.enter_context(nc.Block())
        xh, xl = x

        @block.sync
        def _(sp):
            for i, (c, k) in enumerate(pieces):
                sp.dma_start(raw[:, c, k:k + 2, :],
                             w.rearrange("(k p) n -> p k n", p=P)[:, k:k + 2, at + 512 * c:at + 512 * (c + 1)])\
                    .then_inc(loaded[i], 16)

        @block.tensor
        def _(pe):
            for i, (c, k0) in enumerate(pieces):
                pe.wait_ge(lo_ready, i + 1)
                for t in range(TT):
                    ts = slice(t * P, (t + 1) * P)
                    bank = ps[:, c * TT + t, :]
                    for k in (k0, k0 + 1):
                        nc.tensor.matmul(bank, xh[:, k, ts], wh[:, c, k, :], start=k == 0, stop=False)
                        nc.tensor.matmul(bank, xh[:, k, ts], wl[:, c, k, :], start=False, stop=False)
                        last = nc.tensor.matmul(bank, xl[:, k, ts], wh[:, c, k, :], start=False, stop=k == kt - 1)
                    if k0 == kt - 2:
                        last.then_inc(mm_done, 1)

        @block.scalar
        def _(act):
            for i, (c, k) in enumerate(pieces):
                act.wait_ge(loaded[i], 16)
                nc.scalar.activation(wh[:, c, k:k + 2, :], raw[:, c, k:k + 2, :], ACT.Copy).then_inc(hi_ready, 1)
            for n in range(n_chunks * TT):
                act.wait_ge(mm_done, n + 1)
                nc.scalar.activation(dst[:, n % TT, n // TT * 512:(n // TT + 1) * 512], ps[:, n, :], ACT.Copy)

        @block.vector
        def _(dve):
            for i, (c, k) in enumerate(pieces):
                dve.wait_ge(hi_ready, i + 1)
                nc.vector.tensor_tensor(wl[:, c, k:k + 2, :], raw[:, c, k:k + 2, :],
                                        wh[:, c, k:k + 2, :].bitcast(F32), ALU.subtract).then_inc(lo_ready, 1)


def two_parts(nc, stack, name, n):
    return [stack.enter_context(nc.sbuf_tensor(f"{name}_{p}", [P, n, L], F32R)) for p in ("hi", "lo")]


def normed(nc, e, src, n, x, gain, shift=None, scale=None, root=None, known=False):
    return lambda *a: norm_programs(nc, e, *a[:3], src, n, x[0], x[1], gain, shift, scale, root, known, *a[3:])


def cut(nc, e, src, n, x):
    return lambda *a: cut_programs(nc, e, *a[:3], src, n, x[0], x[1])


def ffn_swiglu(nc, e, tag, norm, w_gu, w_down, side_up, side_down):
    with ExitStack() as s:
        ff = two_parts(nc, s, f"{tag}_ff", D_FF // P)
        with ExitStack() as s2:
            h = two_parts(nc, s2, f"{tag}_h", DT)
            gemm(nc, e, f"{tag}_up", w_gu, DT, h, D_FF // P // 2, 2, 2, "swiglu", dst=ff, side=side_up,
                 before=normed(nc, e, e.x, DT, h, lambda k: col(e, norm, k)))
        gemm(nc, e, f"{tag}_down", w_down, D_FF // P, ff, 4, 2, 1, "add", dst=e.x, factor=0.5, side=side_down)


def load_tables(nc, tag, pairs):
    with ExitStack() as s:
        sb, pb, sem = opened(nc, s, tag)
        loaded = sem("loaded")
        block = s.enter_context(nc.Block())

        @block.sync
        def _(sp):
            for dst, src in pairs:
                sp.dma_start(dst, src).then_inc(loaded, 16)
            sp.wait_ge(loaded, 16 * len(pairs))



def position_order():
    return np.concatenate([np.arange(0, L, 2), np.arange(1, L, 2)])


def shape_tables():
    f32 = np.float32
    t = {"c_ident": np.eye(P, dtype=f32)}
    half = np.arange(P) // CH
    t["c_heads"] = (half[:, None] == half[None, :]).astype(f32)
    order = position_order()
    ang = 2 * np.pi * ((2 * np.arange(L // 2)[None, :] + 1) * order[:, None] % (4 * L)) / (4 * L)
    t["c_cos"], t["c_sin"] = np.cos(ang).astype(f32), np.sin(ang).astype(f32)
    t["c_cosT"], t["c_sinT"] = np.ascontiguousarray(t["c_cos"].T), np.ascontiguousarray(t["c_sin"].T)
    pos = np.arange(L, dtype=f32)
    tt = (pos / f32(L - 1))[:, None]
    w = (f32(TWO_PI / L) * pos)[:, None]
    bands = np.linspace(1e-4, 15, 16).astype(f32)[None, :]
    feats = np.concatenate([tt, np.cos(bands * w), -np.sin(bands * w)], axis=-1).astype(f32)
    t["c_feats"] = np.ascontiguousarray(feats[order].T)
    t["c_negt"] = np.ascontiguousarray(-tt[order].reshape(TT, P).T)
    nz = np.ones((P, TT), f32)
    nz[0, 0] = 0
    t["c_notfirst"] = nz
    i = np.arange(P)
    r, c = i[:, None], i[None, :]
    lev = []
    for k in range(LEVELS):
        b = 2**k
        lev.append((r // (2 * b) == c // (2 * b)) & (r // b % 2 == 1) & (c // b % 2 == 0))
    lower = np.stack(lev).astype(f32)
    t["c_levels"] = np.ascontiguousarray(
        np.stack([lower, lower.transpose(0, 2, 1)]).transpose(2, 0, 1, 3).reshape(P, -1))
    sC, tC = i % CH, i % CH
    strict, incl = sC[:, None] < tC[None, :CH], sC[:, None] <= tC[None, :CH]
    fwd = np.concatenate([strict, incl], 1)
    strict, incl = sC[:, None] > tC[None, :CH], sC[:, None] >= tC[None, :CH]
    bwd = np.concatenate([strict, incl], 1)
    t["c_scan"] = np.ascontiguousarray(np.concatenate([fwd, bwd], 1).astype(f32))
    reset = np.ones((P, L), f32)
    reset[:, ::CH] = 0
    t["c_reset"] = reset
    t["c_causal"] = (r <= c).astype(f32)
    t["c_causal_row"] = np.where(c <= r, 0, -1e30).astype(f32)
    sel = np.zeros((A_HEADS, A_HEADS, P), f32)
    for h in range(A_HEADS):
        sel[h, h, :] = 1
    t["c_sel"] = sel.reshape(A_HEADS, -1)
    inv = (10000.0 ** (-np.arange(32, dtype=f32).astype(np.float64) / 32)).astype(f32)
    t["c_invfreq"] = np.tile(inv, 4).reshape(P, 1)
    return t



def hyena_filter_mlp(nc, e, I, h2, tables):
    with ExitStack() as s:
        sb, pb, sem = opened(nc, s, "hyf")
        feats, w1, w2 = sb("feats", [EMB, L]), sb("w1", [EMB, FILT]), sb("w2", [FILT, FILT])
        h1, y, n = sb("h1", [FILT, L]), sb("y", [FILT, L]), sb("n", [FILT, L])
        ps = pb("ps", [FILT, 2, L])
        loaded, tables_in, z_ready, y_ready = sem("loaded"), sem("tables_in"), sem("z"), sem("y")
        sin_ready, steps = sem("sin"), sem("steps")
        block = s.enter_context(nc.Block())

        @block.sync
        def _(sp):
            sp.dma_start(feats[:, :], I["c_feats"]).then_inc(loaded, 16)
            sp.dma_start(w1[:, :], I["hy_ffn_w1"]).then_inc(loaded, 16)
            sp.dma_start(w2[:, :], I["hy_ffn_w2"]).then_inc(loaded, 16)
            for dst, src in tables:
                sp.dma_start(dst, src).then_inc(tables_in, 16)
            sp.wait_ge(tables_in, 16 * len(tables))

        @block.tensor
        def _(pe):
            pe.wait_ge(loaded, 48)
            nc.tensor.matmul(ps[:, 0, :], w1[:, :], feats[:, :], start=True, stop=True).then_inc(z_ready, 1)
            pe.wait_ge(sin_ready, 1)
            nc.tensor.matmul(ps[:, 1, :], w2[:, :], h1[:, :], start=True, stop=True).then_inc(z_ready, 1)

        @block.vector
        def _(dve):
            st = Steps(steps)

            def then(ins):
                dve.wait_ge(steps, st.mark(ins))

            nc.vector.memset(h2[FILT:FILT + 1, :], 1.0)
            for layer, bias in enumerate(("hy_ffn_b1", "hy_ffn_b2")):
                dve.wait_ge(z_ready, layer + 1)
                then(nc.vector.tensor_scalar(y[:, :], ps[:, layer, :], col(e, bias, 0, FILT),
                                             col(e, "hy_sin_freq", 0, FILT), ALU.add, ALU.mult))
                then(nc.vector.tensor_scalar(n[:, :], y[:, :], 1 / TWO_PI, ROUND, ALU.mult, ALU.add))
                then(nc.vector.tensor_scalar(n[:, :], n[:, :], ROUND, None, ALU.subtract))
                for part in (PI_A, PI_B, PI_C):
                    then(nc.vector.scalar_tensor_tensor(y[:, :], n[:, :], -part, y[:, :], ALU.mult, ALU.add))
                nc.vector.tensor_scalar(y[:, :], y[:, :], math.pi, -math.pi, ALU.min, ALU.max)\
                    .then_inc(y_ready, 1)
                if layer == 0:
                    dve.wait_ge(sin_ready, 1)

        @block.scalar
        def _(act):
            for layer, dst in enumerate((h1, h2)):
                act.wait_ge(y_ready, layer + 1)
                nc.scalar.activation(dst[0:FILT, :], y[:, :], ACT.Sin).then_inc(sin_ready, 1)


def hyena_spectra(nc, e, I, h2, cos, sin, spec):
    with ExitStack() as s:
        sb, pb, sem = opened(nc, s, "hys")
        w3 = sb("w3", [FILT + 1, 4, D_HY])
        dec = sb("dec", [P, 4, D_HY])
        negt, notfirst = sb("negt", [P, TT]), sb("notfirst", [P, TT])
        env = sb("env", [P, 2, D_HY])
        fb = sb("fb", [P, 2, D_HY])
        sq = sb("sq", [P, 2, D_HY])
        ab = sb("ab", [P, 2, TT, D_HY])
        rs = sb("rs", [P, 2, D_HY])
        even = sb("even", [P, 2, D_HY])
        ps = pb("ps", [P, 2, D_HY])
        pn = pb("pn", [P, D_HY])
        pk = pb("pk", [P, 2, 2, D_HY])
        loaded, dec_abs, env_ready, raw_done = sem("loaded"), sem("dec_abs"), sem("env_ready"), sem("raw_done")
        fb_ready, sq_ready, sq_used, ab_ready = sem("fb_ready"), sem("sq_ready"), sem("sq_used"), sem("ab_ready")
        inv_ready, rs_ready, k_done, k_out = sem("inv_ready"), sem("rs_ready"), sem("k_done"), sem("k_out")
        even_out, scaled = sem("even_out"), sem("scaled")
        steps = sem("steps")
        block = s.enter_context(nc.Block())
        N = 2 * TT

        @block.sync
        def _(sp):
            sp.dma_start(w3[0:FILT, :, :], I["hy_ffn_w3"].rearrange("k (g c) -> k g c", g=4)).then_inc(loaded, 16)
            sp.dma_start(w3[FILT:FILT + 1, :, :],
                         I["hy_ffn_b3"].rearrange("(o g c) -> o g c", o=1, g=4)).then_inc(loaded, 16)
            decay = I["hy_decay"].rearrange("d o c -> (d o) c")
            sp.dma_start(dec[:, :, :], decay.partition_broadcast(P)).then_inc(loaded, 16)
            sp.dma_start(negt[:, :], I["c_negt"]).then_inc(loaded, 16)
            sp.dma_start(notfirst[:, :], I["c_notfirst"]).then_inc(loaded, 16)

        @block.tensor
        def _(pe):
            pe.wait_ge(loaded, 80)
            for o in range(2):
                for t in range(TT):
                    n = o * TT + t
                    for d in range(2):
                        if n > 0:
                            pe.wait_ge(fb_ready, 2 * (n - 1) + d + 1)
                        nc.tensor.matmul(ps[:, d, :], h2[:, t * P:(t + 1) * P], w3[:, 2 * d + o, :],
                                         start=True, stop=True).then_inc(raw_done, 1)
                    for d in range(2):
                        pe.wait_ge(sq_ready, 2 * n + d + 1)
                        nc.tensor.matmul(pn[:, :], e.ones[:, :], sq[:, d, :], start=t == 0 and d == 0,
                                         stop=t == TT - 1 and d == 1).then_inc(sq_used, 1)
                pe.wait_ge(ab_ready, 2 * TT * (o + 1))
                for j in range(4):
                    m = o * 4 + j
                    part, f = j // 2, j % 2
                    table = (cos, sin)[part]
                    if m >= 2:
                        pe.wait_ge(k_out, 2 * (m - 1))
                    for t in range(TT):
                        last = nc.tensor.matmul(pk[:, m % 2, t // 2, :], table[:, t, f * P:(f + 1) * P],
                                                ab[:, part, t, :], start=t % 2 == 0, stop=t % 2 == 1)
                        if t % 2 == 1:
                            last.then_inc(k_done, 1)

        @block.scalar
        def _(act):
            act.wait_ge(loaded, 80)
            nc.scalar.activation(dec[:, :, :], dec[:, :, :], ACT.Abs).then_inc(dec_abs, 1)
            act.wait_ge(dec_abs, 1)
            for o in range(2):
                for t in range(TT):
                    n = o * TT + t
                    for d in range(2):
                        if n > 0:
                            act.wait_ge(fb_ready, 2 * (n - 1) + d + 1)
                        nc.scalar.activation(env[:, d, :], dec[:, 2 * d + o, :], ACT.Exp,
                                             scale=negt[:, t:t + 1]).then_inc(env_ready, 1)
                    for d in range(2):
                        act.wait_ge(fb_ready, 2 * n + d + 1)
                        if n > 0:
                            act.wait_ge(sq_used, 2 * (n - 1) + d + 1)
                        nc.scalar.activation(sq[:, d, :], fb[:, d, :], ACT.Square).then_inc(sq_ready, 1)
                act.wait_ge(inv_ready, o + 1)
                if o > 0:
                    act.wait_ge(scaled, 8 * o)
                nc.scalar.activation(rs[:, 1, :], rs[:, 0, :], ACT.Sqrt).then_inc(rs_ready, 1)
                for j in range(4):
                    m = o * 4 + j
                    act.wait_ge(k_done, 2 * m + 1)
                    if m >= 2:
                        act.wait_ge(k_out, 2 * (m - 1))
                    nc.scalar.activation(even[:, m % 2, :], pk[:, m % 2, 0, :], ACT.Copy, scale=1.0 / L)\
                        .then_inc(even_out, 1)

        @block.vector
        def _(dve):
            st = Steps(steps)
            for o in range(2):
                if o == 1:
                    dve.wait_ge(k_done, 8)
                for t in range(TT):
                    n = o * TT + t
                    for d in range(2):
                        dve.wait_ge(raw_done, 2 * n + d + 1)
                        dve.wait_ge(env_ready, 2 * n + d + 1)
                        if n > 0:
                            dve.wait_ge(sq_ready, 2 * (n - 1) + d + 1)
                            dve.wait_ge(ab_ready, 2 * n)
                        scalar = 1.0 if d == 0 else notfirst[:, t:t + 1]
                        nc.vector.scalar_tensor_tensor(fb[:, d, :], ps[:, d, :], scalar, env[:, d, :],
                                                       ALU.mult, ALU.mult).then_inc(fb_ready, 1)
                    dve.wait_ge(fb_ready, 2 * n + 2)
                    nc.vector.tensor_tensor(ab[:, 0, t, :], fb[:, 0, :], fb[:, 1, :], ALU.add).then_inc(ab_ready, 1)
                    nc.vector.tensor_tensor(ab[:, 1, t, :], fb[:, 0, :], fb[:, 1, :], ALU.subtract)\
                        .then_inc(ab_ready, 1)
                dve.wait_ge(sq_used, 2 * TT * (o + 1))
                dve.wait_ge(steps, st.mark(nc.vector.tensor_scalar(rs[:, 0, :], pn[:, :], EPS, None, ALU.add)))
                nc.vector.reciprocal(rs[:, 0, :], rs[:, 0, :]).then_inc(inv_ready, 1)
                for j in range(4):
                    m = o * 4 + j
                    part, f = j // 2, j % 2
                    dve.wait_ge(even_out, m + 1)
                    dve.wait_ge(k_done, 2 * m + 2)
                    ev, odd = even[:, m % 2, :], pk[:, m % 2, 1, :]
                    nc.vector.scalar_tensor_tensor(spec[:, o, part, f, :], odd, 1.0 / L, ev,
                                                   ALU.mult, ALU.add).then_inc(k_out, 1)
                    if part == 0:
                        ins = nc.vector.scalar_tensor_tensor(spec[:, o, part, 2 + f, :], odd, -1.0 / L, ev,
                                                             ALU.mult, ALU.add)
                    else:
                        ins = nc.vector.scalar_tensor_tensor(spec[:, o, part, 2 + f, :], odd, 1.0 / L, ev,
                                                             ALU.mult, ALU.subtract)
                    ins.then_inc(k_out, 1)

        @block.gpsimd
        def _(pool):
            for o in range(2):
                pool.wait_ge(rs_ready, o + 1)
                for j in range(4):
                    for i in range(2):
                        pool.wait_ge(k_out, 2 * (o * 4 + j) + i + 1)
                        d = spec[:, o, j // 2, 2 * i + j % 2, :]
                        nc.gpsimd.tensor_tensor(d, d, rs[:, 1, :], ALU.mult).then_inc(scaled, 1)


def hyena_long_conv(nc, e, o, z, gate, dst, cos, sin, cosT, sinT, spec):
    with ExitStack() as s:
        sb, pb, sem = opened(nc, s, f"hyl{o}")
        zt = sb("zt", [P, TT, D_HY])
        zf = sb("zf", [P, 2, 2, D_HY])
        yf = sb("yf", [P, 2, TT, D_HY])
        back = sb("back", [P, 2, 2, 2, D_HY])
        tmp = sb("tmp", [P, 4, D_HY])
        dz = zt[:, 0:2, :]
        pt = pb("pt", [P, 2, D_HY])
        pf = pb("pf", [P, 2, 2, D_HY])
        po = pb("po", [P, 2, L])
        turned, zt_ready, f_done, even_out = sem("turned"), sem("zt_ready"), sem("f_done"), sem("even_out")
        zf_ready, prod, yf_ready, back_ready = sem("zf"), sem("prod"), sem("yf"), sem("back")
        real_ready = sem("real")
        o_done, o_out, gated = sem("o_done"), sem("o_out"), sem("gated")
        block = s.enter_context(nc.Block())
        M = TT // 2

        @block.tensor
        def _(pe):
            for t in range(TT):
                if t >= 2:
                    pe.wait_ge(zt_ready, t - 1)
                at = t % M * 2 * P + t // M
                for c in range(HT):
                    last = nc.tensor.transpose(pt[:, t % 2, c * P:(c + 1) * P], z[:, c, at:at + 2 * P - 1:2],
                                               e.ident[:, :])
                last.then_inc(turned, 1)
            pe.wait_ge(zt_ready, TT)
            for f in range(M):
                for part, table in enumerate((cos, sin)):
                    if f > 0:
                        pe.wait_ge(zf_ready, 4 * (f - 1) + 2 * part + 2)
                    for t in range(TT):
                        last = nc.tensor.matmul(pf[:, part, t // M, :], table[:, t, f * P:(f + 1) * P], zt[:, t, :],
                                                start=t % M == 0, stop=t % M == M - 1)
                        if t % M == M - 1:
                            last.then_inc(f_done, 1)
            for c in range(HT):
                if c >= 2:
                    pe.wait_ge(o_out, c - 1)
                for odd in range(2):
                    half = slice(odd * L // 2, (odd + 1) * L // 2)
                    for f in range(M):
                        pe.wait_ge(back_ready, 4 * f + 2 * odd + 2)
                        for part, table in enumerate((cosT, sinT)):
                            last = nc.tensor.matmul(po[:, c % 2, half], back[:, odd, part, f, c * P:(c + 1) * P],
                                                    table[:, f, half], start=part + f == 0,
                                                    stop=part == 1 and f == M - 1)
                last.then_inc(o_done, 1)

        @block.scalar
        def _(act):
            for t in range(TT):
                act.wait_ge(turned, t + 1)
                nc.scalar.activation(zt[:, t, :], pt[:, t % 2, :], ACT.Copy).then_inc(zt_ready, 1)
            for f in range(M):
                for part in range(2):
                    act.wait_ge(f_done, 4 * f + 2 * part + 1)
                    if f > 0:
                        act.wait_ge(prod, 8 * f)
                    nc.scalar.activation(zf[:, part, 0, :], pf[:, part, 0, :], ACT.Copy).then_inc(even_out, 1)

        @block.vector
        def _(dve):
            for f in range(M):
                for part in range(2):
                    dve.wait_ge(f_done, 4 * f + 2 * part + 2)
                    dve.wait_ge(even_out, 2 * f + part + 1)
                    ev, odd = zf[:, part, 0, :], pf[:, part, 1, :]
                    a, b = (ev, odd) if part == 0 else (odd, ev)
                    nc.vector.tensor_tensor(zf[:, part, 1, :], a, b, ALU.subtract).then_inc(zf_ready, 1)
                    dve.wait_ge(zf_ready, 4 * f + 2 * part + 1)
                    nc.vector.tensor_tensor(ev, ev, odd, ALU.add).then_inc(zf_ready, 1)
                for i in range(2):
                    n = 2 * f + i
                    dve.wait_ge(zf_ready, 4 * f + 4)
                    kr, ks = spec[:, o, 0, 2 * i + f, :], spec[:, o, 1, 2 * i + f, :]
                    for done_before, js in ((yf_ready, (2, 3)), (real_ready, (0, 1))):
                        if n > 0:
                            dve.wait_ge(done_before, n)
                        for j in js:
                            a, b = ((0, kr), (1, ks), (0, ks), (1, kr))[j]
                            nc.vector.tensor_tensor(tmp[:, j, :], zf[:, a, i, :], b, ALU.mult).then_inc(prod, 1)
                    dve.wait_ge(prod, 4 * n + 4)
                    nc.vector.tensor_tensor(yf[:, 0, 2 * i + f, :], tmp[:, 0, :], tmp[:, 1, :], ALU.subtract)\
                        .then_inc(real_ready, 1)
                dve.wait_ge(real_ready, 2 * f + 2)
                dve.wait_ge(yf_ready, 2 * f + 2)
                for odd in range(2):
                    for part in range(2):
                        op = ALU.add if odd == part else ALU.subtract
                        nc.vector.tensor_tensor(back[:, odd, part, f, :], yf[:, part, f, :], yf[:, part, 2 + f, :], op)\
                            .then_inc(back_ready, 1)
            for c in range(HT):
                dve.wait_ge(o_done, c + 1)
                if c >= 2:
                    dve.wait_ge(gated, c - 1)
                sums = po[:, c % 2, :].rearrange("p (two n) -> p n two", two=2)
                nc.vector.scalar_tensor_tensor(dz[:, c % 2, :].rearrange("p (n two) -> p n two", two=2),
                                               z[:, c, :].rearrange("p (n two) -> p n two", two=2),
                                               col(e, "hy_bias_d", o * HT + c), sums, ALU.mult, ALU.add).then_inc(o_out, 1)
                dve.wait_ge(o_out, c + 1)
                nc.vector.tensor_tensor(dst[:, c, :], dz[:, c % 2, :], gate[:, c, :], ALU.mult).then_inc(gated, 1)

        @block.gpsimd
        def _(pool):
            for n in range(TT):
                f = n % 2 * 2 + n // 2
                pool.wait_ge(prod, 4 * n + 2)
                nc.gpsimd.tensor_tensor(yf[:, 1, f, :], tmp[:, 2, :], tmp[:, 3, :], ALU.add)\
                    .then_inc(yf_ready, 1)


def hyena_branch(nc, e, I, h, merged, root):
    with ExitStack() as s:
        keep = lambda name, shape: s.enter_context(nc.sbuf_tensor(f"hy_{name}", shape, F32))
        z2 = keep("z2", [P, HT, L])
        with ExitStack() as s2:
            part = lambda name, shape: s2.enter_context(nc.sbuf_tensor(f"hy_{name}", shape, F32))
            uc = part("uc", [P, N_HY // P, L])
            cos, sin = part("cos", [P, TT, L // 2]), part("sin", [P, TT, L // 2])
            cosT, sinT = part("cosT", [P, TT // 2, L]), part("sinT", [P, TT // 2, L])
            table = lambda name: I[name].rearrange("(t p) f -> p t f", p=P)
            tables = [(cos[:, :, :], table("c_cos")), (sin[:, :, :], table("c_sin")),
                      (cosT[:, :, :], table("c_cosT")), (sinT[:, :, :], table("c_sinT"))]
            h2 = part("h2", [FILT + 1, L])
            conv = lambda i: (lambda j: col_at(e.cols, COL["hy_conv_w"] + i * (N_HY // P) + j))
            with nc.sbuf_tensor("hy_u", [P, N_HY // P, L], F32) as u:
                gemm(nc, e, "hy_in", I["w_in"][:, 0:N_HY], DT, h, 3, 2, 2, "copy", dst=u,
                     before=normed(nc, e, e.x, DT, h, lambda k: col(e, "mix_norm", k), root=root),
                     taps=(lambda j: tile_at(uc, j), conv(1), conv(0), conv(2),
                           lambda j: col_at(e.cols, COL["hy_conv_b"] + j)))
            hyena_filter_mlp(nc, e, I, h2, tables)
            spec = part("spec", [P, 2, 2, TT, D_HY])
            hyena_spectra(nc, e, I, h2, cos, sin, spec)
            x1, x2, v = uc[:, 0:HT, :], uc[:, HT:2 * HT, :], uc[:, 2 * HT:3 * HT, :]
            hyena_long_conv(nc, e, 0, v, x1, x1, cos, sin, cosT, sinT, spec)
            hyena_long_conv(nc, e, 1, x1, x2, z2, cos, sin, cosT, sinT, spec)
        gated_output(nc, e, "hy", I["w_in"][:, N_HY + N_RW:N_HY + N_RW + D], h, None, I["hy_out"], HT, z2, merged, 0)


def gated_output(nc, e, tag, w_gate, h, before, w_o, k_tiles, z, merged, add):
    with ExitStack() as s:
        g = s.enter_context(nc.sbuf_tensor(f"{tag}_sig", [P, DT, L], F32))
        stream = Stream(nc, e, s, tag, DT * 2 * P)
        gemm(nc, e, f"{tag}_gate", w_gate, DT, h, 2, 2, 2, "copy", dst=g, func=ACT.Sigmoid, before=before,
             stream=stream, following=(w_o, k_tiles, 2 * P))
        zp = two_parts(nc, s, f"{tag}_z", k_tiles)
        gemm(nc, e, f"{tag}_out", w_o, k_tiles, zp, 2, 2, 2, "gate", dst=merged, gate=g, factor=add,
             before=cut(nc, e, z, k_tiles, zp), stream=stream)



def rwkv_inputs(nc, e, I, h, rkv, lora, root):
    n = MU_ROWS + 1
    mu = COL["rw_mu"]
    with nc.sbuf_tensor("rw_u", [P, n, L], F32) as u:
        result = lambda j: lora[:, j - 3 * RT, :] if isinstance(j, int) else tile_at(rkv, j)
        gemm(nc, e, "rw_in", I["w_in"][:, N_HY:N_HY + n * P], DT, h, n // 4, 2, 2, "copy", dst=u,
             before=normed(nc, e, e.x, DT, h, lambda k: col(e, "mix_norm", k), root=root, known=True),
             taps=(result, lambda j: col_at(e.shift_keep, j), lambda j: col_at(e.cols, mu + j),
                   lambda j: col_at(e.cols, mu + n + j), None))


def rwkv_features(nc, e, I, rkv, lora, lw, a, g, kk, bonus):
    r, k, v = rkv[:, 0:RT, :], rkv[:, RT:2 * RT, :], rkv[:, 2 * RT:3 * RT, :]
    us = lora
    WD, AD, GD = 0, 1, 2
    rest = N_RW - MU_ROWS * P
    with ExitStack() as s:
        sb, pb, sem = opened(nc, s, "rwf")
        w2, a2 = sb("w2", [P, D_RW]), sb("a2", [P, D_RW])
        g2, g2b = sb("g2", [P, D_RW]), sb("g2b", [rest, D_RW])
        kks = sb("kks", [P, RT, L])
        sq = sb("sq", [P, RT, L])
        nrm = sb("nrm", [P, RT, L])
        kd = sb("kd", [P, 2, L])
        rk = sb("rk", [P, 2, L])
        ps = pb("ps", [P, 4, L])
        pn = pb("pn", [P, RT, L])
        loaded, act_in, done, taken = sem("loaded"), sem("act_in"), sem("done"), sem("taken")
        kks_ready, sq_ready, n_done, n_root, steps = sem("kks"), sem("sq"), sem("n_done"), sem("n_root"), sem("steps")
        rk_ready, b_done, b_out = sem("rk"), sem("b_done"), sem("b_out")
        block = s.enter_context(nc.Block())

        @block.sync
        def _(sp):
            sp.dma_start(w2[:, :], I["rw_w2"].rearrange("d r c -> (d r) c")).then_inc(loaded, 16)
            sp.dma_start(a2[:, :], I["rw_a2"].rearrange("d r c -> (d r) c")).then_inc(loaded, 16)
            sp.dma_start(g2[:, :], I["rw_g2"][0:P, :]).then_inc(loaded, 16)
            sp.dma_start(g2b[:, :], I["rw_g2"][P:P + rest, :]).then_inc(loaded, 16)

        jobs = [("a", d, c) for c in range(RT) for d in range(2)] + \
               [("w", d, c) for d in range(2) for c in range(RT)] + [("g", 0, c) for c in range(RT)]

        @block.tensor
        def _(pe):
            for c in range(RT):
                pe.wait_ge(sq_ready, c + 1)
                nc.tensor.matmul(pn[:, c, :], e.heads[:, :], sq[:, c, :], start=True, stop=True)\
                    .then_inc(n_done, 1)
            pe.wait_ge(loaded, 64)
            for n, (kind, d, c) in enumerate(jobs):
                if n >= 4:
                    pe.wait_ge(taken, n - 3)
                cs = slice(c * P, (c + 1) * P)
                hd = slice(64 * d, 64 * d + 64)
                if kind == "g":
                    pe.wait_ge(act_in, 3)
                    nc.tensor.matmul(ps[:, n % 4, :], g2[:, cs], us[:, GD, :], start=True, stop=False)
                    last = nc.tensor.matmul(ps[:, n % 4, :], g2b[:, cs], us[0:rest, GD + 1, :], start=False, stop=True)
                else:
                    wt, src = (w2, WD) if kind == "w" else (a2, AD)
                    if kind == "w":
                        pe.wait_ge(act_in, 1)
                    last = nc.tensor.matmul(ps[:, n % 4, :], wt[hd, cs], us[hd, src, :], start=True, stop=True)
                last.then_inc(done, 1)
            for c in range(RT):
                pe.wait_ge(rk_ready, c + 1)
                pe.wait_ge(n_root, c + 1)
                nc.tensor.matmul(pn[:, c, :], e.heads[:, :], rk[:, c % 2, :], start=True, stop=True)\
                    .then_inc(b_done, 1)

        @block.scalar
        def _(act):
            for c in range(RT):
                nc.scalar.activation(sq[:, c, :], k[:, c, :], ACT.Square, scale=col(e, "rw_k_k", c))\
                    .then_inc(sq_ready, 1)
            for c in range(RT):
                act.wait_ge(n_done, c + 1)
                nc.scalar.activation(nrm[:, c, :], pn[:, c, :], ACT.Sqrt).then_inc(n_root, 1)
            nc.scalar.activation(us[:, WD, :], us[:, WD, :], ACT.Tanh).then_inc(act_in, 1)
            nc.scalar.activation(us[:, GD, :], us[:, GD, :], ACT.Sigmoid).then_inc(act_in, 1)
            nc.scalar.activation(us[0:rest, GD + 1, :], us[0:rest, GD + 1, :], ACT.Sigmoid).then_inc(act_in, 1)
            for n, (kind, d, c) in enumerate(jobs):
                act.wait_ge(done, n + 1)
                if kind == "g":
                    ins = nc.scalar.activation(g[:, c, :], ps[:, n % 4, :], ACT.Copy)
                else:
                    dst, bias = (lw, "rw_w0") if kind == "w" else (a, "rw_a0")
                    ins = nc.scalar.activation(dst[:, d, c, :], ps[:, n % 4, :], ACT.Sigmoid,
                                               bias=col(e, bias, d * RT + c))
                ins.then_inc(taken, 1)

        @block.gpsimd
        def _(pool):
            for c in range(RT):
                nc.gpsimd.tensor_scalar(kks[:, c, :], k[:, c, :], col(e, "rw_k_k", c), None, ALU.mult)\
                    .then_inc(kks_ready, 1)
            for d in range(2):
                for c in range(RT):
                    pool.wait_ge(taken, 2 * RT + d * RT + c + 1)
                    nc.gpsimd.tensor_scalar(lw[:, d, c, :], lw[:, d, c, :], LOG_DECAY_MAX, None, ALU.mult)

        @block.vector
        def _(dve):
            st = Steps(steps)

            def then(ins):
                dve.wait_ge(steps, st.mark(ins))

            for c in range(RT):
                dve.wait_ge(n_root, c + 1)
                then(nc.vector.tensor_scalar(nrm[:, c, :], nrm[:, c, :], 1e-12, None, ALU.max))
                then(nc.vector.reciprocal(nrm[:, c, :], nrm[:, c, :]))
                dve.wait_ge(kks_ready, c + 1)
                nc.vector.tensor_tensor(kk[:, c, :], kks[:, c, :], nrm[:, c, :], ALU.mult)
            for c in range(RT):
                dve.wait_ge(taken, 2 * c + 2)
                then(nc.vector.scalar_tensor_tensor(kd[:, 0, :], a[:, 0, c, :], -2.0, a[:, 1, c, :],
                                                    ALU.add, ALU.add))
                then(nc.vector.tensor_scalar(kd[:, 0, :], kd[:, 0, :], col(e, "rw_k_a", c), 2.0,
                                             ALU.mult, ALU.add))
                then(nc.vector.tensor_tensor(kd[:, 0, :], kd[:, 0, :], k[:, c, :], ALU.mult))
                if c >= 2:
                    dve.wait_ge(b_done, c - 1)
                nc.vector.scalar_tensor_tensor(rk[:, c % 2, :], kd[:, 0, :], col(e, "rw_r_k", c), r[:, c, :],
                                               ALU.mult, ALU.mult).then_inc(rk_ready, 1)
                dve.wait_ge(rk_ready, c + 1)
            for c in range(RT):
                dve.wait_ge(b_done, c + 1)
                nc.vector.tensor_tensor(bonus[:, c, :], pn[:, c, :], v[:, c, :], ALU.mult).then_inc(b_out, 1)


class Scaled:
    pass


def scaled_programs(nc, e, sb, sem, d, half, nb, rkv, lw, a, kk, reset, ar, kb, pend):
    toks = slice(half * LH, half * LH + LH)
    r, k = rkv[:, 0:RT, toks], rkv[:, RT:2 * RT, toks]
    lw, a, kk = lw[:, :, :, toks], a[:, :, :, toks], kk[:, :, toks]
    chunks = lambda t: t.rearrange("p (n c) -> p n c", c=CH)
    N = Scaled()
    inc, kd = (sb(f"s_{n}", [P, nb, LH]) for n in ("inc", "kd"))
    inv = kb[:, :, :, CH:2 * CH]
    steps, pin, pout, kd_ready = sem("s_steps"), sem("s_logs"), sem("s_powers"), sem("s_kd")
    pn, pn_used = sem("s_inverse"), sem("s_pn_used")
    st = Steps(steps)

    def pool_program(pool):
        for c in range(RT):
            b = c % nb
            if c >= nb:
                pool.wait_ge(pn_used, c - nb + 1)
            nc.gpsimd.tensor_scalar(kd[:, b, :], a[:, d, c, :], -1.0, col(e, "rw_k_a", c),
                                    ALU.add, ALU.mult).then_inc(kd_ready, 1)
            pool.wait_ge(kd_ready, 3 * c + 1)
            nc.gpsimd.tensor_scalar(kd[:, b, :], kd[:, b, :], 1.0, None, ALU.add).then_inc(kd_ready, 1)
            pool.wait_ge(kd_ready, 3 * c + 2)
            nc.gpsimd.tensor_tensor(kd[:, b, :], kd[:, b, :], k[:, c, :], ALU.mult).then_inc(kd_ready, 1)

    def act_program(act, c):
        b = c % nb
        act.wait_ge(pin, c + 1)
        if c >= nb:
            act.wait_ge(pn_used, c - nb + 1)
        nc.scalar.activation(inv[:, c, :, :], chunks(inc[:, b, :]), ACT.Exp, scale=-1.0).then_inc(pn, 1)
        act.wait_ge(pn, c + 1)
        nc.scalar.activation(inc[:, b, :], inc[:, b, :], ACT.Exp).then_inc(pout, 1)
        nc.scalar.activation(ar[:, c, :, 0:CH], ar[:, c, :, 0:CH], ACT.Exp).then_inc(pout, 1)

    def then(dve, ins):
        dve.wait_ge(steps, st.mark(ins))

    def logs(dve, c):
        b = c % nb
        w, exc = lw[:, d, c, :], ar[:, c, :, 0:CH]
        then(dve, nc.vector.tensor_tensor_scan(inc[:, b, :], reset[:, :], w, 0.0, ALU.mult, ALU.add))
        if d == 0:
            nc.vector.tensor_tensor(exc, chunks(inc[:, b, :]), chunks(w), ALU.subtract).then_inc(pin, 1)
        else:
            whole = chunks(inc[:, b, :])[:, :, CH - 1:CH]
            then(dve, nc.vector.tensor_copy(pend[:, c, :], whole.rearrange("p n o -> p (n o)")))
            then(dve, nc.vector.tensor_tensor(exc, pend[:, c, :].unsqueeze(2).to_broadcast([P, HCH, CH]),
                                              chunks(inc[:, b, :]), ALU.subtract))
            nc.vector.tensor_tensor(chunks(inc[:, b, :]), exc, chunks(w), ALU.add).then_inc(pin, 1)

    def products(dve, c):
        b = c % nb
        dve.wait_ge(pout, 2 * c + 2)
        dve.wait_ge(kd_ready, 3 * c + 3)
        nc.vector.scalar_tensor_tensor(ar[:, c, :, 0:CH], chunks(kk[:, c, :]), -1.0, ar[:, c, :, 0:CH],
                                       ALU.mult, ALU.mult)
        nc.vector.tensor_tensor(ar[:, c, :, CH:2 * CH], chunks(r[:, c, :]), chunks(inc[:, b, :]), ALU.mult)
        then(dve, nc.vector.tensor_tensor(kb[:, c, :, 0:CH], chunks(kd[:, b, :]), inv[:, c, :, :], ALU.mult))
        at = CH - 1 if d == 0 else 0
        nc.vector.tensor_copy(pend[:, c, :].unsqueeze(2), chunks(inc[:, b, :])[:, :, at:at + 1])
        then(dve, nc.vector.tensor_tensor(chunks(kd[:, b, :]), chunks(kk[:, c, :]), chunks(a[:, d, c, :]), ALU.mult))
        nc.vector.tensor_tensor(inv[:, c, :, :], inv[:, c, :, :], chunks(kd[:, b, :]), ALU.mult).then_inc(pn_used, 1)
        dve.wait_ge(pn_used, c + 1)

    N.pool, N.act, N.logs, N.products = pool_program, act_program, logs, products
    return N


def rwkv_scaled(nc, e, d, half, *operands):
    with ExitStack() as s:
        sb, pb, sem = opened(nc, s, f"rws{d}{half}")
        N = scaled_programs(nc, e, sb, sem, d, half, 1, *operands)
        block = s.enter_context(nc.Block())
        block.gpsimd(N.pool)

        @block.scalar
        def _(act):
            for c in range(RT):
                N.act(act, c)

        @block.vector
        def _(dve):
            for c in range(RT):
                N.logs(dve, c)
                N.products(dve, c)


def rwkv_matrices(nc, e, d, half, rkv, ar, kb, scan_mask, gt, kbt, vu, bv):
    v = rkv[:, 2 * RT:3 * RT, half * LH:half * LH + LH]
    with ExitStack() as s:
        sb, pb, sem = opened(nc, s, f"rwm{d}{half}")
        pg = pb("pg", [P, 2, 2, HCH, P])
        pk, pv, pbv = pb("pk", [P, 2, HCH, P]), pb("pv", [CH, HCH, P]), pb("pbv", [P, L])
        g_done, k_done, v_done = sem("g_done"), sem("k_done"), sem("v_done")
        g_out, k_out, v_out = sem("g_out"), sem("k_out"), sem("v_out")
        b_done, b_out = sem("b_done"), sem("b_out")
        block = s.enter_context(nc.Block())
        hs = [slice(0, 64), slice(64, 128)]

        @block.tensor
        def _(pe):
            def b_times_v(c):
                pe.wait_ge(g_out, 2 * c + 2)
                pe.wait_ge(v_out, c + 1)
                if c >= 1:
                    pe.wait_ge(b_out, c)
                for ch in range(HCH):
                    for hd in range(2):
                        last = nc.tensor.matmul(pbv[hs[hd], ch * CH:(ch + 1) * CH], gt[0:CH, c, ch, hd, 0:CH],
                                                vu[0:CH, c, ch, hs[hd]], start=True, stop=True)
                last.then_inc(b_done, 1)

            for c in range(RT):
                for hd in range(2):
                    if c >= 2:
                        pe.wait_ge(g_out, 2 * (c - 2) + hd + 1)
                    for ch in range(HCH):
                        last = nc.tensor.matmul(pg[:, c % 2, hd, ch, :], kb[hs[hd], c, ch, :], ar[hs[hd], c, ch, :],
                                                start=True, stop=True)
                    last.then_inc(g_done, 1)
                if c >= 2:
                    pe.wait_ge(k_out, c - 1)
                for ch in range(HCH):
                    last = nc.tensor.transpose(pk[:, c % 2, ch, :], kb[:, c, ch, :], e.ident[:, :])
                last.then_inc(k_done, 1)
                if c > 0:
                    pe.wait_ge(v_out, c)
                for ch in range(HCH):
                    last = nc.tensor.transpose(pv[:, ch, :], v[:, c, ch * CH:(ch + 1) * CH], e.ident[:, :])
                last.then_inc(v_done, 1)
                if c > 0:
                    b_times_v(c - 1)
            b_times_v(RT - 1)

        @block.scalar
        def _(act):
            for c in range(RT):
                act.wait_ge(k_done, c + 1)
                nc.scalar.activation(kbt[:, c, :, :], pk[:, c % 2, :, :], ACT.Copy).then_inc(k_out, 1)
                act.wait_ge(b_done, c + 1)
                nc.scalar.activation(bv[:, :, c, :], pbv[:, 0:LH].rearrange("p (n i) -> p n i", n=HCH),
                                     ACT.Copy).then_inc(b_out, 1)

        @block.vector
        def _(dve):
            for c in range(RT):
                for hd in range(2):
                    dve.wait_ge(g_done, 2 * c + hd + 1)
                    mask = scan_mask[:, d, :].unsqueeze(1).to_broadcast([P, HCH, P])
                    nc.vector.tensor_tensor(gt[:, c, :, hd, :], pg[:, c % 2, hd, :, :], mask, ALU.mult)\
                        .then_inc(g_out, 1)
                dve.wait_ge(v_done, c + 1)
                nc.vector.tensor_copy(vu[0:CH, c, :, :], pv[:, :, :]).then_inc(v_out, 1)


def rwkv_inverse(nc, e, d, half, gt, levels, xt, spare, xw):
    with ExitStack() as s:
        sb, pb, sem = opened(nc, s, f"rwi{d}{half}")
        at, a = spare[:, 0:2, :, :], spare[:, 2:4, :, :]
        x, w = xw[:, 0:2, :, :], xw[:, 2:4, :, :]
        pw, pt, px = (pb(n, [P, 2, 4, P]) for n in ("pw", "pt", "px"))
        zeroed, at_ready, a_turned, a_ready = sem("zeroed"), sem("at"), sem("a_turned"), sem("a")
        start_ready, w_done, w_out = sem("start"), sem("w_done"), sem("w_out")
        t_done, t_out, x_done, x_out, steps = sem("t_done"), sem("t_out"), sem("x_done"), sem("x_out"), sem("steps")
        block = s.enter_context(nc.Block())
        rounds = RT // 2
        K = LEVELS - 1
        below, above = (levels[:, d, :, :], levels[:, 1 - d, :, :])
        mask4 = lambda m: m.unsqueeze(1).to_broadcast([P, 4, P])

        @block.tensor
        def _(pe):
            for c in range(rounds):
                for q in range(2):
                    pe.wait_ge(at_ready, 2 * c + q + 1)
                    if c > 0:
                        pe.wait_ge(x_out, (K - 1) * (2 * (c - 1) + q + 1))
                    for m in range(4):
                        last = nc.tensor.transpose(px[:, q, m, :], at[:, q, m, :], e.ident[:, :])
                    last.then_inc(a_turned, 1)
                for k in range(K):
                    for q in range(2):
                        i = (c * K + k) * 2 + q
                        if k == 0:
                            pe.wait_ge(start_ready, 2 * c + q + 1)
                        else:
                            pe.wait_ge(t_out, i - 1)
                            pe.wait_ge(x_out, (c * (K - 1) + k - 1) * 2 + q + 1)
                        for m in range(4):
                            last = nc.tensor.matmul(pw[:, q, m, :], a[:, q, m, :], xt[:, 2 * c + q, m, :],
                                                    start=True, stop=True)
                        last.then_inc(w_done, 1)
                    for q in range(2):
                        i = (c * K + k) * 2 + q
                        pe.wait_ge(w_out, i + 1)
                        for m in range(4):
                            last = nc.tensor.matmul(pt[:, q, m, :], x[:, q, m, :], w[:, q, m, :],
                                                    start=True, stop=True)
                        last.then_inc(t_done, 1)
                        if k < K - 1:
                            for m in range(4):
                                last = nc.tensor.matmul(px[:, q, m, :], w[:, q, m, :], x[:, q, m, :],
                                                        start=True, stop=True)
                            last.then_inc(x_done, 1)

        @block.scalar
        def _(act):
            for c in range(rounds):
                for q in range(2):
                    act.wait_ge(a_turned, 2 * c + q + 1)
                    if c > 0:
                        act.wait_ge(w_done, 2 * K * c)
                    nc.scalar.activation(a[:, q, :, :], px[:, q, :, :], ACT.Copy).then_inc(a_ready, 1)

        @block.vector
        def _(dve):
            st = Steps(steps)
            nc.vector.memset(at[:, :, :, :], 0.0).then_inc(zeroed, 1)
            dve.wait_ge(zeroed, 1)
            for c in range(rounds):
                for q in range(2):
                    if c > 0:
                        dve.wait_ge(start_ready, 2 * c)
                    for hd in range(2):
                        hs = slice(64 * hd, 64 * hd + 64)
                        ins = nc.vector.tensor_copy(at[hs, q, :, hs], gt[CH:P, 2 * c + q, :, hd, 0:CH])
                        st.mark(ins) if hd == 0 else ins.then_inc(at_ready, 1)
                for q in range(2):
                    dve.wait_ge(a_ready, 2 * c + q + 1)
                    dve.wait_ge(at_ready, 2 * c + q + 1)
                    dve.wait_ge(steps, st.n)
                    if c > 0:
                        dve.wait_ge(t_done, 2 * K * (c - 1) + 2 * K)
                    xq, xtq = x[:, q, :, :], xt[:, 2 * c + q, :, :]
                    st.mark(nc.vector.tensor_tensor(xq, a[:, q, :, :], mask4(below[:, 0, :]), ALU.mult))
                    st.mark(nc.vector.tensor_tensor(xtq, at[:, q, :, :], mask4(above[:, 0, :]), ALU.mult))
                    dve.wait_ge(steps, st.n)
                    st.mark(nc.vector.tensor_tensor(xq, xq, mask4(e.ident[:, :]), ALU.add))
                    nc.vector.tensor_tensor(xtq, xtq, mask4(e.ident[:, :]), ALU.add).then_inc(start_ready, 1)
                    dve.wait_ge(steps, st.n)
                for k in range(K):
                    for q in range(2):
                        i = (c * K + k) * 2 + q
                        dve.wait_ge(w_done, i + 1)
                        if i >= 2:
                            dve.wait_ge(t_done, i - 1)
                        nc.vector.tensor_tensor(w[:, q, :, :], pw[:, q, :, :], mask4(above[:, k + 1, :]),
                                                ALU.mult).then_inc(w_out, 1)
                    for q in range(2):
                        i = (c * K + k) * 2 + q
                        xq, xtq = x[:, q, :, :], xt[:, 2 * c + q, :, :]
                        dve.wait_ge(t_done, i + 1)
                        nc.vector.tensor_tensor(xtq, xtq, pt[:, q, :, :], ALU.add).then_inc(t_out, 1)
                        if k < K - 1:
                            dve.wait_ge(x_done, (c * (K - 1) + k) * 2 + q + 1)
                            nc.vector.tensor_tensor(xq, xq, px[:, q, :, :], ALU.add).then_inc(x_out, 1)


def rwkv_chain(nc, e, d, half, state, ar, gt, kbt, xt, vu, bv, pend, y, following):
    with ExitStack() as s:
        sb, pb, sem = opened(nc, s, f"rwc{d}{half}")
        first = half == d
        rhs = sb("rhs", [P, RT, CH])
        grown = sb("grown", [P, RT, CH])
        pr, pu, py, pt = (pb(n, [P, RT, CH]) for n in ("pr", "pu", "py", "pt"))
        zeroed, r_done, r_out, u_done, u_out = sem("zeroed"), sem("r_done"), sem("r_out"), sem("u_done"), sem("u_out")
        u_out2, y_done, y_out = sem("u_out2"), sem("y_done"), sem("y_out")
        t_done, grown_ready, state_ready = sem("t_done"), sem("grown"), sem("state_ready")
        ahead = scaled_programs(nc, e, sb, sem, *following) if following else None
        block = s.enter_context(nc.Block())
        order = list(range(HCH)) if d == 0 else list(range(HCH - 1, -1, -1))
        hs = [slice(0, 64), slice(64, 128)]

        @block.tensor
        def _(pe):
            if first:
                pe.wait_ge(zeroed, 1)
            for n, ch in enumerate(order):
                if n > 0:
                    pe.wait_ge(state_ready, n)
                    pe.wait_ge(r_out, n)
                for c in range(RT):
                    for hd in range(2):
                        last = nc.tensor.matmul(pr[hs[hd], c, :], ar[hs[hd], c, ch, 0:CH], state[hs[hd], n % 2, c, :],
                                                start=True, stop=True)
                last.then_inc(r_done, 1)
                pe.wait_ge(r_out, n + 1)
                if n > 0:
                    pe.wait_ge(u_out, n)
                    pe.wait_ge(u_out2, n)
                for c in range(RT):
                    last = nc.tensor.matmul(pu[:, c, :], xt[:, c, ch, :], rhs[:, c, :], start=True, stop=True)
                last.then_inc(u_done, 1)
                pe.wait_ge(u_out, n + 1)
                pe.wait_ge(u_out2, n + 1)
                if n > 0:
                    pe.wait_ge(grown_ready, n)
                for c in range(RT):
                    for hd in range(2):
                        last = nc.tensor.matmul(pt[hs[hd], c, :], kbt[:, c, ch, hs[hd]], vu[:, c, ch, hs[hd]],
                                                start=True, stop=True)
                last.then_inc(t_done, 1)
                if n > 0:
                    pe.wait_ge(y_out, n)
                for c in range(RT):
                    for hd in range(2):
                        nc.tensor.matmul(py[hs[hd], c, :], vu[:, c, ch, hs[hd]], gt[:, c, ch, hd, CH:2 * CH],
                                         start=True, stop=False)
                        last = nc.tensor.matmul(py[hs[hd], c, :], state[hs[hd], n % 2, c, :], ar[hs[hd], c, ch, CH:2 * CH],
                                                start=False, stop=True)
                last.then_inc(y_done, 1)

        @block.scalar
        def _(act):
            for n, ch in enumerate(order):
                act.wait_ge(u_done, n + 1)
                nc.scalar.activation(vu[CH:P, :, ch, 0:CH], pu[0:CH, :, :], ACT.Copy).then_inc(u_out, 1)
                if ahead:
                    ahead.act(act, n)

        @block.vector
        def _(dve):
            if first:
                nc.vector.memset(state[:, 0, :, :], 0.0).then_inc(zeroed, 1)
                dve.wait_ge(zeroed, 1)
            for n, ch in enumerate(order):
                dve.wait_ge(r_done, n + 1)
                if n > 0:
                    dve.wait_ge(u_done, n)
                nc.vector.tensor_tensor(rhs[:, :, :], bv[:, ch, :, :], pr[:, :, :], ALU.add).then_inc(r_out, 1)
                if ahead:
                    ahead.logs(dve, n)
                dve.wait_ge(u_done, n + 1)
                nc.vector.tensor_copy(vu[CH:P, :, ch, CH:P], pu[CH:P, :, :]).then_inc(u_out2, 1)
                dve.wait_ge(t_done, n + 1)
                if n > 0:
                    dve.wait_ge(state_ready, n)
                nc.vector.tensor_tensor(grown[:, :, :], state[:, n % 2, :, :], pt[:, :, :], ALU.add)\
                    .then_inc(grown_ready, 1)
                dve.wait_ge(grown_ready, n + 1)
                if n > 0:
                    dve.wait_ge(y_done, n)
                decay = pend[:, :, ch:ch + 1].to_broadcast([P, RT, CH])
                nc.vector.tensor_tensor(state[:, (n + 1) % 2, :, :], grown[:, :, :], decay, ALU.mult)\
                    .then_inc(state_ready, 1)
                if ahead:
                    ahead.products(dve, n)
                dve.wait_ge(y_done, n + 1)
                ys = y[:, :, half * LH + ch * CH:half * LH + (ch + 1) * CH]
                if d == 0:
                    nc.vector.tensor_copy(ys, py[:, :, :]).then_inc(y_out, 1)
                else:
                    nc.vector.tensor_tensor(ys, ys, py[:, :, :], ALU.add).then_inc(y_out, 1)
        if ahead:
            block.gpsimd(ahead.pool)


def rwkv_group_norm(nc, e, y, bonus, g):
    with ExitStack() as s:
        sb, pb, sem = opened(nc, s, "rwn")
        cen, sq, rs = sb("cen", [P, RT, L]), sb("sq", [P, RT, L]), sb("rs", [P, RT, L])
        ps, pv = pb("ps", [P, 2, L]), pb("pv", [P, 2, L])
        m_done, cen_ready, sq_ready, v_done = sem("m_done"), sem("cen"), sem("sq"), sem("v_done")
        inv_ready, rs_ready, steps = sem("inv"), sem("rs_ready"), sem("steps")
        block = s.enter_context(nc.Block())

        @block.tensor
        def _(pe):
            for c in range(RT):
                if c >= 2:
                    pe.wait_ge(cen_ready, c - 1)
                nc.tensor.matmul(ps[:, c % 2, :], e.heads[:, :], y[:, c, :], start=True, stop=True).then_inc(m_done, 1)
            for c in range(RT):
                pe.wait_ge(sq_ready, c + 1)
                if c >= 2:
                    pe.wait_ge(inv_ready, c - 1)
                nc.tensor.matmul(pv[:, c % 2, :], e.heads[:, :], sq[:, c, :], start=True, stop=True).then_inc(v_done, 1)

        @block.scalar
        def _(act):
            for c in range(RT):
                act.wait_ge(cen_ready, c + 1)
                nc.scalar.activation(sq[:, c, :], cen[:, c, :], ACT.Square).then_inc(sq_ready, 1)
            for c in range(RT):
                act.wait_ge(inv_ready, c + 1)
                nc.scalar.activation(rs[:, c, :], rs[:, c, :], ACT.Sqrt).then_inc(rs_ready, 1)

        @block.vector
        def _(dve):
            st = Steps(steps)

            def then(ins):
                dve.wait_ge(steps, st.mark(ins))

            for c in range(RT):
                dve.wait_ge(m_done, c + 1)
                nc.vector.scalar_tensor_tensor(cen[:, c, :], ps[:, c % 2, :], -1.0 / CH, y[:, c, :],
                                               ALU.mult, ALU.add).then_inc(cen_ready, 1)
            for c in range(RT):
                dve.wait_ge(v_done, c + 1)
                then(nc.vector.tensor_scalar(rs[:, c, :], pv[:, c % 2, :], 1.0 / CH, GN_EPS, ALU.mult, ALU.add))
                nc.vector.reciprocal(rs[:, c, :], rs[:, c, :]).then_inc(inv_ready, 1)
            for c in range(RT):
                dve.wait_ge(rs_ready, c + 1)
                dve.wait_ge(cen_ready, c + 1)
                then(nc.vector.scalar_tensor_tensor(cen[:, c, :], cen[:, c, :], col(e, "rw_ln_w", c), rs[:, c, :],
                                                    ALU.mult, ALU.mult))
                then(nc.vector.scalar_tensor_tensor(cen[:, c, :], cen[:, c, :], col(e, "rw_ln_b", c),
                                                    bonus[:, c, :], ALU.add, ALU.add))
                nc.vector.tensor_tensor(y[:, c, :], cen[:, c, :], g[:, c, :], ALU.mult)


def rwkv_branch(nc, e, I, merged, root):
    with ExitStack() as s:
        keep = lambda name, shape: s.enter_context(nc.sbuf_tensor(f"rw_{name}", shape, F32))
        y = keep("y", [P, RT, L])
        with ExitStack() as s2:
            part = lambda name, shape: s2.enter_context(nc.sbuf_tensor(f"rw_{name}", shape, F32))
            rkv = part("rkv", [P, 3 * RT, L])
            lora = y
            with ExitStack() as s3:
                rwkv_inputs(nc, e, I, two_parts(nc, s3, "rw_h", DT), rkv, lora, root)
            lw, a = part("lw", [P, 2, RT, L]), part("a", [P, 2, RT, L])
            g, kk, bonus = (part(n, [P, RT, L]) for n in ("g", "kk", "bonus"))
            rwkv_features(nc, e, I, rkv, lora, lw, a, g, kk, bonus)
            with ExitStack() as s3:
                scan = lambda name, shape: s3.enter_context(nc.sbuf_tensor(f"rw_{name}", shape, F32))
                gt = scan("gt", [P, RT, HCH, 2, P])
                kbt, vu, xt, kb = (scan(n, [P, RT, HCH, P]) for n in ("kbt", "vu", "xt", "kb"))
                place = [scan(f"place{i}", [P, RT, HCH, P]) for i in range(2)]
                pend = [scan(f"pend{i}", [P, RT, HCH]) for i in range(2)]
                state = scan("state", [P, 2, RT, CH])
                bv = scan("bv", [P, HCH, RT, CH])
                reset, scan_mask = scan("reset", [P, LH]), scan("scan_mask", [P, 2, P])
                levels = scan("levels", [P, 2, LEVELS, P])
                load_tables(nc, "scan_tables", [
                    (reset[:, :], I["c_reset"][:, 0:LH]),
                    (scan_mask[:, :, :], I["c_scan"].rearrange("p (d t) -> p d t", d=2)),
                    (levels[:, :, :, :], I["c_levels"].rearrange("p (a k t) -> p a k t", a=2, k=LEVELS))])
                units = [(0, 0), (0, 1), (1, 1), (1, 0)]
                inputs = lambda n: (rkv, lw, a, kk, reset, place[n % 2], kb, pend[n % 2])
                rwkv_scaled(nc, e, *units[0], *inputs(0))
                for n, (d, half) in enumerate(units):
                    ar = place[n % 2]
                    rwkv_matrices(nc, e, d, half, rkv, ar, kb, scan_mask, gt, kbt, vu, bv)
                    rwkv_inverse(nc, e, d, half, gt, levels, xt, kb, place[(n + 1) % 2])
                    following = (*units[n + 1], 1, *inputs(n + 1)) if n + 1 < len(units) else None
                    rwkv_chain(nc, e, d, half, state, ar, gt, kbt, xt, vu, bv, pend[n % 2], y, following)
            rwkv_group_norm(nc, e, y, bonus, g)
        h = two_parts(nc, s, "rw_h3", DT)
        gated_output(nc, e, "rw", I["w_in"][:, N_HY + N_RW + D:N_HY + N_RW + 2 * D], h,
                     normed(nc, e, e.x, DT, h, lambda k: col(e, "mix_norm", k), root=root, known=True), I["rw_out"], RT, y, merged, 1)



def prepare_columns(nc, e):
    with ExitStack() as s:
        sb, pb, sem = opened(nc, s, "columns")
        summed = sem("summed")
        block = s.enter_context(nc.Block())
        n, mu = MU_ROWS + 1, COL["rw_mu"]

        @block.scalar
        def _(act):
            nc.scalar.activation(e.cond[:, :], e.cols[:, COL["c_2"]:COL["c_2"] + DT], ACT.Silu)

        @block.vector
        def _(dve):
            nc.vector.tensor_tensor(e.shift_keep[:, :], e.cols[:, mu:mu + n], e.cols[:, mu + n:mu + 2 * n],
                                    ALU.add).then_inc(summed, 1)
            dve.wait_ge(summed, 1)
            nc.vector.tensor_scalar(e.shift_keep[:, :], e.shift_keep[:, :], -1.0, 1.0, ALU.mult, ALU.add)


def add_condition_bias(nc, e):
    with ExitStack() as s:
        block = s.enter_context(nc.Block())

        @block.vector
        def _(dve):
            for dst, name, at in ((e.ada[:, 0, :], "ada_b_2", 0), (e.kvada[:, :], "kv_ada_b_2", 0)):
                n = dst.shape[-1]
                nc.vector.tensor_tensor(dst, dst, e.cols[:, COL[name] + at:COL[name] + at + n], ALU.add)


def add_condition_bias_1(nc, e):
    with ExitStack() as s:
        block = s.enter_context(nc.Block())

        @block.vector
        def _(dve):
            at = COL["ada_b_2"] + 6 * DT
            nc.vector.tensor_tensor(e.ada[:, 1, :], e.ada[:, 1, :], e.cols[:, at:at + 6 * DT], ALU.add)


def mlstm_gates(nc, e, I, h, rows, ccol):
    H = A_HEADS
    with ExitStack() as s:
        sb, pb, sem = opened(nc, s, "mg")
        raw = sb("raw", [P, 2, DT, P])
        wh, wl = (s.enter_context(nc.sbuf_tensor(f"mg_{n}", [P, 2, DT, P], F32R)) for n in ("wh", "wl"))
        ones, zeros = sb("ones", [H, L]), sb("zeros", [H, L])
        ig, f, af, m, F, M = (sb(n, [H, L]) for n in ("ig", "f", "af", "m", "cf", "mx"))
        pi, pf, pc = pb("pi", [P, L]), pb("pf", [P, L]), pb("pc", [P, TT, H])
        loaded, mm_done, act_done, dve_done = sem("loaded"), sem("mm_done"), sem("act_done"), sem("dve_done")
        steps, turned, hi_ready, lo_ready = sem("steps"), sem("turned"), sem("hi_ready"), sem("lo_ready")
        xh, xl = h
        block = s.enter_context(nc.Block())
        at = 2 * H * A_QK + A_HEADS * P

        @block.sync
        def _(sp):
            for g in range(2):
                sp.dma_start(raw[:, g, :, :], I["a_w_in_2"][0, :, at + g * H:at + g * H + P]
                             .rearrange("(k p) n -> p k n", p=P)).then_inc(loaded, 16)

        @block.tensor
        def _(pe):
            pe.wait_ge(lo_ready, 1)
            for g, ps in enumerate((pi, pf)):
                for k in range(DT):
                    nc.tensor.matmul(ps[:, :], wh[:, g, k, :], xh[:, k, :], start=k == 0, stop=False)
                    nc.tensor.matmul(ps[:, :], wh[:, g, k, :], xl[:, k, :], start=False, stop=False)
                    last = nc.tensor.matmul(ps[:, :], wl[:, g, k, :], xh[:, k, :], start=False, stop=k == DT - 1)
                last.then_inc(mm_done, 1)
            pe.wait_ge(dve_done, 2)
            for t in range(TT):
                last = nc.tensor.transpose(pc[:, t, :], ig[:, t * P:(t + 1) * P], e.ident[0:H, 0:H])
            last.then_inc(turned, 1)

        @block.scalar
        def _(act):
            act.wait_ge(loaded, 32)
            nc.scalar.activation(wh[:, :, :, :], raw[:, :, :, :], ACT.Copy).then_inc(hi_ready, 1)
            b = COL["a_gate_b_2"]
            act.wait_ge(mm_done, 1)
            nc.scalar.activation(ig[:, :], pi[0:H, :], ACT.Identity, bias=e.cols[0:H, b:b + 1]).then_inc(act_done, 1)
            act.wait_ge(mm_done, 2)
            nc.scalar.activation(f[:, :], pf[0:H, :], ACT.Identity, bias=e.cols[0:H, b + 1:b + 2]).then_inc(act_done, 1)
            act.wait_ge(act_done, 2)
            nc.scalar.activation(af[:, :], f[:, :], ACT.Abs).then_inc(act_done, 1)
            act.wait_ge(act_done, 3)
            nc.scalar.activation(af[:, :], af[:, :], ACT.Exp, scale=-1.0).then_inc(act_done, 1)
            act.wait_ge(act_done, 4)
            nc.scalar.activation(af[:, :], af[:, :], ACT.Ln, bias=1.0).then_inc(act_done, 1)
            act.wait_ge(dve_done, 1)
            nc.scalar.activation(rows[:, 1, :], m[:, :], ACT.Exp, scale=-1.0)
            act.wait_ge(turned, 1)
            nc.scalar.activation(ccol[:, :, :], pc[:, :, :], ACT.Copy)

        @block.vector
        def _(dve):
            st = Steps(steps)

            def then(ins):
                dve.wait_ge(steps, st.mark(ins))

            dve.wait_ge(hi_ready, 1)
            nc.vector.tensor_tensor(wl[:, :, :, :], raw[:, :, :, :], wh[:, :, :, :].bitcast(F32), ALU.subtract)\
                .then_inc(lo_ready, 1)
            then(nc.vector.memset(ones[:, :], 1.0))
            then(nc.vector.memset(zeros[:, :], 0.0))
            dve.wait_ge(act_done, 5)
            then(nc.vector.scalar_tensor_tensor(f[:, :], f[:, :], 0.0, af[:, :], ALU.min, ALU.subtract))
            then(nc.vector.tensor_tensor_scan(F[:, :], ones[:, :], f[:, :], 0.0, ALU.mult, ALU.add))
            then(nc.vector.tensor_tensor(ig[:, :], ig[:, :], F[:, :], ALU.subtract))
            then(nc.vector.tensor_tensor_scan(M[:, :], zeros[:, :], ig[:, :], 0.0, ALU.add, ALU.max))
            nc.vector.tensor_tensor(m[:, :], F[:, :], M[:, :], ALU.add).then_inc(dve_done, 1)
            nc.vector.tensor_scalar(rows[:, 0, :], M[:, :], -1.0, None, ALU.mult).then_inc(dve_done, 1)


def mlstm_heads(nc, e, I, qk, v, rows, ccol, out, inv):
    H = A_HEADS
    with ExitStack() as s:
        sb, pb, sem = opened(nc, s, "mh")
        sel, causal = sb("sel", [H, H, P]), sb("causal", [P, P])
        dT, pT = sb("dT", [P, 3, L]), sb("pT", [P, 3, L])
        negM, floor, den = sb("negM", [P, 3, L]), sb("floor", [P, 3, L]), sb("den", [P, 2, L])
        sq = sb("sq", [P, 2, L])
        pm, pe_, pS, pn, pd = (pb("pm", [P, L]), pb("pe", [P, L]), pb("pS", [P, 2, L]),
                               pb("pn", [P, 2, L]), pb("pd", [P, 2, L]))
        loaded, rows_done, rows_out, s_done = sem("loaded"), sem("rows_done"), sem("rows_out"), sem("s_done")
        arg_ready, d_ready, p_ready, p_masked = sem("arg"), sem("d_ready"), sem("p_ready"), sem("p_masked")
        used, head_done, abs_ready, out_done, steps = (sem("used"), sem("head_done"), sem("abs"),
                                                       sem("out_done"), sem("steps"))
        squared, mean_done = sem("squared"), sem("mean_done")
        block = s.enter_context(nc.Block())
        units = [(h, j) for h in range(H) for j in range(TT)]

        @block.sync
        def _(sp):
            sp.dma_start(sel[:, :, :], I["c_sel"].rearrange("k (h p) -> k h p", h=H)).then_inc(loaded, 16)
            sp.dma_start(causal[:, :], I["c_causal"]).then_inc(loaded, 16)

        @block.tensor
        def _(pe):
            def broadcast(h):
                if h > 0:
                    pe.wait_ge(rows_out, 2 * h)
                nc.tensor.matmul(pm[:, :], sel[:, h, :], rows[:, 0, :], start=True, stop=True)
                nc.tensor.matmul(pe_[:, :], sel[:, h, :], rows[:, 1, :], start=True, stop=True)\
                    .then_inc(rows_done, 1)

            def mean(h):
                pe.wait_ge(squared, 2 * h + 1)
                pe.wait_ge(abs_ready, h + 1)
                nc.tensor.matmul(pd[:, h % 2, :], e.ones[:, :], sq[:, h % 2, :], start=True, stop=True)\
                    .then_inc(mean_done, 1)

            def scores(n):
                h, j = units[n]
                hs = slice(64 * (h % 2), 64 * (h % 2) + 64)
                if n >= 2:
                    pe.wait_ge(p_ready, n - 1)
                nc.tensor.matmul(pS[:, n % 2, j * P:L], qk[hs, H // 2 + h // 2, j * P:(j + 1) * P],
                                 qk[hs, h // 2, j * P:L], start=True, stop=True).then_inc(s_done, 1)

            pe.wait_ge(loaded, 32)
            broadcast(0)
            scores(0)
            scores(1)
            for n, (h, j) in enumerate(units):
                if j == 1 and h + 1 < H:
                    broadcast(h + 1)
                if n + 2 < len(units):
                    scores(n + 2)
                if j == 2 and h > 0:
                    mean(h - 1)
                pe.wait_ge(p_masked, n + 1)
                if j == 0 and h >= 2:
                    pe.wait_ge(out_done, h - 1)
                    pe.wait_ge(squared, 2 * (h - 1))
                first, last_j = j == 0, j == TT - 1
                nc.tensor.matmul(pn[:, h % 2, j * P:L], v[:, j, h * P:(h + 1) * P], pT[:, n % 3, j * P:L],
                                 start=first, stop=last_j)
                last = nc.tensor.matmul(pd[:, h % 2, j * P:L], e.ones[:, :], pT[:, n % 3, j * P:L],
                                        start=first, stop=last_j)
                last.then_inc(used, 1)
            mean(H - 1)

        @block.scalar
        def _(act):
            def take_rows(h):
                act.wait_ge(rows_done, h + 1)
                if h >= 3:
                    act.wait_ge(out_done, h - 2)
                nc.scalar.activation(negM[:, h % 3, :], pm[:, :], ACT.Copy).then_inc(rows_out, 1)
                nc.scalar.activation(floor[:, h % 3, :], pe_[:, :], ACT.Copy).then_inc(rows_out, 1)

            def take_sum(h):
                act.wait_ge(used, TT * (h + 1))
                if h >= 2:
                    act.wait_ge(out_done, h - 1)
                nc.scalar.activation(den[:, h % 2, :], pd[:, h % 2, :], ACT.Abs).then_inc(abs_ready, 1)
                nc.scalar.activation(sq[:, h % 2, :], pn[:, h % 2, :], ACT.Square).then_inc(squared, 1)
                nc.scalar.activation(out[:, h, :], pn[:, h % 2, :], ACT.Copy).then_inc(squared, 1)

            take_rows(0)
            for n, (h, j) in enumerate(units):
                act.wait_ge(arg_ready, n + 1)
                nc.scalar.activation(dT[:, n % 3, j * P:L], dT[:, n % 3, j * P:L], ACT.Exp).then_inc(d_ready, 1)
                if j == 0 and h > 0:
                    take_sum(h - 1)
                if j == 2 and h + 1 < H:
                    take_rows(h + 1)
            take_sum(H - 1)

        @block.vector
        def _(dve):
            st = Steps(steps)

            def then(ins):
                dve.wait_ge(steps, st.mark(ins))

            def floored(h):
                d = den[:, h % 2, :]
                dve.wait_ge(abs_ready, h + 1)
                then(nc.vector.tensor_tensor(d, d, floor[:, h % 3, :], ALU.max))
                st.mark(nc.vector.scalar_tensor_tensor(d, d, EPS, d, ALU.mult, ALU.mult))

            def finish(h):
                dve.wait_ge(steps, st.n)
                dve.wait_ge(mean_done, h + 1)
                nc.vector.scalar_tensor_tensor(inv[:, h, :], pd[:, h % 2, :], 1.0 / P, den[:, h % 2, :],
                                               ALU.mult, ALU.add).then_inc(out_done, 1)

            def invert(h, j):
                part = inv[:, h, j * P:(j + 1) * P]
                dve.wait_ge(out_done, h + 1)
                nc.vector.reciprocal(part, part)

            def argument(n):
                h, j = units[n]
                if j == 0:
                    dve.wait_ge(rows_out, 2 * h + 2)
                if n >= 3:
                    dve.wait_ge(p_ready, n - 2)
                nc.vector.tensor_scalar(dT[:, n % 3, j * P:L], negM[:, h % 3, j * P:L], ccol[:, j, h:h + 1], 0.0,
                                        ALU.add, ALU.min).then_inc(arg_ready, 1)

            argument(0)
            argument(1)
            for n, (h, j) in enumerate(units):
                dve.wait_ge(d_ready, n + 1)
                dve.wait_ge(s_done, n + 1)
                if n >= 3:
                    dve.wait_ge(used, n - 2)
                nc.vector.scalar_tensor_tensor(pT[:, n % 3, j * P:L], pS[:, n % 2, j * P:L], A_QK**-0.5,
                                               dT[:, n % 3, j * P:L], ALU.mult, ALU.mult).then_inc(p_ready, 1)
                if n + 2 < len(units):
                    argument(n + 2)
                if j == 1 and h > 0:
                    floored(h - 1)
                if j == 3 and h > 0:
                    finish(h - 1)
                if h > 1:
                    invert(h - 2, j)
            floored(H - 1)
            finish(H - 1)
            for h in (H - 2, H - 1):
                for j in range(TT):
                    invert(h, j)

        @block.gpsimd
        def _(pool):
            pool.wait_ge(loaded, 32)
            for n, (h, j) in enumerate(units):
                pool.wait_ge(p_ready, n + 1)
                diag = pT[:, n % 3, j * P:(j + 1) * P]
                nc.gpsimd.tensor_tensor(diag, diag, causal[:, :], ALU.mult).then_inc(p_masked, 1)


def head_norm_gate(nc, e, hh, inv, og):
    n = A_HEADS
    with ExitStack() as s:
        sb, pb, sem = opened(nc, s, "hn")
        rs_ready, normed_ = sem("rs_ready"), sem("normed")
        block = s.enter_context(nc.Block())

        @block.scalar
        def _(act):
            for k in range(n):
                nc.scalar.activation(inv[:, k, :], inv[:, k, :], ACT.Sqrt).then_inc(rs_ready, 1)

        @block.vector
        def _(dve):
            for k in range(n):
                dve.wait_ge(rs_ready, k + 1)
                nc.vector.scalar_tensor_tensor(hh[:, k, :], hh[:, k, :], col(e, "a_head_g_2", k), inv[:, k, :],
                                               ALU.mult, ALU.mult).then_inc(normed_, 1)
                if k % 2 == 1:
                    dve.wait_ge(normed_, k)
                    nc.vector.tensor_tensor(hh[:, k - 1, :], hh[:, k - 1, :], og[:, k - 1, :], ALU.mult)

        @block.gpsimd
        def _(pool):
            for k in range(1, n, 2):
                pool.wait_ge(normed_, k + 1)
                nc.gpsimd.tensor_tensor(hh[:, k, :], hh[:, k, :], og[:, k, :], ALU.mult)


def mlstm_mixer(nc, e, I, h, before, y):
    H = A_HEADS
    with ExitStack() as s:
        part = lambda name, shape: s.enter_context(nc.sbuf_tensor(f"ml_{name}", shape, F32))
        w = I["a_w_in_2"][0]
        qk, v = part("qk", [P, H, L]), part("v", [P, TT, H * P])
        rows, ccol = part("rows", [H, 2, L]), part("ccol", [P, TT, H])
        gemm(nc, e, "ml_qk", w[:, 0:2 * H * A_QK], DT, h, 2, 2, 2, "copy", dst=qk, before=before)
        gemm_tokens(nc, e, "ml_v", w, DT, h, 2, v, 2 * H * A_QK)
        mlstm_gates(nc, e, I, h, rows, ccol)
        at = 2 * H * A_QK + H * P + 2 * H
        og = part("og", [P, H, L])
        gemm(nc, e, "ml_og", w[:, at:at + H * P], DT, h, 4, 2, 1, "copy", dst=og, func=ACT.Sigmoid)
        with nc.sbuf_tensor("ml_inv", [P, H, L], F32) as inv:
            mlstm_heads(nc, e, I, qk, v, rows, ccol, y, inv)
            head_norm_gate(nc, e, y, inv, og)
        hp = two_parts(nc, s, "ml_hp", H)
        gemm(nc, e, "ml_out", I["a_w_out_2"][0], H, hp, 2, 2, 2, "copy", dst=y, before=cut(nc, e, y, H, hp))


def rope_tables(nc, e, I, cosr, sinr):
    def programs(sb, pb, sem):
        pos = sb("rope_pos", [P, L])[:, :].bitcast(mybir.dt.int32)
        inv, ang, n, r = sb("rope_inv", [P, 1]), sb("rope_ang", [P, L]), sb("rope_n", [P, L]), sb("rope_r", [P, L])
        loaded, steps, r_ready, abs_ready, c_ready = (sem("rope_in"), sem("rope_steps"), sem("rope_r"),
                                                      sem("rope_abs"), sem("rope_c"))

        def sync(sp):
            sp.dma_start(pos, I["positions_2"][0, :].partition_broadcast(P)).then_inc(loaded, 16)
            sp.dma_start(inv[:, :], I["c_invfreq"]).then_inc(loaded, 16)

        def vector(dve):
            st = Steps(steps)

            def then(ins):
                dve.wait_ge(steps, st.mark(ins))

            dve.wait_ge(loaded, 32)
            then(nc.vector.tensor_copy(ang[:, :], pos))
            then(nc.vector.tensor_scalar(ang[:, :], ang[:, :], inv[:, 0:1], None, ALU.mult))
            then(nc.vector.tensor_scalar(n[:, :], ang[:, :], 1 / TWO_PI, ROUND, ALU.mult, ALU.add))
            then(nc.vector.tensor_scalar(n[:, :], n[:, :], ROUND, None, ALU.subtract))
            for part in (PI_A, PI_B, PI_C):
                then(nc.vector.scalar_tensor_tensor(ang[:, :], n[:, :], -part, ang[:, :], ALU.mult, ALU.add))
            nc.vector.tensor_scalar(ang[:, :], ang[:, :], math.pi, -math.pi, ALU.min, ALU.max).then_inc(r_ready, 1)
            dve.wait_ge(abs_ready, 1)
            nc.vector.tensor_scalar(r[:, :], r[:, :], -1.0, math.pi / 2, ALU.mult, ALU.add).then_inc(c_ready, 1)

        def scalar(act):
            act.wait_ge(r_ready, 1)
            nc.scalar.activation(sinr[:, :], ang[:, :], ACT.Sin)
            nc.scalar.activation(r[:, :], ang[:, :], ACT.Abs).then_inc(abs_ready, 1)
            act.wait_ge(c_ready, 1)
            nc.scalar.activation(cosr[:, :], r[:, :], ACT.Sin)

        return sync, scalar, vector

    return programs


def rotate(nc, dve, steps, st, p1, p2, cosr, sinr, parts, t1, t2, t3, t4):
    cs, sn = cosr[0:parts, :], sinr[0:parts, :]
    st.mark(nc.vector.tensor_tensor(t1, p1, cs, ALU.mult))
    st.mark(nc.vector.tensor_tensor(t2, p2, sn, ALU.mult))
    st.mark(nc.vector.tensor_tensor(t3, p2, cs, ALU.mult))
    dve.wait_ge(steps, st.mark(nc.vector.tensor_tensor(t4, p1, sn, ALU.mult)))


def three_passes(nc, ps, wh, wl, xh, xl, kt):
    for k in range(kt):
        nc.tensor.matmul(ps, wh(k), xh(k), start=k == 0, stop=False)
        nc.tensor.matmul(ps, wh(k), xl(k), start=False, stop=False)
        last = nc.tensor.matmul(ps, wl(k), xh(k), start=False, stop=k == kt - 1)
    return last


def mla_keys_a(nc, e, I, h, before, ckv, cosr, sinr, kr, early):
    with ExitStack() as s:
        sb, pb, sem = opened(nc, s, "ka")
        raw = sb("raw", [P, 2, DT, P])
        wh, wl = (s.enter_context(nc.sbuf_tensor(f"ka_{n}", [P, 4, DT, P], F32R)) for n in ("wh", "wl"))
        t1, t2, t3, t4 = (sb(n, [32, L]) for n in ("t1", "t2", "t3", "t4"))
        ps = pb("ps", [P, 4, L])
        loaded = [sem(f"loaded{i}") for i in range(2)]
        hi_ready, lo_ready, early_in = sem("hi_ready"), sem("lo_ready"), sem("early_in")
        done, steps = sem("done"), sem("steps")
        first = before(sb, pb, sem)
        block = s.enter_context(nc.Block())
        block.gpsimd(first.pool)

        @block.sync
        def _(sp):
            w = I["kv_w_a_2"].rearrange("(k p) n -> p k n", p=P)
            for j in range(4):
                if j >= 2:
                    sp.wait_ge(lo_ready, j - 1)
                    sp.dma_start(raw[:, j % 2, :, :], w[:, :, (j - 2) * P:(j - 1) * P]).then_inc(loaded[j % 2], 16)
                else:
                    at = KV_LORA + 32 * j
                    sp.dma_start(raw[:, j, :, 0:32], w[:, :, at:at + 32]).then_inc(loaded[j], 16)
                    sp.dma_start(raw[:, j, :, 32:P], w[:, :, 0:P - 32]).then_inc(loaded[j], 16)
            for dst, src in early:
                sp.dma_start(dst, src).then_inc(early_in, 16)
            sp.wait_ge(early_in, 16 * len(early))

        @block.tensor
        def _(pe):
            for k in range(first.count):
                first.wait_part(pe, k)
            for j in range(4):
                pe.wait_ge(lo_ready, j + 1)
                three_passes(nc, ps[:, j, :], lambda k: wh[:, j, k, :], lambda k: wl[:, j, k, :],
                             lambda k: h[0][:, k, :], lambda k: h[1][:, k, :], DT).then_inc(done, 1)

        def upper(act, j):
            act.wait_ge(loaded[j % 2], 32 if j < 2 else 48)
            nc.scalar.activation(wh[:, j, :, :], raw[:, j % 2, :, :], ACT.Copy).then_inc(hi_ready, 1)

        def lower(dve, j):
            dve.wait_ge(hi_ready, j + 1)
            nc.vector.tensor_tensor(wl[:, j, :, :], raw[:, j % 2, :, :], wh[:, j, :, :].bitcast(F32), ALU.subtract)\
                .then_inc(lo_ready, 1)

        @block.scalar
        def _(act):
            first.act[0](act)
            first.act[1](act)
            for j in range(4):
                upper(act, j)
            for j in range(2):
                act.wait_ge(done, j + 3)
                nc.scalar.activation(ckv[:, j, :], ps[:, 2 + j, :], ACT.Copy)

        @block.vector
        def _(dve):
            first.dve[0](dve)
            first.dve[1](dve)
            for j in range(4):
                lower(dve, j)
            st = Steps(steps)
            dve.wait_ge(done, 2)
            rotate(nc, dve, steps, st, ps[0:32, 0, :], ps[0:32, 1, :], cosr, sinr, 32,
                   t1[:, :], t2[:, :], t3[:, :], t4[:, :])
            nc.vector.tensor_tensor(kr[0:32, :], t1[:, :], t2[:, :], ALU.subtract)
            nc.vector.tensor_tensor(kr[32:64, :], t3[:, :], t4[:, :], ALU.add)


def mla_queries(nc, e, I, cq, before, cosr, sinr, qn, qr):
    H, KT = B_HEADS, Q_LORA // P
    with ExitStack() as s:
        sb, pb, sem = opened(nc, s, "qb")
        raw = sb("raw", [P, KT, H, NOPE + ROPE])
        rope = sb("rope", [P, KT, 2, H, 32])
        wh, wl = (s.enter_context(nc.sbuf_tensor(f"qb_{n}", [P, KT, H, NOPE], F32R)) for n in ("wh", "wl"))
        rh, rl = (s.enter_context(nc.sbuf_tensor(f"qb_{n}", [P, KT, 2, H, 32], F32R)) for n in ("rh", "rl"))
        t = sb("t", [P, 4, L])
        pn, pr = pb("pn", [P, 2, L]), pb("pr", [P, 2, 2, L])
        loaded, sorted_, n_done, n_out = sem("loaded"), sem("sorted"), sem("n_done"), sem("n_out")
        hi_ready, lo_ready, r_done, steps = sem("hi_ready"), sem("lo_ready"), sem("r_done"), sem("steps")
        first = before(sb, pb, sem)
        block = s.enter_context(nc.Block())

        @block.sync
        def _(sp):
            sp.dma_start(raw[:, :, :, :], I["b_w_q_b_2"][0].rearrange("(k p) (h n) -> p k h n", p=P, h=H))\
                .then_inc(loaded, 16)

        @block.gpsimd
        def _(pool):
            pool.wait_ge(loaded, 16)
            for k in range(KT):
                for half in range(2):
                    at = NOPE + 32 * half
                    nc.gpsimd.tensor_copy(rope[:, k, half, :, :], raw[:, k, :, at:at + 32]).then_inc(sorted_, 1)
            first.pool(pool)

        @block.tensor
        def _(pe):
            first.pe(pe)
            for k in range(first.count):
                first.wait_part(pe, k)
            xh, xl = (lambda k: cq[0][:, k, :]), (lambda k: cq[1][:, k, :])
            pe.wait_ge(lo_ready, 2)
            for g in range(2):
                for half in range(2):
                    of = lambda w: (lambda k: w[:, k, half, 4 * g:4 * g + 4, :].rearrange("p h n -> p (h n)"))
                    last = three_passes(nc, pr[:, g, half, :], of(rh), of(rl), xh, xl, KT)
                last.then_inc(r_done, 1)
            for h in range(H):
                if h >= 2:
                    pe.wait_ge(n_out, h - 1)
                three_passes(nc, pn[:, h % 2, :], lambda k: wh[:, k, h, :], lambda k: wl[:, k, h, :], xh, xl, KT)\
                    .then_inc(n_done, 1)

        @block.scalar
        def _(act):
            first.act[0](act)
            act.wait_ge(loaded, 16)
            for k in range(KT):
                ins = nc.scalar.activation(wh[:, k, :, :], raw[:, k, :, 0:NOPE], ACT.Copy)
            ins.then_inc(hi_ready, 1)
            act.wait_ge(sorted_, 2 * KT)
            nc.scalar.activation(rh[:, :, :, :, :], rope[:, :, :, :, :], ACT.Copy).then_inc(hi_ready, 1)
            first.act[1](act)
            for h in range(H):
                act.wait_ge(n_done, h + 1)
                nc.scalar.activation(qn[:, h, :], pn[:, h % 2, :], ACT.Copy).then_inc(n_out, 1)

        @block.vector
        def _(dve):
            first.dve[0](dve)
            dve.wait_ge(hi_ready, 1)
            for k in range(KT):
                ins = nc.vector.tensor_tensor(wl[:, k, :, :], raw[:, k, :, 0:NOPE], wh[:, k, :, :].bitcast(F32),
                                              ALU.subtract)
            ins.then_inc(lo_ready, 1)
            dve.wait_ge(hi_ready, 2)
            nc.vector.tensor_tensor(rl[:, :, :, :, :], rope[:, :, :, :, :], rh[:, :, :, :, :].bitcast(F32),
                                    ALU.subtract).then_inc(lo_ready, 1)
            first.dve[1](dve)
            st = Steps(steps)
            for g in range(2):
                dve.wait_ge(r_done, g + 1)
                rotate(nc, dve, steps, st, pr[:, g, 0, :], pr[:, g, 1, :], cosr, sinr, P,
                       t[:, 0, :], t[:, 1, :], t[:, 2, :], t[:, 3, :])
                for i in range(4):
                    hp = slice(32 * i, 32 * i + 32)
                    st.mark(nc.vector.tensor_tensor(qr[0:32, 4 * g + i, :], t[hp, 0, :], t[hp, 1, :], ALU.subtract))
                    st.mark(nc.vector.tensor_tensor(qr[32:64, 4 * g + i, :], t[hp, 2, :], t[hp, 3, :], ALU.add))
                dve.wait_ge(steps, st.n)


def mla_attention(nc, e, I, qn, qr, kn, kr, v, out):
    H = B_HEADS
    scale = (NOPE + ROPE) ** -0.5
    with ExitStack() as s:
        sb, pb, sem = opened(nc, s, "at")
        mask = sb("mask", [P, P])
        mx, nm, total, inv = (sb(n, [P, 3]) for n in ("mx", "nm", "total", "inv"))
        p, pT = sb("p", [P, 3, L]), sb("pT", [P, 3, L])
        pS, pt, po = pb("pS", [P, 3, L]), pb("pt", [P, 3, L]), pb("po", [P, 2, L])
        loaded, s_done, nm_ready, p_ready = sem("loaded"), sem("s_done"), sem("nm"), sem("p_ready")
        p_normed, turned, pT_ready, used = sem("p_normed"), sem("turned"), sem("pT_ready"), sem("used")
        out_done, steps = sem("out_done"), sem("steps")
        block = s.enter_context(nc.Block())
        units = [(h, i) for h in range(H) for i in range(TT)]
        N = len(units)

        @block.sync
        def _(sp):
            sp.dma_start(mask[:, :], I["c_causal_row"]).then_inc(loaded, 16)

        @block.tensor
        def _(pe):
            def scores(n):
                h, i = units[n]
                w = (i + 1) * P
                if n >= 3:
                    pe.wait_ge(p_ready, n - 2)
                ts = slice(i * P, (i + 1) * P)
                nc.tensor.matmul(pS[:, n % 3, 0:w], qn[:, h, ts], kn[:, h, 0:w], start=True, stop=False)
                nc.tensor.matmul(pS[:, n % 3, 0:w], qr[0:ROPE, h, ts], kr[0:ROPE, 0:w], start=False, stop=True)\
                    .then_inc(s_done, 1)

            def turn(n):
                h, i = units[n]
                pe.wait_ge(p_normed, n + 1)
                if n >= 3:
                    pe.wait_ge(pT_ready, n - 2)
                for j in range(i + 1):
                    js = slice(j * P, (j + 1) * P)
                    last = nc.tensor.transpose(pt[:, n % 3, js], p[:, n % 3, js], e.ident[:, :])
                last.then_inc(turned, 1)

            def values(n):
                h, i = units[n]
                pe.wait_ge(pT_ready, n + 1)
                if i == 0 and h >= 2:
                    pe.wait_ge(out_done, h - 1)
                for j in range(i + 1):
                    last = nc.tensor.matmul(po[:, h % 2, i * P:(i + 1) * P], v[:, j, h * P:(h + 1) * P],
                                            pT[:, n % 3, j * P:(j + 1) * P], start=j == 0, stop=j == i)
                last.then_inc(used, 1)

            for n in range(N + 3):
                if n < N:
                    scores(n)
                if 2 <= n < N + 2:
                    turn(n - 2)
                if n >= 3:
                    values(n - 3)

        @block.vector
        def _(dve):
            st = Steps(steps)

            def then(ins):
                dve.wait_ge(steps, st.mark(ins))

            def maximum(n):
                h, i = units[n]
                b = n % 3
                dve.wait_ge(s_done, n + 1)
                diag = pS[:, b, i * P:(i + 1) * P]
                then(nc.vector.tensor_tensor(diag, diag, mask[:, :], ALU.add))
                then(nc.vector.reduce_max(mx[:, b:b + 1], pS[:, b, 0:(i + 1) * P], AX.X))
                if n >= 3:
                    dve.wait_ge(p_ready, n - 2)
                nc.vector.tensor_scalar(nm[:, b:b + 1], mx[:, b:b + 1], -scale, None, ALU.mult).then_inc(nm_ready, 1)

            def normalise(n):
                h, i = units[n]
                b = n % 3
                dve.wait_ge(p_ready, n + 1)
                then(nc.vector.reciprocal(inv[:, b:b + 1], total[:, b:b + 1]))
                nc.vector.tensor_scalar(p[:, b, 0:(i + 1) * P], p[:, b, 0:(i + 1) * P], inv[:, b:b + 1], None,
                                        ALU.mult).then_inc(p_normed, 1)

            dve.wait_ge(loaded, 16)
            maximum(0)
            maximum(1)
            for n in range(N):
                normalise(n)
                if n + 2 < N:
                    maximum(n + 2)

        @block.scalar
        def _(act):
            def copies(n):
                h, i = units[n]
                act.wait_ge(turned, n + 1)
                if n >= 3:
                    act.wait_ge(used, n - 2)
                nc.scalar.activation(pT[:, n % 3, 0:(i + 1) * P], pt[:, n % 3, 0:(i + 1) * P], ACT.Copy)\
                    .then_inc(pT_ready, 1)

            def take_out(n):
                h, i = units[n]
                if i == TT - 1:
                    act.wait_ge(used, n + 1)
                    nc.scalar.activation(out[:, h, :], po[:, h % 2, :], ACT.Copy).then_inc(out_done, 1)

            for n in range(N):
                h, i = units[n]
                b = n % 3
                act.wait_ge(nm_ready, n + 1)
                if n >= 3:
                    act.wait_ge(turned, n - 2)
                nc.scalar.activation(p[:, b, 0:(i + 1) * P], pS[:, b, 0:(i + 1) * P], ACT.Exp, bias=nm[:, b:b + 1],
                                     scale=scale, accum_out=total[:, b:b + 1]).then_inc(p_ready, 1)
                if n >= 2:
                    copies(n - 2)
                if n >= 4:
                    take_out(n - 4)
            copies(N - 2)
            copies(N - 1)
            for n in range(N - 4, N):
                take_out(n)


def mla_keys_values_b(nc, e, raw_k, raw_v, c, before, kn, v):
    H = B_HEADS
    with ExitStack() as s:
        sb, pb, sem = opened(nc, s, "kvb")
        (kh, kl), (vh, vl) = ([s.enter_context(nc.sbuf_tensor(f"kvb_{n}{p}", [P, 2, H, P], F32R))
                               for p in ("h", "l")] for n in ("k", "v"))
        ps = pb("ps", [P, 4, L])
        hi_ready, lo_ready, done, taken = sem("hi_ready"), sem("lo_ready"), sem("done"), sem("taken")
        first = before(sb, pb, sem)
        block = s.enter_context(nc.Block())
        block.gpsimd(first.pool)
        N = H + 2 * TT

        @block.tensor
        def _(pe):
            first.pe(pe)
            for k in range(first.count):
                first.wait_part(pe, k)
            pe.wait_ge(lo_ready, 1)
            for n in range(N):
                if n >= 4:
                    pe.wait_ge(taken, n - 3)
                if n == H:
                    pe.wait_ge(lo_ready, 2)
                if n < H:
                    last = three_passes(nc, ps[:, n % 4, :], lambda k: kh[:, k, n, :], lambda k: kl[:, k, n, :],
                                        lambda k: c[0][:, k, :], lambda k: c[1][:, k, :], 2)
                else:
                    t, half = (n - H) % TT, (n - H) // TT
                    ts = slice(t * P, (t + 1) * P)
                    columns = lambda w: (lambda k: w[:, k, 4 * half:4 * half + 4, :].rearrange("p h n -> p (h n)"))
                    last = three_passes(nc, ps[:, n % 4, :], lambda k: c[0][:, k, ts], lambda k: c[1][:, k, ts],
                                        columns(vh), columns(vl), 2)
                last.then_inc(done, 1)

        @block.scalar
        def _(act):
            first.act[0](act)
            nc.scalar.activation(kh[:, :, :, :], raw_k[:, :, :, :], ACT.Copy).then_inc(hi_ready, 1)
            first.act[1](act)
            nc.scalar.activation(vh[:, :, :, :], raw_v[:, :, :, :], ACT.Copy).then_inc(hi_ready, 1)
            for n in range(N):
                act.wait_ge(done, n + 1)
                t, half = (n - H) % TT, (n - H) // TT
                dst = kn[:, n, :] if n < H else v[:, t, half * 512:(half + 1) * 512]
                nc.scalar.activation(dst, ps[:, n % 4, :], ACT.Copy).then_inc(taken, 1)

        @block.vector
        def _(dve):
            first.dve[0](dve)
            for i, (raw, wh, wl) in enumerate(((raw_k, kh, kl), (raw_v, vh, vl))):
                dve.wait_ge(hi_ready, i + 1)
                nc.vector.tensor_tensor(wl[:, :, :, :], raw[:, :, :, :], wh[:, :, :, :].bitcast(F32), ALU.subtract)\
                    .then_inc(lo_ready, 1)
                if i == 0:
                    first.dve[1](dve)


def mla_mixer(nc, e, I, before, y):
    H = B_HEADS
    with ExitStack() as s:
        keep = lambda name, shape: s.enter_context(nc.sbuf_tensor(f"mla_{name}", shape, F32))
        cosr, sinr = keep("cos", [P, L]), keep("sin", [P, L])
        kr, cq = keep("kr", [ROPE, L]), keep("cq", [P, Q_LORA // P, L])
        root = keep("root", [P, L])
        with ExitStack() as s2:
            h = two_parts(nc, s2, "mla_h", DT)
            gemm(nc, e, "q_a", I["b_w_q_a_2"][0], DT, h, 1, 3, 1, "copy", dst=cq, before=before(h, root=root[:, :]),
                 also=rope_tables(nc, e, I, cosr, sinr))
        kn, v = keep("kn", [P, H, L]), keep("v", [P, TT, H * P])
        with ExitStack() as s2:
            part = lambda name, shape: s2.enter_context(nc.sbuf_tensor(f"mla_{name}", shape, F32))
            ckv = part("ckv", [P, 2, L])
            raw_k, raw_v = part("raw_k", [P, 2, H, P]), part("raw_v", [P, 2, H, P])
            kv_b = I["kv_w_b_2"].rearrange("(k p) (h two n) -> p k h two n", p=P, h=H, two=2)
            early = [(raw[:, k, :, :], kv_b[:, k, :, i, :]) for i, raw in enumerate((raw_k, raw_v)) for k in range(2)]
            with ExitStack() as s3:
                hk = two_parts(nc, s3, "mla_hk", DT)
                mla_keys_a(nc, e, I, hk, normed(nc, e, e.x, DT, hk, lambda k: col(e, "kv_norm_g_2", k),
                                                shift=lambda k: e.kvada[:, k:k + 1],
                                                scale=lambda k: e.kvada[:, DT + k:DT + k + 1],
                                                root=root[:, :], known=True),
                           ckv, cosr, sinr, kr, early)
            cp = two_parts(nc, s2, "mla_cp", 2)
            mla_keys_values_b(nc, e, raw_k, raw_v, cp,
                              normed(nc, e, ckv, 2, cp, lambda k: col(e, "kv_latent_g_2", k)), kn, v)
        qn, qr = keep("qn", [P, H, L]), keep("qr", [ROPE, H, L])
        with ExitStack() as s2:
            qp = two_parts(nc, s2, "mla_qp", Q_LORA // P)
            mla_queries(nc, e, I, qp, normed(nc, e, cq, Q_LORA // P, qp, lambda k: col(e, "b_q_latent_g_2", k)),
                        cosr, sinr, qn, qr)
        mla_attention(nc, e, I, qn, qr, kn, kr, v, y)
    with ExitStack() as s:
        yp = two_parts(nc, s, "mla_yp", H)
        gemm(nc, e, "mla_out", I["b_w_out_2"][0], H, yp, 2, 2, 2, "copy", dst=y, before=cut(nc, e, y, H, yp))


def second_block(nc, e, I, sides):
    add_condition_bias(nc, e)
    for l in range(2):
        part = lambda i: (lambda k: e.ada[:, l, i * DT + k:i * DT + k + 1])
        gain = lambda i: (lambda k: col(e, "norm_g_2", (4 * l + i) * DT + k))
        with ExitStack() as s:
            y = s.enter_context(nc.sbuf_tensor(f"l{l}_y", [P, DT, L], F32))
            before = lambda h, **kept: normed(nc, e, e.x, DT, h, gain(0), shift=part(0), scale=part(1), **kept)
            if l == 0:
                with ExitStack() as s2:
                    h = two_parts(nc, s2, "ml_h", DT)
                    mlstm_mixer(nc, e, I, h, before(h), y)
            else:
                mla_mixer(nc, e, I, before, y)
            norm_stage(nc, e, f"l{l}_mixed", y, DT, y, gain(1), gate=part(2), onto=e.x)
            h = two_parts(nc, s, f"l{l}_h2", DT)
            ff = two_parts(nc, s, f"l{l}_ff", D_FF2 // P // 2)
            stream = Stream(nc, e, s, f"l{l}", DT * 2 * P)
            w1, w2 = I["mlp_w1_2"][l], I["mlp_w2_2"][l]
            for half in range(2):
                cols = slice(half * D_FF2 // 2, (half + 1) * D_FF2 // 2)
                gemm(nc, e, f"l{l}_up{half}", w1[:, cols], DT, h, 4, 2, 2, "sqrelu", dst=ff,
                     before=normed(nc, e, e.x, DT, h, gain(2), shift=part(3), scale=part(4)) if half == 0 else None,
                     side=sides[0] if (l, half) == (0, 1) else None, stream=stream,
                     following=(w2[cols, :], D_FF2 // P // 2, P))
                gemm(nc, e, f"l{l}_down{half}", w2[cols, :], D_FF2 // P // 2, ff, 4, 2, 1,
                     "copy" if half == 0 else "add", dst=y, side=sides[1] if (l, half) == (0, 1) else None,
                     stream=stream,
                     following=(w1[:, D_FF2 // 2:], DT, 2 * P) if half == 0 else None)
            norm_stage(nc, e, f"l{l}_out", y, DT, y, gain(3), gate=part(5), onto=e.x)
        if l == 0:
            add_condition_bias_1(nc, e)


def store_output(nc, e, out):
    with ExitStack() as s:
        sb, pb, sem = opened(nc, s, "store")
        rows = sb("rows", [P, TT, D])
        ps = pb("ps", [P, 4, L])
        turned, taken, stored = sem("turned"), sem("taken"), sem("stored")
        block = s.enter_context(nc.Block())

        @block.tensor
        def _(pe):
            for n in range(2 * TT):
                t, half = n // 2, n % 2
                if n >= 4:
                    pe.wait_ge(taken, n - 3)
                for i in range(4):
                    last = nc.tensor.transpose(ps[:, n % 4, i * P:(i + 1) * P],
                                               e.x[:, 4 * half + i, t * P:(t + 1) * P], e.ident[:, :])
                last.then_inc(turned, 1)

        @block.scalar
        def _(act):
            for n in range(2 * TT):
                t, half = n // 2, n % 2
                act.wait_ge(turned, n + 1)
                nc.scalar.activation(rows[:, t, half * 512:(half + 1) * 512], ps[:, n % 4, :], ACT.Copy)\
                    .then_inc(taken, 1)

        @block.sync
        def _(sp):
            for t in range(TT):
                sp.wait_ge(taken, 2 * t + 2)
                sp.dma_start(out[0, t * P:(t + 1) * P, :], rows[:, t, :]).then_inc(stored, 16)
            sp.wait_ge(stored, 16 * TT)



def program(nc, I, out):
    with ExitStack() as s:
        e = Kept()
        e.side_in, e.side_loads = s.enter_context(nc.semaphore("side_in")), 0
        e.loaded, e.loads = [s.enter_context(nc.semaphore(f"stream_loaded{i}")) for i in range(2)], [0, 0]
        Semaphores.start(nc)
        keep = lambda name, shape: s.enter_context(nc.sbuf_tensor(name, shape, F32))
        e.x = keep("resid", [P, DT, L])
        e.ident, e.ones, e.heads = keep("ident", [P, P]), keep("ones", [P, P]), keep("heads", [P, P])
        e.cols = keep("cols", [P, ROW_TILES * P])
        load_constants(nc, e, I)
        e.cond, e.kvada, e.ada = keep("cond", [P, DT]), keep("kvada", [P, 2 * DT]), keep("ada", [P, 2, 6 * DT])
        e.shift_keep = keep("shift_keep", [P, MU_ROWS + 1])
        prepare_columns(nc, e)
        most, rest = 33, 6 * DT - 16
        side = lambda w, at, n, cols, dst: (w[:, at * P:(at + n) * P], cols, e.cond, dst[:, at:at + n])
        ada0, ada1, kvada = I["ada_w_2"][0], I["ada_w_2"][1], I["kv_ada_w_2"]
        ffn_swiglu(nc, e, "ffn1", "ffn1_norm", I["ffn1_w_gu"], I["ffn1_w_down"],
                   side(ada0, 0, most, 3 * P, e.ada[:, 0, :]), side(ada0, rest, 16, 4 * P, e.ada[:, 0, :]))
        with ExitStack() as s2:
            part = lambda name, shape: s2.enter_context(nc.sbuf_tensor(name, shape, F32))
            merged = part("merged", [P, DT, L])
            root = part("mix_root", [P, L])[:, :]
            with ExitStack() as s3:
                hyena_branch(nc, e, I, two_parts(nc, s3, "h_mix", DT), merged, root)
            rwkv_branch(nc, e, I, merged, root)
            mp = two_parts(nc, s2, "merged", DT)
            gemm(nc, e, "mix_out", I["w_out"], DT, mp, 2, 2, 2, "add", dst=e.x, before=cut(nc, e, merged, DT, mp))
        ffn_swiglu(nc, e, "ffn2", "ffn2_norm", I["ffn2_w_gu"], I["ffn2_w_down"],
                   side(ada1, 0, most, 3 * P, e.ada[:, 1, :]), side(kvada, 0, 2 * DT, 4 * P, e.kvada))
        norm_stage(nc, e, "final", e.x, DT, e.x, lambda k: col(e, "final_norm", k))
        second_block(nc, e, I, [side(ada1, rest + 8 * i, 8, 2 * P, e.ada[:, 1, :]) for i in range(2)])
        store_output(nc, e, out)




_OUT = (1, L, D)


def kernel(**inputs):
    import concourse.bacc as bacc
    from concourse.bass_utils import run_bass_kernel_spmd

    nc = bacc.Bacc("TRN2", target_bir_lowering=False, num_devices=1)
    arrays, aps = {}, {}
    for name, a in list(inputs.items()) + list(shape_tables().items()):
        a = np.ascontiguousarray(a)
        arrays[f"in_{name}"] = a
        aps[name] = nc.dram_tensor(f"in_{name}", a.shape, mybir.dt.from_np(a.dtype), kind="ExternalInput").ap()
    out = nc.dram_tensor("out_0", _OUT, F32, kind="ExternalOutput").ap()
    program(nc, aps, out)
    return run_bass_kernel_spmd(nc, [arrays], core_ids=[0]).results[0]["out_0"]
```
